# Optimizing a Trainium2 kernel written in Bass

```python
import math
import jax
import jax.numpy as jnp
from jax import lax
import numpy as np
import jax, jax.numpy as jnp

D_MODEL = 1024
BATCH = 1
SEQ = 1024
DEPTH = 2

F32 = jnp.float32

GDN_HEADS = 6
GDN_DK = 64
GDN_DV = 64
GDN_CONV = 5
GDN_CHUNK = 64
GDN_QK_W = GDN_HEADS * GDN_DK
GDN_W = GDN_HEADS * GDN_DV
GDN_QKV_W = 2 * GDN_QK_W + GDN_W

MLA_HEADS = 6
MLA_NOPE = 64
MLA_ROPE = 32
MLA_V = 64
MLA_Q_RANK = 192
MLA_KV_RANK = 128
MLA_QBLOCK = 128
ROPE_THETA = 10000.0
MLA_W = MLA_HEADS * MLA_V

RWKV_HEADS = 4
RWKV_HD = 64
RWKV_DECAY_LORA = 64
RWKV_ICLR_LORA = 64
RWKV_W = RWKV_HEADS * RWKV_HD
RWKV_SHIFT_W = 3 * RWKV_W + RWKV_DECAY_LORA + RWKV_ICLR_LORA
RWKV_LN_EPS = 64e-5

D_MIX = GDN_W + MLA_W + RWKV_W
NORM_EPS = 1e-6

IN_LAYOUT = (
    ('gate', D_MIX),
    ('gdn_q', GDN_QK_W), ('gdn_k', GDN_QK_W), ('gdn_v', GDN_W),
    ('gdn_a', 2 * GDN_HEADS), ('gdn_b', 2 * GDN_HEADS),
    ('mla_cq', MLA_Q_RANK), ('mla_ckv', MLA_KV_RANK), ('mla_kr', MLA_ROPE),
    ('rw_r', RWKV_W), ('rw_k', RWKV_W), ('rw_v', RWKV_W),
    ('rw_wd', RWKV_DECAY_LORA), ('rw_ad', RWKV_ICLR_LORA),
)
N_IN = sum(width for _, width in IN_LAYOUT)


def split_columns(p):
    cols = {}
    off = 0
    for name, width in IN_LAYOUT:
        cols[name] = p[..., off:off + width]
        off += width
    return cols

def rms_norm(x, g, eps=NORM_EPS):
    xf = x.astype(F32)
    y = xf * lax.rsqrt(jnp.mean(xf * xf, axis=-1, keepdims=True) + eps)
    return (y * g.astype(F32)).astype(x.dtype)

def l2_normalize(x, eps=1e-6):
    xf = x.astype(F32)
    return xf * lax.rsqrt(jnp.sum(xf * xf, axis=-1, keepdims=True) + eps)

def centred_depthwise_conv(x, w):
    pad = w.shape[0] // 2
    return lax.conv_general_dilated(
        x, w[:, None, :].astype(x.dtype), window_strides=(1,), padding=[(pad, pad)],
        dimension_numbers=('NWC', 'WIO', 'NWC'), feature_group_count=x.shape[-1])

def centred_token_shift(x, mu):
    zeros = jnp.zeros_like(x[:, :1])
    x_prev = jnp.concatenate([zeros, x[:, :-1]], axis=1)
    x_next = jnp.concatenate([x[:, 1:], zeros], axis=1)
    return x + mu[0] * (x_prev - x) + mu[1] * (x_next - x)

def bidir_stack(t_fwd, t_bwd):
    return jnp.concatenate([t_fwd, jnp.flip(t_bwd, axis=1)], axis=0)

def bidir_merge(y):
    b = y.shape[0] // 2
    return y[:b] + jnp.flip(y[b:], axis=1)

def gated_delta_chunked(q, k, v, g, beta):
    n, l, h, dk = q.shape
    dv = v.shape[-1]
    c = GDN_CHUNK
    nc = l // c

    def chunks(t):
        return jnp.moveaxis(t.reshape((n, nc, c, h) + t.shape[3:]), 3, 1)

    q, k, v, g, beta = chunks(q), chunks(k), chunks(v), chunks(g), chunks(beta)
    cum = jnp.cumsum(g, axis=-1)
    diff = cum[..., :, None] - cum[..., None, :]
    idx = jnp.arange(c)
    incl = idx[:, None] >= idx[None, :]
    strict = idx[:, None] > idx[None, :]
    d_incl = jnp.exp(jnp.where(incl, diff, -jnp.inf))
    d_strict = jnp.where(strict, d_incl, 0.0)
    a_mat = beta[..., :, None] * jnp.einsum('nhcid,nhcjd->nhcij', k, k) * d_strict
    gam = jnp.exp(cum)
    rhs = jnp.concatenate([beta[..., None] * v, (beta * gam)[..., None] * k], axis=-1)
    sol = lax.linalg.triangular_solve(a_mat, rhs, left_side=True, lower=True, unit_diagonal=True)
    u0, w = sol[..., :dv], sol[..., dv:]
    p_intra = jnp.einsum('nhcid,nhcjd->nhcij', q, k) * d_incl
    q_g = q * gam[..., None]
    k_d = k * jnp.exp(cum[..., -1:] - cum)[..., None]
    g_end = jnp.exp(cum[..., -1])
    xs = tuple(jnp.moveaxis(t, 2, 0) for t in (w, u0, p_intra, q_g, k_d, g_end))

    def step(s, inp):
        w_c, u0_c, p_c, qg_c, kd_c, ge_c = inp
        u = u0_c - jnp.einsum('nhcd,nhde->nhce', w_c, s)
        o = jnp.einsum('nhcd,nhde->nhce', qg_c, s) + jnp.einsum('nhij,nhje->nhie', p_c, u)
        s = ge_c[..., None, None] * s + jnp.einsum('nhcd,nhce->nhde', kd_c, u)
        return s, o

    s0 = jnp.zeros((n, h, dk, dv), F32)
    _, o = lax.scan(step, s0, xs)
    return jnp.transpose(o, (1, 0, 3, 2, 4)).reshape(n, l, h, dv)

def gdn_branch(cols, conv_w, a_log, dt_bias, norm_g):
    b, l = cols['gdn_q'].shape[:2]
    qkv = jnp.concatenate([cols['gdn_q'], cols['gdn_k'], cols['gdn_v']], axis=-1)
    qkv = jax.nn.silu(centred_depthwise_conv(qkv, conv_w))
    q, k, v = jnp.split(qkv, [GDN_QK_W, 2 * GDN_QK_W], axis=-1)
    q = l2_normalize(q.reshape(b, l, GDN_HEADS, GDN_DK)) * (GDN_DK ** -0.5)
    k = l2_normalize(k.reshape(b, l, GDN_HEADS, GDN_DK))
    v = v.reshape(b, l, GDN_HEADS, GDN_DV).astype(F32)
    a = cols['gdn_a'].astype(F32).reshape(b, l, 2, GDN_HEADS)
    bt = cols['gdn_b'].astype(F32).reshape(b, l, 2, GDN_HEADS)
    g = -jnp.exp(a_log.astype(F32)) * jax.nn.softplus(a + dt_bias.astype(F32))
    beta = jax.nn.sigmoid(bt)
    o = gated_delta_chunked(
        bidir_stack(q, q), bidir_stack(k, k), bidir_stack(v, v),
        bidir_stack(g[:, :, 0], g[:, :, 1]), bidir_stack(beta[:, :, 0], beta[:, :, 1]))
    o = rms_norm(bidir_merge(o), norm_g)
    return o.reshape(b, l, GDN_W)

def apply_rope(x, cos, sin):
    xf = x.astype(F32)
    x1, x2 = jnp.split(xf, 2, axis=-1)
    return jnp.concatenate([x1 * cos - x2 * sin, x2 * cos + x1 * sin], axis=-1)

def mla_branch(cols, positions, q_norm_g, w_uq, kv_norm_g, w_ukv):
    b, l = cols['mla_cq'].shape[:2]
    q = (rms_norm(cols['mla_cq'], q_norm_g) @ w_uq).reshape(b, l, MLA_HEADS, MLA_NOPE + MLA_ROPE)
    kv = (rms_norm(cols['mla_ckv'], kv_norm_g) @ w_ukv).reshape(b, l, MLA_HEADS, MLA_NOPE + MLA_V)
    q_nope, q_rot = q[..., :MLA_NOPE], q[..., MLA_NOPE:]
    k_nope, v = kv[..., :MLA_NOPE], kv[..., MLA_NOPE:]
    half = MLA_ROPE // 2
    inv_freq = ROPE_THETA ** (-jnp.arange(half, dtype=F32) / half)
    ang = positions.astype(F32)[..., None] * inv_freq
    cos, sin = jnp.cos(ang), jnp.sin(ang)
    q_rot = apply_rope(q_rot, cos[:, :, None], sin[:, :, None])
    k_rot = apply_rope(cols['mla_kr'], cos, sin)
    scale = (MLA_NOPE + MLA_ROPE) ** -0.5
    q = jnp.concatenate([q_nope.astype(F32), q_rot], axis=-1) * scale
    k = jnp.concatenate([k_nope.astype(F32),
                         jnp.broadcast_to(k_rot[:, :, None], (b, l, MLA_HEADS, MLA_ROPE))], axis=-1)
    v = v.astype(F32)
    nb = l // MLA_QBLOCK
    q_blocks = jnp.moveaxis(q.reshape(b, nb, MLA_QBLOCK, MLA_HEADS, MLA_NOPE + MLA_ROPE), 1, 0)

    def attend(q_blk):
        s = jnp.einsum('bqhd,bkhd->bhqk', q_blk, k)
        p = jax.nn.softmax(s, axis=-1)
        return jnp.einsum('bhqk,bkhd->bqhd', p, v)

    o = lax.map(attend, q_blocks)
    return jnp.moveaxis(o, 0, 1).reshape(b, l, MLA_W)

def to_heads(t):
    return t.reshape(t.shape[:-1] + (RWKV_HEADS, RWKV_HD))

def rwkv7_branch(cols, mu, w0, w2, a0, a2, k_k, k_a, r_k, ln_g, ln_b):
    b, l = cols['rw_r'].shape[:2]
    feats = jnp.concatenate([cols['rw_r'], cols['rw_k'], cols['rw_v'], cols['rw_wd'], cols['rw_ad']],
                            axis=-1).astype(F32)
    feats = centred_token_shift(feats, mu.astype(F32))
    r, k, v, wd, ad = jnp.split(feats, [RWKV_W, 2 * RWKV_W, 3 * RWKV_W, 3 * RWKV_W + RWKV_DECAY_LORA], axis=-1)
    w_log = -jax.nn.softplus(-(w0.astype(F32)[:, None, None]
                               + jnp.einsum('bld,edc->eblc', jnp.tanh(wd), w2.astype(F32)))) - 0.5
    decay = jnp.exp(-jnp.exp(w_log))
    a = jax.nn.sigmoid(a0.astype(F32)[:, None, None] + jnp.einsum('bld,edc->eblc', ad, a2.astype(F32)))
    kk = l2_normalize(to_heads(k * k_k.astype(F32)))
    k_mod = k[None] * (1.0 + (a - 1.0) * k_a.astype(F32))
    r_h, v_h = to_heads(r), to_heads(v)
    a_h = to_heads(a)
    xs = (
        bidir_stack(r_h, r_h),
        bidir_stack(to_heads(decay[0]), to_heads(decay[1])),
        bidir_stack(to_heads(k_mod[0]), to_heads(k_mod[1])),
        bidir_stack(v_h, v_h),
        bidir_stack(kk, kk),
        bidir_stack(a_h[0] * kk, a_h[1] * kk),
    )
    xs = tuple(jnp.moveaxis(t, 1, 0) for t in xs)

    def step(s, inp):
        r_t, w_t, k_t, v_t, kk_t, b_t = inp
        sa = jnp.einsum('nhij,nhj->nhi', s, -kk_t)
        s = s * w_t[:, :, None, :] + sa[..., None] * b_t[:, :, None, :] + v_t[..., None] * k_t[:, :, None, :]
        y = jnp.einsum('nhij,nhj->nhi', s, r_t)
        return s, y

    s0 = jnp.zeros((2 * b, RWKV_HEADS, RWKV_HD, RWKV_HD), F32)
    _, y = lax.scan(step, s0, xs)
    y = bidir_merge(jnp.moveaxis(y, 0, 1))
    mean = jnp.mean(y, axis=-1, keepdims=True)
    var = jnp.mean(jnp.square(y - mean), axis=-1, keepdims=True)
    y = ((y - mean) * lax.rsqrt(var + RWKV_LN_EPS)).reshape(b, l, RWKV_W) * ln_g.astype(F32) + ln_b.astype(F32)
    k_bonus = to_heads(0.5 * (k_mod[0] + k_mod[1]))
    bonus = jnp.sum(r_h * k_bonus * r_k.astype(F32), axis=-1, keepdims=True) * v_h
    return y + bonus.reshape(b, l, RWKV_W)

def first_inputs(seed: int = 0) -> dict:
    key = jax.random.key(seed)
    ks = jax.random.split(key, 24)

    def nrm(k, shape, scale):
        return jax.random.normal(k, shape, F32) * scale

    x = nrm(ks[0], (BATCH, SEQ, D_MODEL), 1.0)
    positions = (jnp.arange(SEQ, dtype=jnp.int32)[None, :]
                 + jax.random.randint(ks[1], (BATCH, 1), 0, 512, dtype=jnp.int32))
    norm_g = 1.0 + nrm(ks[2], (DEPTH, D_MODEL), 0.02)
    w_in = nrm(ks[3], (DEPTH, D_MODEL, N_IN), D_MODEL ** -0.5)
    gdn_conv = nrm(ks[4], (DEPTH, GDN_CONV, GDN_QKV_W), GDN_CONV ** -0.5)
    gdn_a_log = jnp.log(jax.random.uniform(ks[5], (DEPTH, 2, GDN_HEADS), F32, 1.0, 16.0))
    dt = jnp.exp(jax.random.uniform(ks[6], (DEPTH, 2, GDN_HEADS), F32, math.log(1e-3), math.log(1e-1)))
    gdn_dt_bias = dt + jnp.log(-jnp.expm1(-dt))
    gdn_norm_g = 1.0 + nrm(ks[7], (DEPTH, GDN_DV), 0.02)
    mla_q_norm_g = 1.0 + nrm(ks[8], (DEPTH, MLA_Q_RANK), 0.02)
    mla_w_uq = nrm(ks[9], (DEPTH, MLA_Q_RANK, MLA_HEADS * (MLA_NOPE + MLA_ROPE)), MLA_Q_RANK ** -0.5)
    mla_kv_norm_g = 1.0 + nrm(ks[10], (DEPTH, MLA_KV_RANK), 0.02)
    mla_w_ukv = nrm(ks[11], (DEPTH, MLA_KV_RANK, MLA_HEADS * (MLA_NOPE + MLA_V)), MLA_KV_RANK ** -0.5)
    rwkv_mu = jax.random.uniform(ks[12], (DEPTH, 2, RWKV_SHIFT_W), F32, 0.0, 0.5)
    rwkv_w0 = jax.random.uniform(ks[13], (DEPTH, 2, RWKV_W), F32, -6.0, -1.0)
    rwkv_w2 = nrm(ks[14], (DEPTH, 2, RWKV_DECAY_LORA, RWKV_W), 0.1)
    rwkv_a0 = nrm(ks[15], (DEPTH, 2, RWKV_W), 0.1)
    rwkv_a2 = nrm(ks[16], (DEPTH, 2, RWKV_ICLR_LORA, RWKV_W), 0.1)
    rwkv_k_k = 0.85 + nrm(ks[17], (DEPTH, RWKV_W), 0.02)
    rwkv_k_a = 1.0 + nrm(ks[18], (DEPTH, RWKV_W), 0.02)
    rwkv_r_k = nrm(ks[19], (DEPTH, RWKV_HEADS, RWKV_HD), 0.1)
    rwkv_ln_g = 1.0 + nrm(ks[20], (DEPTH, RWKV_W), 0.02)
    rwkv_ln_b = nrm(ks[21], (DEPTH, RWKV_W), 0.02)
    w_out = nrm(ks[22], (DEPTH, D_MIX, D_MODEL), D_MIX ** -0.5)
    final_norm_g = 1.0 + nrm(ks[23], (D_MODEL,), 0.02)
    return {
        'x': x, 'positions': positions, 'norm_g': norm_g, 'w_in': w_in,
        'gdn_conv': gdn_conv, 'gdn_a_log': gdn_a_log, 'gdn_dt_bias': gdn_dt_bias, 'gdn_norm_g': gdn_norm_g,
        'mla_q_norm_g': mla_q_norm_g, 'mla_w_uq': mla_w_uq, 'mla_kv_norm_g': mla_kv_norm_g, 'mla_w_ukv': mla_w_ukv,
        'rwkv_mu': rwkv_mu, 'rwkv_w0': rwkv_w0, 'rwkv_w2': rwkv_w2, 'rwkv_a0': rwkv_a0, 'rwkv_a2': rwkv_a2,
        'rwkv_k_k': rwkv_k_k, 'rwkv_k_a': rwkv_k_a, 'rwkv_r_k': rwkv_r_k,
        'rwkv_ln_g': rwkv_ln_g, 'rwkv_ln_b': rwkv_ln_b,
        'w_out': w_out, 'final_norm_g': final_norm_g,
    }

def first_block(x, positions, norm_g, w_in, gdn_conv, gdn_a_log, gdn_dt_bias, gdn_norm_g,
              mla_q_norm_g, mla_w_uq, mla_kv_norm_g, mla_w_ukv,
              rwkv_mu, rwkv_w0, rwkv_w2, rwkv_a0, rwkv_a2, rwkv_k_k, rwkv_k_a, rwkv_r_k,
              rwkv_ln_g, rwkv_ln_b, w_out, final_norm_g):
    for layer in range(DEPTH):
        h = rms_norm(x, norm_g[layer])
        cols = split_columns(h @ w_in[layer])
        y_gdn = gdn_branch(cols, gdn_conv[layer], gdn_a_log[layer], gdn_dt_bias[layer], gdn_norm_g[layer])
        y_mla = mla_branch(cols, positions, mla_q_norm_g[layer], mla_w_uq[layer],
                           mla_kv_norm_g[layer], mla_w_ukv[layer])
        y_rwkv = rwkv7_branch(cols, rwkv_mu[layer], rwkv_w0[layer], rwkv_w2[layer], rwkv_a0[layer],
                              rwkv_a2[layer], rwkv_k_k[layer], rwkv_k_a[layer], rwkv_r_k[layer],
                              rwkv_ln_g[layer], rwkv_ln_b[layer])
        mix = jnp.concatenate([y_gdn.astype(F32), y_mla.astype(F32), y_rwkv.astype(F32)], axis=-1)
        mix = mix * jax.nn.silu(cols['gate'].astype(F32))
        x = x + mix.astype(x.dtype) @ w_out[layer]
    return rms_norm(x, final_norm_g)


DEPTH_2 = 1

N_META = 16
D_CONV = D_MODEL
CONV_WIDTH = 31
HG_HEADS = 8
HG_DK = 128
HG_DV = D_MODEL // HG_HEADS
D_HK = HG_HEADS * HG_DK
D_HV = HG_HEADS * HG_DV
CHUNK = 64
EPS = 1e-6
SPLIT_SIZES = (D_CONV, D_CONV, D_CONV, D_HK, D_HK, D_HV, D_HV, D_MODEL, D_MODEL)
D_IN = D_CONV * 3 + D_HK * 2 + D_HV * 2 + D_MODEL * 2


def rmsnorm(x, g):
    xf = x.astype(jnp.float32)
    y = xf * lax.rsqrt(jnp.mean(xf * xf, axis=-1, keepdims=True) + EPS)
    return (y * g.astype(jnp.float32)).astype(x.dtype)

def layernorm(x, g, b):
    xf = x.astype(jnp.float32)
    mu = jnp.mean(xf, axis=-1, keepdims=True)
    var = jnp.mean(jnp.square(xf - mu), axis=-1, keepdims=True)
    y = (xf - mu) * lax.rsqrt(var + EPS)
    return (y * g.astype(jnp.float32) + b.astype(jnp.float32)).astype(x.dtype)

def conformer_branch(u_a, u_b, z, conv_w, conv_b, ln_g, ln_b, w_out):
    a = u_a * jax.nn.sigmoid(u_b)
    c = lax.conv_general_dilated(
        a, conv_w[:, None, :].astype(a.dtype), window_strides=(1,),
        padding=[(CONV_WIDTH - 1, 0)],
        dimension_numbers=('NWC', 'WIO', 'NWC'),
        feature_group_count=D_CONV) + conv_b
    c = jax.nn.silu(layernorm(c, ln_g, ln_b))
    return (c * jax.nn.silu(z)) @ w_out

def hgrn2_branch(q_raw, f_raw, i_raw, g, lb, gnorm_g, w_out):
    bsz, seqlen, _ = q_raw.shape
    out_dtype = i_raw.dtype
    q = jax.nn.silu(q_raw.astype(jnp.float32))
    f = lb + (1.0 - lb) * jax.nn.sigmoid(f_raw.astype(jnp.float32))
    log_f = jnp.log(f)
    k = 1.0 - f
    v = i_raw.astype(jnp.float32)
    pad = (-seqlen) % CHUNK
    n_chunks = (seqlen + pad) // CHUNK

    def to_chunks(t, d):
        t = jnp.pad(t, ((0, 0), (pad, 0), (0, 0)))
        t = t.reshape(bsz, n_chunks, CHUNK, HG_HEADS, d)
        return jnp.transpose(t, (1, 0, 3, 2, 4))

    qc = to_chunks(q, HG_DK)
    kc = to_chunks(k, HG_DK)
    vc = to_chunks(v, HG_DV)
    bc = jnp.cumsum(to_chunks(log_f, HG_DK), axis=3)
    causal = jnp.tril(jnp.ones((CHUNK, CHUNK), dtype=bool))[None, None, :, :, None]

    def step(S, inp):
        qi, ki, vi, bi = inp
        o_inter = jnp.einsum('bhtk,bhkv->bhtv', qi * jnp.exp(bi), S)
        diff = bi[:, :, :, None, :] - bi[:, :, None, :, :]
        decay = jnp.exp(jnp.where(causal, diff, -jnp.inf))
        attn = jnp.einsum('bhtk,bhsk,bhtsk->bhts', qi, ki, decay)
        o_intra = jnp.einsum('bhts,bhsv->bhtv', attn, vi)
        b_last = bi[:, :, -1:, :]
        S_new = jnp.exp(b_last[:, :, 0, :])[..., None] * S + jnp.einsum(
            'bhsk,bhsv->bhkv', ki * jnp.exp(b_last - bi), vi)
        return S_new, o_inter + o_intra

    S0 = jnp.zeros((bsz, HG_HEADS, HG_DK, HG_DV), jnp.float32)
    _, o = lax.scan(step, S0, (qc, kc, vc, bc))
    o = jnp.transpose(o, (1, 0, 3, 2, 4)).reshape(bsz, n_chunks * CHUNK, HG_HEADS, HG_DV)
    o = o[:, pad:]
    o = o * lax.rsqrt(jnp.mean(o * o, axis=-1, keepdims=True) + EPS)
    o = o * gnorm_g.astype(jnp.float32).reshape(HG_HEADS, HG_DV)
    o = o.reshape(bsz, seqlen, D_HV).astype(out_dtype)
    return (o * jax.nn.silu(g)) @ w_out

def second_inputs(seed: int = 0) -> dict:
    key = jax.random.key(seed)
    ks = jax.random.split(key, 16)
    f32 = jnp.float32
    nrm = lambda k, shape, s: jax.random.normal(k, shape, f32) * s
    return {
        "x": nrm(ks[0], (BATCH, SEQ, D_MODEL), 1.0),
        "meta_tokens": nrm(ks[1], (N_META, D_MODEL), 1.0),
        "norm_g": 1.0 + nrm(ks[2], (DEPTH_2, D_MODEL), 0.02),
        "w_in": nrm(ks[3], (DEPTH_2, D_MODEL, D_IN), D_MODEL ** -0.5),
        "conv_w": nrm(ks[4], (DEPTH_2, CONV_WIDTH, D_CONV), CONV_WIDTH ** -0.5),
        "conv_b": nrm(ks[5], (DEPTH_2, D_CONV), 0.02),
        "ln_g": 1.0 + nrm(ks[6], (DEPTH_2, D_CONV), 0.02),
        "ln_b": nrm(ks[7], (DEPTH_2, D_CONV), 0.02),
        "w_conv_out": nrm(ks[8], (DEPTH_2, D_CONV, D_MODEL), D_CONV ** -0.5),
        "lb_logits": nrm(ks[9], (DEPTH_2 + 1, D_HK), 0.5),
        "gnorm_g": 1.0 + nrm(ks[10], (DEPTH_2, D_HV), 0.02),
        "w_rec_out": nrm(ks[11], (DEPTH_2, D_HV, D_MODEL), D_HV ** -0.5),
        "w_out": nrm(ks[12], (DEPTH_2, D_MODEL, D_MODEL), D_MODEL ** -0.5),
        "final_g": 1.0 + nrm(ks[13], (D_MODEL,), 0.02),
    }

def second_block(x, meta_tokens, norm_g, w_in, conv_w, conv_b, ln_g, ln_b, w_conv_out,
              lb_logits, gnorm_g, w_rec_out, w_out, final_g):
    bsz = x.shape[0]
    meta = jnp.broadcast_to(meta_tokens.astype(x.dtype)[None], (bsz, N_META, D_MODEL))
    h_res = jnp.concatenate([meta, x], axis=1)
    lb_all = jnp.cumsum(jax.nn.softmax(lb_logits.astype(jnp.float32), axis=0), axis=0)
    split_idx = [int(v) for v in np.cumsum(SPLIT_SIZES)[:-1]]
    for l in range(DEPTH_2):
        h = rmsnorm(h_res, norm_g[l])
        proj = h @ w_in[l]
        glu_a, glu_b, z_conv, q, f, i, g_rec, m_conv, m_rec = jnp.split(proj, split_idx, axis=-1)
        y_conv = conformer_branch(glu_a, glu_b, z_conv, conv_w[l], conv_b[l],
                                  ln_g[l], ln_b[l], w_conv_out[l])
        y_rec = hgrn2_branch(q, f, i, g_rec, lb_all[l], gnorm_g[l], w_rec_out[l])
        merged = jax.nn.sigmoid(m_conv) * y_conv + jax.nn.sigmoid(m_rec) * y_rec
        h_res = h_res + merged @ w_out[l]
    return rmsnorm(h_res[:, N_META:], final_g)


_first_inputs = second_inputs


def second_inputs(seed=0):
    import zlib

    import numpy as np

    out = dict(_first_inputs(seed))
    spreads = {}
    factors = {'norm_g': 5.198,
     'conv_b': 7.996,
     'ln_g': 8.0,
     'ln_b': 8.0,
     'lb_logits': 3.279,
     'gnorm_g': 8.0,
     'final_g': 2.742}
    for name, (base, spread) in spreads.items():
        noise = np.random.default_rng([zlib.crc32(name.encode()), seed]).standard_normal(out[name].shape)
        drawn = base * np.exp(spread * noise) if base else spread * noise
        out[name] = __import__('jax').numpy.asarray(drawn.astype(out[name].dtype))
    for name, factor in factors.items():
        out[name] = (out[name] * factor).astype(out[name].dtype)
    return out


_narrow_inputs = second_inputs


def second_inputs(seed=0):

    out = dict(_narrow_inputs(seed))
    wider = {'ln_g': 5.31, 'ln_b': 5.58, 'gnorm_g': 4.03, 'final_g': 3.09}
    for name, times in wider.items():
        mean = out[name].mean()
        out[name] = (mean + times * (out[name] - mean)).astype(out[name].dtype)
    return out


def setup_inputs(seed=0):
    out = dict(first_inputs(seed))
    for name, value in second_inputs(seed + 1).items():
        if name != "x":
            out[name + "_2"] = value
    return out


def reference(
    x, positions, norm_g, w_in, gdn_conv, gdn_a_log, gdn_dt_bias, gdn_norm_g, mla_q_norm_g,
    mla_w_uq, mla_kv_norm_g, mla_w_ukv, rwkv_mu, rwkv_w0, rwkv_w2, rwkv_a0, rwkv_a2, rwkv_k_k,
    rwkv_k_a, rwkv_r_k, rwkv_ln_g, rwkv_ln_b, w_out, final_norm_g, meta_tokens_2, norm_g_2,
    w_in_2, conv_w_2, conv_b_2, ln_g_2, ln_b_2, w_conv_out_2, lb_logits_2, gnorm_g_2,
    w_rec_out_2, w_out_2, final_g_2,
):
    x = first_block(
        x, positions, norm_g, w_in, gdn_conv, gdn_a_log, gdn_dt_bias, gdn_norm_g, mla_q_norm_g,
        mla_w_uq, mla_kv_norm_g, mla_w_ukv, rwkv_mu, rwkv_w0, rwkv_w2, rwkv_a0, rwkv_a2,
        rwkv_k_k, rwkv_k_a, rwkv_r_k, rwkv_ln_g, rwkv_ln_b, w_out, final_norm_g,
    )
    return second_block(
        x, meta_tokens_2, norm_g_2, w_in_2, conv_w_2, conv_b_2, ln_g_2, ln_b_2, w_conv_out_2,
        lb_logits_2, gnorm_g_2, w_rec_out_2, w_out_2, final_g_2,
    )


_drawn_inputs = setup_inputs


def setup_inputs(seed=0):
    import zlib

    import numpy as np

    out = dict(_drawn_inputs(seed))
    spreads = {}
    factors = {'gdn_norm_g': 3.007,
     'mla_q_norm_g': 8.0,
     'mla_kv_norm_g': 8.0,
     'rwkv_k_k': 3.812,
     'rwkv_k_a': 3.398,
     'rwkv_ln_g': 4.195,
     'rwkv_ln_b': 3.82}
    for name, (base, spread) in spreads.items():
        noise = np.random.default_rng([zlib.crc32(name.encode()), seed]).standard_normal(out[name].shape)
        drawn = base * np.exp(spread * noise) if base else spread * noise
        out[name] = jnp.asarray(drawn.astype(out[name].dtype))
    for name, factor in factors.items():
        out[name] = (out[name] * factor).astype(out[name].dtype)
    return out
```

```python
from contextlib import ExitStack

import concourse.bass as bass
import numpy as np
from concourse import mybir

F32 = mybir.dt.float32
I32 = mybir.dt.int32
U32 = mybir.dt.uint32
FN = mybir.ActivationFunctionType
ALU = mybir.AluOpType
AX = mybir.AxisListType.X
ds = bass.ds

P = 128
DEPTH, DM, SEQ = 2, 1024, 1024
KD = DM // P
NT = SEQ // P
GH, GD = 6, 64
GW = GH * GD
CONV = 5
MH, NOPE, ROPE, MV = 6, 64, 32, 64
QR, KVR = 192, 128
QK = NOPE + ROPE
RH, RD = 4, 64
RW = RH * RD
N_IN = 3448
COL_GDN, COL_AB, COL_RW = 1024, 2176, 2552
TM_W = COL_RW - COL_AB
NLEV = 7
T2 = SEQ + P
NT2 = T2 // P
META = 16
TAPS = 31
D_IN2 = 9216
NORM_EPS = 1e-6
RWKV_EPS = 64e-5

PARAMS = [("norm_g", KD), ("conv", 9 * CONV), ("a_log", 2 * GH), ("dt", 2 * GH), ("gdn_g", GD), ("q_g", 2), ("kv_g", 1),
          ("mu", 14), ("w0", 4), ("a0", 4), ("k_k", 2), ("k_a", 2), ("r_k", 2), ("ln_g", RW), ("ln_b", RW)]
PARAMS2 = [("norm_g", KD), ("conv_w", KD * TAPS), ("conv_b", KD), ("ln_g", KD), ("ln_b", KD), ("lb", KD * 2),
           ("gnorm", KD)]
CONSTS = [("ident", P), ("tri_f", P), ("tri_b", P), ("aft", P), ("bef", P), ("ones", P), ("blk", P), ("sel", 2),
          ("freq", ROPE // 2), ("eps", 1), ("rw_eps", 1), ("lo", NLEV * P), ("up", NLEV * P)]


def offsets(fields):
    at, out = 0, {}
    for name, n in fields:
        out[name] = (at, n)
        at += n
    return out, at


def shape_constants():
    i = np.arange(P)
    r, c = i[:, None], i[None, :]
    lo = np.stack([((r >> (k + 1)) == (c >> (k + 1))) & (((r >> k) & 1) == 1) & (((c >> k) & 1) == 0) for k in range(NLEV)], 1)
    up = np.stack([((r >> (k + 1)) == (c >> (k + 1))) & (((r >> k) & 1) == 0) & (((c >> k) & 1) == 1) for k in range(NLEV)], 1)
    half = ROPE // 2
    parts = {
        "ident": r == c, "tri_f": r <= c, "tri_b": r >= c, "aft": r > c, "bef": r < c, "ones": np.ones((P, P)),
        "blk": (r // 64) == (c // 64), "sel": (r // 64) == np.arange(2)[None, :],
        "freq": np.broadcast_to(np.float32(10000.0) ** (-np.arange(half, dtype=np.float32) / half), (P, half)),
        "eps": np.full((P, 1), NORM_EPS), "rw_eps": np.full((P, 1), RWKV_EPS),
        "lo": lo.reshape(P, -1), "up": up.reshape(P, -1),
    }
    return np.ascontiguousarray(np.concatenate([np.asarray(parts[n], np.float32) for n, _ in CONSTS], 1))


class Steps:

    def __init__(self, sem, label, unit, values):
        self.sem, self.label, self.unit, self.values = sem, label, unit, values
        self.stage, self.count = "", 0

    def begin(self, stage):
        self.stage, self.count = stage, 0

    def __call__(self, name):
        self.count += self.unit
        self.values[self.stage, self.label, name] = self.count
        return self.sem, self.unit

    def __getitem__(self, name):
        return self.sem, self.values.get((self.stage, self.label, name), 1)


class Transfers:

    def __init__(self, nc, ctx, values):
        self.nc, self.ctx, self.values, self.sems = nc, ctx, values, {}

    def begin(self, stage):
        self.stage, self.counts = stage, {}

    def sem(self, name):
        if name not in self.sems:
            self.sems[name] = self.ctx.enter_context(self.nc.semaphore("dma_" + name))
        return self.sems[name]

    def __call__(self, name):
        self.counts[name] = self.counts.get(name, 0) + 16
        self.values[self.stage, "dma", name] = self.counts[name]
        return self.sem(name), 16

    def __getitem__(self, name):
        return self.sem(name), self.values.get((self.stage, "dma", name), 16)


def build(nc, io, values):
    with ExitStack() as ctx:
        def sem(name):
            return ctx.enter_context(nc.semaphore(name))

        VEC = Steps(sem("vector_steps"), "vec", 1, values)
        ACT = Steps(sem("scalar_steps"), "act", 1, values)
        PE = Steps(sem("tensor_steps"), "pe", 1, values)
        POOL = Steps(sem("gpsimd_steps"), "pool", 1, values)
        DMA = Transfers(nc, ctx, values)

        def begin(stage):
            for s in (VEC, ACT, PE, POOL, DMA):
                s.begin(stage)

        def clear():
            for s in (VEC, ACT, PE, POOL):
                nc.sync.sem_clear(s.sem)
            for name in DMA.counts:
                nc.sync.sem_clear(DMA.sem(name))
            nc.all_engine_barrier()

        def sbuf(stack, name, shape, dt=F32):
            return stack.enter_context(nc.sbuf_tensor(name, shape, dt))

        def rep(ap, n):
            return ap[:, None, :].broadcast_to([ap.shape[0], n, ap.shape[1]])

        def col(ap, m):
            return ap[:, :, None].broadcast_to([ap.shape[0], ap.shape[1], m])

        def hbm(name, shape):
            return nc.dram_tensor(name, shape, F32).ap()

        gate_hbm = hbm("gate_hbm", (SEQ, DM))
        gdn_hbm = hbm("gdn_hbm", (2, SEQ, GW))
        rwkv_hbm = hbm("rwkv_hbm", (3, SEQ, RW))
        mla_hbm = hbm("mla_hbm", (SEQ, GW))
        x_hbm = hbm("x_hbm", (T2, DM))
        conv_hbm = hbm("conv_hbm", (KD, P, T2))
        rec_hbm = hbm("rec_hbm", (KD, P, T2))
        tm_hbm = hbm("tm_hbm", (SEQ, TM_W))

        C_AT, C_N = offsets(CONSTS)
        P_AT, P_N = offsets(PARAMS)
        P2_AT, P2_N = offsets(PARAMS2)
        consts = sbuf(ctx, "consts", [P, C_N])
        ps = ctx.enter_context(nc.psum_tensor("ps", [P, 8, 512], F32))

        def cst(name, k=None):
            a, n = C_AT[name]
            return consts[:, a:a + n] if k is None else consts[:, a + k * P:a + (k + 1) * P]

        ident, ones, blk = cst("ident"), cst("ones"), cst("blk")
        hT = sbuf(ctx, "hT", [P, KD, T2])
        params = sbuf(ctx, "params", [P, max(P_N, P2_N)])

        def par(name, table=P_AT):
            a, n = table[name]
            return params[:, a:a + n]

        def w_rows(w):
            return w.rearrange("(k p) n -> p k n", p=P)

        def norm_scalar(act, x_tile, work):
            act.wait_ge(*DMA["x_tile"])
            act.activation(work["sq"][:, :], x_tile, FN.Square, accum_out=work["ss"][:, :]).then_inc(*ACT("norm_sum"))
            act.wait_ge(*ACT["norm_sum"])
            act.activation(work["ln"][:, :], work["ss"][:, :], FN.Ln, bias=cst("eps"), scale=1.0 / DM).then_inc(*ACT("norm_ln"))
            act.wait_ge(*ACT["norm_ln"])
            act.activation(work["rstd"][:, :], work["ln"][:, :], FN.Exp, scale=-0.5).then_inc(*ACT("norm_rstd"))

        def norm_vector(vec, x_tile, g, work):
            vec.wait_ge(*ACT["norm_rstd"])
            vec.tensor_scalar(work["xn"][:, :], x_tile, work["rstd"][:, :], None, ALU.mult).then_inc(*VEC("normed"))
            for b in range(2):
                vec.wait_ge(*PE[f"turned{b}"])
                vec.tensor_tensor(work["hs"][:, 4 * b:4 * b + 4, :], ps[:, b, :].rearrange("p (k n) -> p k n", k=4),
                                  col(g[:, 4 * b:4 * b + 4], P), ALU.mult).then_inc(*VEC(f"h_tile{b}"))

        def norm_tensor(pe, work):
            pe.wait_ge(*VEC["normed"])
            for b in range(2):
                for k in range(4):
                    m = pe.transpose(ps[:, b, k * P:(k + 1) * P], work["xn"][:, (4 * b + k) * P:(4 * b + k + 1) * P], ident)
                m.then_inc(*PE(f"turned{b}"))

        def norm_pool(pool, t, work):
            pool.wait_ge(*VEC["h_tile1"])
            pool.tensor_copy(hT[:, :, ds(t * P, P)], work["hs"][:, :, :]).then_inc(*POOL("h_kept"))

        def norm_buffers(stack, tag):
            return {"x": sbuf(stack, "x" + tag, [P, DM]), "sq": sbuf(stack, "sq" + tag, [P, DM]), "xn": sbuf(stack, "xn" + tag, [P, DM]),
                    "hs": sbuf(stack, "hs" + tag, [P, KD, P]), "ss": sbuf(stack, "ss" + tag, [P, 1]),
                    "ln": sbuf(stack, "ln" + tag, [P, 1]), "rstd": sbuf(stack, "rstd" + tag, [P, 1])}

        first = ExitStack()
        cs = sbuf(first, "cos_sin", [P, NT, 2, ROPE // 2])
        begin("load")
        with ExitStack() as st, nc.Block() as block:
            pos_i = sbuf(st, "pos_i", [P, NT], I32)
            pos = sbuf(st, "pos", [P, NT])
            ang = sbuf(st, "ang", [P, 2, NT, ROPE // 2])
            turns = sbuf(st, "turns", [P, 2, NT, ROPE // 2])
            whole = sbuf(st, "whole", [P, 2, NT, ROPE // 2])

            @block.sync
            def _(sp):
                sp.dma_start(consts[:, :], io["consts"]).then_inc(*DMA("consts"))
                sp.dma_start(pos_i[:, :], io["positions"]).then_inc(*DMA("positions"))
                sp.dma_start(x_hbm[P:T2, :], io["x"]).then_inc(*DMA("x"))
                sp.wait_ge(*DMA["x"])

            @block.vector
            def _(vec):
                two_pi = 2 * np.pi
                c1 = float(np.float32(6.28125))
                c2 = float(np.float32(np.round((two_pi - c1) * 2**19) / 2**19))
                c3 = float(np.float32(two_pi - c1 - c2))
                magic = float(np.float32(1.5 * 2**23))
                vec.wait_ge(*DMA["positions"])
                vec.tensor_copy(pos[:, :], pos_i[:, :]).then_inc(*VEC("pos"))
                vec.wait_ge(*DMA["consts"])
                vec.wait_ge(*VEC["pos"])
                vec.tensor_tensor(ang[:, 1, :, :], col(pos[:, :], ROPE // 2), rep(cst("freq"), NT), ALU.mult).then_inc(*VEC("ang"))
                vec.wait_ge(*VEC["ang"])
                vec.tensor_scalar(turns[:, 1], ang[:, 1], 1.0 / two_pi, magic, ALU.mult, ALU.add).then_inc(*VEC("turns1"))
                vec.tensor_scalar(turns[:, 0], ang[:, 1], 1.0 / two_pi, 0.25, ALU.mult, ALU.add).then_inc(*VEC("turns0a"))
                vec.wait_ge(*VEC["turns0a"])
                vec.tensor_scalar(turns[:, 0], turns[:, 0], magic, None, ALU.add).then_inc(*VEC("turns0"))
                vec.wait_ge(*VEC["turns0"])
                vec.tensor_scalar(whole[:, :], turns[:, :], magic, None, ALU.subtract).then_inc(*VEC("whole"))
                vec.tensor_copy(ang[:, 0], ang[:, 1]).then_inc(*VEC("ang0"))
                for n, c in enumerate((c1, c2, c3)):
                    vec.wait_ge(*VEC["ang0" if n == 0 else f"cut{n - 1}"])
                    vec.scalar_tensor_tensor(out=ang[:, :], in0=whole[:, :], scalar=-c, in1=ang[:, :], op0=ALU.mult,
                                             op1=ALU.add).then_inc(*VEC(f"cut{n}"))
                vec.wait_ge(*VEC["cut2"])
                vec.tensor_scalar(ang[:, 0], ang[:, 0], float(np.float32(np.pi / 2)), None, ALU.add).then_inc(*VEC("quarter"))
                vec.wait_ge(*VEC["quarter"])
                vec.tensor_scalar(ang[:, :], ang[:, :], 3.1415925, -3.1415925, ALU.min, ALU.max).then_inc(*VEC("range"))

            @block.scalar
            def _(act):
                act.wait_ge(*VEC["range"])
                act.activation(cs[:, :, :, :].rearrange("p t c f -> p c t f"), ang[:, :, :, :], FN.Sin).then_inc(*ACT("cos_sin"))
        clear()

        with nc.Fori(0, DEPTH) as L:
            w_in = io["w_in"][ds(L, 1)].rearrange("a r n -> (a r) n")
            w_uq = io["w_uq"][ds(L, 1)].rearrange("a r n -> (a r) n")

            with ExitStack() as st:
                work = norm_buffers(st, "_1")
                wg = sbuf(st, "w_gate", [P, KD, DM])
                wt = sbuf(st, "w_tm", [P, KD, TM_W])
                gate = sbuf(st, "gate", [P, DM])
                tm_out = sbuf(st, "tm_out", [P, TM_W])
                begin("load1")
                with nc.Block() as block:
                    @block.sync
                    def _(sp):
                        sp.dma_start(params[:, 0:P_N], io["params"][ds(L, 1)].rearrange("a p n -> (a p) n")).then_inc(*DMA("params"))
                        sp.dma_start(wt[:, :, :], w_rows(w_in[:, COL_AB:COL_RW])).then_inc(*DMA("w_tm"))
                        sp.dma_start(wg[:, :, :], w_rows(w_in[:, 0:DM])).then_inc(*DMA("w_gate"))
                        sp.wait_ge(*DMA["params"])
                        sp.wait_ge(*DMA["w_tm"])
                        sp.wait_ge(*DMA["w_gate"])
                clear()
                with nc.Fori(1, NT2) as t:
                    begin("stage1")
                    with nc.Block() as block:
                        @block.scalar
                        def _(act):
                            norm_scalar(act, work["x"][:, :], work)
                            for b in range(2):
                                act.wait_ge(*PE[f"gate{b}"])
                                act.copy(gate[:, b * 512:(b + 1) * 512], ps[:, 2 + b, :]).then_inc(*ACT(f"gate{b}"))

                        @block.vector
                        def _(vec):
                            norm_vector(vec, work["x"][:, :], par("norm_g"), work)
                            vec.wait_ge(*PE["tm"])
                            vec.tensor_copy(tm_out[:, :], ps[:, 4, 0:TM_W]).then_inc(*VEC("tm"))

                        @block.tensor
                        def _(pe):
                            norm_tensor(pe, work)
                            pe.wait_ge(*VEC["h_tile1"])
                            for b in range(3):
                                for k in range(KD):
                                    if b == 0:
                                        m = pe.matmul(ps[:, 4, 0:TM_W], lhsT=work["hs"][:, k, :], rhs=wt[:, k, :],
                                                      start=(k == 0), stop=(k == KD - 1))
                                    else:
                                        m = pe.matmul(ps[:, 1 + b, :], lhsT=work["hs"][:, k, :], rhs=wg[:, k, (b - 1) * 512:b * 512],
                                                      start=(k == 0), stop=(k == KD - 1))
                                m.then_inc(*PE("tm" if b == 0 else f"gate{b - 1}"))

                        @block.gpsimd
                        def _(pool):
                            norm_pool(pool, t, work)

                        @block.sync
                        def _(sp):
                            sp.dma_start(work["x"][:, :], x_hbm[ds(t * P, P), :]).then_inc(*DMA("x_tile"))
                            row = (t - 1) * P
                            sp.wait_ge(*VEC["tm"])
                            sp.dma_start(tm_hbm[ds(row, P), :], tm_out[:, :]).then_inc(*DMA("tm_out"))
                            sp.wait_ge(*ACT["gate1"])
                            sp.dma_start(gate_hbm[ds(row, P), :], gate[:, :]).then_inc(*DMA("gate_out"))
                            sp.wait_ge(*DMA["tm_out"])
                            sp.wait_ge(*DMA["gate_out"])
                    clear()

            def project_tensor(pe, wc):
                for b in range(2):
                    for k in range(KD):
                        m = pe.matmul(ps[:, b, :], lhsT=wc[:, k, :], rhs=hT[:, k, P + b * 512:P + (b + 1) * 512],
                                      start=(k == 0), stop=(k == KD - 1))
                    m.then_inc(*PE(f"proj{b}"))

            def project_copy(act, xp):
                for b in range(2):
                    act.wait_ge(*PE[f"proj{b}"])
                    act.copy(xp[:, 2 + b * 512:2 + (b + 1) * 512], ps[:, b, :]).then_inc(*ACT(f"proj{b}"))

            def load_columns(wc, column):
                begin("columns")
                with nc.Block() as block:
                    @block.sync
                    def _(sp):
                        sp.dma_start(wc[:, :, :], w_rows(w_in[:, column:column + P])).then_inc(*DMA("w_cols"))
                        sp.wait_ge(*DMA["w_cols"])
                clear()

            def invert_tensor(pe, n_groups, size, ready, AT, X, Y, Pm):
                def bank(kind, g):
                    return ps[:, 2 * kind + g % 2, :].rearrange("p (u n) -> p u n", u=4)
                for k in range(NLEV):
                    for g in range(n_groups):
                        us = range(size * g, size * (g + 1))
                        if k == 0:
                            pe.wait_ge(*VEC[ready[g]])
                        else:
                            pe.wait_ge(*POOL[f"X0_{g}"] if k == 1 else VEC[f"Xn{k - 1}_{g}"])
                        if g >= 2:
                            pe.wait_ge(*VEC[f"P{k}_{g - 2}"])
                        elif k > 0:
                            last = max(q for q in range(n_groups) if q % 2 == g % 2)
                            pe.wait_ge(*VEC[f"P{k - 1}_{last}"])
                        for n, u in enumerate(us):
                            m = pe.matmul(bank(0, g)[:, n, :], lhsT=AT(u), rhs=ident if k == 0 else X[:, u, :],
                                          start=True, stop=True)
                        m.then_inc(*PE(f"P{k}_{g}"))
                    if k == 0:
                        continue
                    for g in range(n_groups):
                        us = range(size * g, size * (g + 1))
                        pe.wait_ge(*VEC[f"P{k}_{g}"])
                        if k == 1:
                            pe.wait_ge(*POOL[f"Y0_{g}"])
                        else:
                            pe.wait_ge(*VEC[f"Yn{k - 1}_{g}"])
                        prev = (k, g - 2) if g >= 2 else (k - 1, max(q for q in range(n_groups) if q % 2 == g % 2))
                        if prev[0] >= 1:
                            pe.wait_ge(*VEC[f"Yn{prev[0]}_{prev[1]}"])
                            pe.wait_ge(*VEC[f"Xn{prev[0]}_{prev[1]}"] if prev[0] < NLEV - 1 else VEC[f"Yn{prev[0]}_{prev[1]}"])
                        if k < NLEV - 1:
                            for n, u in enumerate(us):
                                m = pe.matmul(bank(1, g)[:, n, :], lhsT=Y[:, u, :], rhs=Pm[:, u, :], start=True, stop=True)
                            m.then_inc(*PE(f"Xd{k}_{g}"))
                        for n, u in enumerate(us):
                            m = pe.matmul(bank(2, g)[:, n, :], lhsT=Pm[:, u, :], rhs=Y[:, u, :], start=True, stop=True)
                        m.then_inc(*PE(f"Yd{k}_{g}"))

            def invert_vector(vec, n_groups, size, parts, X, Y, Pm):
                def bank(kind, g):
                    return ps[:, 2 * kind + g % 2, :].rearrange("p (u n) -> p u n", u=4)
                for k in range(NLEV):
                    for g in range(n_groups):
                        vec.wait_ge(*PE[f"P{k}_{g}"])
                        for n, (a, b, lower) in enumerate(parts(g)):
                            a0 = a - size * g
                            m = vec.tensor_tensor(Pm[:, a:b, :], bank(0, g)[:, a0:a0 + b - a, :],
                                                  rep(cst("lo" if lower else "up", k), b - a), ALU.mult)
                        m.then_inc(*VEC(f"P{k}_{g}"))
                    if k == 0:
                        continue
                    for g in range(n_groups):
                        us = slice(size * g, size * (g + 1))
                        if k < NLEV - 1:
                            vec.wait_ge(*PE[f"Xd{k}_{g}"])
                            vec.tensor_tensor(X[:, us, :], X[:, us, :], bank(1, g)[:, 0:size, :], ALU.subtract).then_inc(*VEC(f"Xn{k}_{g}"))
                        vec.wait_ge(*PE[f"Yd{k}_{g}"])
                        vec.tensor_tensor(Y[:, us, :], Y[:, us, :], bank(2, g)[:, 0:size, :], ALU.subtract).then_inc(*VEC(f"Yn{k}_{g}"))

            def invert_pool(pool, n_groups, size, ready, parts, AT_all, X, Y, Pm):
                for g in range(n_groups):
                    us = slice(size * g, size * (g + 1))
                    pool.wait_ge(*VEC[ready[g]])
                    for a, b, lower in parts(g):
                        m = pool.tensor_tensor(Y[:, a:b, :], AT_all(a, b), rep(cst("up" if lower else "lo", 0), b - a), ALU.mult)
                    m.then_inc(*POOL(f"Y00_{g}"))
                    pool.wait_ge(*POOL[f"Y00_{g}"])
                    pool.tensor_tensor(Y[:, us, :], rep(ident, size), Y[:, us, :], ALU.subtract).then_inc(*POOL(f"Y0_{g}"))
                    pool.wait_ge(*VEC[f"P0_{g}"])
                    pool.tensor_tensor(X[:, us, :], rep(ident, size), Pm[:, us, :], ALU.subtract).then_inc(*POOL(f"X0_{g}"))

            with ExitStack() as st:
                rw = sbuf(st, "rw", [P, 7, SEQ])
                dec = sbuf(st, "dec", [P, 2, 2, SEQ])
                kmod = sbuf(st, "kmod", [P, 2, 2, SEQ])
                bb = sbuf(st, "bb", [P, 2, 2, SEQ])
                bonus = sbuf(st, "bonus", [P, 2, SEQ])
                with ExitStack() as st2:
                    wc = sbuf(st2, "w_cols", [P, KD, P])
                    xp = sbuf(st2, "x_pad", [P, SEQ + 4])
                    acc = sbuf(st2, "acc", [P, SEQ])
                    mu0 = sbuf(st2, "mu0", [P, 7])
                    load_columns(wc, COL_RW + 6 * P)
                    begin("rw_zero")
                    with nc.Block() as block:
                        @block.vector
                        def _(vec):
                            vec.memset(xp[:, :], 0.0).then_inc(*VEC("pad"))
                            mu = par("mu").rearrange("p (i c) -> p i c", c=2)
                            vec.tensor_tensor(mu0[:, :], mu[:, :, 0], mu[:, :, 1], ALU.add).then_inc(*VEC("mu_sum"))
                            vec.wait_ge(*VEC["mu_sum"])
                            vec.tensor_scalar(mu0[:, :], mu0[:, :], -1.0, 1.0, ALU.mult, ALU.add).then_inc(*VEC("mu0"))
                    clear()
                    with nc.Fori(0, 7) as i:
                        begin("rw_proj")
                        with nc.Block() as block:
                            @block.tensor
                            def _(pe):
                                project_tensor(pe, wc)

                            @block.scalar
                            def _(act):
                                project_copy(act, xp)

                            @block.sync
                            def _(sp):
                                sp.wait_ge(*PE["proj1"])
                                sp.dma_start(wc[:, :, :], w_rows(w_in[:, ds((6 - i) * P + (COL_RW - P), P)])).then_inc(*DMA("w_cols"))
                                sp.wait_ge(*DMA["w_cols"])

                            @block.vector
                            def _(vec):
                                vec.wait_ge(*ACT["proj1"])
                                vec.tensor_scalar(acc[:, :], xp[:, 2:2 + SEQ], mu0[:, ds(6 - i, 1)], None, ALU.mult).then_inc(*VEC("centre"))
                                vec.wait_ge(*VEC["centre"])
                                mu_at = P_AT["mu"][0]
                                vec.scalar_tensor_tensor(out=acc[:, :], in0=xp[:, 1:1 + SEQ], scalar=params[:, ds((6 - i) * 2 + mu_at, 1)],
                                                         in1=acc[:, :], op0=ALU.mult, op1=ALU.add).then_inc(*VEC("before"))
                                vec.wait_ge(*VEC["before"])
                                vec.scalar_tensor_tensor(out=rw[:, ds(6 - i, 1), :], in0=xp[:, 3:3 + SEQ],
                                                         scalar=params[:, ds((6 - i) * 2 + (mu_at + 1), 1)],
                                                         in1=acc[:, :], op0=ALU.mult, op1=ALU.add).then_inc(*VEC("after"))
                        clear()

                begin("rw_feat")
                with ExitStack() as st2, nc.Block() as block:
                    th = sbuf(st2, "th", [64, SEQ])
                    kx = sbuf(st2, "kx", [P, 2, SEQ])
                    a_all = sbuf(st2, "a_all", [P, 2, 2, SEQ])
                    sq = sbuf(st2, "sq_f", [P, SEQ])
                    ksum = sbuf(st2, "ksum", [P, SEQ])
                    omka = sbuf(st2, "omka", [P, 2])
                    w2a2 = sbuf(st2, "w2a2", [P, 2, RW])
                    PAIRS = [(e, m) for e in range(2) for m in range(2)]

                    @block.sync
                    def _(sp):
                        sp.dma_start(w2a2[:, :, :], io["w2a2"][ds(L, 1)].rearrange("a p e n -> (a p) e n")).then_inc(*DMA("w2a2"))

                    @block.tensor
                    def _(pe):
                        pe.wait_ge(*DMA["w2a2"])
                        pe.wait_ge(*ACT["tanh"])
                        for n, (e, m) in enumerate(PAIRS):
                            if n:
                                pe.wait_ge(*ACT[f"dec{n - 1}"])
                            for b in range(2):
                                t = slice(b * 512, (b + 1) * 512)
                                q = pe.matmul(ps[:, b, :], lhsT=w2a2[0:64, e, m * P:(m + 1) * P], rhs=th[:, t], start=True, stop=True)
                            q.then_inc(*PE(f"dec{n}"))
                            if n:
                                pe.wait_ge(*ACT[f"rate{n - 1}"])
                            for b in range(2):
                                t = slice(b * 512, (b + 1) * 512)
                                q = pe.matmul(ps[:, 2 + b, :], lhsT=w2a2[64:128, e, m * P:(m + 1) * P], rhs=rw[64:128, 6, t],
                                              start=True, stop=True)
                            q.then_inc(*PE(f"rate{n}"))
                        for m in range(2):
                            pe.wait_ge(*VEC[f"sq{m}"])
                            if m:
                                pe.wait_ge(*ACT["kk_ln0"])
                            for b in range(2):
                                q = pe.matmul(ps[:, 4 + b, :], lhsT=blk, rhs=sq[:, b * 512:(b + 1) * 512], start=True, stop=True)
                            q.then_inc(*PE(f"sumsq{m}"))

                    @block.scalar
                    def _(act):
                        act.activation(th[:, :], rw[0:64, 6, :], FN.Tanh).then_inc(*ACT("tanh"))
                        for n, (e, m) in enumerate(PAIRS):
                            c = P_AT["w0"][0] + 2 * e + m
                            act.wait_ge(*PE[f"dec{n}"])
                            act.activation(dec[:, e, m, :].rearrange("p (b n) -> p b n", b=2), ps[:, 0:2, :], FN.Sigmoid,
                                           bias=params[:, c:c + 1]).then_inc(*ACT(f"dec{n}"))
                            c = P_AT["a0"][0] + 2 * e + m
                            act.wait_ge(*PE[f"rate{n}"])
                            act.activation(a_all[:, e, m, :].rearrange("p (b n) -> p b n", b=2), ps[:, 2:4, :], FN.Sigmoid,
                                           bias=params[:, c:c + 1]).then_inc(*ACT(f"rate{n}"))
                        act.wait_ge(*ACT["dec3"])
                        act.activation(dec[:, :, :, :], dec[:, :, :, :], FN.Exp, scale=-float(np.exp(-0.5))).then_inc(*ACT("decay"))
                        for m in range(2):
                            act.wait_ge(*PE[f"sumsq{m}"])
                            if m:
                                act.wait_ge(*VEC["kk0"])
                            act.activation(ksum[:, :].rearrange("p (b n) -> p b n", b=2), ps[:, 4:6, :], FN.Ln,
                                           bias=cst("eps")).then_inc(*ACT(f"kk_ln{m}"))
                            act.wait_ge(*ACT[f"kk_ln{m}"])
                            act.activation(ksum[:, :], ksum[:, :], FN.Exp, scale=-0.5).then_inc(*ACT(f"kk_rs{m}"))

                    @block.vector
                    def _(vec):
                        vec.tensor_scalar(omka[:, :], par("k_a"), -1.0, 1.0, ALU.mult, ALU.add).then_inc(*VEC("omka"))
                        for m in range(2):
                            c = P_AT["k_k"][0] + m
                            vec.tensor_scalar(kx[:, m, :], rw[:, 2 + m, :], params[:, c:c + 1], None, ALU.mult).then_inc(*VEC(f"kx{m}"))
                        for m in range(2):
                            vec.wait_ge(*VEC[f"kx{m}"])
                            if m:
                                vec.wait_ge(*PE["sumsq0"])
                            vec.tensor_tensor(sq[:, :], kx[:, m, :], kx[:, m, :], ALU.mult).then_inc(*VEC(f"sq{m}"))
                        for n, (e, m) in enumerate(PAIRS):
                            c = P_AT["k_a"][0] + m
                            vec.wait_ge(*ACT[f"rate{n}"])
                            vec.wait_ge(*VEC["omka"])
                            vec.tensor_scalar(kmod[:, e, m, :], a_all[:, e, m, :], params[:, c:c + 1], omka[:, m:m + 1],
                                              ALU.mult, ALU.add).then_inc(*VEC(f"kf{n}"))
                            vec.wait_ge(*VEC[f"kf{n}"])
                            vec.tensor_tensor(kmod[:, e, m, :], kmod[:, e, m, :], rw[:, 2 + m, :], ALU.mult).then_inc(*VEC(f"km{n}"))
                        for m in range(2):
                            c = P_AT["r_k"][0] + m
                            vec.wait_ge(*VEC[f"km{2 + m}"])
                            vec.tensor_tensor(bonus[:, m, :], kmod[:, 0, m, :], kmod[:, 1, m, :], ALU.add).then_inc(*VEC(f"bo{m}a"))
                            vec.wait_ge(*VEC[f"bo{m}a"])
                            vec.scalar_tensor_tensor(out=bonus[:, m, :], in0=bonus[:, m, :], scalar=0.5, in1=rw[:, m, :],
                                                     op0=ALU.mult, op1=ALU.mult).then_inc(*VEC(f"bo{m}b"))
                            vec.wait_ge(*VEC[f"bo{m}b"])
                            vec.tensor_scalar(bonus[:, m, :], bonus[:, m, :], params[:, c:c + 1], None, ALU.mult).then_inc(*VEC(f"bo{m}"))
                        for m in range(2):
                            vec.wait_ge(*ACT[f"kk_rs{m}"])
                            vec.tensor_tensor(rw[:, 2 + m, :], kx[:, m, :], ksum[:, :], ALU.mult).then_inc(*VEC(f"kk{m}"))
                            for e in range(2):
                                vec.wait_ge(*VEC[f"kk{m}"])
                                vec.tensor_tensor(bb[:, e, m, :], a_all[:, e, m, :], rw[:, 2 + m, :], ALU.mult).then_inc(*VEC(f"b{e}{m}"))
                clear()

                with ExitStack() as st2:
                    dch = sbuf(st2, "dch", [P, 4, P])
                    vs = sbuf(st2, "vs", [P, 4, P])
                    bs = sbuf(st2, "bs", [P, 2, P])
                    pp = sbuf(st2, "pp", [P, 4, P + 1])
                    pc = sbuf(st2, "pc", [P, 4, P + 1])
                    ip = sbuf(st2, "ip", [P, 4, P + 1])
                    cinv = sbuf(st2, "cinv", [P, 4])
                    wcm = sbuf(st2, "wcm", [P, 4])
                    KR = sbuf(st2, "KR", [P, 4, 2, P])
                    KB = sbuf(st2, "KB", [P, 4, 2, P])
                    KBt = sbuf(st2, "KBt", [P, 4, 2, P])
                    vt = sbuf(st2, "vt", [P, 4, P])
                    MT = sbuf(st2, "MT", [P, 8, 4, P])
                    X = sbuf(st2, "X", [P, 8, P])
                    Y = sbuf(st2, "Y", [P, 8, P])
                    Pm = sbuf(st2, "Pm", [P, 8, P])
                    Rs = sbuf(st2, "Rs", [P, 4, P])
                    sa = sbuf(st2, "sa", [P, 4, P])
                    yo = sbuf(st2, "yo", [P, 3, RW])
                    Z = sbuf(st2, "Z", [P, 4, P])
                    Zc = sbuf(st2, "Zc", [P, 4, P])
                    Zt = sbuf(st2, "Zt", [P, 4, P])
                    bon = sbuf(st2, "bon", [P, 4])
                    zero = sbuf(st2, "zero", [P, P])
                    begin("rw_state")
                    with nc.Block() as block:
                        @block.vector
                        def _(vec):
                            vec.memset(Z[:, :, :], 0.0).then_inc(*VEC("z"))
                            vec.memset(zero[:, :], 0.0).then_inc(*VEC("zero"))
                            vec.memset(pp[:, :, :], 1.0).then_inc(*VEC("edges"))
                    clear()
                    MID = P // 2
                    with nc.Fori(0, NT) as c:
                        begin("rw_chunk")
                        with nc.Block() as block:
                            off = [c * P, (NT - 1 - c) * P]

                            @block.scalar
                            def _(act):
                                for e in range(2):
                                    act.copy(dch[:, 2 * e:2 * e + 2, :], dec[:, e, :, ds(off[e], P)]).then_inc(*ACT(f"dch{e}"))
                                for e in range(2):
                                    act.copy(vs[:, 2 * e:2 * e + 2, :], rw[:, 4:6, ds(off[e], P)]).then_inc(*ACT(f"vs{e}"))
                                act.copy(bs[:, :, :], bonus[:, :, ds(off[0], P)]).then_inc(*ACT("bs"))
                                act.wait_ge(*PE["vt"])
                                act.copy(vt[:, :, :], ps[:, 6, :].rearrange("p (u n) -> p u n", u=4)).then_inc(*ACT("vt"))
                                for b in range(2):
                                    act.wait_ge(*PE[f"KBt{b}"])
                                    act.copy(KBt[:, 2 * b:2 * b + 2, :, :].rearrange("p a k n -> p (a k) n"),
                                             ps[:, 6 + b, :].rearrange("p (u n) -> p u n", u=4)).then_inc(*ACT(f"KBt{b}"))
                                act.wait_ge(*PE["bon"])
                                act.copy(bon[:, :], ps[:, 7, 0:4]).then_inc(*ACT("bon"))
                                act.wait_ge(*PE["R"])
                                act.mul(Rs[:, :, :], ps[:, 6, :].rearrange("p (u n) -> p u n", u=4), -1.0).then_inc(*ACT("R"))
                                act.wait_ge(*PE["sa"])
                                act.copy(sa[:, :, :], ps[:, 7, :].rearrange("p (u n) -> p u n", u=4)).then_inc(*ACT("sa"))
                                act.wait_ge(*PE["y"])
                                act.copy(yo[:, 0:2, :], ps[:, 6, :].rearrange("p (u n) -> p u n", u=2)).then_inc(*ACT("y"))

                            @block.vector
                            def _(vec):
                                for e in range(2):
                                    vec.wait_ge(*ACT[f"dch{e}"])
                                    for m in range(2):
                                        u = 2 * e + m
                                        if e == 0:
                                            o, d = pp[:, u, 1:P + 1], dch[:, u, :]
                                        else:
                                            o, d = pp[:, u, 0:P][:, ::-1], dch[:, u, :][:, ::-1]
                                        q = vec.tensor_tensor_scan(o, d, zero[:, :], 1.0, ALU.mult, ALU.add)
                                    q.then_inc(*VEC(f"scan{e}"))
                                vec.wait_ge(*VEC["scan0"])
                                vec.wait_ge(*VEC["scan1"])
                                vec.reciprocal(cinv[:, :], pp[:, :, MID]).then_inc(*VEC("cinv"))
                                vec.wait_ge(*VEC["cinv"])
                                vec.tensor_tensor(pc[:, :, :], pp[:, :, :], col(cinv[:, :], P + 1), ALU.mult).then_inc(*VEC("pc"))
                                vec.wait_ge(*VEC["pc"])
                                vec.reciprocal(ip[:, :, :], pc[:, :, :]).then_inc(*VEC("ip"))
                                for e in range(2):
                                    u = slice(2 * e, 2 * e + 2)
                                    inc, exc = (slice(1, P + 1), slice(0, P)) if e == 0 else (slice(0, P), slice(1, P + 1))
                                    vec.tensor_tensor(KR[:, u, 0, :], rw[:, 2:4, ds(off[e], P)], pc[:, u, exc], ALU.mult)
                                    vec.tensor_tensor(KR[:, u, 1, :], rw[:, 0:2, ds(off[e], P)], pc[:, u, inc], ALU.mult).then_inc(*VEC(f"KR{e}"))
                                    vec.wait_ge(*VEC["ip"])
                                    vec.tensor_tensor(KB[:, u, 0, :], bb[:, e, :, ds(off[e], P)], ip[:, u, inc], ALU.mult)
                                    vec.tensor_tensor(KB[:, u, 1, :], kmod[:, e, :, ds(off[e], P)], ip[:, u, inc], ALU.mult).then_inc(*VEC(f"KB{e}"))
                                vec.tensor_tensor(Zc[:, :, :], Z[:, :, :], col(pp[:, :, MID], P), ALU.mult).then_inc(*VEC("Zc"))
                                for e in range(2):
                                    for n in range(4):
                                        u = 4 * e + n
                                        vec.wait_ge(*PE[f"pairs{u}"])
                                        bank = ps[:, u % 6, :].rearrange("p (a b n) -> p a b n", a=2, b=2)
                                        before = cst("bef" if e == 0 else "aft")
                                        upto = cst("tri_f" if e == 0 else "tri_b")
                                        M4 = MT[:, u, :, :].rearrange("p (a b) n -> p a b n", a=2)
                                        vec.tensor_tensor(M4[:, :, 0, :], bank[:, :, 0, :], rep(before, 2), ALU.mult)
                                        q = vec.tensor_tensor(M4[:, :, 1, :], bank[:, :, 1, :], rep(upto, 2), ALU.mult)
                                        q.then_inc(*VEC(f"MT{u}" if n < 3 else f"AT{e}"))
                                invert_vector(vec, 2, 4, lambda g: [(4 * g, 4 * g + 4, g == 0)], X, Y, Pm)
                                vec.wait_ge(*ACT["bon"])
                                vec.tensor_tensor(yo[:, 2, :].rearrange("p (h n) -> p h n", h=4),
                                                  vt[:, 0:2, :].rearrange("p m (h n) -> p (m h) n", h=2), col(bon[:, :], RD),
                                                  ALU.mult).then_inc(*VEC("bonus"))
                                for e in range(2):
                                    at = P if e == 0 else 0
                                    q = vec.tensor_tensor(wcm[:, 2 * e:2 * e + 2], pp[:, 2 * e:2 * e + 2, at], cinv[:, 2 * e:2 * e + 2], ALU.mult)
                                q.then_inc(*VEC("wcm"))
                                for e in range(2):
                                    at = P if e == 0 else 0
                                    u = slice(2 * e, 2 * e + 2)
                                    q = vec.tensor_tensor(Z[:, u, :], Z[:, u, :], col(pp[:, u, at], P), ALU.mult)
                                q.then_inc(*VEC("Zdec"))
                                vec.wait_ge(*PE["Zn"])
                                vec.tensor_tensor(Zt[:, :, :], ps[:, 4, :].rearrange("p (u n) -> p u n", u=4), rep(blk, 4), ALU.mult).then_inc(*VEC("Zt"))
                                vec.wait_ge(*VEC["wcm"])
                                vec.wait_ge(*VEC["Zt"])
                                vec.tensor_tensor(Zt[:, :, :], Zt[:, :, :], col(wcm[:, :], P), ALU.mult).then_inc(*VEC("Zt2"))
                                vec.wait_ge(*VEC["Zt2"])
                                vec.tensor_tensor(Z[:, :, :], Z[:, :, :], Zt[:, :, :], ALU.add).then_inc(*VEC("Z"))

                            @block.gpsimd
                            def _(pool):
                                invert_pool(pool, 2, 4, ("AT0", "AT1"), lambda g: [(4 * g, 4 * g + 4, g == 0)], lambda a, b: MT[:, a:b, 0, :], X, Y, Pm)

                            @block.tensor
                            def _(pe):
                                pe.wait_ge(*ACT["vs1"])
                                for u in range(4):
                                    q = pe.transpose(ps[:, 6, u * P:(u + 1) * P], vs[:, u, :], ident)
                                q.then_inc(*PE("vt"))
                                for e in range(2):
                                    pe.wait_ge(*VEC[f"KR{e}"])
                                    pe.wait_ge(*VEC[f"KB{e}"])
                                    for m in range(2):
                                        for h in range(2):
                                            u, c0 = 4 * e + 2 * m + h, slice(64 * h, 64 * h + 64)
                                            if u >= 6:
                                                pe.wait_ge(*VEC[f"MT{u - 6}"])
                                            for kb in range(2):
                                                q = pe.matmul(ps[:, u % 6, 256 * kb:256 * kb + 256], lhsT=KB[c0, 2 * e + m, kb, :],
                                                              rhs=KR[c0, 2 * e + m, :, :], start=True, stop=True)
                                            q.then_inc(*PE(f"pairs{u}"))
                                for b in range(2):
                                    pe.wait_ge(*ACT["vt"])
                                    for u in range(2):
                                        for kb in range(2):
                                            q = pe.transpose(ps[:, 6 + b, (2 * u + kb) * P:(2 * u + kb + 1) * P], KB[:, 2 * b + u, kb, :], ident)
                                    q.then_inc(*PE(f"KBt{b}"))
                                pe.wait_ge(*ACT["KBt1"])
                                pe.wait_ge(*ACT["bs"])
                                for m in range(2):
                                    q = pe.matmul(ps[:, 7, 2 * m:2 * m + 2], lhsT=bs[:, m, :], rhs=cst("sel"), start=True, stop=True)
                                q.then_inc(*PE("bon"))
                                pe.wait_ge(*VEC["AT1"])
                                invert_tensor(pe, 2, 4, ("AT0", "AT1"), lambda u: MT[:, u, 0, :], X, Y, Pm)
                                pe.wait_ge(*VEC["Zc"])
                                pe.wait_ge(*ACT["bon"])
                                for em in range(4):
                                    pe.matmul(ps[:, 6, em * P:(em + 1) * P], lhsT=KR[:, em, 0, :], rhs=Zc[:, em, :], start=True, stop=False,
                                              skip_group_check=True)
                                    for h in range(2):
                                        n = slice(em * P + 64 * h, em * P + 64 * h + 64)
                                        q = pe.matmul(ps[:, 6, n], lhsT=MT[:, 2 * em + h, 2, :], rhs=vt[:, em, 64 * h:64 * h + 64],
                                                      start=False, stop=True, skip_group_check=True)
                                q.then_inc(*PE("R"))
                                pe.wait_ge(*VEC[f"Yn{NLEV - 1}_1"])
                                pe.wait_ge(*ACT["R"])
                                for u in range(8):
                                    n = slice(64 * u, 64 * u + 64)
                                    q = pe.matmul(ps[:, 7, n], lhsT=Y[:, u, :], rhs=Rs[:, u // 2, 64 * (u % 2):64 * (u % 2) + 64], start=True, stop=True)
                                q.then_inc(*PE("sa"))
                                pe.wait_ge(*ACT["sa"])
                                for em in range(4):
                                    pe.matmul(ps[:, 6, em * P:(em + 1) * P], lhsT=KR[:, em, 1, :], rhs=Zc[:, em, :], start=True, stop=False,
                                              skip_group_check=True)
                                    for h in range(2):
                                        n, hs = slice(em * P + 64 * h, em * P + 64 * h + 64), slice(64 * h, 64 * h + 64)
                                        pe.matmul(ps[:, 6, n], lhsT=MT[:, 2 * em + h, 1, :], rhs=sa[:, em, hs], start=False, stop=False,
                                                  skip_group_check=True)
                                        q = pe.matmul(ps[:, 6, n], lhsT=MT[:, 2 * em + h, 3, :], rhs=vt[:, em, hs], start=False, stop=True,
                                                      skip_group_check=True)
                                q.then_inc(*PE("y"))
                                for em in range(4):
                                    pe.matmul(ps[:, 4, em * P:(em + 1) * P], lhsT=KBt[:, em, 0, :], rhs=sa[:, em, :], start=True, stop=False)
                                    q = pe.matmul(ps[:, 4, em * P:(em + 1) * P], lhsT=KBt[:, em, 1, :], rhs=vt[:, em, :], start=False, stop=True)
                                q.then_inc(*PE("Zn"))

                            @block.sync
                            def _(sp):
                                sp.wait_ge(*VEC["bonus"])
                                sp.dma_start(rwkv_hbm[2, ds(off[0], P), :], yo[:, 2, :]).then_inc(*DMA("y_out"))
                                sp.wait_ge(*ACT["y"])
                                for e in range(2):
                                    sp.dma_start(rwkv_hbm[e, ds(off[e], P), :], yo[:, e, :]).then_inc(*DMA("y_out"))
                                sp.wait_ge(*DMA["y_out"])
                        clear()

            with ExitStack() as st:
                gq = sbuf(st, "gq", [P, 9, SEQ])
                with ExitStack() as st2:
                    wc = sbuf(st2, "w_cols_g", [P, KD, P])
                    xp = sbuf(st2, "x_pad_g", [P, SEQ + 4])
                    acc = sbuf(st2, "acc_g", [P, SEQ])
                    act_out = sbuf(st2, "act_out", [P, SEQ])
                    sq = sbuf(st2, "sq_g", [P, SEQ])
                    rs = sbuf(st2, "rs_g", [P, SEQ])
                    load_columns(wc, COL_GDN)
                    begin("gdn_zero")
                    with nc.Block() as block:
                        @block.vector
                        def _(vec):
                            vec.memset(xp[:, :], 0.0).then_inc(*VEC("pad"))
                    clear()
                    for first_tile, last_tile, normed in ((0, 6, True), (6, 9, False)):
                        with nc.Fori(first_tile, last_tile) as i:
                            begin(f"gdn_proj{first_tile}")
                            with nc.Block() as block:
                                @block.tensor
                                def _(pe):
                                    project_tensor(pe, wc)
                                    if normed:
                                        for b in range(2):
                                            pe.wait_ge(*POOL[f"sq{b}"])
                                            pe.matmul(ps[:, 2 + b, :], lhsT=blk, rhs=sq[:, b * 512:(b + 1) * 512], start=True,
                                                      stop=True).then_inc(*PE(f"sumsq{b}"))

                                @block.sync
                                def _(sp):
                                    sp.wait_ge(*PE["proj1"])
                                    sp.dma_start(wc[:, :, :], w_rows(w_in[:, ds(i * P + (COL_GDN + P), P)])).then_inc(*DMA("w_cols"))
                                    sp.wait_ge(*DMA["w_cols"])

                                @block.scalar
                                def _(act):
                                    project_copy(act, xp)
                                    act.wait_ge(*VEC[f"tap{CONV - 1}"])
                                    if not normed:
                                        act.activation(gq[:, ds(i, 1), :], acc[:, :], FN.Silu).then_inc(*ACT("silu"))
                                    else:
                                        act.activation(act_out[:, :], acc[:, :], FN.Silu).then_inc(*ACT("silu"))
                                        for b in range(2):
                                            t = slice(b * 512, (b + 1) * 512)
                                            act.wait_ge(*PE[f"sumsq{b}"])
                                            act.activation(rs[:, t], ps[:, 2 + b, :], FN.Ln, bias=cst("eps")).then_inc(*ACT(f"ln{b}"))
                                        for b in range(2):
                                            t = slice(b * 512, (b + 1) * 512)
                                            act.wait_ge(*ACT[f"ln{b}"])
                                            act.activation(rs[:, t], rs[:, t], FN.Exp, scale=-0.5).then_inc(*ACT(f"rs{b}"))

                                @block.vector
                                def _(vec):
                                    vec.wait_ge(*ACT["proj1"])
                                    at = P_AT["conv"][0]
                                    vec.tensor_scalar(acc[:, :], xp[:, 0:SEQ], params[:, ds(i * CONV + at, 1)], None, ALU.mult).then_inc(*VEC("tap0"))
                                    for n in range(1, CONV):
                                        vec.wait_ge(*VEC[f"tap{n - 1}"])
                                        vec.scalar_tensor_tensor(out=acc[:, :], in0=xp[:, n:n + SEQ], scalar=params[:, ds(i * CONV + (at + n), 1)],
                                                                 in1=acc[:, :], op0=ALU.mult, op1=ALU.add).then_inc(*VEC(f"tap{n}"))
                                    if normed:
                                        vec.wait_ge(*ACT["rs1"])
                                        vec.tensor_tensor(gq[:, ds(i, 1), :], act_out[:, :], rs[:, :], ALU.mult).then_inc(*VEC("normed"))

                                @block.gpsimd
                                def _(pool):
                                    if normed:
                                        pool.wait_ge(*ACT["silu"])
                                        for b in range(2):
                                            t = slice(b * 512, (b + 1) * 512)
                                            pool.tensor_tensor(sq[:, t], act_out[:, t], act_out[:, t], ALU.mult).then_inc(*POOL(f"sq{b}"))
                            clear()

                G2 = 2 * GH
                tm_ab = sbuf(st, "tm_ab", [P, NT, 2 * G2])
                gb = sbuf(st, "gb", [P, NT, 2, G2])
                begin("gdn_gates")
                with ExitStack() as st2, nc.Block() as block:
                    pre = sbuf(st2, "pre", [P, NT, G2])
                    mag = sbuf(st2, "mag", [P, NT, G2])
                    soft = sbuf(st2, "soft", [P, NT, G2])
                    rate = sbuf(st2, "rate", [P, G2])

                    @block.sync
                    def _(sp):
                        sp.dma_start(tm_ab[:, :, :], tm_hbm[:, 0:2 * G2].rearrange("(t p) n -> p t n", p=P)).then_inc(*DMA("ab"))
                        sp.wait_ge(*DMA["ab"])

                    @block.vector
                    def _(vec):
                        vec.wait_ge(*DMA["ab"])
                        vec.tensor_tensor(pre[:, :, :], tm_ab[:, :, 0:G2], rep(par("dt"), NT), ALU.add).then_inc(*VEC("pre"))
                        vec.wait_ge(*VEC["pre"])
                        vec.scalar_tensor_tensor(out=mag[:, :, :], in0=pre[:, :, :], scalar=-1.0, in1=pre[:, :, :], op0=ALU.mult,
                                                 op1=ALU.max).then_inc(*VEC("mag"))
                        vec.wait_ge(*ACT["soft"])
                        vec.scalar_tensor_tensor(out=soft[:, :, :], in0=pre[:, :, :], scalar=0.0, in1=soft[:, :, :], op0=ALU.max,
                                                 op1=ALU.add).then_inc(*VEC("soft"))
                        vec.wait_ge(*VEC["soft"])
                        vec.wait_ge(*ACT["rate"])
                        vec.tensor_tensor(soft[:, :, :], soft[:, :, :], rep(rate[:, :], NT), ALU.mult).then_inc(*VEC("soft2"))
                        vec.wait_ge(*VEC["soft2"])
                        vec.tensor_scalar(gb[:, :, 0, :], soft[:, :, :], -1.0, None, ALU.mult).then_inc(*VEC("g"))

                    @block.scalar
                    def _(act):
                        act.activation(rate[:, :], par("a_log"), FN.Exp).then_inc(*ACT("rate"))
                        act.wait_ge(*VEC["mag"])
                        act.activation(soft[:, :, :], mag[:, :, :], FN.Exp, scale=-1.0).then_inc(*ACT("exp"))
                        act.wait_ge(*ACT["exp"])
                        act.activation(soft[:, :, :], soft[:, :, :], FN.Ln, bias=1.0).then_inc(*ACT("soft"))
                        act.activation(gb[:, :, 1, :], tm_ab[:, :, G2:2 * G2], FN.Sigmoid).then_inc(*ACT("beta"))
                clear()

                with ExitStack() as st2:
                    kq = sbuf(st2, "kq", [P, 6, 2, P])
                    vs = sbuf(st2, "vs_g", [P, 6, P])
                    gch = sbuf(st2, "gch", [P, 2, 2, GH])
                    Gm = sbuf(st2, "Gm", [P, 12, P])
                    DT = sbuf(st2, "DT", [P, 12, P])
                    DTb = sbuf(st2, "DTb", [P, 12, P])
                    gx = sbuf(st2, "gx", [P, 2, 3, GH])
                    AT = sbuf(st2, "AT", [P, 12, P])
                    PT = sbuf(st2, "PT", [P, 12, P])
                    kt = sbuf(st2, "kt", [P, 2, GW])
                    vt = sbuf(st2, "vt_g", [P, 2, GW])
                    X = Gm
                    Y = sbuf(st2, "Y_g", [P, 12, P])
                    Pm = DTb
                    R = sbuf(st2, "R_g", [P, 2, GW])
                    U = sbuf(st2, "U_g", [P, 2, GW])
                    Ur = sbuf(st2, "Ur_g", [P, 2, GW])
                    o = sbuf(st2, "o_g", [P, 2, GW])
                    S = sbuf(st2, "S_g", [P, 6, P])
                    St = sbuf(st2, "St_g", [P, 6, P])
                    begin("gdn_state")
                    with nc.Block() as block:
                        @block.vector
                        def _(vec):
                            vec.memset(S[:, :, :], 0.0).then_inc(*VEC("s"))
                    clear()

                    def heads(ap):
                        return ap.rearrange("p (h n) -> p h n", n=GD)

                    def parts(g):
                        cuts = sorted({4 * g, 4 * g + 4} | ({6} if g == 1 else set()))
                        return [(a, b, a < 6) for a, b in zip(cuts, cuts[1:])]

                    def units(b0, n, w):
                        return ps[:, b0:b0 + (n * w + 511) // 512, :].rearrange("p b n -> p (b n)")[:, 0:n * w].rearrange("p (u n) -> p u n", u=n)

                    with nc.Fori(0, NT) as c:
                        begin("gdn_chunk")
                        with nc.Block() as block:
                            chunk = [c, NT - 1 - c]
                            off = [c * P, (NT - 1 - c) * P]

                            @block.scalar
                            def _(act):
                                for e in range(2):
                                    u = slice(3 * e, 3 * e + 3)
                                    act.copy(kq[:, u, 0, :], gq[:, 3:6, ds(off[e], P)]).then_inc(*ACT(f"k{e}"))
                                    act.copy(kq[:, u, 1, :], gq[:, 0:3, ds(off[e], P)]).then_inc(*ACT(f"kq{e}"))
                                    act.copy(vs[:, u, :], gq[:, 6:9, ds(off[e], P)]).then_inc(*ACT(f"v{e}"))
                                for e in range(2):
                                    act.wait_ge(*PE[f"diff{e}"])
                                    act.activation(DT[:, 6 * e:6 * e + 6, :], units(2 * e, 6, P), FN.Exp).then_inc(*ACT(f"DT{e}"))
                                act.wait_ge(*PE["small"])
                                act.activation(gx[:, :, :, :].rearrange("p e a h -> p (e a h)"), ps[:, 4, 0:36], FN.Exp).then_inc(*ACT("gx"))
                                for e in range(2):
                                    act.wait_ge(*PE[f"turned{e}"])
                                    act.copy(kt[:, e, :], ps[:, 6, 0:GW]).then_inc(*ACT(f"kt{e}"))
                                    act.copy(vt[:, e, :], ps[:, 7, 0:GW]).then_inc(*ACT(f"vt{e}"))

                            @block.gpsimd
                            def _(pool):
                                for e in range(2):
                                    pool.wait_ge(*VEC["gch"])
                                    pool.tensor_tensor(Gm[:, 6 * e:6 * e + 6, :], col(gch[:, e, 0, :], P), rep(cst("tri_f" if e == 0 else "tri_b"), 6),
                                                       ALU.mult).then_inc(*POOL(f"Gm{e}"))
                                for e in range(2):
                                    u = slice(6 * e, 6 * e + 6)
                                    pool.wait_ge(*ACT[f"DT{e}"])
                                    pool.tensor_tensor(DT[:, u, :], DT[:, u, :], rep(cst("tri_f" if e == 0 else "tri_b"), 6), ALU.mult).then_inc(*POOL(f"DTm{e}"))
                                    pool.wait_ge(*POOL[f"DTm{e}"])
                                    pool.tensor_tensor(DTb[:, u, :], DT[:, u, :], col(gch[:, e, 1, :], P), ALU.mult).then_inc(*POOL(f"DTb{e}"))
                                invert_pool(pool, 3, 4, ("PT1", "PT1", "PT1"), parts, lambda a, b: AT[:, a:b, :], X, Y, Pm)

                            @block.tensor
                            def _(pe):
                                for e in range(2):
                                    behind = cst("aft" if e == 0 else "bef")
                                    pe.wait_ge(*POOL[f"Gm{e}"])
                                    g = Gm[:, 6 * e:6 * e + 6, :].rearrange("p u n -> p (u n)")
                                    pe.matmul(ps[:, 2 * e, :], lhsT=behind, rhs=g[:, 0:512], start=True, stop=True)
                                    pe.matmul(ps[:, 2 * e + 1, 0:256], lhsT=behind, rhs=g[:, 512:768], start=True, stop=True).then_inc(*PE(f"diff{e}"))
                                for e in range(2):
                                    mats = (cst("tri_f"), cst("aft"), ones) if e == 0 else (cst("tri_b"), cst("bef"), ones)
                                    for n, mat in enumerate(mats):
                                        q = pe.matmul(ps[:, 4, (3 * e + n) * GH:(3 * e + n + 1) * GH], lhsT=mat, rhs=gch[:, e, 0, :], start=True, stop=True)
                                q.then_inc(*PE("small"))
                                for e in range(2):
                                    pe.wait_ge(*ACT[f"v{e}"])
                                    if e:
                                        pe.wait_ge(*ACT["vt0"])
                                    for m in range(3):
                                        pe.transpose(ps[:, 6, m * P:(m + 1) * P], kq[:, 3 * e + m, 0, :], ident)
                                        q = pe.transpose(ps[:, 7, m * P:(m + 1) * P], vs[:, 3 * e + m, :], ident)
                                    q.then_inc(*PE(f"turned{e}"))
                                pe.wait_ge(*ACT["gx"])
                                for h in range(2):
                                    c0 = slice(64 * h, 64 * h + 64)
                                    for em in range(6):
                                        q = pe.matmul(ps[:, 3 * h + em // 2, 256 * (em % 2):256 * (em % 2) + 256], lhsT=kq[c0, em, 0, :],
                                                      rhs=kq[c0, em, :, :], start=True, stop=True)
                                    q.then_inc(*PE(f"pairs{h}"))
                                pe.wait_ge(*ACT["vt1"])
                                for e in range(2):
                                    for m in range(3):
                                        q = pe.matmul(ps[:, 6 + e, m * P:(m + 1) * P], lhsT=kq[:, 3 * e + m, 0, :], rhs=S[:, 3 * e + m, :], start=True, stop=True)
                                q.then_inc(*PE("kS"))
                                pe.wait_ge(*VEC["PT1"])
                                invert_tensor(pe, 3, 4, ("PT1", "PT1", "PT1"), lambda u: AT[:, u, :], X, Y, Pm)
                                pe.wait_ge(*VEC["R"])
                                pe.wait_ge(*VEC[f"Yn{NLEV - 1}_2"])
                                for u in range(12):
                                    e, n = u // 6, slice(64 * (u % 6), 64 * (u % 6) + 64)
                                    q = pe.matmul(ps[:, 6 + e, n], lhsT=Y[:, u, :], rhs=R[:, e, n], start=True, stop=True)
                                q.then_inc(*PE("w"))
                                for e in range(2):
                                    for m in range(3):
                                        q = pe.matmul(ps[:, e, m * P:(m + 1) * P], lhsT=kq[:, 3 * e + m, 1, :], rhs=S[:, 3 * e + m, :], start=True, stop=True)
                                q.then_inc(*PE("qS"))
                                pe.wait_ge(*VEC["U"])
                                for u in range(12):
                                    e, n = u // 6, slice(64 * (u % 6), 64 * (u % 6) + 64)
                                    q = pe.matmul(ps[:, 2 + e, n], lhsT=PT[:, u, :], rhs=U[:, e, n], start=True, stop=True)
                                q.then_inc(*PE("PU"))
                                pe.wait_ge(*VEC["Ur"])
                                for e in range(2):
                                    for m in range(3):
                                        n = slice(m * P, (m + 1) * P)
                                        q = pe.matmul(ps[:, 4 + e, n], lhsT=kt[:, e, n], rhs=Ur[:, e, n], start=True, stop=True)
                                q.then_inc(*PE("Sn"))

                            @block.vector
                            def _(vec):
                                for e in range(2):
                                    q = vec.tensor_copy(gch[:, e, :, :], gb[:, ds(chunk[e], 1), :, GH * e:GH * e + GH])
                                q.then_inc(*VEC("gch"))
                                for h in range(2):
                                    bank = units(3 * h, 12, P).rearrange("p (u k) n -> p u k n", k=2)
                                    vec.wait_ge(*PE[f"pairs{h}"])
                                    vec.wait_ge(*POOL["DTb1"])

                                    def of_head(ap):
                                        return ap.rearrange("p (u h) n -> p u h n", h=2)[:, :, h, :]
                                    vec.tensor_tensor(of_head(AT[:, :, :]), bank[:, :, 0, :], of_head(DTb[:, :, :]), ALU.mult)
                                    vec.scalar_tensor_tensor(out=of_head(PT[:, :, :]), in0=bank[:, :, 1, :], scalar=GD ** -0.5,
                                                             in1=of_head(DT[:, :, :]), op0=ALU.mult, op1=ALU.mult).then_inc(*VEC(f"PT{h}"))
                                vec.wait_ge(*PE["kS"])
                                for e in range(2):
                                    q = vec.tensor_tensor(heads(R[:, e, :]), heads(ps[:, 6 + e, 0:GW]), col(gx[:, e, 0, :], GD), ALU.mult)
                                q.then_inc(*VEC("gkS"))
                                vec.wait_ge(*VEC["gkS"])
                                vec.tensor_tensor(R[:, :, :], vt[:, :, :], R[:, :, :], ALU.subtract).then_inc(*VEC("R"))
                                invert_vector(vec, 3, 4, parts, X, Y, Pm)
                                vec.wait_ge(*PE["w"])
                                for e in range(2):
                                    q = vec.tensor_tensor(heads(U[:, e, :]), heads(ps[:, 6 + e, 0:GW]), col(gch[:, e, 1, :], GD), ALU.mult)
                                q.then_inc(*VEC("U"))
                                vec.wait_ge(*VEC["U"])
                                for e in range(2):
                                    q = vec.tensor_tensor(heads(Ur[:, e, :]), heads(U[:, e, :]), col(gx[:, e, 1, :], GD), ALU.mult)
                                q.then_inc(*VEC("Ur"))
                                vec.wait_ge(*PE["qS"])
                                for e in range(2):
                                    q = vec.tensor_tensor(heads(o[:, e, :]), heads(ps[:, e, 0:GW]), col(gx[:, e, 0, :], GD), ALU.mult)
                                q.then_inc(*VEC("gqS"))
                                vec.wait_ge(*VEC["gqS"])
                                vec.wait_ge(*PE["PU"])
                                vec.scalar_tensor_tensor(out=o[:, :, :], in0=o[:, :, :], scalar=GD ** -0.5, in1=ps[:, 2:4, 0:GW],
                                                         op0=ALU.mult, op1=ALU.add).then_inc(*VEC("o"))
                                for e in range(2):
                                    su = S[:, 3 * e:3 * e + 3, :].rearrange("p m (h n) -> p (m h) n", h=2)
                                    q = vec.tensor_tensor(su, su, col(gx[:, e, 2, :], GD), ALU.mult)
                                q.then_inc(*VEC("Sdec"))
                                vec.wait_ge(*PE["Sn"])
                                for e in range(2):
                                    q = vec.tensor_tensor(St[:, 3 * e:3 * e + 3, :], ps[:, 4 + e, 0:GW].rearrange("p (m n) -> p m n", n=P), rep(blk, 3), ALU.mult)
                                q.then_inc(*VEC("St"))
                                vec.wait_ge(*VEC["St"])
                                vec.tensor_tensor(S[:, :, :], S[:, :, :], St[:, :, :], ALU.add).then_inc(*VEC("S"))

                            @block.sync
                            def _(sp):
                                sp.wait_ge(*VEC["o"])
                                for e in range(2):
                                    sp.dma_start(gdn_hbm[e, ds(off[e], P), :], o[:, e, :]).then_inc(*DMA("o_out"))
                                sp.wait_ge(*DMA["o_out"])
                        clear()

            with ExitStack() as st:
                qT = sbuf(st, "qT", [QK, MH, SEQ])
                kT = sbuf(st, "kT", [QK, MH, SEQ])
                V = sbuf(st, "V", [P, NT, MH, MV])
                with ExitStack() as st2:
                    wq = sbuf(st2, "w_uq", [P, 2, MH * QK])
                    wkv = sbuf(st2, "w_ukv", [P, MH * (NOPE + MV)])
                    begin("mla_load")
                    with nc.Block() as block:
                        @block.sync
                        def _(sp):
                            sp.dma_start(wq[:, 0, :], w_uq[0:P, :]).then_inc(*DMA("w_mla"))
                            sp.dma_start(wq[0:QR - P, 1, :], w_uq[P:QR, :]).then_inc(*DMA("w_mla"))
                            sp.dma_start(wkv[:, :], io["w_ukv"][ds(L, 1)].rearrange("a r n -> (a r) n")).then_inc(*DMA("w_mla"))
                            sp.wait_ge(*DMA["w_mla"])
                    clear()
                    lat = sbuf(st2, "lat", [P, QR + KVR + ROPE])
                    junk = sbuf(st2, "junk", [P, QR])
                    ss = sbuf(st2, "ss_m", [P, 2])
                    rs = sbuf(st2, "rs_m", [P, 2])
                    cn = sbuf(st2, "cn", [P, QR + KVR])
                    cT = sbuf(st2, "cT", [P, 3, P])
                    qk = sbuf(st2, "qk", [P, 2 * MH, QK])
                    tr = sbuf(st2, "tr", [P, 2, MH, ROPE])
                    tk = sbuf(st2, "tk", [P, 2, ROPE])
                    kr = sbuf(st2, "kr", [P, ROPE])
                    csn = sbuf(st2, "csn", [P, 2, ROPE // 2])
                    H2 = ROPE // 2
                    with nc.Fori(0, NT) as t:
                        begin("mla_up")
                        with nc.Block() as block:
                            @block.sync
                            def _(sp):
                                sp.dma_start(lat[:, :], tm_hbm[ds(t * P, P), 4 * GH:TM_W]).then_inc(*DMA("lat"))

                            @block.scalar
                            def _(act):
                                act.wait_ge(*DMA["lat"])
                                act.activation(junk[:, :], lat[:, 0:QR], FN.Square, accum_out=ss[:, 0:1]).then_inc(*ACT("ss0"))
                                act.activation(cn[:, 0:KVR], lat[:, QR:QR + KVR], FN.Square, accum_out=ss[:, 1:2]).then_inc(*ACT("ss1"))
                                act.wait_ge(*ACT["ss1"])
                                act.activation(rs[:, 0:1], ss[:, 0:1], FN.Ln, bias=cst("eps"), scale=1.0 / QR).then_inc(*ACT("ln0"))
                                act.activation(rs[:, 1:2], ss[:, 1:2], FN.Ln, bias=cst("eps"), scale=1.0 / KVR).then_inc(*ACT("ln1"))
                                act.wait_ge(*ACT["ln1"])
                                act.activation(rs[:, :], rs[:, :], FN.Exp, scale=-0.5).then_inc(*ACT("rs"))
                                for b in range(2):
                                    act.wait_ge(*PE[f"q{b}"])
                                    act.copy(qk[:, 3 * b:3 * b + 3, :], ps[:, 1 + b, 0:3 * QK].rearrange("p (h n) -> p h n", n=QK)).then_inc(*ACT(f"q{b}"))
                                for b in range(2):
                                    act.wait_ge(*PE[f"kv{b}"])
                                    kv = ps[:, 3 + b, 0:3 * (NOPE + MV)].rearrange("p (h n) -> p h n", h=3)
                                    act.copy(qk[:, MH + 3 * b:MH + 3 * b + 3, 0:NOPE], kv[:, :, 0:NOPE]).then_inc(*ACT(f"k{b}"))
                                    act.copy(V[:, ds(t, 1), 3 * b:3 * b + 3, :], kv[:, None, :, NOPE:NOPE + MV]).then_inc(*ACT(f"v{b}"))
                                for b in range(3):
                                    act.wait_ge(*PE[f"qkT{b}"])
                                    if b == 0:
                                        act.copy(qT[:, 0:4, ds(t * P, P)], ps[0:QK, 5, :].rearrange("p (h n) -> p h n", h=4)).then_inc(*ACT("qT0"))
                                    elif b == 1:
                                        act.copy(qT[:, 4:6, ds(t * P, P)], ps[0:QK, 6, 0:256].rearrange("p (h n) -> p h n", h=2)).then_inc(*ACT("qT1"))
                                        act.copy(kT[:, 0:2, ds(t * P, P)], ps[0:QK, 6, 256:512].rearrange("p (h n) -> p h n", h=2)).then_inc(*ACT("kT1"))
                                    else:
                                        act.copy(kT[:, 2:6, ds(t * P, P)], ps[0:QK, 7, :].rearrange("p (h n) -> p h n", h=4)).then_inc(*ACT("kT2"))

                            @block.vector
                            def _(vec):
                                vec.wait_ge(*ACT["rs"])
                                vec.tensor_scalar(cn[:, 0:QR], lat[:, 0:QR], rs[:, 0:1], None, ALU.mult).then_inc(*VEC("cq"))
                                vec.tensor_scalar(cn[:, QR:QR + KVR], lat[:, QR:QR + KVR], rs[:, 1:2], None, ALU.mult).then_inc(*VEC("ckv"))
                                vec.wait_ge(*PE["cT"])
                                g = P_AT["q_g"][0]
                                vec.tensor_scalar(cT[:, 0, :], ps[:, 0, 0:P], params[:, g:g + 1], None, ALU.mult).then_inc(*VEC("cT0"))
                                vec.tensor_scalar(cT[0:QR - P, 1, :], ps[0:QR - P, 0, P:2 * P], params[0:QR - P, g + 1:g + 2], None, ALU.mult).then_inc(*VEC("cT1"))
                                vec.tensor_scalar(cT[:, 2, :], ps[:, 0, 2 * P:3 * P], par("kv_g"), None, ALU.mult).then_inc(*VEC("cT2"))
                                cos1, sin1 = csn[:, 0, :], csn[:, 1, :]
                                vec.tensor_copy(csn[:, 0, :], cs[:, ds(t, 1), 0, :]).then_inc(*VEC("cos"))
                                vec.tensor_copy(csn[:, 1, :], cs[:, ds(t, 1), 1, :]).then_inc(*VEC("sin"))
                                k1, k2 = lat[:, QR + KVR:QR + KVR + H2], lat[:, QR + KVR + H2:]
                                vec.wait_ge(*VEC["sin"])
                                vec.tensor_tensor(tk[:, 0, 0:H2], k1, cos1, ALU.mult)
                                vec.tensor_tensor(tk[:, 1, 0:H2], k2, sin1, ALU.mult)
                                vec.tensor_tensor(tk[:, 0, H2:], k2, cos1, ALU.mult)
                                vec.tensor_tensor(tk[:, 1, H2:], k1, sin1, ALU.mult).then_inc(*VEC("tk"))
                                vec.wait_ge(*VEC["tk"])
                                vec.tensor_tensor(kr[:, 0:H2], tk[:, 0, 0:H2], tk[:, 1, 0:H2], ALU.subtract)
                                vec.tensor_tensor(kr[:, H2:], tk[:, 0, H2:], tk[:, 1, H2:], ALU.add).then_inc(*VEC("kr"))
                                vec.wait_ge(*VEC["kr"])
                                vec.tensor_copy(qk[:, MH:2 * MH, NOPE:QK], rep(kr[:, :], MH)).then_inc(*VEC("k_rot"))
                                vec.wait_ge(*ACT["q1"])
                                q1, q2 = qk[:, 0:MH, NOPE:NOPE + H2], qk[:, 0:MH, NOPE + H2:QK]
                                vec.tensor_tensor(tr[:, 0, :, 0:H2], q1, rep(cos1, MH), ALU.mult)
                                vec.tensor_tensor(tr[:, 1, :, 0:H2], q2, rep(sin1, MH), ALU.mult)
                                vec.tensor_tensor(tr[:, 0, :, H2:], q2, rep(cos1, MH), ALU.mult)
                                vec.tensor_tensor(tr[:, 1, :, H2:], q1, rep(sin1, MH), ALU.mult).then_inc(*VEC("tr"))
                                vec.wait_ge(*VEC["tr"])
                                vec.tensor_tensor(q1, tr[:, 0, :, 0:H2], tr[:, 1, :, 0:H2], ALU.subtract)
                                vec.tensor_tensor(q2, tr[:, 0, :, H2:], tr[:, 1, :, H2:], ALU.add).then_inc(*VEC("q_rot"))

                            @block.tensor
                            def _(pe):
                                pe.wait_ge(*VEC["ckv"])
                                pe.transpose(ps[:, 0, 0:P], cn[:, 0:P], ident)
                                pe.transpose(ps[0:QR - P, 0, P:2 * P], cn[:, P:QR], ident)
                                pe.transpose(ps[:, 0, 2 * P:3 * P], cn[:, QR:QR + KVR], ident).then_inc(*PE("cT"))
                                pe.wait_ge(*VEC["cT2"])
                                for b in range(2):
                                    n = slice(3 * QK * b, 3 * QK * (b + 1))
                                    pe.matmul(ps[:, 1 + b, 0:3 * QK], lhsT=cT[:, 0, :], rhs=wq[:, 0, n], start=True, stop=False)
                                    pe.matmul(ps[:, 1 + b, 0:3 * QK], lhsT=cT[0:QR - P, 1, :], rhs=wq[0:QR - P, 1, n], start=False,
                                              stop=True).then_inc(*PE(f"q{b}"))
                                for b in range(2):
                                    w = 3 * (NOPE + MV)
                                    pe.matmul(ps[:, 3 + b, 0:w], lhsT=cT[:, 2, :], rhs=wkv[:, w * b:w * (b + 1)], start=True,
                                              stop=True).then_inc(*PE(f"kv{b}"))
                                pe.wait_ge(*VEC["q_rot"])
                                pe.wait_ge(*ACT["v1"])
                                for b in range(3):
                                    for n in range(4):
                                        q = pe.transpose(ps[0:QK, 5 + b, n * P:(n + 1) * P], qk[:, 4 * b + n, :], ident)
                                    q.then_inc(*PE(f"qkT{b}"))
                        clear()

                with ExitStack() as st2:
                    qs = sbuf(st2, "qs", [QK, MH, P])
                    pr = sbuf(st2, "pr", [P, 2, SEQ])
                    pT = sbuf(st2, "pT", [P, 2, NT, P])
                    mx = sbuf(st2, "mx", [P, MH])
                    nm = sbuf(st2, "nm", [P, MH])
                    den = sbuf(st2, "den", [P, MH])
                    om = sbuf(st2, "om", [P, GW])
                    SC = QK ** -0.5
                    with nc.Fori(0, NT) as t:
                        begin("attend")
                        with nc.Block() as block:
                            @block.gpsimd
                            def _(pool):
                                pool.tensor_copy(qs[:, :, :], qT[:, :, ds(t * P, P)]).then_inc(*POOL("qs"))

                            @block.tensor
                            def _(pe):
                                def scores(h):
                                    s = h % 2
                                    if h >= 2:
                                        pe.wait_ge(*ACT[f"p{h - 2}"])
                                    for b in range(2):
                                        q = pe.matmul(ps[:, 2 * s + b, :], lhsT=qs[:, h, :], rhs=kT[:, h, b * 512:(b + 1) * 512], start=True, stop=True)
                                    q.then_inc(*PE(f"s{h}"))
                                pe.wait_ge(*POOL["qs"])
                                scores(0)
                                for h in range(MH):
                                    s = h % 2
                                    if h + 1 < MH:
                                        scores(h + 1)
                                    pe.wait_ge(*ACT[f"p{h}"])
                                    if h >= 1:
                                        pe.wait_ge(*VEC[f"pT{h - 1}"])
                                        pe.wait_ge(*ACT[f"pT{h - 1}"])
                                    for b in range(2):
                                        for n in range(4):
                                            q = pe.transpose(ps[:, 4 + b, n * P:(n + 1) * P], pr[:, s, (4 * b + n) * P:(4 * b + n + 1) * P], ident)
                                        q.then_inc(*PE(f"t{h}_{b}"))
                                    pe.wait_ge(*VEC[f"pT{h}"])
                                    pe.wait_ge(*ACT[f"pT{h}"])
                                    if h >= 2:
                                        pe.wait_ge(*VEC[f"o{h - 2}"])
                                    for k in range(NT):
                                        q = pe.matmul(ps[:, 6 + s, 0:MV], lhsT=pT[:, s, k, :], rhs=V[:, k, h, :], start=(k == 0), stop=(k == NT - 1))
                                    q.then_inc(*PE(f"o{h}"))

                            @block.scalar
                            def _(act):
                                def expo(h):
                                    s = h % 2
                                    act.wait_ge(*VEC[f"nm{h}"])
                                    if h >= 2:
                                        act.wait_ge(*PE[f"t{h - 2}_1"])
                                    act.activation(pr[:, s, :].rearrange("p (b n) -> p b n", b=2), ps[:, 2 * s:2 * s + 2, :], FN.Exp,
                                                   bias=nm[:, h:h + 1], scale=SC, accum_out=den[:, h:h + 1]).then_inc(*ACT(f"p{h}"))
                                expo(0)
                                for h in range(MH):
                                    s = h % 2
                                    if h + 1 < MH:
                                        expo(h + 1)
                                    act.wait_ge(*PE[f"t{h}_1"])
                                    if h >= 2:
                                        act.wait_ge(*PE[f"o{h - 2}"])
                                    act.copy(pT[:, s, 4:8, :], ps[:, 5, :].rearrange("p (k n) -> p k n", k=4)).then_inc(*ACT(f"pT{h}"))

                            @block.vector
                            def _(vec):
                                def top(h):
                                    s = h % 2
                                    vec.wait_ge(*PE[f"s{h}"])
                                    vec.tensor_reduce(mx[:, h:h + 1], ps[:, 2 * s:2 * s + 2, :].rearrange("p b n -> p (b n)"), AX, ALU.max).then_inc(*VEC(f"mx{h}"))
                                    vec.wait_ge(*VEC[f"mx{h}"])
                                    vec.tensor_scalar(nm[:, h:h + 1], mx[:, h:h + 1], -SC, None, ALU.mult).then_inc(*VEC(f"nm{h}"))
                                top(0)
                                for h in range(MH):
                                    s = h % 2
                                    if h + 1 < MH:
                                        top(h + 1)
                                    vec.wait_ge(*PE[f"t{h}_0"])
                                    if h >= 2:
                                        vec.wait_ge(*PE[f"o{h - 2}"])
                                    vec.tensor_copy(pT[:, s, 0:4, :], ps[:, 4, :].rearrange("p (k n) -> p k n", k=4)).then_inc(*VEC(f"pT{h}"))
                                    vec.wait_ge(*ACT[f"p{h}"])
                                    vec.reciprocal(mx[:, h:h + 1], den[:, h:h + 1]).then_inc(*VEC(f"inv{h}"))
                                    vec.wait_ge(*VEC[f"inv{h}"])
                                    vec.wait_ge(*PE[f"o{h}"])
                                    vec.tensor_scalar(om[:, h * MV:(h + 1) * MV], ps[:, 6 + s, 0:MV], mx[:, h:h + 1], None, ALU.mult).then_inc(*VEC(f"o{h}"))

                            @block.sync
                            def _(sp):
                                sp.wait_ge(*VEC[f"o{MH - 1}"])
                                sp.dma_start(mla_hbm[ds(t * P, P), :], om[:, :]).then_inc(*DMA("o_out"))
                                sp.wait_ge(*DMA["o_out"])
                        clear()

            with ExitStack() as st:
                wo = sbuf(st, "w_out", [P, KD, DM])
                gi = sbuf(st, "gi", [P, 2, GW])
                ri = sbuf(st, "ri", [P, 3, RW])
                gate = sbuf(st, "gate_in", [P, DM])
                sg = sbuf(st, "sg", [P, DM])
                mix = sbuf(st, "mix", [P, DM])
                mT = sbuf(st, "mT", [P, KD, P])
                xt = sbuf(st, "x_t", [P, DM])
                s = sbuf(st, "s_sum", [P, GW])
                y = sbuf(st, "y_sum", [P, RW])
                sq = sbuf(st, "sq_o", [P, GW + RW])
                ssum = sbuf(st, "ssum", [P, GH + RH])
                mean = sbuf(st, "mean", [P, RH])
                rs = sbuf(st, "rs_o", [P, GH + RH])
                begin("out_load")
                with nc.Block() as block:
                    @block.sync
                    def _(sp):
                        sp.dma_start(wo[:, :, :], w_rows(io["w_out"][ds(L, 1)].rearrange("a r n -> (a r) n"))).then_inc(*DMA("w_out"))
                        sp.wait_ge(*DMA["w_out"])
                clear()
                with nc.Fori(0, NT) as t:
                    begin("out")
                    with nc.Block() as block:
                        @block.sync
                        def _(sp):
                            row = t * P
                            sp.dma_start(gi[:, :, :], gdn_hbm[:, ds(row, P), :].rearrange("e p n -> p e n")).then_inc(*DMA("gdn_in"))
                            sp.dma_start(ri[:, :, :], rwkv_hbm[:, ds(row, P), :].rearrange("e p n -> p e n")).then_inc(*DMA("rwkv_in"))
                            sp.dma_start(mix[:, GW:2 * GW], mla_hbm[ds(row, P), :]).then_inc(*DMA("mla_in"))
                            sp.dma_start(gate[:, :], gate_hbm[ds(row, P), :]).then_inc(*DMA("gate_in"))
                            sp.dma_start(xt[:, :], x_hbm[ds(row + P, P), :]).then_inc(*DMA("x_in"))
                            sp.wait_ge(*VEC["x1"])
                            sp.dma_start(x_hbm[ds(row + P, P), :], xt[:, :]).then_inc(*DMA("x_out"))
                            sp.wait_ge(*DMA["x_out"])

                        @block.scalar
                        def _(act):
                            act.wait_ge(*DMA["gate_in"])
                            act.activation(sg[:, :], gate[:, :], FN.Silu).then_inc(*ACT("gate"))
                            act.wait_ge(*VEC["gss"])
                            act.activation(rs[:, 0:GH], ssum[:, 0:GH], FN.Ln, bias=cst("eps"), scale=1.0 / GD).then_inc(*ACT("ln_g"))
                            act.wait_ge(*VEC["rss"])
                            act.activation(rs[:, GH:GH + RH], ssum[:, GH:GH + RH], FN.Ln, bias=cst("rw_eps"), scale=1.0 / RD).then_inc(*ACT("ln_r"))
                            act.wait_ge(*ACT["ln_r"])
                            act.activation(rs[:, :], rs[:, :], FN.Exp, scale=-0.5).then_inc(*ACT("rs"))
                            for b in range(2):
                                act.wait_ge(*PE[f"mT{b}"])
                                act.copy(mT[:, 4 * b:4 * b + 4, :], ps[:, b, :].rearrange("p (k n) -> p k n", k=4)).then_inc(*ACT(f"mT{b}"))

                        @block.vector
                        def _(vec):
                            def h6(ap):
                                return ap.rearrange("p (h n) -> p h n", n=GD)
                            vec.wait_ge(*DMA["gdn_in"])
                            vec.tensor_tensor(s[:, :], gi[:, 0, :], gi[:, 1, :], ALU.add).then_inc(*VEC("s"))
                            vec.wait_ge(*DMA["rwkv_in"])
                            vec.tensor_tensor(y[:, :], ri[:, 0, :], ri[:, 1, :], ALU.add).then_inc(*VEC("y"))
                            vec.wait_ge(*VEC["s"])
                            vec.tensor_tensor(sq[:, 0:GW], s[:, :], s[:, :], ALU.mult).then_inc(*VEC("gsq"))
                            vec.wait_ge(*VEC["y"])
                            vec.tensor_reduce(mean[:, :], h6(y[:, :]), AX, ALU.add).then_inc(*VEC("ysum"))
                            vec.wait_ge(*VEC["gsq"])
                            vec.tensor_reduce(ssum[:, 0:GH], h6(sq[:, 0:GW]), AX, ALU.add).then_inc(*VEC("gss"))
                            vec.wait_ge(*VEC["ysum"])
                            vec.tensor_scalar(mean[:, :], mean[:, :], 1.0 / RD, None, ALU.mult).then_inc(*VEC("mean"))
                            vec.wait_ge(*VEC["mean"])
                            vec.tensor_tensor(h6(y[:, :]), h6(y[:, :]), col(mean[:, :], RD), ALU.subtract).then_inc(*VEC("yc"))
                            vec.wait_ge(*VEC["yc"])
                            vec.tensor_tensor(sq[:, GW:GW + RW], y[:, :], y[:, :], ALU.mult).then_inc(*VEC("rsq"))
                            vec.wait_ge(*VEC["rsq"])
                            vec.tensor_reduce(ssum[:, GH:GH + RH], h6(sq[:, GW:GW + RW]), AX, ALU.add).then_inc(*VEC("rss"))
                            vec.wait_ge(*ACT["rs"])
                            vec.tensor_tensor(h6(s[:, :]), h6(s[:, :]), col(rs[:, 0:GH], GD), ALU.mult).then_inc(*VEC("g1"))
                            vec.tensor_tensor(h6(y[:, :]), h6(y[:, :]), col(rs[:, GH:GH + RH], RD), ALU.mult).then_inc(*VEC("r1"))
                            vec.wait_ge(*VEC["g1"])
                            vec.tensor_tensor(h6(mix[:, 0:GW]), h6(s[:, :]), rep(par("gdn_g"), GH), ALU.mult).then_inc(*VEC("g2"))
                            vec.wait_ge(*VEC["r1"])
                            vec.tensor_tensor(y[:, :], y[:, :], par("ln_g"), ALU.mult).then_inc(*VEC("r2"))
                            vec.tensor_tensor(ri[:, 2, :], ri[:, 2, :], par("ln_b"), ALU.add).then_inc(*VEC("r3"))
                            vec.wait_ge(*VEC["r3"])
                            vec.tensor_tensor(mix[:, 2 * GW:], y[:, :], ri[:, 2, :], ALU.add).then_inc(*VEC("r4"))
                            vec.wait_ge(*VEC["r4"])
                            vec.wait_ge(*DMA["mla_in"])
                            vec.wait_ge(*ACT["gate"])
                            vec.tensor_tensor(mix[:, :], mix[:, :], sg[:, :], ALU.mult).then_inc(*VEC("mix"))
                            vec.wait_ge(*DMA["x_in"])
                            for b in range(2):
                                n = slice(512 * b, 512 * (b + 1))
                                vec.wait_ge(*PE[f"o{b}"])
                                vec.tensor_tensor(xt[:, n], xt[:, n], ps[:, 2 + b, :], ALU.add).then_inc(*VEC(f"x{b}"))

                        @block.tensor
                        def _(pe):
                            pe.wait_ge(*VEC["mix"])
                            for b in range(2):
                                for k in range(4):
                                    q = pe.transpose(ps[:, b, k * P:(k + 1) * P], mix[:, (4 * b + k) * P:(4 * b + k + 1) * P], ident)
                                q.then_inc(*PE(f"mT{b}"))
                            pe.wait_ge(*ACT["mT1"])
                            for b in range(2):
                                for k in range(KD):
                                    q = pe.matmul(ps[:, 2 + b, :], lhsT=mT[:, k, :], rhs=wo[:, k, 512 * b:512 * (b + 1)], start=(k == 0), stop=(k == KD - 1))
                                q.then_inc(*PE(f"o{b}"))
                    clear()
        first.close()

        with ExitStack() as st:
            work = norm_buffers(st, "_2")
            fg = sbuf(st, "fg", [P, DM])
            meta = sbuf(st, "meta", [P, DM])
            begin("load2")
            with nc.Block() as block:
                @block.vector
                def _(vec):
                    vec.memset(meta[:, :], 0.0).then_inc(*VEC("zero"))

                @block.sync
                def _(sp):
                    sp.dma_start(params[:, 0:P2_N], io["params2"]).then_inc(*DMA("params2"))
                    sp.dma_start(fg[:, :], io["final_g"]).then_inc(*DMA("final_g"))
                    sp.wait_ge(*VEC["zero"])
                    sp.dma_start(meta[P - META:P, :], io["meta"]).then_inc(*DMA("meta"))
                    sp.wait_ge(*DMA["meta"])
                    sp.dma_start(x_hbm[0:P, :], meta[:, :]).then_inc(*DMA("meta_out"))
                    sp.wait_ge(*DMA["meta_out"])
                    sp.wait_ge(*DMA["params2"])
                    sp.wait_ge(*DMA["final_g"])
            clear()
            with nc.Fori(1, NT2) as t:
                begin("final1")
                with nc.Block() as block:
                    @block.sync
                    def _(sp):
                        sp.dma_start(work["x"][:, :], x_hbm[ds(t * P, P), :]).then_inc(*DMA("x_tile"))
                        sp.wait_ge(*VEC["final"])
                        sp.dma_start(x_hbm[ds(t * P, P), :], work["xn"][:, :]).then_inc(*DMA("x_out"))
                        sp.wait_ge(*DMA["x_out"])

                    @block.scalar
                    def _(act):
                        norm_scalar(act, work["x"][:, :], work)

                    @block.vector
                    def _(vec):
                        vec.wait_ge(*ACT["norm_rstd"])
                        vec.scalar_tensor_tensor(out=work["xn"][:, :], in0=work["x"][:, :], scalar=work["rstd"][:, :], in1=fg[:, :],
                                                 op0=ALU.mult, op1=ALU.mult).then_inc(*VEC("final"))
                clear()
            with nc.Fori(0, NT2) as t:
                begin("norm2")
                with nc.Block() as block:
                    @block.sync
                    def _(sp):
                        sp.dma_start(work["x"][:, :], x_hbm[ds(t * P, P), :]).then_inc(*DMA("x_tile"))

                    @block.scalar
                    def _(act):
                        norm_scalar(act, work["x"][:, :], work)

                    @block.vector
                    def _(vec):
                        norm_vector(vec, work["x"][:, :], par("norm_g", P2_AT), work)

                    @block.tensor
                    def _(pe):
                        norm_tensor(pe, work)

                    @block.gpsimd
                    def _(pool):
                        norm_pool(pool, t, work)
                clear()

        w_in2 = io["w_in_2"]
        THIRD = T2 // 3

        def project3(pe, banks, w, x_in):
            for b in range(3):
                for k in range(KD):
                    q = pe.matmul(ps[:, banks + b, 0:THIRD], lhsT=w[:, k, :], rhs=x_in[:, k, b * THIRD:(b + 1) * THIRD],
                                  start=(k == 0), stop=(k == KD - 1))
            return q

        def bank3(banks):
            return ps[:, banks:banks + 3, 0:THIRD]

        def tok3(ap):
            return ap.rearrange("p (b n) -> p b n", b=3)

        def tiles(ap):
            return ap.rearrange("p (t n) -> p t n", n=P)

        with ExitStack() as st:
            NAMES = ("glu_a", "glu_b", "q", "f", "i", "g")
            COLS = dict(zip(NAMES, (0, DM, 3 * DM, 4 * DM, 5 * DM, 6 * DM)))
            wt = {n: sbuf(st, "w2_" + n, [P, KD, P]) for n in NAMES}
            glu = sbuf(st, "glu", [P, T2])
            sgb = sbuf(st, "sgb", [P, T2])
            cv = sbuf(st, "cv", [P, T2])
            q_ = sbuf(st, "q_", [P, T2])
            k_ = sbuf(st, "k_", [P, T2])
            Rp = sbuf(st, "Rp", [P, T2])
            Sp = sbuf(st, "Sp", [P, T2])
            W = sbuf(st, "W", [P, 2, T2])
            v = sbuf(st, "v2", [P, T2])
            kS = sbuf(st, "kS", [P, T2])
            at = sbuf(st, "attn", [P, T2])
            Sst = sbuf(st, "Sst", [P, NT2, P])
            sgg = sbuf(st, "sgg", [P, T2])
            orec = sbuf(st, "orec", [P, T2])
            osq = sbuf(st, "osq", [P, T2])
            lb = sbuf(st, "lb", [P, KD])
            omlb = sbuf(st, "omlb", [P, KD])
            diff = sbuf(st, "lb_diff", [P, KD])
            begin("hg_load")
            with nc.Block() as block:
                @block.sync
                def _(sp):
                    for n in NAMES:
                        sp.dma_start(wt[n][:, :, :], w_rows(w_in2[:, COLS[n]:COLS[n] + P])).then_inc(*DMA("w2"))
                    sp.wait_ge(*DMA["w2"])

                @block.vector
                def _(vec):
                    l = par("lb", P2_AT).rearrange("p (k c) -> p k c", c=2)
                    mxl, e2 = Sp[:, 0:KD], Rp[:, 0:2 * KD].rearrange("p (c k) -> p c k", c=2)
                    vec.tensor_tensor(mxl, l[:, :, 0], l[:, :, 1], ALU.max).then_inc(*VEC("lb_max"))
                    vec.wait_ge(*VEC["lb_max"])
                    vec.tensor_tensor(e2[:, 0, :], l[:, :, 0], mxl, ALU.subtract)
                    vec.tensor_tensor(e2[:, 1, :], l[:, :, 1], mxl, ALU.subtract).then_inc(*VEC("lb_shift"))
                    vec.wait_ge(*ACT["lb_exp"])
                    vec.tensor_tensor(diff[:, :], e2[:, 0, :], e2[:, 1, :], ALU.add).then_inc(*VEC("lb_sum"))
                    vec.wait_ge(*VEC["lb_sum"])
                    vec.reciprocal(diff[:, :], diff[:, :]).then_inc(*VEC("lb_inv"))
                    vec.wait_ge(*VEC["lb_inv"])
                    vec.tensor_tensor(lb[:, :], e2[:, 0, :], diff[:, :], ALU.mult).then_inc(*VEC("lb"))
                    vec.wait_ge(*VEC["lb"])
                    vec.tensor_scalar(omlb[:, :], lb[:, :], -1.0, 1.0, ALU.mult, ALU.add).then_inc(*VEC("omlb"))
                    vec.memset(at[:, :], 0.0).then_inc(*VEC("attn0"))
                    vec.memset(cv[:, :], 0.0).then_inc(*VEC("cv0"))
                    vec.memset(Sst[:, 0, :], 0.0).then_inc(*VEC("state0"))

                @block.scalar
                def _(act):
                    act.wait_ge(*VEC["lb_shift"])
                    act.activation(Rp[:, 0:2 * KD], Rp[:, 0:2 * KD], FN.Exp).then_inc(*ACT("lb_exp"))
            clear()

            def level(ap, k):
                return ap.rearrange("p (a s n) -> p a s n", s=2, n=1 << k)

            with nc.Fori(0, KD) as i:
                begin("hg")
                with nc.Block() as block:
                    at_w = P2_AT["conv_w"][0]

                    @block.sync
                    def _(sp):
                        for n, used in (("f", "f"), ("q", "q"), ("i", "v"), ("glu_b", "glu_b"), ("glu_a", "glu_a"), ("g", "g")):
                            sp.wait_ge(*PE[used])
                            sp.dma_start(wt[n][:, :, :], w_rows(w_in2[:, ds(i * P + (COLS[n] + P), P)])).then_inc(*DMA("w2"))
                        sp.wait_ge(*VEC[f"tap{TAPS - 1}"])
                        sp.dma_start(conv_hbm[ds(i, 1)].rearrange("a p n -> (a p) n"), cv[:, :]).then_inc(*DMA("out2"))
                        sp.wait_ge(*VEC["orec"])
                        sp.dma_start(rec_hbm[ds(i, 1)].rearrange("a p n -> (a p) n"), orec[:, :]).then_inc(*DMA("out2"))
                        sp.wait_ge(*DMA["w2"])
                        sp.wait_ge(*DMA["out2"])

                    @block.tensor
                    def _(pe):
                        project3(pe, 0, wt["f"], hT).then_inc(*PE("f"))
                        project3(pe, 3, wt["q"], hT).then_inc(*PE("q"))
                        pe.wait_ge(*ACT["f"])
                        for t in range(NT2):
                            for k in range(KD):
                                q = pe.matmul(ps[:, t // 3, (t % 3) * P:(t % 3 + 1) * P], lhsT=hT[:, k, t * P:(t + 1) * P], rhs=wt["i"][:, k, :],
                                              start=(k == 0), stop=(k == KD - 1))
                        q.then_inc(*PE("v"))
                        pe.wait_ge(*ACT["q"])
                        project3(pe, 3, wt["glu_b"], hT).then_inc(*PE("glu_b"))
                        pe.wait_ge(*ACT["v"])
                        project3(pe, 0, wt["glu_a"], hT).then_inc(*PE("glu_a"))
                        pe.wait_ge(*ACT["glu_b"])
                        project3(pe, 3, wt["g"], hT).then_inc(*PE("g"))
                        for n in range(NLEV + 1):
                            pe.wait_ge(*VEC["glu"] if n == 0 else VEC[f"kept{n - 1}"])
                            if n == 0:
                                pe.wait_ge(*VEC["k"])
                                pe.wait_ge(*ACT["q"])
                            else:
                                pe.wait_ge(*VEC[f"W{n - 1}"])
                            for t in range(NT2):
                                u = slice(t * P, (t + 1) * P)
                                a, b = (k_[:, u], q_[:, u]) if n == 0 else (W[:, (n - 1) % 2, u],) * 2
                                q = pe.matmul(ps[:, t // 3, (t % 3) * P:(t % 3 + 1) * P], lhsT=a, rhs=b, start=True, stop=True)
                            q.then_inc(*PE(f"pairs{n}"))
                        pe.wait_ge(*VEC["kS"])
                        pe.wait_ge(*ACT["g"])
                        for t in range(NT2):
                            q = pe.transpose(ps[:, 3 + t // 3, (t % 3) * P:(t % 3 + 1) * P], kS[:, t * P:(t + 1) * P], ident)
                        q.then_inc(*PE("kS"))
                        pe.wait_ge(*ACT["kS"])
                        pe.wait_ge(*VEC[f"kept{NLEV}"])
                        for t in range(NT2 - 1):
                            q = pe.matmul(ps[:, t // 4, (t % 4) * P:(t % 4 + 1) * P], lhsT=kS[:, t * P:(t + 1) * P], rhs=v[:, t * P:(t + 1) * P],
                                          start=True, stop=True)
                        q.then_inc(*PE("kv"))
                        pe.wait_ge(*VEC[f"state{NT2 - 2}"])
                        pe.wait_ge(*VEC["qR"])
                        for t in range(NT2):
                            u = slice(t * P, (t + 1) * P)
                            o_ap = ps[:, 3 + t // 3, (t % 3) * P:(t % 3 + 1) * P]
                            pe.matmul(o_ap, lhsT=v[:, u], rhs=at[:, u], start=True, stop=False)
                            q = pe.matmul(o_ap, lhsT=Sst[:, t, :], rhs=q_[:, u], start=False, stop=True)
                        q.then_inc(*PE("o"))
                        pe.wait_ge(*ACT["osq"])
                        for b in range(3):
                            q = pe.matmul(ps[:, b, 0:THIRD], lhsT=ones, rhs=osq[:, b * THIRD:(b + 1) * THIRD], start=True, stop=True)
                        q.then_inc(*PE("oss"))

                    @block.scalar
                    def _(act):
                        act.wait_ge(*PE["f"])
                        act.activation(tok3(sgb[:, :]), bank3(0), FN.Sigmoid).then_inc(*ACT("f"))
                        act.wait_ge(*PE["q"])
                        act.activation(tok3(q_[:, :]), bank3(3), FN.Silu).then_inc(*ACT("q"))
                        act.wait_ge(*PE["v"])
                        act.copy(tok3(v[:, :]), bank3(0)).then_inc(*ACT("v"))
                        act.wait_ge(*PE["glu_b"])
                        act.wait_ge(*VEC["f"])
                        act.activation(tok3(sgb[:, :]), bank3(3), FN.Sigmoid).then_inc(*ACT("glu_b"))
                        act.wait_ge(*PE["g"])
                        act.activation(tok3(sgg[:, :]), bank3(3), FN.Silu).then_inc(*ACT("g"))
                        act.wait_ge(*PE["kS"])
                        act.copy(tok3(kS[:, :]), bank3(3)).then_inc(*ACT("kS"))
                        act.wait_ge(*PE["o"])
                        act.activation(tok3(osq[:, :]), bank3(3), FN.Square).then_inc(*ACT("osq"))
                        act.copy(tok3(orec[:, :]), bank3(3)).then_inc(*ACT("o"))
                        act.wait_ge(*PE["oss"])
                        act.activation(tok3(osq[:, :]), bank3(0), FN.Ln, bias=cst("eps"), scale=1.0 / P).then_inc(*ACT("o_ln"))
                        act.wait_ge(*ACT["o_ln"])
                        act.activation(osq[:, :], osq[:, :], FN.Exp, scale=-0.5).then_inc(*ACT("o_rs"))

                    @block.gpsimd
                    def _(pool):
                        pool.memset(Sp[:, :], 1.0).then_inc(*POOL("S_"))
                        for k in range(NLEV):
                            R4, S4 = level(Rp[:, :], k), level(Sp[:, :], k)
                            n = T2 >> (k + 1)
                            pool.wait_ge(*POOL["S_"] if k == 0 else POOL[f"R{k - 1}"])
                            pool.wait_ge(*VEC[f"W{k}"])
                            pool.tensor_tensor(S4[:, :, 0, :], S4[:, :, 0, :], R4[:, :, 1, (1 << k) - 1:1 << k].broadcast_to([P, n, 1 << k]),
                                               ALU.mult).then_inc(*POOL(f"S{k}"))
                            pool.wait_ge(*POOL[f"S{k}"])
                            pool.tensor_tensor(R4[:, :, 1, :], R4[:, :, 1, :], R4[:, :, 0, (1 << k) - 1:1 << k].broadcast_to([P, n, 1 << k]),
                                               ALU.mult).then_inc(*POOL(f"R{k}"))

                    @block.vector
                    def _(vec):
                        vec.wait_ge(*ACT["f"])
                        vec.tensor_scalar(Rp[:, :], sgb[:, :], omlb[:, ds(i, 1)], lb[:, ds(i, 1)], ALU.mult, ALU.add).then_inc(*VEC("f"))
                        vec.wait_ge(*VEC["f"])
                        vec.tensor_scalar(k_[:, :], Rp[:, :], -1.0, 1.0, ALU.mult, ALU.add).then_inc(*VEC("k"))
                        vec.wait_ge(*ACT["q"])
                        vec.wait_ge(*VEC["k"])
                        vec.wait_ge(*POOL["S_"])

                        def weights(k):
                            Wk, q4, k4, R4, S4 = (level(a, k) for a in (W[:, k % 2, :], q_[:, :], k_[:, :], Rp[:, :], Sp[:, :]))
                            if k >= 1:
                                vec.wait_ge(*POOL[f"R{k - 1}"])
                            if k >= 2:
                                vec.wait_ge(*PE[f"pairs{k - 1}"])
                            vec.tensor_tensor(Wk[:, :, 1, :], q4[:, :, 1, :], R4[:, :, 1, :], ALU.mult)
                            vec.tensor_tensor(Wk[:, :, 0, :], k4[:, :, 0, :], S4[:, :, 0, :], ALU.mult).then_inc(*VEC(f"W{k}"))

                        weights(0)
                        weights(1)
                        vec.wait_ge(*PE["glu_a"])
                        vec.wait_ge(*ACT["glu_b"])
                        vec.tensor_tensor(tok3(glu[:, :]), bank3(0), tok3(sgb[:, :]), ALU.mult).then_inc(*VEC("glu"))
                        T0 = P - META
                        NW = T2 - T0

                        def tap(n):
                            src = glu[:, T0 - (TAPS - 1) + n:T0 - (TAPS - 1) + n + NW]
                            w = params[:, ds(i * TAPS + (at_w + n), 1)]
                            vec.wait_ge(*VEC["glu" if n == 0 else f"tap{n - 1}"])
                            if n == 0:
                                vec.tensor_scalar(cv[:, T0:], src, w, params[:, ds(i + P2_AT["conv_b"][0], 1)], ALU.mult,
                                                  ALU.add).then_inc(*VEC("tap0"))
                            else:
                                vec.scalar_tensor_tensor(out=cv[:, T0:], in0=src, scalar=w, in1=cv[:, T0:], op0=ALU.mult,
                                                         op1=ALU.add).then_inc(*VEC(f"tap{n}"))
                        done = 0
                        for n in range(NLEV + 1):
                            vec.wait_ge(*PE[f"pairs{n}"])
                            mask = ident if n == 0 else cst("up", n - 1)
                            for b in range(3):
                                q = vec.copy_predicated(at[:, b * THIRD:(b + 1) * THIRD].rearrange("p (t n) -> p t n", n=P),
                                                        rep(mask, 3).bitcast(U32),
                                                        ps[:, b, 0:THIRD].rearrange("p (t n) -> p t n", n=P))
                            q.then_inc(*VEC(f"kept{n}"))
                            if 2 <= n + 1 < NLEV:
                                weights(n + 1)
                            for _ in range(2):
                                tap(done)
                                done += 1
                        vec.wait_ge(*POOL[f"R{NLEV - 1}"])
                        vec.tensor_tensor(kS[:, :], k_[:, :], Sp[:, :], ALU.mult).then_inc(*VEC("kS"))
                        vec.wait_ge(*PE["pairs0"])
                        vec.tensor_tensor(q_[:, :], q_[:, :], Rp[:, :], ALU.mult).then_inc(*VEC("qR"))
                        for _ in range(4):
                            tap(done)
                            done += 1
                        vec.wait_ge(*PE["kv"])
                        for t in range(NT2 - 1):
                            if t:
                                vec.wait_ge(*VEC[f"state{t - 1}"])
                            vec.scalar_tensor_tensor(out=Sst[:, t + 1, :], in0=Sst[:, t, :], scalar=Rp[:, (t + 1) * P - 1:(t + 1) * P],
                                                     in1=ps[:, t // 4, (t % 4) * P:(t % 4 + 1) * P], op0=ALU.mult, op1=ALU.add).then_inc(*VEC(f"state{t}"))
                        while done < TAPS:
                            tap(done)
                            done += 1
                        vec.wait_ge(*ACT["o_rs"])
                        vec.tensor_tensor(orec[:, :], orec[:, :], osq[:, :], ALU.mult).then_inc(*VEC("o_normed"))
                        vec.wait_ge(*VEC["o_normed"])
                        vec.scalar_tensor_tensor(out=orec[:, :], in0=orec[:, :], scalar=params[:, ds(i + P2_AT["gnorm"][0], 1)],
                                                 in1=sgg[:, :], op0=ALU.mult, op1=ALU.mult).then_inc(*VEC("orec"))
                clear()

        merged_stack = ExitStack()
        cz = sbuf(merged_stack, "cz", [P, KD, T2])
        rec = sbuf(merged_stack, "rec", [P, KD, T2])
        merged = sbuf(merged_stack, "merged", [P, KD, T2])
        with ExitStack() as st:
            wz = sbuf(st, "wz", [P, KD, P])
            mu = sbuf(st, "mu", [P, T2])
            sq = sbuf(st, "sq_l", [P, 2, T2])
            zs = sbuf(st, "zs", [P, T2])
            begin("ln")
            with nc.Block() as block:
                @block.sync
                def _(sp):
                    sp.dma_start(wz[:, :, :], w_rows(w_in2[:, 2 * DM:2 * DM + P])).then_inc(*DMA("wz"))
                    sp.dma_start(cz[:, :, :], conv_hbm.rearrange("k p n -> p k n")).then_inc(*DMA("cz"))
                    sp.dma_start(rec[:, :, :], rec_hbm.rearrange("k p n -> p k n")).then_inc(*DMA("rec"))
                    sp.wait_ge(*DMA["rec"])
                    sp.wait_ge(*DMA["wz"])

                @block.tensor
                def _(pe):
                    pe.wait_ge(*DMA["cz"])
                    for b in range(3):
                        for k in range(KD):
                            q = pe.matmul(ps[:, b, 0:THIRD], lhsT=ones, rhs=cz[:, k, b * THIRD:(b + 1) * THIRD], start=(k == 0), stop=(k == KD - 1))
                    q.then_inc(*PE("sum"))
                    for k in range(KD):
                        pe.wait_ge(*ACT[f"sq{k}"])
                        for b in range(3):
                            q = pe.matmul(ps[:, 3 + b, 0:THIRD], lhsT=ones, rhs=sq[:, k % 2, b * THIRD:(b + 1) * THIRD], start=(k == 0),
                                          stop=(k == KD - 1))
                        q.then_inc(*PE(f"sumsq{k}"))

                @block.scalar
                def _(act):
                    act.wait_ge(*PE["sum"])
                    act.mul(tok3(mu[:, :]), bank3(0), 1.0 / DM).then_inc(*ACT("mu"))
                    for k in range(KD):
                        act.wait_ge(*VEC[f"centred{k}"])
                        if k >= 2:
                            act.wait_ge(*PE[f"sumsq{k - 2}"])
                        act.activation(sq[:, k % 2, :], cz[:, k, :], FN.Square).then_inc(*ACT(f"sq{k}"))
                    act.wait_ge(*PE[f"sumsq{KD - 1}"])
                    act.activation(tok3(zs[:, :]), bank3(3), FN.Ln, bias=cst("eps"), scale=1.0 / DM).then_inc(*ACT("ln"))
                    act.wait_ge(*ACT["ln"])
                    act.activation(zs[:, :], zs[:, :], FN.Exp, scale=-0.5).then_inc(*ACT("rs"))

                @block.vector
                def _(vec):
                    vec.wait_ge(*ACT["mu"])
                    for k in range(KD):
                        vec.tensor_tensor(cz[:, k, :], cz[:, k, :], mu[:, :], ALU.subtract).then_inc(*VEC(f"centred{k}"))
                    vec.wait_ge(*ACT["rs"])
                    for k in range(KD):
                        vec.tensor_tensor(cz[:, k, :], cz[:, k, :], zs[:, :], ALU.mult).then_inc(*VEC(f"scaled{k}"))
            clear()
            with nc.Fori(0, KD) as i:
                begin("z")
                with nc.Block() as block:
                    @block.sync
                    def _(sp):
                        sp.wait_ge(*PE["z"])
                        sp.dma_start(wz[:, :, :], w_rows(w_in2[:, ds(i * P + (2 * DM + P), P)])).then_inc(*DMA("wz"))
                        sp.wait_ge(*DMA["wz"])

                    @block.tensor
                    def _(pe):
                        project3(pe, 0, wz, hT).then_inc(*PE("z"))

                    @block.scalar
                    def _(act):
                        act.wait_ge(*VEC["affine"])
                        act.activation(mu[:, :], mu[:, :], FN.Silu).then_inc(*ACT("c"))
                        act.wait_ge(*PE["z"])
                        act.activation(tok3(zs[:, :]), bank3(0), FN.Silu).then_inc(*ACT("z"))

                    @block.vector
                    def _(vec):
                        vec.tensor_scalar(mu[:, :], cz[:, ds(i, 1), :], params[:, ds(i + P2_AT["ln_g"][0], 1)],
                                          params[:, ds(i + P2_AT["ln_b"][0], 1)], ALU.mult, ALU.add).then_inc(*VEC("affine"))
                        vec.wait_ge(*ACT["z"])
                        vec.tensor_tensor(cz[:, ds(i, 1), :], mu[:, :], zs[:, :], ALU.mult).then_inc(*VEC("cz"))
                clear()

        with ExitStack() as st:
            wm = {n: sbuf(st, "wm_" + n, [P, KD, P]) for n in ("m_conv", "m_rec", "conv", "rec")}
            src = {"m_conv": (w_in2, 7 * DM), "m_rec": (w_in2, 8 * DM), "conv": (io["w_conv_out_2"], 0), "rec": (io["w_rec_out_2"], 0)}
            gm = sbuf(st, "gm", [P, 2, T2])
            with nc.Fori(0, KD) as i:
                begin("merge")
                with nc.Block() as block:
                    @block.sync
                    def _(sp):
                        for n in ("m_conv", "conv", "m_rec", "rec"):
                            w, c0 = src[n]
                            sp.dma_start(wm[n][:, :, :], w_rows(w[:, ds(i * P + c0, P)])).then_inc(*DMA("w_" + n))

                    @block.tensor
                    def _(pe):
                        pe.wait_ge(*DMA["w_m_conv"])
                        project3(pe, 0, wm["m_conv"], hT).then_inc(*PE("m_conv"))
                        pe.wait_ge(*DMA["w_conv"])
                        project3(pe, 3, wm["conv"], cz).then_inc(*PE("conv"))
                        pe.wait_ge(*DMA["w_m_rec"])
                        pe.wait_ge(*ACT["m_conv"])
                        project3(pe, 0, wm["m_rec"], hT).then_inc(*PE("m_rec"))
                        pe.wait_ge(*DMA["w_rec"])
                        pe.wait_ge(*VEC["conv"])
                        project3(pe, 3, wm["rec"], rec).then_inc(*PE("rec"))

                    @block.scalar
                    def _(act):
                        act.wait_ge(*PE["m_conv"])
                        act.activation(tok3(gm[:, 0, :]), bank3(0), FN.Sigmoid).then_inc(*ACT("m_conv"))
                        act.wait_ge(*PE["m_rec"])
                        act.activation(tok3(gm[:, 1, :]), bank3(0), FN.Sigmoid).then_inc(*ACT("m_rec"))

                    @block.vector
                    def _(vec):
                        vec.wait_ge(*PE["conv"])
                        vec.wait_ge(*ACT["m_conv"])
                        vec.tensor_tensor(tok3(gm[:, 0, :]), tok3(gm[:, 0, :]), bank3(3), ALU.mult).then_inc(*VEC("conv"))
                        vec.wait_ge(*PE["rec"])
                        vec.wait_ge(*ACT["m_rec"])
                        vec.tensor_tensor(tok3(gm[:, 1, :]), tok3(gm[:, 1, :]), bank3(3), ALU.mult).then_inc(*VEC("rec"))
                        vec.wait_ge(*VEC["rec"])
                        vec.tensor_tensor(merged[:, ds(i, 1), :], gm[:, 0, :], gm[:, 1, :], ALU.add).then_inc(*VEC("merged"))
                clear()

        with ExitStack() as st:
            wo = cz[:, :, 0:DM]
            mT = sbuf(st, "mT2", [P, KD, P])
            xt = sbuf(st, "x_o", [P, DM])
            sq = sbuf(st, "sq_e", [P, DM])
            fg = sbuf(st, "fg2", [P, DM])
            ss = sbuf(st, "ss_e", [P, 1])
            rs = sbuf(st, "rs_e", [P, 1])
            begin("end_load")
            with nc.Block() as block:
                @block.sync
                def _(sp):
                    sp.dma_start(wo, w_rows(io["w_out_2"])).then_inc(*DMA("end"))
                    sp.dma_start(fg[:, :], io["final_g_2"]).then_inc(*DMA("end"))
                    sp.wait_ge(*DMA["end"])
            clear()
            with nc.Fori(1, NT2) as t:
                begin("end")
                with nc.Block() as block:
                    @block.sync
                    def _(sp):
                        sp.dma_start(xt[:, :], x_hbm[ds(t * P, P), :]).then_inc(*DMA("x_in"))
                        sp.wait_ge(*VEC["y"])
                        sp.dma_start(io["out"][ds((t - 1) * P, P), :], sq[:, :]).then_inc(*DMA("y_out"))
                        sp.wait_ge(*DMA["y_out"])

                    @block.gpsimd
                    def _(pool):
                        pool.tensor_copy(mT[:, :, :], merged[:, :, ds(t * P, P)]).then_inc(*POOL("mT"))

                    @block.tensor
                    def _(pe):
                        pe.wait_ge(*POOL["mT"])
                        for b in range(2):
                            for k in range(KD):
                                q = pe.matmul(ps[:, b, :], lhsT=mT[:, k, :], rhs=wo[:, k, 512 * b:512 * (b + 1)], start=(k == 0), stop=(k == KD - 1))
                            q.then_inc(*PE(f"o{b}"))

                    @block.vector
                    def _(vec):
                        vec.wait_ge(*DMA["x_in"])
                        for b in range(2):
                            n = slice(512 * b, 512 * (b + 1))
                            vec.wait_ge(*PE[f"o{b}"])
                            vec.tensor_tensor(xt[:, n], xt[:, n], ps[:, b, :], ALU.add).then_inc(*VEC(f"x{b}"))
                        vec.wait_ge(*ACT["rs"])
                        vec.scalar_tensor_tensor(out=sq[:, :], in0=xt[:, :], scalar=rs[:, :], in1=fg[:, :], op0=ALU.mult,
                                                 op1=ALU.mult).then_inc(*VEC("y"))

                    @block.scalar
                    def _(act):
                        act.wait_ge(*VEC["x1"])
                        act.activation(sq[:, :], xt[:, :], FN.Square, accum_out=ss[:, :]).then_inc(*ACT("ss"))
                        act.wait_ge(*ACT["ss"])
                        act.activation(rs[:, :], ss[:, :], FN.Ln, bias=cst("eps"), scale=1.0 / DM).then_inc(*ACT("ln"))
                        act.wait_ge(*ACT["ln"])
                        act.activation(rs[:, :], rs[:, :], FN.Exp, scale=-0.5).then_inc(*ACT("rs"))
                clear()
        merged_stack.close()


def kernel(**inputs):
    import numpy as _np
    import concourse.bacc as _bacc
    from concourse import mybir as _mybir
    from concourse.bass_utils import run_bass_kernel_spmd as _run

    a = {k: _np.asarray(v) for k, v in inputs.items()}

    def channels(v, n):
        return v.reshape(v.shape[0], n, P).transpose(0, 2, 1)

    def everywhere(v):
        return _np.broadcast_to(v[:, None, :], (v.shape[0], P, v.shape[1]))

    def both(v, n):
        return v.reshape(v.shape[0], v.shape[1], n, P).transpose(0, 3, 1, 2).reshape(v.shape[0], P, -1)

    q_g = _np.zeros((DEPTH, 2 * P), _np.float32)
    q_g[:, :QR] = a["mla_q_norm_g"]
    laid = {
        "norm_g": channels(a["norm_g"], KD),
        "conv": a["gdn_conv"].reshape(DEPTH, CONV, 9, P).transpose(0, 3, 2, 1).reshape(DEPTH, P, -1),
        "a_log": everywhere(a["gdn_a_log"].reshape(DEPTH, -1)), "dt": everywhere(a["gdn_dt_bias"].reshape(DEPTH, -1)),
        "gdn_g": everywhere(a["gdn_norm_g"]), "q_g": channels(q_g, 2), "kv_g": channels(a["mla_kv_norm_g"], 1),
        "mu": a["rwkv_mu"].reshape(DEPTH, 2, 7, P).transpose(0, 3, 2, 1).reshape(DEPTH, P, -1),
        "w0": both(a["rwkv_w0"], 2), "a0": both(a["rwkv_a0"], 2), "k_k": channels(a["rwkv_k_k"], 2),
        "k_a": channels(a["rwkv_k_a"], 2), "r_k": channels(a["rwkv_r_k"].reshape(DEPTH, RW), 2),
        "ln_g": everywhere(a["rwkv_ln_g"]), "ln_b": everywhere(a["rwkv_ln_b"]),
    }
    laid2 = {
        "norm_g": channels(a["norm_g_2"], KD)[0],
        "conv_w": a["conv_w_2"][0].reshape(TAPS, KD, P).transpose(2, 1, 0).reshape(P, -1),
        "conv_b": channels(a["conv_b_2"], KD)[0], "ln_g": channels(a["ln_g_2"], KD)[0], "ln_b": channels(a["ln_b_2"], KD)[0],
        "lb": a["lb_logits_2"].reshape(2, KD, P).transpose(2, 1, 0).reshape(P, -1), "gnorm": channels(a["gnorm_g_2"], KD)[0],
    }
    w2a2 = _np.concatenate([a["rwkv_w2"].transpose(0, 2, 1, 3), a["rwkv_a2"].transpose(0, 2, 1, 3)], 1)
    arrays = {
        "consts": shape_constants(), "positions": a["positions"].reshape(NT, P).T, "x": a["x"].reshape(SEQ, DM),
        "params": _np.concatenate([laid[n] for n, _ in PARAMS], 2), "params2": _np.concatenate([laid2[n] for n, _ in PARAMS2], 1),
        "w_in": a["w_in"], "w_uq": a["mla_w_uq"], "w_ukv": a["mla_w_ukv"], "w2a2": w2a2, "w_out": a["w_out"],
        "final_g": everywhere(a["final_norm_g"][None])[0], "meta": a["meta_tokens_2"], "w_in_2": a["w_in_2"][0],
        "w_conv_out_2": a["w_conv_out_2"][0], "w_rec_out_2": a["w_rec_out_2"][0], "w_out_2": a["w_out_2"][0],
        "final_g_2": everywhere(a["final_g_2"][None])[0],
    }
    arrays = {"in_" + n: _np.ascontiguousarray(v) for n, v in arrays.items()}

    def program(values):
        nc = _bacc.Bacc("TRN2", target_bir_lowering=False, num_devices=1)
        io = {n[3:]: nc.dram_tensor(n, v.shape, _mybir.dt.from_np(v.dtype), kind="ExternalInput").ap() for n, v in arrays.items()}
        io["out"] = nc.dram_tensor("out", (SEQ, DM), F32, kind="ExternalOutput").ap()
        build(nc, io, values)
        return nc

    values = {}
    program(values)
    r = _run(program(values), [arrays], core_ids=[0])
    return r.results[0]["out"].reshape(1, SEQ, DM)
```

```python
from contextlib import ExitStack

import concourse.bass as bass
import numpy as np
from concourse import mybir

F32 = mybir.dt.float32
I32 = mybir.dt.int32
U32 = mybir.dt.uint32
FN = mybir.ActivationFunctionType
ALU = mybir.AluOpType
AX = mybir.AxisListType.X
ds = bass.ds

P = 128
DEPTH, DM, SEQ = 2, 1024, 1024
KD = DM // P
NT = SEQ // P
GH, GD = 6, 64
GW = GH * GD
CONV = 5
MH, NOPE, ROPE, MV = 6, 64, 32, 64
QR, KVR = 192, 128
QK = NOPE + ROPE
RH, RD = 4, 64
RW = RH * RD
N_IN = 3448
COL_GDN, COL_AB, COL_RW = 1024, 2176, 2552
TM_W = COL_RW - COL_AB
NLEV = 7
T2 = SEQ + P
NT2 = T2 // P
META = 16
TAPS = 31
D_IN2 = 9216
NORM_EPS = 1e-6
RWKV_EPS = 64e-5

PARAMS = [("norm_g", KD), ("conv", 9 * CONV), ("a_log", 2 * GH), ("dt", 2 * GH), ("gdn_g", GD), ("q_g", 2), ("kv_g", 1),
          ("mu", 14), ("w0", 4), ("a0", 4), ("k_k", 2), ("k_a", 2), ("r_k", 2), ("ln_g", RW), ("ln_b", RW)]
PARAMS2 = [("norm_g", KD), ("conv_w", KD * TAPS), ("conv_b", KD), ("ln_g", KD), ("ln_b", KD), ("lb", KD * 2),
           ("gnorm", KD)]
CONSTS = [("ident", P), ("tri_f", P), ("tri_b", P), ("aft", P), ("bef", P), ("ones", P), ("blk", P), ("sel", 2),
          ("freq", ROPE // 2), ("eps", 1), ("rw_eps", 1), ("lo", NLEV * P), ("up", NLEV * P)]


def offsets(fields):
    at, out = 0, {}
    for name, n in fields:
        out[name] = (at, n)
        at += n
    return out, at


def shape_constants():
    i = np.arange(P)
    r, c = i[:, None], i[None, :]
    lo = np.stack([((r >> (k + 1)) == (c >> (k + 1))) & (((r >> k) & 1) == 1) & (((c >> k) & 1) == 0) for k in range(NLEV)], 1)
    up = np.stack([((r >> (k + 1)) == (c >> (k + 1))) & (((r >> k) & 1) == 0) & (((c >> k) & 1) == 1) for k in range(NLEV)], 1)
    half = ROPE // 2
    parts = {
        "ident": r == c, "tri_f": r <= c, "tri_b": r >= c, "aft": r > c, "bef": r < c, "ones": np.ones((P, P)),
        "blk": (r // 64) == (c // 64), "sel": (r // 64) == np.arange(2)[None, :],
        "freq": np.broadcast_to(np.float32(10000.0) ** (-np.arange(half, dtype=np.float32) / half), (P, half)),
        "eps": np.full((P, 1), NORM_EPS), "rw_eps": np.full((P, 1), RWKV_EPS),
        "lo": lo.reshape(P, -1), "up": up.reshape(P, -1),
    }
    return np.ascontiguousarray(np.concatenate([np.asarray(parts[n], np.float32) for n, _ in CONSTS], 1))


class Steps:

    def __init__(self, sem, label, unit, values):
        self.sem, self.label, self.unit, self.values = sem, label, unit, values
        self.stage, self.count = "", 0

    def begin(self, stage):
        self.stage, self.count = stage, 0

    def __call__(self, name):
        self.count += self.unit
        self.values[self.stage, self.label, name] = self.count
        return self.sem, self.unit

    def __getitem__(self, name):
        return self.sem, self.values.get((self.stage, self.label, name), 1)


class Transfers:

    def __init__(self, nc, ctx, values):
        self.nc, self.ctx, self.values, self.sems = nc, ctx, values, {}

    def begin(self, stage):
        self.stage, self.counts = stage, {}

    def sem(self, name):
        if name not in self.sems:
            self.sems[name] = self.ctx.enter_context(self.nc.semaphore("dma_" + name))
        return self.sems[name]

    def __call__(self, name):
        self.counts[name] = self.counts.get(name, 0) + 16
        self.values[self.stage, "dma", name] = self.counts[name]
        return self.sem(name), 16

    def __getitem__(self, name):
        return self.sem(name), self.values.get((self.stage, "dma", name), 16)


def build(nc, io, values):
    with ExitStack() as ctx:
        def sem(name):
            return ctx.enter_context(nc.semaphore(name))

        VEC = Steps(sem("vector_steps"), "vec", 1, values)
        ACT = Steps(sem("scalar_steps"), "act", 1, values)
        PE = Steps(sem("tensor_steps"), "pe", 1, values)
        POOL = Steps(sem("gpsimd_steps"), "pool", 1, values)
        DMA = Transfers(nc, ctx, values)

        def begin(stage):
            for s in (VEC, ACT, PE, POOL, DMA):
                s.begin(stage)

        def clear():
            for s in (VEC, ACT, PE, POOL):
                nc.sync.sem_clear(s.sem)
            for name in DMA.counts:
                nc.sync.sem_clear(DMA.sem(name))
            nc.all_engine_barrier()

        def sbuf(stack, name, shape, dt=F32):
            return stack.enter_context(nc.sbuf_tensor(name, shape, dt))

        def rep(ap, n):
            return ap[:, None, :].broadcast_to([ap.shape[0], n, ap.shape[1]])

        def col(ap, m):
            return ap[:, :, None].broadcast_to([ap.shape[0], ap.shape[1], m])

        def hbm(name, shape):
            return nc.dram_tensor(name, shape, F32).ap()

        gate_hbm = hbm("gate_hbm", (SEQ, DM))
        gdn_hbm = hbm("gdn_hbm", (2, SEQ, GW))
        rwkv_hbm = hbm("rwkv_hbm", (3, SEQ, RW))
        mla_hbm = hbm("mla_hbm", (SEQ, GW))
        x_hbm = hbm("x_hbm", (T2, DM))
        conv_hbm = hbm("conv_hbm", (KD, P, T2))
        rec_hbm = hbm("rec_hbm", (KD, P, T2))
        tm_hbm = hbm("tm_hbm", (SEQ, TM_W))

        C_AT, C_N = offsets(CONSTS)
        P_AT, P_N = offsets(PARAMS)
        P2_AT, P2_N = offsets(PARAMS2)
        consts = sbuf(ctx, "consts", [P, C_N])
        ps = ctx.enter_context(nc.psum_tensor("ps", [P, 8, 512], F32))

        def cst(name, k=None):
            a, n = C_AT[name]
            return consts[:, a:a + n] if k is None else consts[:, a + k * P:a + (k + 1) * P]

        ident, ones, blk = cst("ident"), cst("ones"), cst("blk")
        hT = sbuf(ctx, "hT", [P, KD, T2])
        params = sbuf(ctx, "params", [P, max(P_N, P2_N)])

        def par(name, table=P_AT):
            a, n = table[name]
            return params[:, a:a + n]

        def w_rows(w):
            return w.rearrange("(k p) n -> p k n", p=P)

        def norm_tiles(stage, n, row, g, work, final=None, loads=None):
            X, ss, rs = work["x"], work["ss"], work["rs"]
            rounds = 2 if final is not None else 1
            begin(stage)
            with nc.Block() as block:
                @block.sync
                def _(sp):
                    for j in range(n):
                        sp.dma_start(X[:, j, :], x_hbm[ds(row(j), P), :]).then_inc(*DMA(f"x_tile{j}"))
                    if loads is not None:
                        loads(sp)
                    if final is not None:
                        for j in range(n):
                            sp.wait_ge(*VEC[f"final{j}"])
                            sp.dma_start(x_hbm[ds(row(j), P), :], X[:, j, :]).then_inc(*DMA("x_out"))
                        sp.wait_ge(*DMA["x_out"])

                @block.scalar
                def _(act):
                    for r in range(rounds):
                        for j in range(n):
                            act.wait_ge(*(DMA[f"x_tile{j}"] if r == 0 else VEC[f"final{j}"]))
                            if r + j > 0:
                                act.wait_ge(*(ACT[f"sum{r}_{j - 1}"] if j > 0 else ACT[f"sum0_{n - 1}"]))
                            act.activation(work["sq"][:, :], X[:, j, :], FN.Square, accum_out=ss[:, r, j:j + 1]).then_inc(*ACT(f"sum{r}_{j}"))
                        act.wait_ge(*ACT[f"sum{r}_{n - 1}"])
                        act.activation(rs[:, r, 0:n], ss[:, r, 0:n], FN.Ln, bias=cst("eps"), scale=1.0 / DM).then_inc(*ACT(f"ln{r}"))
                        act.wait_ge(*ACT[f"ln{r}"])
                        act.activation(rs[:, r, 0:n], rs[:, r, 0:n], FN.Exp, scale=-0.5).then_inc(*ACT(f"rs{r}"))

                @block.vector
                def _(vec):
                    if final is not None:
                        for j in range(n):
                            vec.wait_ge(*ACT["rs0"])
                            vec.scalar_tensor_tensor(out=X[:, j, :], in0=X[:, j, :], scalar=rs[:, 0, j:j + 1], in1=final, op0=ALU.mult,
                                                     op1=ALU.mult).then_inc(*VEC(f"final{j}"))
                    for j in range(n + 1):
                        if j < n:
                            vec.wait_ge(*ACT[f"rs{rounds - 1}"])
                            vec.tensor_scalar(work["xn"][:, j % 2, :], X[:, j, :], rs[:, rounds - 1, j:j + 1], None,
                                              ALU.mult).then_inc(*VEC(f"normed{j}"))
                        if j > 0:
                            for b in range(2):
                                vec.wait_ge(*PE[f"turned{j - 1}_{b}"])
                                bank = (2 * (j - 1) + b) % 8
                                vec.tensor_tensor(hT[:, 4 * b:4 * b + 4, ds(row(j - 1), P)], ps[:, bank, :].rearrange("p (k n) -> p k n", k=4),
                                                  col(g[:, 4 * b:4 * b + 4], P), ALU.mult).then_inc(*VEC(f"h{j - 1}_{b}"))

                @block.tensor
                def _(pe):
                    for j in range(n):
                        pe.wait_ge(*VEC[f"normed{j}"])
                        for b in range(2):
                            for k in range(4):
                                q = pe.transpose(ps[:, (2 * j + b) % 8, k * P:(k + 1) * P], work["xn"][:, j % 2, (4 * b + k) * P:(4 * b + k + 1) * P], ident)
                            q.then_inc(*PE(f"turned{j}_{b}"))
            clear()

        def norm_buffers(stack, tag, n):
            return {"x": sbuf(stack, "x" + tag, [P, n, DM]), "sq": sbuf(stack, "sq" + tag, [P, DM]), "xn": sbuf(stack, "xn" + tag, [P, 2, DM]),
                    "ss": sbuf(stack, "ss" + tag, [P, 2, n]), "rs": sbuf(stack, "rs" + tag, [P, 2, n])}

        first = ExitStack()
        cs = sbuf(first, "cos_sin", [P, NT, 2, ROPE // 2])
        begin("load")
        with ExitStack() as st, nc.Block() as block:
            pos_i = sbuf(st, "pos_i", [P, NT], I32)
            pos = sbuf(st, "pos", [P, NT])
            ang = sbuf(st, "ang", [P, 2, NT, ROPE // 2])
            turns = sbuf(st, "turns", [P, 2, NT, ROPE // 2])
            whole = sbuf(st, "whole", [P, 2, NT, ROPE // 2])
            meta = sbuf(st, "meta", [P, DM])

            @block.sync
            def _(sp):
                sp.dma_start(consts[:, :], io["consts"]).then_inc(*DMA("consts"))
                sp.dma_start(pos_i[:, :], io["positions"]).then_inc(*DMA("positions"))
                sp.dma_start(x_hbm[P:T2, :], io["x"]).then_inc(*DMA("x"))
                sp.wait_ge(*VEC["zero"])
                sp.dma_start(meta[P - META:P, :], io["meta"]).then_inc(*DMA("meta"))
                sp.wait_ge(*DMA["meta"])
                sp.dma_start(x_hbm[0:P, :], meta[:, :]).then_inc(*DMA("meta_out"))
                sp.wait_ge(*DMA["meta_out"])
                sp.wait_ge(*DMA["x"])

            @block.vector
            def _(vec):
                vec.memset(meta[:, :], 0.0).then_inc(*VEC("zero"))
                two_pi = 2 * np.pi
                c1 = float(np.float32(6.28125))
                c2 = float(np.float32(np.round((two_pi - c1) * 2**19) / 2**19))
                c3 = float(np.float32(two_pi - c1 - c2))
                magic = float(np.float32(1.5 * 2**23))
                vec.wait_ge(*DMA["positions"])
                vec.tensor_copy(pos[:, :], pos_i[:, :]).then_inc(*VEC("pos"))
                vec.wait_ge(*DMA["consts"])
                vec.wait_ge(*VEC["pos"])
                vec.tensor_tensor(ang[:, 1, :, :], col(pos[:, :], ROPE // 2), rep(cst("freq"), NT), ALU.mult).then_inc(*VEC("ang"))
                vec.wait_ge(*VEC["ang"])
                vec.tensor_scalar(turns[:, 1], ang[:, 1], 1.0 / two_pi, magic, ALU.mult, ALU.add).then_inc(*VEC("turns1"))
                vec.tensor_scalar(turns[:, 0], ang[:, 1], 1.0 / two_pi, 0.25, ALU.mult, ALU.add).then_inc(*VEC("turns0a"))
                vec.wait_ge(*VEC["turns0a"])
                vec.tensor_scalar(turns[:, 0], turns[:, 0], magic, None, ALU.add).then_inc(*VEC("turns0"))
                vec.wait_ge(*VEC["turns0"])
                vec.tensor_scalar(whole[:, :], turns[:, :], magic, None, ALU.subtract).then_inc(*VEC("whole"))
                vec.tensor_copy(ang[:, 0], ang[:, 1]).then_inc(*VEC("ang0"))
                for n, c in enumerate((c1, c2, c3)):
                    vec.wait_ge(*VEC["ang0" if n == 0 else f"cut{n - 1}"])
                    vec.scalar_tensor_tensor(out=ang[:, :], in0=whole[:, :], scalar=-c, in1=ang[:, :], op0=ALU.mult,
                                             op1=ALU.add).then_inc(*VEC(f"cut{n}"))
                vec.wait_ge(*VEC["cut2"])
                vec.tensor_scalar(ang[:, 0], ang[:, 0], float(np.float32(np.pi / 2)), None, ALU.add).then_inc(*VEC("quarter"))
                vec.wait_ge(*VEC["quarter"])
                vec.tensor_scalar(ang[:, :], ang[:, :], 3.1415925, -3.1415925, ALU.min, ALU.max).then_inc(*VEC("range"))

            @block.scalar
            def _(act):
                act.wait_ge(*VEC["range"])
                act.activation(cs[:, :, :, :].rearrange("p t c f -> p c t f"), ang[:, :, :, :], FN.Sin).then_inc(*ACT("cos_sin"))
        clear()

        with nc.Fori(0, DEPTH) as L:
            w_in = io["w_in"][ds(L, 1)].rearrange("a r n -> (a r) n")
            w_uq = io["w_uq"][ds(L, 1)].rearrange("a r n -> (a r) n")

            with ExitStack() as st:
                wg = sbuf(st, "w_gate", [P, KD, DM])
                wt = sbuf(st, "w_tm", [P, KD, TM_W])
                with ExitStack() as st2:
                    work = norm_buffers(st2, "_1", 4)
                    begin("load1")
                    with nc.Block() as block:
                        @block.sync
                        def _(sp):
                            sp.dma_start(params[:, 0:P_N], io["params"][ds(L, 1)].rearrange("a p n -> (a p) n")).then_inc(*DMA("params"))
                            sp.wait_ge(*DMA["params"])
                    clear()
                    with nc.Fori(0, 2) as i:
                        def load_gate(sp):
                            sp.dma_start(wg[:, ds(i * (KD // 2), KD // 2), :], w_rows(w_in[ds(i * (DM // 2), DM // 2), 0:DM])).then_inc(*DMA("w"))
                            sp.dma_start(wt[:, ds(i * (KD // 2), KD // 2), :], w_rows(w_in[ds(i * (DM // 2), DM // 2), COL_AB:COL_RW])).then_inc(*DMA("w"))
                            sp.wait_ge(*DMA["w"])
                        norm_tiles("norm1", 4, lambda j: i * (4 * P) + (j + 1) * P, par("norm_g"), work, loads=load_gate)

                def token_major(stage, w, columns, out, dst):
                    begin(stage)
                    with nc.Block() as block:
                        @block.tensor
                        def _(pe):
                            for t in range(NT):
                                for k in range(KD):
                                    q = pe.matmul(ps[:, t, 0:columns], lhsT=hT[:, k, (t + 1) * P:(t + 2) * P], rhs=w(k), start=(k == 0),
                                                  stop=(k == KD - 1))
                                q.then_inc(*PE(f"tile{t}"))

                        @block.scalar
                        def _(act):
                            for t in range(0, NT, 2):
                                act.wait_ge(*PE[f"tile{t}"])
                                act.copy(out[:, t, 0:columns], ps[:, t, 0:columns]).then_inc(*ACT(f"tile{t}"))

                        @block.vector
                        def _(vec):
                            for t in range(1, NT, 2):
                                vec.wait_ge(*PE[f"tile{t}"])
                                vec.tensor_copy(out[:, t, 0:columns], ps[:, t, 0:columns]).then_inc(*VEC(f"tile{t}"))

                        @block.sync
                        def _(sp):
                            for t in range(NT):
                                sp.wait_ge(*(VEC if t % 2 else ACT)[f"tile{t}"])
                                sp.dma_start(dst(t), out[:, t, 0:columns]).then_inc(*DMA("out"))
                            sp.wait_ge(*DMA["out"])
                    clear()

                tm_out = sbuf(st, "tm_out", [P, NT, 512])
                token_major("tm", lambda k: wt[:, k, :], TM_W, tm_out, lambda t: tm_hbm[t * P:(t + 1) * P, :])
                with nc.Fori(0, 2) as i:
                    token_major("gate", lambda k: wg[:, k, ds(i * 512, 512)], 512, tm_out,
                                lambda t: gate_hbm[t * P:(t + 1) * P, ds(i * 512, 512)])

            def project_tensor(pe, wc):
                for b in range(2):
                    for k in range(KD):
                        m = pe.matmul(ps[:, b, :], lhsT=wc[:, k, :], rhs=hT[:, k, P + b * 512:P + (b + 1) * 512],
                                      start=(k == 0), stop=(k == KD - 1))
                    m.then_inc(*PE(f"proj{b}"))

            def project_copy(act, xp):
                for b in range(2):
                    act.wait_ge(*PE[f"proj{b}"])
                    act.copy(xp[:, 2 + b * 512:2 + (b + 1) * 512], ps[:, b, :]).then_inc(*ACT(f"proj{b}"))

            def load_columns(wc, column):
                begin("columns")
                with nc.Block() as block:
                    @block.sync
                    def _(sp):
                        sp.dma_start(wc[:, :, :], w_rows(w_in[:, column:column + P])).then_inc(*DMA("w_cols"))
                        sp.wait_ge(*DMA["w_cols"])
                clear()

            def side(ap, k, g):
                if len(ap.shape) == 2:
                    return ap.rearrange("p (a s n) -> p a s n", s=2, n=1 << k)[:, :, g, :]
                return ap.rearrange("p u (a s n) -> p u a s n", s=2, n=1 << k)[:, :, :, g, :]

            def half_bank(b, k, n):
                return ps[:, b, 0:64 * n].rearrange("p (u a n) -> p u a n", u=n, n=1 << k)

            def invert_tensor(pe, n, ready, turn_bank, AT, X, Y, Pm):
                def product(k, g):
                    pe.wait_ge(*VEC[ready[g]] if k == 0 else VEC[f"X{k - 1}_{g}"])
                    for w in range(n):
                        u = n * g + w
                        q = pe.matmul(ps[:, g, 64 * w:64 * w + 64], lhsT=AT(u), rhs=side(ident if k == 0 else X[:, u, :], k, g),
                                      start=True, stop=True)
                    q.then_inc(*PE(f"P{k}_{g}"))
                for g in range(2):
                    product(0, g)
                for k in range(NLEV):
                    if k > 0:
                        for g in range(2):
                            pe.wait_ge(*VEC[f"P{k}_{g}"])
                            pe.wait_ge(*ACT[f"Y{k - 1}_{g}"])
                            for w in range(n):
                                u = n * g + w
                                q = pe.matmul(ps[:, 2 + g, 64 * w:64 * w + 64], lhsT=Y[:, u, :], rhs=Pm[:, u, :], start=True, stop=True)
                            q.then_inc(*PE(f"Xd{k}_{g}"))
                    for g in range(2):
                        if k + 1 < NLEV:
                            product(k + 1, g)
                        pe.wait_ge(*VEC[f"X{k}_{g}"])
                        for w in range(n):
                            q = pe.transpose(ps[:, turn_bank(g) + w // 4, (w % 4) * P:(w % 4 + 1) * P], X[:, n * g + w, :], ident)
                        q.then_inc(*PE(f"Y{k}_{g}"))

            def invert_vector(vec, n, X, Pm):
                for k in range(NLEV):
                    for g in range(2):
                        us = slice(n * g, n * g + n)
                        mask = side(cst("lo" if g == 0 else "up", k), k, g)
                        pm = Pm[:, us, :].rearrange("p u (a n) -> p u a n", n=1 << k)
                        vec.wait_ge(*PE[f"P{k}_{g}"])
                        vec.tensor_tensor(pm, half_bank(g, k, n), mask[:, None, :, :].broadcast_to([P, n, 64 >> k, 1 << k]),
                                          ALU.mult).then_inc(*VEC(f"P{k}_{g}"))
                        if k == 0:
                            vec.wait_ge(*VEC[f"P0_{g}"])
                            vec.wait_ge(*POOL[f"I{g}"])
                            vec.tensor_tensor(side(X[:, us, :], k, g), side(X[:, us, :], k, g), pm, ALU.subtract).then_inc(*VEC(f"X0_{g}"))
                    if k > 0:
                        for g in range(2):
                            us = slice(n * g, n * g + n)
                            vec.wait_ge(*PE[f"Xd{k}_{g}"])
                            vec.tensor_tensor(side(X[:, us, :], k, g), side(X[:, us, :], k, g), half_bank(2 + g, k, n),
                                              ALU.subtract).then_inc(*VEC(f"X{k}_{g}"))

            def invert_scalar(act, n, turn_bank, Y):
                for k in range(NLEV):
                    for g in range(2):
                        act.wait_ge(*PE[f"Y{k}_{g}"])
                        banks = ps[:, turn_bank(g):turn_bank(g) + (n + 3) // 4, :].rearrange("p b n -> p (b n)")[:, 0:n * P]
                        act.copy(Y[:, n * g:n * g + n, :].rearrange("p u n -> p (u n)"), banks).then_inc(*ACT(f"Y{k}_{g}"))

            def invert_pool(pool, n, X):
                for g in range(2):
                    pool.tensor_copy(X[:, n * g:n * g + n, :], rep(ident, n)).then_inc(*POOL(f"I{g}"))

            with ExitStack() as st:
                rw = sbuf(st, "rw", [P, 7, SEQ])
                dec = sbuf(st, "dec", [P, 2, 2, SEQ])
                kmod = sbuf(st, "kmod", [P, 2, 2, SEQ])
                bb = sbuf(st, "bb", [P, 2, 2, SEQ])
                bonus = sbuf(st, "bonus", [P, 2, SEQ])
                with ExitStack() as st2:
                    wc = sbuf(st2, "w_cols", [P, KD, P])
                    xp = sbuf(st2, "x_pad", [P, SEQ + 4])
                    acc = sbuf(st2, "acc", [P, SEQ])
                    mu0 = sbuf(st2, "mu0", [P, 7])
                    load_columns(wc, COL_RW + 6 * P)
                    begin("rw_zero")
                    with nc.Block() as block:
                        @block.vector
                        def _(vec):
                            vec.memset(xp[:, :], 0.0).then_inc(*VEC("pad"))
                            mu = par("mu").rearrange("p (i c) -> p i c", c=2)
                            vec.tensor_tensor(mu0[:, :], mu[:, :, 0], mu[:, :, 1], ALU.add).then_inc(*VEC("mu_sum"))
                            vec.wait_ge(*VEC["mu_sum"])
                            vec.tensor_scalar(mu0[:, :], mu0[:, :], -1.0, 1.0, ALU.mult, ALU.add).then_inc(*VEC("mu0"))
                    clear()
                    with nc.Fori(0, 7) as i:
                        begin("rw_proj")
                        with nc.Block() as block:
                            @block.tensor
                            def _(pe):
                                project_tensor(pe, wc)

                            @block.scalar
                            def _(act):
                                project_copy(act, xp)

                            @block.sync
                            def _(sp):
                                sp.wait_ge(*PE["proj1"])
                                sp.dma_start(wc[:, :, :], w_rows(w_in[:, ds((6 - i) * P + (COL_RW - P), P)])).then_inc(*DMA("w_cols"))
                                sp.wait_ge(*DMA["w_cols"])

                            @block.vector
                            def _(vec):
                                vec.wait_ge(*ACT["proj1"])
                                vec.tensor_scalar(acc[:, :], xp[:, 2:2 + SEQ], mu0[:, ds(6 - i, 1)], None, ALU.mult).then_inc(*VEC("centre"))
                                vec.wait_ge(*VEC["centre"])
                                mu_at = P_AT["mu"][0]
                                vec.scalar_tensor_tensor(out=acc[:, :], in0=xp[:, 1:1 + SEQ], scalar=params[:, ds((6 - i) * 2 + mu_at, 1)],
                                                         in1=acc[:, :], op0=ALU.mult, op1=ALU.add).then_inc(*VEC("before"))
                                vec.wait_ge(*VEC["before"])
                                vec.scalar_tensor_tensor(out=rw[:, ds(6 - i, 1), :], in0=xp[:, 3:3 + SEQ],
                                                         scalar=params[:, ds((6 - i) * 2 + (mu_at + 1), 1)],
                                                         in1=acc[:, :], op0=ALU.mult, op1=ALU.add).then_inc(*VEC("after"))
                        clear()

                begin("rw_feat")
                with ExitStack() as st2, nc.Block() as block:
                    th = sbuf(st2, "th", [64, SEQ])
                    kx = sbuf(st2, "kx", [P, 2, SEQ])
                    a_all = sbuf(st2, "a_all", [P, 2, 2, SEQ])
                    sq = sbuf(st2, "sq_f", [P, SEQ])
                    ksum = sbuf(st2, "ksum", [P, SEQ])
                    omka = sbuf(st2, "omka", [P, 2])
                    w2a2 = sbuf(st2, "w2a2", [P, 2, RW])
                    PAIRS = [(e, m) for e in range(2) for m in range(2)]

                    @block.sync
                    def _(sp):
                        sp.dma_start(w2a2[:, :, :], io["w2a2"][ds(L, 1)].rearrange("a p e n -> (a p) e n")).then_inc(*DMA("w2a2"))

                    @block.tensor
                    def _(pe):
                        pe.wait_ge(*DMA["w2a2"])
                        pe.wait_ge(*ACT["tanh"])
                        for n, (e, m) in enumerate(PAIRS):
                            if n:
                                pe.wait_ge(*ACT[f"dec{n - 1}"])
                            for b in range(2):
                                t = slice(b * 512, (b + 1) * 512)
                                q = pe.matmul(ps[:, b, :], lhsT=w2a2[0:64, e, m * P:(m + 1) * P], rhs=th[:, t], start=True, stop=True)
                            q.then_inc(*PE(f"dec{n}"))
                            if n:
                                pe.wait_ge(*ACT[f"rate{n - 1}"])
                            for b in range(2):
                                t = slice(b * 512, (b + 1) * 512)
                                q = pe.matmul(ps[:, 2 + b, :], lhsT=w2a2[64:128, e, m * P:(m + 1) * P], rhs=rw[64:128, 6, t],
                                              start=True, stop=True)
                            q.then_inc(*PE(f"rate{n}"))
                        for m in range(2):
                            pe.wait_ge(*VEC[f"sq{m}"])
                            if m:
                                pe.wait_ge(*ACT["kk_ln0"])
                            for b in range(2):
                                q = pe.matmul(ps[:, 4 + b, :], lhsT=blk, rhs=sq[:, b * 512:(b + 1) * 512], start=True, stop=True)
                            q.then_inc(*PE(f"sumsq{m}"))

                    @block.scalar
                    def _(act):
                        act.activation(th[:, :], rw[0:64, 6, :], FN.Tanh).then_inc(*ACT("tanh"))
                        for n, (e, m) in enumerate(PAIRS):
                            c = P_AT["w0"][0] + 2 * e + m
                            act.wait_ge(*PE[f"dec{n}"])
                            act.activation(dec[:, e, m, :].rearrange("p (b n) -> p b n", b=2), ps[:, 0:2, :], FN.Sigmoid,
                                           bias=params[:, c:c + 1]).then_inc(*ACT(f"dec{n}"))
                            c = P_AT["a0"][0] + 2 * e + m
                            act.wait_ge(*PE[f"rate{n}"])
                            act.activation(a_all[:, e, m, :].rearrange("p (b n) -> p b n", b=2), ps[:, 2:4, :], FN.Sigmoid,
                                           bias=params[:, c:c + 1]).then_inc(*ACT(f"rate{n}"))
                        act.wait_ge(*ACT["dec3"])
                        act.activation(dec[:, :, :, :], dec[:, :, :, :], FN.Exp, scale=-float(np.exp(-0.5))).then_inc(*ACT("decay"))
                        for m in range(2):
                            act.wait_ge(*PE[f"sumsq{m}"])
                            if m:
                                act.wait_ge(*VEC["kk0"])
                            act.activation(ksum[:, :].rearrange("p (b n) -> p b n", b=2), ps[:, 4:6, :], FN.Ln,
                                           bias=cst("eps")).then_inc(*ACT(f"kk_ln{m}"))
                            act.wait_ge(*ACT[f"kk_ln{m}"])
                            act.activation(ksum[:, :], ksum[:, :], FN.Exp, scale=-0.5).then_inc(*ACT(f"kk_rs{m}"))

                    @block.vector
                    def _(vec):
                        vec.tensor_scalar(omka[:, :], par("k_a"), -1.0, 1.0, ALU.mult, ALU.add).then_inc(*VEC("omka"))
                        for m in range(2):
                            c = P_AT["k_k"][0] + m
                            vec.tensor_scalar(kx[:, m, :], rw[:, 2 + m, :], params[:, c:c + 1], None, ALU.mult).then_inc(*VEC(f"kx{m}"))
                        for m in range(2):
                            vec.wait_ge(*VEC[f"kx{m}"])
                            if m:
                                vec.wait_ge(*PE["sumsq0"])
                            vec.tensor_tensor(sq[:, :], kx[:, m, :], kx[:, m, :], ALU.mult).then_inc(*VEC(f"sq{m}"))
                        for n, (e, m) in enumerate(PAIRS):
                            c = P_AT["k_a"][0] + m
                            vec.wait_ge(*ACT[f"rate{n}"])
                            vec.wait_ge(*VEC["omka"])
                            vec.tensor_scalar(kmod[:, e, m, :], a_all[:, e, m, :], params[:, c:c + 1], omka[:, m:m + 1],
                                              ALU.mult, ALU.add).then_inc(*VEC(f"kf{n}"))
                            vec.wait_ge(*VEC[f"kf{n}"])
                            vec.tensor_tensor(kmod[:, e, m, :], kmod[:, e, m, :], rw[:, 2 + m, :], ALU.mult).then_inc(*VEC(f"km{n}"))
                        for m in range(2):
                            c = P_AT["r_k"][0] + m
                            vec.wait_ge(*VEC[f"km{2 + m}"])
                            vec.tensor_tensor(bonus[:, m, :], kmod[:, 0, m, :], kmod[:, 1, m, :], ALU.add).then_inc(*VEC(f"bo{m}a"))
                            vec.wait_ge(*VEC[f"bo{m}a"])
                            vec.scalar_tensor_tensor(out=bonus[:, m, :], in0=bonus[:, m, :], scalar=0.5, in1=rw[:, m, :],
                                                     op0=ALU.mult, op1=ALU.mult).then_inc(*VEC(f"bo{m}b"))
                            vec.wait_ge(*VEC[f"bo{m}b"])
                            vec.tensor_scalar(bonus[:, m, :], bonus[:, m, :], params[:, c:c + 1], None, ALU.mult).then_inc(*VEC(f"bo{m}"))
                        for m in range(2):
                            vec.wait_ge(*ACT[f"kk_rs{m}"])
                            vec.tensor_tensor(rw[:, 2 + m, :], kx[:, m, :], ksum[:, :], ALU.mult).then_inc(*VEC(f"kk{m}"))
                            for e in range(2):
                                vec.wait_ge(*VEC[f"kk{m}"])
                                vec.tensor_tensor(bb[:, e, m, :], a_all[:, e, m, :], rw[:, 2 + m, :], ALU.mult).then_inc(*VEC(f"b{e}{m}"))
                clear()

                with ExitStack() as st2:
                    dch = sbuf(st2, "dch", [P, 4, P])
                    vs = sbuf(st2, "vs", [P, 4, P])
                    bs = sbuf(st2, "bs", [P, 2, P])
                    pp = sbuf(st2, "pp", [P, 4, P + 1])
                    pc = sbuf(st2, "pc", [P, 4, P + 1])
                    ip = sbuf(st2, "ip", [P, 4, P + 1])
                    cinv = sbuf(st2, "cinv", [P, 4])
                    wcm = sbuf(st2, "wcm", [P, 4])
                    KR = sbuf(st2, "KR", [P, 4, 2, P])
                    KB = sbuf(st2, "KB", [P, 4, 2, P])
                    KBt = sbuf(st2, "KBt", [P, 4, 2, P])
                    vt = sbuf(st2, "vt", [P, 4, P])
                    MT = sbuf(st2, "MT", [P, 8, 4, P])
                    X = sbuf(st2, "X", [P, 8, P])
                    Y = sbuf(st2, "Y", [P, 8, P])
                    Pm = sbuf(st2, "Pm", [P, 8, P // 2])
                    Rs = sbuf(st2, "Rs", [P, 4, P])
                    sa = sbuf(st2, "sa", [P, 4, P])
                    yo = sbuf(st2, "yo", [P, 3, RW])
                    Z = sbuf(st2, "Z", [P, 4, P])
                    Zc = sbuf(st2, "Zc", [P, 4, P])
                    Zt = sbuf(st2, "Zt", [P, 4, P])
                    bon = sbuf(st2, "bon", [P, 4])
                    zero = sbuf(st2, "zero", [P, P])
                    begin("rw_state")
                    with nc.Block() as block:
                        @block.vector
                        def _(vec):
                            vec.memset(Z[:, :, :], 0.0).then_inc(*VEC("z"))
                            vec.memset(zero[:, :], 0.0).then_inc(*VEC("zero"))
                            vec.memset(pp[:, :, :], 1.0).then_inc(*VEC("edges"))
                    clear()
                    MID = P // 2
                    with nc.Fori(0, NT) as c:
                        begin("rw_chunk")
                        with nc.Block() as block:
                            off = [c * P, (NT - 1 - c) * P]

                            @block.scalar
                            def _(act):
                                for e in range(2):
                                    act.copy(dch[:, 2 * e:2 * e + 2, :], dec[:, e, :, ds(off[e], P)]).then_inc(*ACT(f"dch{e}"))
                                for e in range(2):
                                    act.copy(vs[:, 2 * e:2 * e + 2, :], rw[:, 4:6, ds(off[e], P)]).then_inc(*ACT(f"vs{e}"))
                                act.copy(bs[:, :, :], bonus[:, :, ds(off[0], P)]).then_inc(*ACT("bs"))
                                act.wait_ge(*PE["vt"])
                                act.copy(vt[:, :, :], ps[:, 6, :].rearrange("p (u n) -> p u n", u=4)).then_inc(*ACT("vt"))
                                for b in range(2):
                                    act.wait_ge(*PE[f"KBt{b}"])
                                    act.copy(KBt[:, 2 * b:2 * b + 2, :, :].rearrange("p a k n -> p (a k) n"),
                                             ps[:, 6 + b, :].rearrange("p (u n) -> p u n", u=4)).then_inc(*ACT(f"KBt{b}"))
                                act.wait_ge(*PE["bon"])
                                act.copy(bon[:, :], ps[:, 7, 0:4]).then_inc(*ACT("bon"))
                                invert_scalar(act, 4, lambda g: 4 + g, Y)
                                act.wait_ge(*PE["R"])
                                act.mul(Rs[:, :, :], ps[:, 6, :].rearrange("p (u n) -> p u n", u=4), -1.0).then_inc(*ACT("R"))
                                act.wait_ge(*PE["sa"])
                                act.copy(sa[:, :, :], ps[:, 7, :].rearrange("p (u n) -> p u n", u=4)).then_inc(*ACT("sa"))
                                act.wait_ge(*PE["y"])
                                act.copy(yo[:, 0:2, :], ps[:, 6, :].rearrange("p (u n) -> p u n", u=2)).then_inc(*ACT("y"))

                            @block.vector
                            def _(vec):
                                for e in range(2):
                                    vec.wait_ge(*ACT[f"dch{e}"])
                                    for m in range(2):
                                        u = 2 * e + m
                                        if e == 0:
                                            o, d = pp[:, u, 1:P + 1], dch[:, u, :]
                                        else:
                                            o, d = pp[:, u, 0:P][:, ::-1], dch[:, u, :][:, ::-1]
                                        q = vec.tensor_tensor_scan(o, d, zero[:, :], 1.0, ALU.mult, ALU.add)
                                    q.then_inc(*VEC(f"scan{e}"))
                                vec.wait_ge(*VEC["scan0"])
                                vec.wait_ge(*VEC["scan1"])
                                vec.reciprocal(cinv[:, :], pp[:, :, MID]).then_inc(*VEC("cinv"))
                                vec.wait_ge(*VEC["cinv"])
                                vec.tensor_tensor(pc[:, :, :], pp[:, :, :], col(cinv[:, :], P + 1), ALU.mult).then_inc(*VEC("pc"))
                                vec.wait_ge(*VEC["pc"])
                                vec.reciprocal(ip[:, :, :], pc[:, :, :]).then_inc(*VEC("ip"))
                                for e in range(2):
                                    u = slice(2 * e, 2 * e + 2)
                                    inc, exc = (slice(1, P + 1), slice(0, P)) if e == 0 else (slice(0, P), slice(1, P + 1))
                                    vec.tensor_tensor(KR[:, u, 0, :], rw[:, 2:4, ds(off[e], P)], pc[:, u, exc], ALU.mult)
                                    vec.tensor_tensor(KR[:, u, 1, :], rw[:, 0:2, ds(off[e], P)], pc[:, u, inc], ALU.mult).then_inc(*VEC(f"KR{e}"))
                                    vec.wait_ge(*VEC["ip"])
                                    vec.tensor_tensor(KB[:, u, 0, :], bb[:, e, :, ds(off[e], P)], ip[:, u, inc], ALU.mult)
                                    vec.tensor_tensor(KB[:, u, 1, :], kmod[:, e, :, ds(off[e], P)], ip[:, u, inc], ALU.mult).then_inc(*VEC(f"KB{e}"))
                                vec.tensor_tensor(Zc[:, :, :], Z[:, :, :], col(pp[:, :, MID], P), ALU.mult).then_inc(*VEC("Zc"))
                                for e in range(2):
                                    for n in range(4):
                                        u = 4 * e + n
                                        vec.wait_ge(*PE[f"pairs{u}"])
                                        bank = ps[:, u % 6, :].rearrange("p (a b n) -> p a b n", a=2, b=2)
                                        before = cst("bef" if e == 0 else "aft")
                                        upto = cst("tri_f" if e == 0 else "tri_b")
                                        M4 = MT[:, u, :, :].rearrange("p (a b) n -> p a b n", a=2)
                                        vec.tensor_tensor(M4[:, :, 0, :], bank[:, :, 0, :], rep(before, 2), ALU.mult)
                                        q = vec.tensor_tensor(M4[:, :, 1, :], bank[:, :, 1, :], rep(upto, 2), ALU.mult)
                                        q.then_inc(*VEC(f"MT{u}" if n < 3 else f"AT{e}"))
                                invert_vector(vec, 4, X, Pm)
                                vec.wait_ge(*ACT["bon"])
                                vec.tensor_tensor(yo[:, 2, :].rearrange("p (h n) -> p h n", h=4),
                                                  vt[:, 0:2, :].rearrange("p m (h n) -> p (m h) n", h=2), col(bon[:, :], RD),
                                                  ALU.mult).then_inc(*VEC("bonus"))
                                for e in range(2):
                                    at = P if e == 0 else 0
                                    q = vec.tensor_tensor(wcm[:, 2 * e:2 * e + 2], pp[:, 2 * e:2 * e + 2, at], cinv[:, 2 * e:2 * e + 2], ALU.mult)
                                q.then_inc(*VEC("wcm"))
                                for e in range(2):
                                    at = P if e == 0 else 0
                                    u = slice(2 * e, 2 * e + 2)
                                    q = vec.tensor_tensor(Z[:, u, :], Z[:, u, :], col(pp[:, u, at], P), ALU.mult)
                                q.then_inc(*VEC("Zdec"))
                                vec.wait_ge(*PE["Zn"])
                                vec.tensor_tensor(Zt[:, :, :], ps[:, 4, :].rearrange("p (u n) -> p u n", u=4), rep(blk, 4), ALU.mult).then_inc(*VEC("Zt"))
                                vec.wait_ge(*VEC["wcm"])
                                vec.wait_ge(*VEC["Zt"])
                                vec.tensor_tensor(Zt[:, :, :], Zt[:, :, :], col(wcm[:, :], P), ALU.mult).then_inc(*VEC("Zt2"))
                                vec.wait_ge(*VEC["Zt2"])
                                vec.tensor_tensor(Z[:, :, :], Z[:, :, :], Zt[:, :, :], ALU.add).then_inc(*VEC("Z"))

                            @block.gpsimd
                            def _(pool):
                                invert_pool(pool, 4, X)

                            @block.tensor
                            def _(pe):
                                pe.wait_ge(*ACT["vs1"])
                                for u in range(4):
                                    q = pe.transpose(ps[:, 6, u * P:(u + 1) * P], vs[:, u, :], ident)
                                q.then_inc(*PE("vt"))
                                for e in range(2):
                                    pe.wait_ge(*VEC[f"KR{e}"])
                                    pe.wait_ge(*VEC[f"KB{e}"])
                                    for m in range(2):
                                        for h in range(2):
                                            u, c0 = 4 * e + 2 * m + h, slice(64 * h, 64 * h + 64)
                                            if u >= 6:
                                                pe.wait_ge(*VEC[f"MT{u - 6}"])
                                            for kb in range(2):
                                                q = pe.matmul(ps[:, u % 6, 256 * kb:256 * kb + 256], lhsT=KB[c0, 2 * e + m, kb, :],
                                                              rhs=KR[c0, 2 * e + m, :, :], start=True, stop=True)
                                            q.then_inc(*PE(f"pairs{u}"))
                                for b in range(2):
                                    pe.wait_ge(*ACT["vt"])
                                    for u in range(2):
                                        for kb in range(2):
                                            q = pe.transpose(ps[:, 6 + b, (2 * u + kb) * P:(2 * u + kb + 1) * P], KB[:, 2 * b + u, kb, :], ident)
                                    q.then_inc(*PE(f"KBt{b}"))
                                pe.wait_ge(*ACT["KBt1"])
                                pe.wait_ge(*ACT["bs"])
                                for m in range(2):
                                    q = pe.matmul(ps[:, 7, 2 * m:2 * m + 2], lhsT=bs[:, m, :], rhs=cst("sel"), start=True, stop=True)
                                q.then_inc(*PE("bon"))
                                pe.wait_ge(*VEC["AT1"])
                                invert_tensor(pe, 4, ("AT0", "AT1"), lambda g: 4 + g, lambda u: MT[:, u, 0, :], X, Y, Pm)
                                pe.wait_ge(*VEC["Zc"])
                                pe.wait_ge(*ACT["bon"])
                                for em in range(4):
                                    pe.matmul(ps[:, 6, em * P:(em + 1) * P], lhsT=KR[:, em, 0, :], rhs=Zc[:, em, :], start=True, stop=False,
                                              skip_group_check=True)
                                    for h in range(2):
                                        n = slice(em * P + 64 * h, em * P + 64 * h + 64)
                                        q = pe.matmul(ps[:, 6, n], lhsT=MT[:, 2 * em + h, 2, :], rhs=vt[:, em, 64 * h:64 * h + 64],
                                                      start=False, stop=True, skip_group_check=True)
                                q.then_inc(*PE("R"))
                                pe.wait_ge(*ACT[f"Y{NLEV - 1}_1"])
                                pe.wait_ge(*ACT["R"])
                                for u in range(8):
                                    n = slice(64 * u, 64 * u + 64)
                                    q = pe.matmul(ps[:, 7, n], lhsT=Y[:, u, :], rhs=Rs[:, u // 2, 64 * (u % 2):64 * (u % 2) + 64], start=True, stop=True)
                                q.then_inc(*PE("sa"))
                                pe.wait_ge(*ACT["sa"])
                                for em in range(4):
                                    pe.matmul(ps[:, 6, em * P:(em + 1) * P], lhsT=KR[:, em, 1, :], rhs=Zc[:, em, :], start=True, stop=False,
                                              skip_group_check=True)
                                    for h in range(2):
                                        n, hs = slice(em * P + 64 * h, em * P + 64 * h + 64), slice(64 * h, 64 * h + 64)
                                        pe.matmul(ps[:, 6, n], lhsT=MT[:, 2 * em + h, 1, :], rhs=sa[:, em, hs], start=False, stop=False,
                                                  skip_group_check=True)
                                        q = pe.matmul(ps[:, 6, n], lhsT=MT[:, 2 * em + h, 3, :], rhs=vt[:, em, hs], start=False, stop=True,
                                                      skip_group_check=True)
                                q.then_inc(*PE("y"))
                                for em in range(4):
                                    pe.matmul(ps[:, 4, em * P:(em + 1) * P], lhsT=KBt[:, em, 0, :], rhs=sa[:, em, :], start=True, stop=False)
                                    q = pe.matmul(ps[:, 4, em * P:(em + 1) * P], lhsT=KBt[:, em, 1, :], rhs=vt[:, em, :], start=False, stop=True)
                                q.then_inc(*PE("Zn"))

                            @block.sync
                            def _(sp):
                                sp.wait_ge(*VEC["bonus"])
                                sp.dma_start(rwkv_hbm[2, ds(off[0], P), :], yo[:, 2, :]).then_inc(*DMA("y_out"))
                                sp.wait_ge(*ACT["y"])
                                for e in range(2):
                                    sp.dma_start(rwkv_hbm[e, ds(off[e], P), :], yo[:, e, :]).then_inc(*DMA("y_out"))
                                sp.wait_ge(*DMA["y_out"])
                        clear()

            with ExitStack() as st:
                gq = sbuf(st, "gq", [P, 9, SEQ])
                with ExitStack() as st2:
                    wc = sbuf(st2, "w_cols_g", [P, KD, P])
                    xp = sbuf(st2, "x_pad_g", [P, SEQ + 4])
                    acc = sbuf(st2, "acc_g", [P, SEQ])
                    act_out = sbuf(st2, "act_out", [P, SEQ])
                    sq = sbuf(st2, "sq_g", [P, SEQ])
                    rs = sbuf(st2, "rs_g", [P, SEQ])
                    load_columns(wc, COL_GDN)
                    begin("gdn_zero")
                    with nc.Block() as block:
                        @block.vector
                        def _(vec):
                            vec.memset(xp[:, :], 0.0).then_inc(*VEC("pad"))
                    clear()
                    for first_tile, last_tile, normed in ((0, 6, True), (6, 9, False)):
                        with nc.Fori(first_tile, last_tile) as i:
                            begin(f"gdn_proj{first_tile}")
                            with nc.Block() as block:
                                @block.tensor
                                def _(pe):
                                    project_tensor(pe, wc)
                                    if normed:
                                        for b in range(2):
                                            pe.wait_ge(*POOL[f"sq{b}"])
                                            pe.matmul(ps[:, 2 + b, :], lhsT=blk, rhs=sq[:, b * 512:(b + 1) * 512], start=True,
                                                      stop=True).then_inc(*PE(f"sumsq{b}"))

                                @block.sync
                                def _(sp):
                                    sp.wait_ge(*PE["proj1"])
                                    sp.dma_start(wc[:, :, :], w_rows(w_in[:, ds(i * P + (COL_GDN + P), P)])).then_inc(*DMA("w_cols"))
                                    sp.wait_ge(*DMA["w_cols"])

                                @block.scalar
                                def _(act):
                                    project_copy(act, xp)
                                    act.wait_ge(*VEC[f"tap{CONV - 1}"])
                                    if not normed:
                                        act.activation(gq[:, ds(i, 1), :], acc[:, :], FN.Silu).then_inc(*ACT("silu"))
                                    else:
                                        act.activation(act_out[:, :], acc[:, :], FN.Silu).then_inc(*ACT("silu"))
                                        for b in range(2):
                                            t = slice(b * 512, (b + 1) * 512)
                                            act.wait_ge(*PE[f"sumsq{b}"])
                                            act.activation(rs[:, t], ps[:, 2 + b, :], FN.Ln, bias=cst("eps")).then_inc(*ACT(f"ln{b}"))
                                        for b in range(2):
                                            t = slice(b * 512, (b + 1) * 512)
                                            act.wait_ge(*ACT[f"ln{b}"])
                                            act.activation(rs[:, t], rs[:, t], FN.Exp, scale=-0.5).then_inc(*ACT(f"rs{b}"))

                                @block.vector
                                def _(vec):
                                    vec.wait_ge(*ACT["proj1"])
                                    at = P_AT["conv"][0]
                                    vec.tensor_scalar(acc[:, :], xp[:, 0:SEQ], params[:, ds(i * CONV + at, 1)], None, ALU.mult).then_inc(*VEC("tap0"))
                                    for n in range(1, CONV):
                                        vec.wait_ge(*VEC[f"tap{n - 1}"])
                                        vec.scalar_tensor_tensor(out=acc[:, :], in0=xp[:, n:n + SEQ], scalar=params[:, ds(i * CONV + (at + n), 1)],
                                                                 in1=acc[:, :], op0=ALU.mult, op1=ALU.add).then_inc(*VEC(f"tap{n}"))
                                    if normed:
                                        vec.wait_ge(*ACT["rs1"])
                                        vec.tensor_tensor(gq[:, ds(i, 1), :], act_out[:, :], rs[:, :], ALU.mult).then_inc(*VEC("normed"))

                                @block.gpsimd
                                def _(pool):
                                    if normed:
                                        pool.wait_ge(*ACT["silu"])
                                        for b in range(2):
                                            t = slice(b * 512, (b + 1) * 512)
                                            pool.tensor_tensor(sq[:, t], act_out[:, t], act_out[:, t], ALU.mult).then_inc(*POOL(f"sq{b}"))
                            clear()

                G2 = 2 * GH
                tm_ab = sbuf(st, "tm_ab", [P, NT, 2 * G2])
                gb = sbuf(st, "gb", [P, NT, 2, G2])
                begin("gdn_gates")
                with ExitStack() as st2, nc.Block() as block:
                    pre = sbuf(st2, "pre", [P, NT, G2])
                    mag = sbuf(st2, "mag", [P, NT, G2])
                    soft = sbuf(st2, "soft", [P, NT, G2])
                    rate = sbuf(st2, "rate", [P, G2])

                    @block.sync
                    def _(sp):
                        sp.dma_start(tm_ab[:, :, :], tm_hbm[:, 0:2 * G2].rearrange("(t p) n -> p t n", p=P)).then_inc(*DMA("ab"))
                        sp.wait_ge(*DMA["ab"])

                    @block.vector
                    def _(vec):
                        vec.wait_ge(*DMA["ab"])
                        vec.tensor_tensor(pre[:, :, :], tm_ab[:, :, 0:G2], rep(par("dt"), NT), ALU.add).then_inc(*VEC("pre"))
                        vec.wait_ge(*VEC["pre"])
                        vec.scalar_tensor_tensor(out=mag[:, :, :], in0=pre[:, :, :], scalar=-1.0, in1=pre[:, :, :], op0=ALU.mult,
                                                 op1=ALU.max).then_inc(*VEC("mag"))
                        vec.wait_ge(*ACT["soft"])
                        vec.scalar_tensor_tensor(out=soft[:, :, :], in0=pre[:, :, :], scalar=0.0, in1=soft[:, :, :], op0=ALU.max,
                                                 op1=ALU.add).then_inc(*VEC("soft"))
                        vec.wait_ge(*VEC["soft"])
                        vec.wait_ge(*ACT["rate"])
                        vec.tensor_tensor(soft[:, :, :], soft[:, :, :], rep(rate[:, :], NT), ALU.mult).then_inc(*VEC("soft2"))
                        vec.wait_ge(*VEC["soft2"])
                        vec.tensor_scalar(gb[:, :, 0, :], soft[:, :, :], -1.0, None, ALU.mult).then_inc(*VEC("g"))

                    @block.scalar
                    def _(act):
                        act.activation(rate[:, :], par("a_log"), FN.Exp).then_inc(*ACT("rate"))
                        act.wait_ge(*VEC["mag"])
                        act.activation(soft[:, :, :], mag[:, :, :], FN.Exp, scale=-1.0).then_inc(*ACT("exp"))
                        act.wait_ge(*ACT["exp"])
                        act.activation(soft[:, :, :], soft[:, :, :], FN.Ln, bias=1.0).then_inc(*ACT("soft"))
                        act.activation(gb[:, :, 1, :], tm_ab[:, :, G2:2 * G2], FN.Sigmoid).then_inc(*ACT("beta"))
                clear()

                with ExitStack() as st2:
                    kq = sbuf(st2, "kq", [P, 6, 2, P])
                    vs = sbuf(st2, "vs_g", [P, 6, P])
                    gch = sbuf(st2, "gch", [P, 2, 2, GH])
                    Gm = sbuf(st2, "Gm", [P, 12, P])
                    DT = sbuf(st2, "DT", [P, 12, P])
                    DTb = sbuf(st2, "DTb", [P, 12, P])
                    gx = sbuf(st2, "gx", [P, 2, 3, GH])
                    AT = sbuf(st2, "AT", [P, 12, P])
                    PT = sbuf(st2, "PT", [P, 12, P])
                    kt = sbuf(st2, "kt", [P, 2, GW])
                    vt = sbuf(st2, "vt_g", [P, 2, GW])
                    X = sbuf(st2, "X_g", [P, 12, P])
                    Y = sbuf(st2, "Y_g", [P, 12, P])
                    Pm = sbuf(st2, "Pm_g", [P, 12, P // 2])
                    R = sbuf(st2, "R_g", [P, 2, GW])
                    U = sbuf(st2, "U_g", [P, 2, GW])
                    Ur = sbuf(st2, "Ur_g", [P, 2, GW])
                    o = sbuf(st2, "o_g", [P, 2, GW])
                    S = sbuf(st2, "S_g", [P, 6, P])
                    St = sbuf(st2, "St_g", [P, 6, P])
                    begin("gdn_state")
                    with nc.Block() as block:
                        @block.vector
                        def _(vec):
                            vec.memset(S[:, :, :], 0.0).then_inc(*VEC("s"))
                    clear()

                    def heads(ap):
                        return ap.rearrange("p (h n) -> p h n", n=GD)

                    def units(b0, n, w):
                        return ps[:, b0:b0 + (n * w + 511) // 512, :].rearrange("p b n -> p (b n)")[:, 0:n * w].rearrange("p (u n) -> p u n", u=n)

                    with nc.Fori(0, NT) as c:
                        begin("gdn_chunk")
                        with nc.Block() as block:
                            chunk = [c, NT - 1 - c]
                            off = [c * P, (NT - 1 - c) * P]

                            @block.scalar
                            def _(act):
                                act.copy(kq[:, 0:3, 0, :], gq[:, 3:6, ds(off[0], P)])
                                act.copy(kq[:, 0:3, 1, :], gq[:, 0:3, ds(off[0], P)])
                                act.copy(vs[:, 0:3, :], gq[:, 6:9, ds(off[0], P)]).then_inc(*ACT("v0"))
                                for e in range(2):
                                    act.wait_ge(*PE[f"diff{e}"])
                                    act.activation(DT[:, 6 * e:6 * e + 6, :], units(2 * e, 6, P), FN.Exp).then_inc(*ACT(f"DT{e}"))
                                act.wait_ge(*PE["small"])
                                act.activation(gx[:, :, :, :].rearrange("p e a h -> p (e a h)"), ps[:, 4, 0:36], FN.Exp).then_inc(*ACT("gx"))
                                for e in range(2):
                                    act.wait_ge(*PE[f"turned{e}"])
                                    act.copy(kt[:, e, :], ps[:, 6, 0:GW]).then_inc(*ACT(f"kt{e}"))
                                    act.copy(vt[:, e, :], ps[:, 7, 0:GW]).then_inc(*ACT(f"vt{e}"))
                                invert_scalar(act, 6, lambda g: 4 + 2 * g, Y)

                            @block.gpsimd
                            def _(pool):
                                pool.wait_ge(*VEC["gch"])
                                pool.tensor_tensor(Gm[:, 6:12, :], col(gch[:, 1, 0, :], P), rep(cst("tri_b"), 6), ALU.mult).then_inc(*POOL("Gm1"))
                                pool.wait_ge(*ACT["DT1"])
                                pool.tensor_tensor(DT[:, 6:12, :], DT[:, 6:12, :], rep(cst("tri_b"), 6), ALU.mult).then_inc(*POOL("DTm1"))
                                invert_pool(pool, 6, X)

                            @block.tensor
                            def _(pe):
                                for e in range(2):
                                    behind = cst("aft" if e == 0 else "bef")
                                    pe.wait_ge(*(POOL["Gm1"] if e else VEC["Gm0"]))
                                    g = Gm[:, 6 * e:6 * e + 6, :].rearrange("p u n -> p (u n)")
                                    pe.matmul(ps[:, 2 * e, :], lhsT=behind, rhs=g[:, 0:512], start=True, stop=True)
                                    pe.matmul(ps[:, 2 * e + 1, 0:256], lhsT=behind, rhs=g[:, 512:768], start=True, stop=True).then_inc(*PE(f"diff{e}"))
                                for e in range(2):
                                    mats = (cst("tri_f"), cst("aft"), ones) if e == 0 else (cst("tri_b"), cst("bef"), ones)
                                    for n, mat in enumerate(mats):
                                        q = pe.matmul(ps[:, 4, (3 * e + n) * GH:(3 * e + n + 1) * GH], lhsT=mat, rhs=gch[:, e, 0, :], start=True, stop=True)
                                q.then_inc(*PE("small"))
                                for e in range(2):
                                    pe.wait_ge(*(VEC["v1"] if e else ACT["v0"]))
                                    if e:
                                        pe.wait_ge(*ACT["vt0"])
                                    for m in range(3):
                                        pe.transpose(ps[:, 6, m * P:(m + 1) * P], kq[:, 3 * e + m, 0, :], ident)
                                        q = pe.transpose(ps[:, 7, m * P:(m + 1) * P], vs[:, 3 * e + m, :], ident)
                                    q.then_inc(*PE(f"turned{e}"))
                                pe.wait_ge(*ACT["gx"])
                                for h in range(2):
                                    c0 = slice(64 * h, 64 * h + 64)
                                    for em in range(6):
                                        q = pe.matmul(ps[:, 3 * h + em // 2, 256 * (em % 2):256 * (em % 2) + 256], lhsT=kq[c0, em, 0, :],
                                                      rhs=kq[c0, em, :, :], start=True, stop=True)
                                    q.then_inc(*PE(f"pairs{h}"))
                                pe.wait_ge(*ACT["vt1"])
                                for e in range(2):
                                    for m in range(3):
                                        q = pe.matmul(ps[:, 6 + e, m * P:(m + 1) * P], lhsT=kq[:, 3 * e + m, 0, :], rhs=S[:, 3 * e + m, :], start=True, stop=True)
                                q.then_inc(*PE("kS"))
                                pe.wait_ge(*VEC["PT1"])
                                pe.wait_ge(*VEC["gkS"])
                                invert_tensor(pe, 6, ("PT1", "PT1"), lambda g: 4 + 2 * g, lambda u: AT[:, u, :], X, Y, Pm)
                                pe.wait_ge(*VEC["R"])
                                pe.wait_ge(*ACT[f"Y{NLEV - 1}_1"])
                                for u in range(12):
                                    e, n = u // 6, slice(64 * (u % 6), 64 * (u % 6) + 64)
                                    q = pe.matmul(ps[:, 6 + e, n], lhsT=Y[:, u, :], rhs=R[:, e, n], start=True, stop=True)
                                q.then_inc(*PE("w"))
                                for e in range(2):
                                    for m in range(3):
                                        q = pe.matmul(ps[:, e, m * P:(m + 1) * P], lhsT=kq[:, 3 * e + m, 1, :], rhs=S[:, 3 * e + m, :], start=True, stop=True)
                                q.then_inc(*PE("qS"))
                                pe.wait_ge(*VEC["U"])
                                for u in range(12):
                                    e, n = u // 6, slice(64 * (u % 6), 64 * (u % 6) + 64)
                                    q = pe.matmul(ps[:, 2 + e, n], lhsT=PT[:, u, :], rhs=U[:, e, n], start=True, stop=True)
                                q.then_inc(*PE("PU"))
                                pe.wait_ge(*VEC["Ur"])
                                for e in range(2):
                                    for m in range(3):
                                        n = slice(m * P, (m + 1) * P)
                                        q = pe.matmul(ps[:, 4 + e, n], lhsT=kt[:, e, n], rhs=Ur[:, e, n], start=True, stop=True)
                                q.then_inc(*PE("Sn"))

                            @block.vector
                            def _(vec):
                                for e in range(2):
                                    q = vec.tensor_copy(gch[:, e, :, :], gb[:, ds(chunk[e], 1), :, GH * e:GH * e + GH])
                                q.then_inc(*VEC("gch"))
                                vec.wait_ge(*VEC["gch"])
                                vec.tensor_tensor(Gm[:, 0:6, :], col(gch[:, 0, 0, :], P), rep(cst("tri_f"), 6), ALU.mult).then_inc(*VEC("Gm0"))
                                vec.tensor_copy(kq[:, 3:6, 0, :], gq[:, 3:6, ds(off[1], P)])
                                vec.tensor_copy(kq[:, 3:6, 1, :], gq[:, 0:3, ds(off[1], P)])
                                vec.tensor_copy(vs[:, 3:6, :], gq[:, 6:9, ds(off[1], P)]).then_inc(*VEC("v1"))
                                vec.wait_ge(*ACT["DT0"])
                                vec.tensor_tensor(DT[:, 0:6, :], DT[:, 0:6, :], rep(cst("tri_f"), 6), ALU.mult).then_inc(*VEC("DTm0"))
                                for e in range(2):
                                    vec.wait_ge(*(POOL["DTm1"] if e else VEC["DTm0"]))
                                    vec.tensor_tensor(DTb[:, 6 * e:6 * e + 6, :], DT[:, 6 * e:6 * e + 6, :], col(gch[:, e, 1, :], P), ALU.mult).then_inc(*VEC(f"DTb{e}"))
                                for h in range(2):
                                    bank = units(3 * h, 12, P).rearrange("p (u k) n -> p u k n", k=2)
                                    vec.wait_ge(*PE[f"pairs{h}"])
                                    vec.wait_ge(*VEC["DTb1"])

                                    def of_head(ap):
                                        return ap.rearrange("p (u h) n -> p u h n", h=2)[:, :, h, :]
                                    vec.tensor_tensor(of_head(AT[:, :, :]), bank[:, :, 0, :], of_head(DTb[:, :, :]), ALU.mult)
                                    vec.scalar_tensor_tensor(out=of_head(PT[:, :, :]), in0=bank[:, :, 1, :], scalar=GD ** -0.5,
                                                             in1=of_head(DT[:, :, :]), op0=ALU.mult, op1=ALU.mult).then_inc(*VEC(f"PT{h}"))
                                vec.wait_ge(*PE["kS"])
                                for e in range(2):
                                    q = vec.tensor_tensor(heads(R[:, e, :]), heads(ps[:, 6 + e, 0:GW]), col(gx[:, e, 0, :], GD), ALU.mult)
                                q.then_inc(*VEC("gkS"))
                                vec.wait_ge(*VEC["gkS"])
                                vec.tensor_tensor(R[:, :, :], vt[:, :, :], R[:, :, :], ALU.subtract).then_inc(*VEC("R"))
                                invert_vector(vec, 6, X, Pm)
                                vec.wait_ge(*PE["w"])
                                for e in range(2):
                                    q = vec.tensor_tensor(heads(U[:, e, :]), heads(ps[:, 6 + e, 0:GW]), col(gch[:, e, 1, :], GD), ALU.mult)
                                q.then_inc(*VEC("U"))
                                vec.wait_ge(*VEC["U"])
                                for e in range(2):
                                    q = vec.tensor_tensor(heads(Ur[:, e, :]), heads(U[:, e, :]), col(gx[:, e, 1, :], GD), ALU.mult)
                                q.then_inc(*VEC("Ur"))
                                vec.wait_ge(*PE["qS"])
                                for e in range(2):
                                    q = vec.tensor_tensor(heads(o[:, e, :]), heads(ps[:, e, 0:GW]), col(gx[:, e, 0, :], GD), ALU.mult)
                                q.then_inc(*VEC("gqS"))
                                vec.wait_ge(*VEC["gqS"])
                                vec.wait_ge(*PE["PU"])
                                vec.scalar_tensor_tensor(out=o[:, :, :], in0=o[:, :, :], scalar=GD ** -0.5, in1=ps[:, 2:4, 0:GW],
                                                         op0=ALU.mult, op1=ALU.add).then_inc(*VEC("o"))
                                for e in range(2):
                                    su = S[:, 3 * e:3 * e + 3, :].rearrange("p m (h n) -> p (m h) n", h=2)
                                    q = vec.tensor_tensor(su, su, col(gx[:, e, 2, :], GD), ALU.mult)
                                q.then_inc(*VEC("Sdec"))
                                vec.wait_ge(*PE["Sn"])
                                for e in range(2):
                                    q = vec.tensor_tensor(St[:, 3 * e:3 * e + 3, :], ps[:, 4 + e, 0:GW].rearrange("p (m n) -> p m n", n=P), rep(blk, 3), ALU.mult)
                                q.then_inc(*VEC("St"))
                                vec.wait_ge(*VEC["St"])
                                vec.tensor_tensor(S[:, :, :], S[:, :, :], St[:, :, :], ALU.add).then_inc(*VEC("S"))

                            @block.sync
                            def _(sp):
                                sp.wait_ge(*VEC["o"])
                                for e in range(2):
                                    sp.dma_start(gdn_hbm[e, ds(off[e], P), :], o[:, e, :]).then_inc(*DMA("o_out"))
                                sp.wait_ge(*DMA["o_out"])
                        clear()

            with ExitStack() as st:
                qT = sbuf(st, "qT", [QK, MH, SEQ])
                kT = sbuf(st, "kT", [QK, MH, SEQ])
                V = sbuf(st, "V", [P, NT, MH, MV])
                with ExitStack() as st2:
                    wq = sbuf(st2, "w_uq", [P, 2, MH * QK])
                    wkv = sbuf(st2, "w_ukv", [P, MH * (NOPE + MV)])
                    begin("mla_load")
                    with nc.Block() as block:
                        @block.sync
                        def _(sp):
                            sp.dma_start(wq[:, 0, :], w_uq[0:P, :]).then_inc(*DMA("w_mla"))
                            sp.dma_start(wq[0:QR - P, 1, :], w_uq[P:QR, :]).then_inc(*DMA("w_mla"))
                            sp.dma_start(wkv[:, :], io["w_ukv"][ds(L, 1)].rearrange("a r n -> (a r) n")).then_inc(*DMA("w_mla"))
                            sp.wait_ge(*DMA["w_mla"])
                    clear()
                    lat = sbuf(st2, "lat", [P, QR + KVR + ROPE])
                    junk = sbuf(st2, "junk", [P, QR])
                    ss = sbuf(st2, "ss_m", [P, 2])
                    rs = sbuf(st2, "rs_m", [P, 2])
                    cn = sbuf(st2, "cn", [P, QR + KVR])
                    cT = sbuf(st2, "cT", [P, 3, P])
                    qk = sbuf(st2, "qk", [P, 2 * MH, QK])
                    tr = sbuf(st2, "tr", [P, 2, MH, ROPE])
                    tk = sbuf(st2, "tk", [P, 2, ROPE])
                    kr = sbuf(st2, "kr", [P, ROPE])
                    csn = sbuf(st2, "csn", [P, 2, ROPE // 2])
                    H2 = ROPE // 2
                    with nc.Fori(0, NT) as t:
                        begin("mla_up")
                        with nc.Block() as block:
                            @block.sync
                            def _(sp):
                                sp.dma_start(lat[:, :], tm_hbm[ds(t * P, P), 4 * GH:TM_W]).then_inc(*DMA("lat"))

                            @block.scalar
                            def _(act):
                                act.wait_ge(*DMA["lat"])
                                act.activation(junk[:, :], lat[:, 0:QR], FN.Square, accum_out=ss[:, 0:1]).then_inc(*ACT("ss0"))
                                act.activation(cn[:, 0:KVR], lat[:, QR:QR + KVR], FN.Square, accum_out=ss[:, 1:2]).then_inc(*ACT("ss1"))
                                act.wait_ge(*ACT["ss1"])
                                act.activation(rs[:, 0:1], ss[:, 0:1], FN.Ln, bias=cst("eps"), scale=1.0 / QR).then_inc(*ACT("ln0"))
                                act.activation(rs[:, 1:2], ss[:, 1:2], FN.Ln, bias=cst("eps"), scale=1.0 / KVR).then_inc(*ACT("ln1"))
                                act.wait_ge(*ACT["ln1"])
                                act.activation(rs[:, :], rs[:, :], FN.Exp, scale=-0.5).then_inc(*ACT("rs"))
                                for b in range(2):
                                    act.wait_ge(*PE[f"q{b}"])
                                    act.copy(qk[:, 3 * b:3 * b + 3, :], ps[:, 1 + b, 0:3 * QK].rearrange("p (h n) -> p h n", n=QK)).then_inc(*ACT(f"q{b}"))
                                for b in range(2):
                                    act.wait_ge(*PE[f"kv{b}"])
                                    kv = ps[:, 3 + b, 0:3 * (NOPE + MV)].rearrange("p (h n) -> p h n", h=3)
                                    act.copy(qk[:, MH + 3 * b:MH + 3 * b + 3, 0:NOPE], kv[:, :, 0:NOPE]).then_inc(*ACT(f"k{b}"))
                                    act.copy(V[:, ds(t, 1), 3 * b:3 * b + 3, :], kv[:, None, :, NOPE:NOPE + MV]).then_inc(*ACT(f"v{b}"))
                                for b in range(3):
                                    act.wait_ge(*PE[f"qkT{b}"])
                                    if b == 0:
                                        act.copy(qT[:, 0:4, ds(t * P, P)], ps[0:QK, 5, :].rearrange("p (h n) -> p h n", h=4)).then_inc(*ACT("qT0"))
                                    elif b == 1:
                                        act.copy(qT[:, 4:6, ds(t * P, P)], ps[0:QK, 6, 0:256].rearrange("p (h n) -> p h n", h=2)).then_inc(*ACT("qT1"))
                                        act.copy(kT[:, 0:2, ds(t * P, P)], ps[0:QK, 6, 256:512].rearrange("p (h n) -> p h n", h=2)).then_inc(*ACT("kT1"))
                                    else:
                                        act.copy(kT[:, 2:6, ds(t * P, P)], ps[0:QK, 7, :].rearrange("p (h n) -> p h n", h=4)).then_inc(*ACT("kT2"))

                            @block.vector
                            def _(vec):
                                vec.wait_ge(*ACT["rs"])
                                vec.tensor_scalar(cn[:, 0:QR], lat[:, 0:QR], rs[:, 0:1], None, ALU.mult).then_inc(*VEC("cq"))
                                vec.tensor_scalar(cn[:, QR:QR + KVR], lat[:, QR:QR + KVR], rs[:, 1:2], None, ALU.mult).then_inc(*VEC("ckv"))
                                vec.wait_ge(*PE["cT"])
                                g = P_AT["q_g"][0]
                                vec.tensor_scalar(cT[:, 0, :], ps[:, 0, 0:P], params[:, g:g + 1], None, ALU.mult).then_inc(*VEC("cT0"))
                                vec.tensor_scalar(cT[0:QR - P, 1, :], ps[0:QR - P, 0, P:2 * P], params[0:QR - P, g + 1:g + 2], None, ALU.mult).then_inc(*VEC("cT1"))
                                vec.tensor_scalar(cT[:, 2, :], ps[:, 0, 2 * P:3 * P], par("kv_g"), None, ALU.mult).then_inc(*VEC("cT2"))
                                cos1, sin1 = csn[:, 0, :], csn[:, 1, :]
                                vec.tensor_copy(csn[:, 0, :], cs[:, ds(t, 1), 0, :]).then_inc(*VEC("cos"))
                                vec.tensor_copy(csn[:, 1, :], cs[:, ds(t, 1), 1, :]).then_inc(*VEC("sin"))
                                k1, k2 = lat[:, QR + KVR:QR + KVR + H2], lat[:, QR + KVR + H2:]
                                vec.wait_ge(*VEC["sin"])
                                vec.tensor_tensor(tk[:, 0, 0:H2], k1, cos1, ALU.mult)
                                vec.tensor_tensor(tk[:, 1, 0:H2], k2, sin1, ALU.mult)
                                vec.tensor_tensor(tk[:, 0, H2:], k2, cos1, ALU.mult)
                                vec.tensor_tensor(tk[:, 1, H2:], k1, sin1, ALU.mult).then_inc(*VEC("tk"))
                                vec.wait_ge(*VEC["tk"])
                                vec.tensor_tensor(kr[:, 0:H2], tk[:, 0, 0:H2], tk[:, 1, 0:H2], ALU.subtract)
                                vec.tensor_tensor(kr[:, H2:], tk[:, 0, H2:], tk[:, 1, H2:], ALU.add).then_inc(*VEC("kr"))
                                vec.wait_ge(*VEC["kr"])
                                vec.tensor_copy(qk[:, MH:2 * MH, NOPE:QK], rep(kr[:, :], MH)).then_inc(*VEC("k_rot"))
                                vec.wait_ge(*ACT["q1"])
                                q1, q2 = qk[:, 0:MH, NOPE:NOPE + H2], qk[:, 0:MH, NOPE + H2:QK]
                                vec.tensor_tensor(tr[:, 0, :, 0:H2], q1, rep(cos1, MH), ALU.mult)
                                vec.tensor_tensor(tr[:, 1, :, 0:H2], q2, rep(sin1, MH), ALU.mult)
                                vec.tensor_tensor(tr[:, 0, :, H2:], q2, rep(cos1, MH), ALU.mult)
                                vec.tensor_tensor(tr[:, 1, :, H2:], q1, rep(sin1, MH), ALU.mult).then_inc(*VEC("tr"))
                                vec.wait_ge(*VEC["tr"])
                                vec.tensor_tensor(q1, tr[:, 0, :, 0:H2], tr[:, 1, :, 0:H2], ALU.subtract)
                                vec.tensor_tensor(q2, tr[:, 0, :, H2:], tr[:, 1, :, H2:], ALU.add).then_inc(*VEC("q_rot"))

                            @block.tensor
                            def _(pe):
                                pe.wait_ge(*VEC["ckv"])
                                pe.transpose(ps[:, 0, 0:P], cn[:, 0:P], ident)
                                pe.transpose(ps[0:QR - P, 0, P:2 * P], cn[:, P:QR], ident)
                                pe.transpose(ps[:, 0, 2 * P:3 * P], cn[:, QR:QR + KVR], ident).then_inc(*PE("cT"))
                                pe.wait_ge(*VEC["cT2"])
                                for b in range(2):
                                    n = slice(3 * QK * b, 3 * QK * (b + 1))
                                    pe.matmul(ps[:, 1 + b, 0:3 * QK], lhsT=cT[:, 0, :], rhs=wq[:, 0, n], start=True, stop=False)
                                    pe.matmul(ps[:, 1 + b, 0:3 * QK], lhsT=cT[0:QR - P, 1, :], rhs=wq[0:QR - P, 1, n], start=False,
                                              stop=True).then_inc(*PE(f"q{b}"))
                                for b in range(2):
                                    w = 3 * (NOPE + MV)
                                    pe.matmul(ps[:, 3 + b, 0:w], lhsT=cT[:, 2, :], rhs=wkv[:, w * b:w * (b + 1)], start=True,
                                              stop=True).then_inc(*PE(f"kv{b}"))
                                pe.wait_ge(*VEC["q_rot"])
                                pe.wait_ge(*ACT["v1"])
                                for b in range(3):
                                    for n in range(4):
                                        q = pe.transpose(ps[0:QK, 5 + b, n * P:(n + 1) * P], qk[:, 4 * b + n, :], ident)
                                    q.then_inc(*PE(f"qkT{b}"))
                        clear()

                with ExitStack() as st2:
                    NU = 2 * MH
                    qs = sbuf(st2, "qs", [QK, NU, P])
                    pr = sbuf(st2, "pr", [P, 2, SEQ])
                    pT = sbuf(st2, "pT", [P, 2, NT, P])
                    mx = sbuf(st2, "mx", [P, NU])
                    nm = sbuf(st2, "nm", [P, NU])
                    den = sbuf(st2, "den", [P, NU])
                    inv = sbuf(st2, "inv", [P, NU])
                    om = sbuf(st2, "om", [P, 2, GW])
                    SC = QK ** -0.5
                    with nc.Fori(0, NT // 2) as t:
                        begin("attend")
                        with nc.Block() as block:
                            @block.tensor
                            def _(pe):
                                def scores(j):
                                    pe.wait_ge(*(VEC if j < MH else ACT)[f"qs{j // MH}"])
                                    if j >= 2:
                                        pe.wait_ge(*ACT[f"p{j - 2}"])
                                    for b in range(2):
                                        q = pe.matmul(ps[:, 2 * (j % 2) + b, :], lhsT=qs[:, j, :], rhs=kT[:, j % MH, b * 512:(b + 1) * 512],
                                                      start=True, stop=True)
                                    q.then_inc(*PE(f"s{j}"))
                                scores(0)
                                scores(1)
                                for j in range(NU):
                                    s = j % 2
                                    pe.wait_ge(*ACT[f"p{j}"])
                                    if j >= 1:
                                        pe.wait_ge(*VEC[f"pT{j - 1}"])
                                        pe.wait_ge(*ACT[f"pT{j - 1}"])
                                    for b in range(2):
                                        for n in range(4):
                                            q = pe.transpose(ps[:, 4 + b, n * P:(n + 1) * P], pr[:, s, (4 * b + n) * P:(4 * b + n + 1) * P], ident)
                                        q.then_inc(*PE(f"t{j}_{b}"))
                                    if j + 2 < NU:
                                        scores(j + 2)
                                    pe.wait_ge(*VEC[f"pT{j}"])
                                    pe.wait_ge(*ACT[f"pT{j}"])
                                    if j >= 2:
                                        pe.wait_ge(*VEC[f"o{j - 2}"])
                                    for k in range(NT):
                                        q = pe.matmul(ps[:, 6 + s, 0:MV], lhsT=pT[:, s, k, :], rhs=V[:, k, j % MH, :], start=(k == 0), stop=(k == NT - 1))
                                    q.then_inc(*PE(f"o{j}"))

                            @block.scalar
                            def _(act):
                                def expo(j):
                                    s = j % 2
                                    act.wait_ge(*VEC[f"nm{j}"])
                                    if j >= 2:
                                        act.wait_ge(*PE[f"t{j - 2}_1"])
                                    act.activation(pr[:, s, :].rearrange("p (b n) -> p b n", b=2), ps[:, 2 * s:2 * s + 2, :], FN.Exp,
                                                   bias=nm[:, j:j + 1], scale=SC, accum_out=den[:, j:j + 1]).then_inc(*ACT(f"p{j}"))
                                act.copy(qs[:, MH:NU, :], qT[:, :, ds(t * (2 * P) + P, P)]).then_inc(*ACT("qs1"))
                                expo(0)
                                expo(1)
                                for j in range(NU):
                                    act.wait_ge(*PE[f"t{j}_1"])
                                    if j >= 2:
                                        act.wait_ge(*PE[f"o{j - 2}"])
                                    act.copy(pT[:, j % 2, 4:8, :], ps[:, 5, :].rearrange("p (k n) -> p k n", k=4)).then_inc(*ACT(f"pT{j}"))
                                    if j + 2 < NU:
                                        expo(j + 2)

                            @block.vector
                            def _(vec):
                                def top(j):
                                    s = j % 2
                                    vec.wait_ge(*PE[f"s{j}"])
                                    vec.tensor_reduce(mx[:, j:j + 1], ps[:, 2 * s:2 * s + 2, :].rearrange("p b n -> p (b n)"), AX, ALU.max).then_inc(*VEC(f"mx{j}"))
                                    vec.wait_ge(*VEC[f"mx{j}"])
                                    vec.tensor_scalar(nm[:, j:j + 1], mx[:, j:j + 1], -SC, None, ALU.mult).then_inc(*VEC(f"nm{j}"))

                                def scale(j):
                                    vec.wait_ge(*PE[f"o{j}"])
                                    vec.tensor_scalar(om[:, j // MH, (j % MH) * MV:(j % MH + 1) * MV], ps[:, 6 + j % 2, 0:MV], inv[:, j:j + 1], None,
                                                      ALU.mult).then_inc(*VEC(f"o{j}"))
                                vec.tensor_copy(qs[:, 0:MH, :], qT[:, :, ds(t * (2 * P), P)]).then_inc(*VEC("qs0"))
                                top(0)
                                top(1)
                                for j in range(NU):
                                    vec.wait_ge(*PE[f"t{j}_0"])
                                    if j >= 2:
                                        vec.wait_ge(*PE[f"o{j - 2}"])
                                    vec.tensor_copy(pT[:, j % 2, 0:4, :], ps[:, 4, :].rearrange("p (k n) -> p k n", k=4)).then_inc(*VEC(f"pT{j}"))
                                    vec.wait_ge(*ACT[f"p{j}"])
                                    vec.reciprocal(inv[:, j:j + 1], den[:, j:j + 1]).then_inc(*VEC(f"inv{j}"))
                                    if j + 2 < NU:
                                        top(j + 2)
                                    if j >= 1:
                                        vec.wait_ge(*VEC[f"inv{j - 1}"])
                                        scale(j - 1)
                                vec.wait_ge(*VEC[f"inv{NU - 1}"])
                                scale(NU - 1)

                            @block.sync
                            def _(sp):
                                for n in range(2):
                                    sp.wait_ge(*VEC[f"o{MH * n + MH - 1}"])
                                    sp.dma_start(mla_hbm[ds(t * (2 * P) + n * P, P), :], om[:, n, :]).then_inc(*DMA("o_out"))
                                sp.wait_ge(*DMA["o_out"])
                        clear()

            with ExitStack() as st:
                wo = sbuf(st, "w_out", [P, KD, DM])
                gi = sbuf(st, "gi", [P, 2, 2, GW])
                ri = sbuf(st, "ri", [P, 2, 3, 2, RW])
                gate = sbuf(st, "gate_in", [P, 2, 2, DM])
                mix = sbuf(st, "mix", [P, 2, 2, DM])
                mT = sbuf(st, "mT", [P, 2, KD, P])
                xt = sbuf(st, "x_t", [P, 4, DM])
                s = sbuf(st, "s_sum", [P, 2, GW])
                y = sbuf(st, "y_sum", [P, 2, RW])
                sq = sbuf(st, "sq_o", [P, 2, GW])
                gi2 = sbuf(st, "gi2", [P, 2, 2, GW])
                g_ss = sbuf(st, "g_ss", [P, 2 * GH])
                r_ss = sbuf(st, "r_ss", [P, 2 * RH])
                mean = sbuf(st, "mean", [P, 2 * RH])
                g_rs = sbuf(st, "g_rs", [P, 2 * GH])
                r_rs = sbuf(st, "r_rs", [P, 2 * RH])
                begin("out_load")
                with nc.Block() as block:
                    @block.sync
                    def _(sp):
                        sp.dma_start(wo[:, :, :], w_rows(io["w_out"][ds(L, 1)].rearrange("a r n -> (a r) n"))).then_inc(*DMA("w_out"))
                        sp.wait_ge(*DMA["w_out"])
                clear()
                with nc.Fori(0, 2) as i:
                    begin("out")
                    with nc.Block() as block:
                        def h64(ap):
                            return ap.rearrange("p t (h n) -> p (t h) n", n=GD)

                        @block.sync
                        def _(sp):
                            for p in range(2):
                                row = i * (4 * P) + 2 * P * p

                                def rows(ap):
                                    return ap.rearrange("(t p) n -> p t n", p=P)
                                for e, dst in enumerate((gi, gi2)):
                                    sp.dma_start(dst[:, p, :, :], rows(gdn_hbm[e, ds(row, 2 * P), :])).then_inc(*DMA(f"gdn_in{p}"))
                                for e in range(3):
                                    sp.dma_start(ri[:, p, e, :, :], rows(rwkv_hbm[e, ds(row, 2 * P), :])).then_inc(*DMA(f"rwkv_in{p}"))
                                sp.dma_start(gate[:, p, :, :], rows(gate_hbm[ds(row, 2 * P), :])).then_inc(*DMA(f"gate_in{p}"))
                                sp.dma_start(mix[:, p, :, GW:2 * GW], rows(mla_hbm[ds(row, 2 * P), :])).then_inc(*DMA(f"mla_in{p}"))
                                sp.dma_start(xt[:, 2 * p:2 * p + 2, :], rows(x_hbm[ds(row + P, 2 * P), :])).then_inc(*DMA(f"x_in{p}"))
                            for t in range(4):
                                sp.wait_ge(*VEC[f"x{t}_1"])
                                sp.dma_start(x_hbm[ds(i * (4 * P) + (t + 1) * P, P), :], xt[:, t, :]).then_inc(*DMA("x_out"))
                            sp.wait_ge(*DMA["x_out"])

                        @block.scalar
                        def _(act):
                            for p in range(2):
                                act.wait_ge(*DMA[f"gate_in{p}"])
                                act.activation(gate[:, p, :, :], gate[:, p, :, :], FN.Silu).then_inc(*ACT(f"gate{p}"))
                            for p in range(2):
                                act.wait_ge(*VEC[f"gss{p}"])
                                act.activation(g_rs[:, :], g_ss[:, :], FN.Ln, bias=cst("eps"), scale=1.0 / GD).then_inc(*ACT(f"ln_g{p}"))
                                act.wait_ge(*VEC[f"rss{p}"])
                                act.activation(r_rs[:, :], r_ss[:, :], FN.Ln, bias=cst("rw_eps"), scale=1.0 / RD).then_inc(*ACT(f"ln_r{p}"))
                                act.wait_ge(*ACT[f"ln_g{p}"])
                                act.activation(g_rs[:, :], g_rs[:, :], FN.Exp, scale=-0.5).then_inc(*ACT(f"g_rs{p}"))
                                act.wait_ge(*ACT[f"ln_r{p}"])
                                act.activation(r_rs[:, :], r_rs[:, :], FN.Exp, scale=-0.5).then_inc(*ACT(f"rs{p}"))
                            for t in range(4):
                                for b in range(2):
                                    act.wait_ge(*PE[f"mT{t}_{b}"])
                                    act.copy(mT[:, t % 2, 4 * b:4 * b + 4, :], ps[:, b, :].rearrange("p (k n) -> p k n", k=4)).then_inc(*ACT(f"mT{t}_{b}"))

                        @block.vector
                        def _(vec):
                            for p in range(2):
                                if p:
                                    vec.wait_ge(*ACT["rs0"])
                                vec.wait_ge(*DMA[f"gdn_in{p}"])
                                vec.tensor_tensor(s[:, :, :], gi[:, p, :, :], gi2[:, p, :, :], ALU.add).then_inc(*VEC(f"s{p}"))
                                vec.wait_ge(*DMA[f"rwkv_in{p}"])
                                vec.tensor_tensor(y[:, :, :], ri[:, p, 0, :, :], ri[:, p, 1, :, :], ALU.add).then_inc(*VEC(f"y{p}"))
                                vec.wait_ge(*VEC[f"s{p}"])
                                vec.tensor_tensor(sq[:, :, :], s[:, :, :], s[:, :, :], ALU.mult).then_inc(*VEC(f"gsq{p}"))
                                vec.wait_ge(*VEC[f"y{p}"])
                                vec.tensor_reduce(mean[:, :], h64(y[:, :, :]), AX, ALU.add).then_inc(*VEC(f"ysum{p}"))
                                vec.wait_ge(*VEC[f"gsq{p}"])
                                vec.tensor_reduce(g_ss[:, :], h64(sq[:, :, :]), AX, ALU.add).then_inc(*VEC(f"gss{p}"))
                                vec.wait_ge(*VEC[f"ysum{p}"])
                                vec.tensor_scalar(mean[:, :], mean[:, :], 1.0 / RD, None, ALU.mult).then_inc(*VEC(f"mean{p}"))
                                vec.wait_ge(*VEC[f"mean{p}"])
                                vec.tensor_tensor(h64(y[:, :, :]), h64(y[:, :, :]), col(mean[:, :], RD), ALU.subtract).then_inc(*VEC(f"yc{p}"))
                                vec.wait_ge(*VEC[f"yc{p}"])
                                vec.wait_ge(*VEC[f"gss{p}"])
                                vec.tensor_tensor(sq[:, :, 0:RW], y[:, :, :], y[:, :, :], ALU.mult).then_inc(*VEC(f"rsq{p}"))
                                vec.wait_ge(*VEC[f"rsq{p}"])
                                vec.tensor_reduce(r_ss[:, :], sq[:, :, 0:RW].rearrange("p t (h n) -> p t h n", n=RD), AX, ALU.add).then_inc(*VEC(f"rss{p}"))
                                vec.tensor_tensor(ri[:, p, 2, :, :], ri[:, p, 2, :, :], rep(par("ln_b"), 2), ALU.add).then_inc(*VEC(f"r3{p}"))
                                vec.wait_ge(*ACT[f"g_rs{p}"])
                                vec.tensor_tensor(h64(s[:, :, :]), h64(s[:, :, :]), col(g_rs[:, :], GD), ALU.mult).then_inc(*VEC(f"g1{p}"))
                                vec.wait_ge(*ACT[f"rs{p}"])
                                vec.tensor_tensor(h64(y[:, :, :]), h64(y[:, :, :]), col(r_rs[:, :], RD), ALU.mult).then_inc(*VEC(f"r1{p}"))
                                vec.wait_ge(*VEC[f"g1{p}"])
                                for t in range(2):
                                    q = vec.tensor_tensor(mix[:, p, t, 0:GW].rearrange("p (h n) -> p h n", n=GD), s[:, t, :].rearrange("p (h n) -> p h n", n=GD),
                                                          rep(par("gdn_g"), GH), ALU.mult)
                                q.then_inc(*VEC(f"g2{p}"))
                                vec.wait_ge(*VEC[f"r1{p}"])
                                vec.tensor_tensor(y[:, :, :], y[:, :, :], rep(par("ln_g"), 2), ALU.mult).then_inc(*VEC(f"r2{p}"))
                                vec.wait_ge(*VEC[f"r3{p}"])
                                vec.wait_ge(*VEC[f"r2{p}"])
                                vec.tensor_tensor(mix[:, p, :, 2 * GW:], y[:, :, :], ri[:, p, 2, :, :], ALU.add).then_inc(*VEC(f"r4{p}"))
                                vec.wait_ge(*VEC[f"r4{p}"])
                                vec.wait_ge(*DMA[f"mla_in{p}"])
                                vec.wait_ge(*ACT[f"gate{p}"])
                                vec.tensor_tensor(mix[:, p, :, :], mix[:, p, :, :], gate[:, p, :, :], ALU.mult).then_inc(*VEC(f"mix{p}"))
                            for t in range(4):
                                vec.wait_ge(*DMA[f"x_in{t // 2}"])
                                for b in range(2):
                                    n = slice(512 * b, 512 * (b + 1))
                                    vec.wait_ge(*PE[f"o{t}_{b}"])
                                    vec.tensor_tensor(xt[:, t, n], xt[:, t, n], ps[:, 2 + (2 * t + b) % 6, :], ALU.add).then_inc(*VEC(f"x{t}_{b}"))

                        @block.tensor
                        def _(pe):
                            def turn(t):
                                pe.wait_ge(*VEC[f"mix{t // 2}"])
                                for b in range(2):
                                    if t >= 1:
                                        pe.wait_ge(*ACT[f"mT{t - 1}_{b}"])
                                    for k in range(4):
                                        q = pe.transpose(ps[:, b, k * P:(k + 1) * P], mix[:, t // 2, t % 2, (4 * b + k) * P:(4 * b + k + 1) * P], ident)
                                    q.then_inc(*PE(f"mT{t}_{b}"))
                            turn(0)
                            for t in range(4):
                                if t == 0:
                                    turn(1)
                                pe.wait_ge(*ACT[f"mT{t}_1"])
                                for b in range(2):
                                    if 2 * t + b >= 6:
                                        pe.wait_ge(*VEC[f"x{(2 * t + b - 6) // 2}_{b}"])
                                    for k in range(KD):
                                        q = pe.matmul(ps[:, 2 + (2 * t + b) % 6, :], lhsT=mT[:, t % 2, k, :], rhs=wo[:, k, 512 * b:512 * (b + 1)],
                                                      start=(k == 0), stop=(k == KD - 1))
                                    q.then_inc(*PE(f"o{t}_{b}"))
                                if t + 2 < 4:
                                    turn(t + 2)
                    clear()
        first.close()

        with ExitStack() as st:
            work = norm_buffers(st, "_2", 4)
            fg = sbuf(st, "fg", [P, DM])
            begin("load2")
            with nc.Block() as block:
                @block.sync
                def _(sp):
                    sp.dma_start(params[:, 0:P2_N], io["params2"]).then_inc(*DMA("params2"))
                    sp.dma_start(fg[:, :], io["final_g"]).then_inc(*DMA("final_g"))
                    sp.wait_ge(*DMA["params2"])
                    sp.wait_ge(*DMA["final_g"])
            clear()
            with nc.Fori(0, 2) as i:
                norm_tiles("norm2", 4, lambda j: i * (4 * P) + (j + 1) * P, par("norm_g", P2_AT), work, final=fg[:, :])
            norm_tiles("norm_meta", 1, lambda j: 0, par("norm_g", P2_AT), work)

        w_in2 = io["w_in_2"]
        THIRD = T2 // 3

        def project3(pe, banks, w, x_in):
            for b in range(3):
                for k in range(KD):
                    q = pe.matmul(ps[:, banks + b, 0:THIRD], lhsT=w[:, k, :], rhs=x_in[:, k, b * THIRD:(b + 1) * THIRD],
                                  start=(k == 0), stop=(k == KD - 1))
            return q

        def bank3(banks):
            return ps[:, banks:banks + 3, 0:THIRD]

        def tok3(ap):
            return ap.rearrange("p (b n) -> p b n", b=3)

        def tiles(ap):
            return ap.rearrange("p (t n) -> p t n", n=P)

        with ExitStack() as st:
            NAMES = ("glu_a", "glu_b", "q", "f", "i", "g")
            COLS = dict(zip(NAMES, (0, DM, 3 * DM, 4 * DM, 5 * DM, 6 * DM)))
            wt = {n: sbuf(st, "w2_" + n, [P, KD, P]) for n in NAMES}
            glu = sbuf(st, "glu", [P, T2])
            sgb = sbuf(st, "sgb", [P, T2])
            cv = sbuf(st, "cv", [P, T2])
            q_ = sbuf(st, "q_", [P, T2])
            k_ = sbuf(st, "k_", [P, T2])
            Rp = sbuf(st, "Rp", [P, T2])
            Sp = sbuf(st, "Sp", [P, T2])
            W = sbuf(st, "W", [P, 2, T2])
            v = sbuf(st, "v2", [P, T2])
            kS = sbuf(st, "kS", [P, T2])
            at = sbuf(st, "attn", [P, T2])
            Sst = sbuf(st, "Sst", [P, NT2, P])
            sgg = sbuf(st, "sgg", [P, T2])
            orec = sbuf(st, "orec", [P, T2])
            osq = sbuf(st, "osq", [P, T2])
            lb = sbuf(st, "lb", [P, KD])
            omlb = sbuf(st, "omlb", [P, KD])
            diff = sbuf(st, "lb_diff", [P, KD])
            begin("hg_load")
            with nc.Block() as block:
                @block.sync
                def _(sp):
                    for n in NAMES:
                        sp.dma_start(wt[n][:, :, :], w_rows(w_in2[:, COLS[n]:COLS[n] + P])).then_inc(*DMA("w2"))
                    sp.wait_ge(*DMA["w2"])

                @block.vector
                def _(vec):
                    l = par("lb", P2_AT).rearrange("p (k c) -> p k c", c=2)
                    mxl, e2 = Sp[:, 0:KD], Rp[:, 0:2 * KD].rearrange("p (c k) -> p c k", c=2)
                    vec.tensor_tensor(mxl, l[:, :, 0], l[:, :, 1], ALU.max).then_inc(*VEC("lb_max"))
                    vec.wait_ge(*VEC["lb_max"])
                    vec.tensor_tensor(e2[:, 0, :], l[:, :, 0], mxl, ALU.subtract)
                    vec.tensor_tensor(e2[:, 1, :], l[:, :, 1], mxl, ALU.subtract).then_inc(*VEC("lb_shift"))
                    vec.wait_ge(*ACT["lb_exp"])
                    vec.tensor_tensor(diff[:, :], e2[:, 0, :], e2[:, 1, :], ALU.add).then_inc(*VEC("lb_sum"))
                    vec.wait_ge(*VEC["lb_sum"])
                    vec.reciprocal(diff[:, :], diff[:, :]).then_inc(*VEC("lb_inv"))
                    vec.wait_ge(*VEC["lb_inv"])
                    vec.tensor_tensor(lb[:, :], e2[:, 0, :], diff[:, :], ALU.mult).then_inc(*VEC("lb"))
                    vec.wait_ge(*VEC["lb"])
                    vec.tensor_scalar(omlb[:, :], lb[:, :], -1.0, 1.0, ALU.mult, ALU.add).then_inc(*VEC("omlb"))
                    vec.memset(at[:, :], 0.0).then_inc(*VEC("attn0"))
                    vec.memset(cv[:, :], 0.0).then_inc(*VEC("cv0"))
                    vec.memset(Sst[:, 0, :], 0.0).then_inc(*VEC("state0"))

                @block.scalar
                def _(act):
                    act.wait_ge(*VEC["lb_shift"])
                    act.activation(Rp[:, 0:2 * KD], Rp[:, 0:2 * KD], FN.Exp).then_inc(*ACT("lb_exp"))
            clear()

            def level(ap, k):
                return ap.rearrange("p (a s n) -> p a s n", s=2, n=1 << k)

            with nc.Fori(0, KD) as i:
                begin("hg")
                with nc.Block() as block:
                    at_w = P2_AT["conv_w"][0]

                    @block.sync
                    def _(sp):
                        for n, used in (("f", "f"), ("q", "q"), ("i", "v"), ("glu_b", "glu_b"), ("glu_a", "glu_a"), ("g", "g")):
                            sp.wait_ge(*PE[used])
                            sp.dma_start(wt[n][:, :, :], w_rows(w_in2[:, ds(i * P + (COLS[n] + P), P)])).then_inc(*DMA("w2"))
                        sp.wait_ge(*VEC[f"tap{TAPS - 1}"])
                        sp.dma_start(conv_hbm[ds(i, 1)].rearrange("a p n -> (a p) n"), cv[:, :]).then_inc(*DMA("out2"))
                        sp.wait_ge(*VEC["orec"])
                        sp.dma_start(rec_hbm[ds(i, 1)].rearrange("a p n -> (a p) n"), orec[:, :]).then_inc(*DMA("out2"))
                        sp.wait_ge(*DMA["w2"])
                        sp.wait_ge(*DMA["out2"])

                    @block.tensor
                    def _(pe):
                        project3(pe, 0, wt["f"], hT).then_inc(*PE("f"))
                        project3(pe, 3, wt["q"], hT).then_inc(*PE("q"))
                        pe.wait_ge(*ACT["f"])
                        for t in range(NT2):
                            for k in range(KD):
                                q = pe.matmul(ps[:, t // 3, (t % 3) * P:(t % 3 + 1) * P], lhsT=hT[:, k, t * P:(t + 1) * P], rhs=wt["i"][:, k, :],
                                              start=(k == 0), stop=(k == KD - 1))
                        q.then_inc(*PE("v"))
                        pe.wait_ge(*ACT["q"])
                        project3(pe, 3, wt["glu_b"], hT).then_inc(*PE("glu_b"))
                        pe.wait_ge(*ACT["v"])
                        project3(pe, 0, wt["glu_a"], hT).then_inc(*PE("glu_a"))
                        pe.wait_ge(*ACT["glu_b"])
                        project3(pe, 3, wt["g"], hT).then_inc(*PE("g"))
                        for n in range(NLEV + 1):
                            pe.wait_ge(*VEC["glu"] if n == 0 else VEC[f"kept{n - 1}"])
                            if n == 0:
                                pe.wait_ge(*VEC["k"])
                                pe.wait_ge(*ACT["q"])
                            else:
                                pe.wait_ge(*VEC[f"W{n - 1}"])
                            for t in range(NT2):
                                u = slice(t * P, (t + 1) * P)
                                a, b = (k_[:, u], q_[:, u]) if n == 0 else (W[:, (n - 1) % 2, u],) * 2
                                q = pe.matmul(ps[:, t // 3, (t % 3) * P:(t % 3 + 1) * P], lhsT=a, rhs=b, start=True, stop=True)
                            q.then_inc(*PE(f"pairs{n}"))
                        pe.wait_ge(*VEC["kS"])
                        pe.wait_ge(*ACT["g"])
                        for t in range(NT2):
                            q = pe.transpose(ps[:, 3 + t // 3, (t % 3) * P:(t % 3 + 1) * P], kS[:, t * P:(t + 1) * P], ident)
                        q.then_inc(*PE("kS"))
                        pe.wait_ge(*ACT["kS"])
                        pe.wait_ge(*VEC[f"kept{NLEV}"])
                        for t in range(NT2 - 1):
                            q = pe.matmul(ps[:, t // 4, (t % 4) * P:(t % 4 + 1) * P], lhsT=kS[:, t * P:(t + 1) * P], rhs=v[:, t * P:(t + 1) * P],
                                          start=True, stop=True)
                        q.then_inc(*PE("kv"))
                        pe.wait_ge(*VEC[f"state{NT2 - 2}"])
                        pe.wait_ge(*VEC["qR"])
                        for t in range(NT2):
                            u = slice(t * P, (t + 1) * P)
                            o_ap = ps[:, 3 + t // 3, (t % 3) * P:(t % 3 + 1) * P]
                            pe.matmul(o_ap, lhsT=v[:, u], rhs=at[:, u], start=True, stop=False)
                            q = pe.matmul(o_ap, lhsT=Sst[:, t, :], rhs=q_[:, u], start=False, stop=True)
                        q.then_inc(*PE("o"))
                        pe.wait_ge(*ACT["osq"])
                        for b in range(3):
                            q = pe.matmul(ps[:, b, 0:THIRD], lhsT=ones, rhs=osq[:, b * THIRD:(b + 1) * THIRD], start=True, stop=True)
                        q.then_inc(*PE("oss"))

                    @block.scalar
                    def _(act):
                        act.wait_ge(*PE["f"])
                        act.activation(tok3(sgb[:, :]), bank3(0), FN.Sigmoid).then_inc(*ACT("f"))
                        act.wait_ge(*PE["q"])
                        act.activation(tok3(q_[:, :]), bank3(3), FN.Silu).then_inc(*ACT("q"))
                        act.wait_ge(*PE["v"])
                        act.copy(tok3(v[:, :]), bank3(0)).then_inc(*ACT("v"))
                        act.wait_ge(*PE["glu_b"])
                        act.wait_ge(*VEC["f"])
                        act.activation(tok3(sgb[:, :]), bank3(3), FN.Sigmoid).then_inc(*ACT("glu_b"))
                        act.wait_ge(*PE["g"])
                        act.activation(tok3(sgg[:, :]), bank3(3), FN.Silu).then_inc(*ACT("g"))
                        act.wait_ge(*PE["kS"])
                        act.copy(tok3(kS[:, :]), bank3(3)).then_inc(*ACT("kS"))
                        act.wait_ge(*PE["o"])
                        act.activation(tok3(osq[:, :]), bank3(3), FN.Square).then_inc(*ACT("osq"))
                        act.copy(tok3(orec[:, :]), bank3(3)).then_inc(*ACT("o"))
                        act.wait_ge(*PE["oss"])
                        act.activation(tok3(osq[:, :]), bank3(0), FN.Ln, bias=cst("eps"), scale=1.0 / P).then_inc(*ACT("o_ln"))
                        act.wait_ge(*ACT["o_ln"])
                        act.activation(osq[:, :], osq[:, :], FN.Exp, scale=-0.5).then_inc(*ACT("o_rs"))

                    @block.gpsimd
                    def _(pool):
                        pool.memset(Sp[:, :], 1.0).then_inc(*POOL("S_"))
                        for k in range(NLEV):
                            R4, S4 = level(Rp[:, :], k), level(Sp[:, :], k)
                            n = T2 >> (k + 1)
                            pool.wait_ge(*POOL["S_"] if k == 0 else POOL[f"R{k - 1}"])
                            pool.wait_ge(*VEC[f"W{k}"])
                            pool.tensor_tensor(S4[:, :, 0, :], S4[:, :, 0, :], R4[:, :, 1, (1 << k) - 1:1 << k].broadcast_to([P, n, 1 << k]),
                                               ALU.mult).then_inc(*POOL(f"S{k}"))
                            pool.wait_ge(*POOL[f"S{k}"])
                            pool.tensor_tensor(R4[:, :, 1, :], R4[:, :, 1, :], R4[:, :, 0, (1 << k) - 1:1 << k].broadcast_to([P, n, 1 << k]),
                                               ALU.mult).then_inc(*POOL(f"R{k}"))

                    @block.vector
                    def _(vec):
                        vec.wait_ge(*ACT["f"])
                        vec.tensor_scalar(Rp[:, :], sgb[:, :], omlb[:, ds(i, 1)], lb[:, ds(i, 1)], ALU.mult, ALU.add).then_inc(*VEC("f"))
                        vec.wait_ge(*VEC["f"])
                        vec.tensor_scalar(k_[:, :], Rp[:, :], -1.0, 1.0, ALU.mult, ALU.add).then_inc(*VEC("k"))
                        vec.wait_ge(*ACT["q"])
                        vec.wait_ge(*VEC["k"])
                        vec.wait_ge(*POOL["S_"])

                        def weights(k):
                            Wk, q4, k4, R4, S4 = (level(a, k) for a in (W[:, k % 2, :], q_[:, :], k_[:, :], Rp[:, :], Sp[:, :]))
                            if k >= 1:
                                vec.wait_ge(*POOL[f"R{k - 1}"])
                            if k >= 2:
                                vec.wait_ge(*PE[f"pairs{k - 1}"])
                            vec.tensor_tensor(Wk[:, :, 1, :], q4[:, :, 1, :], R4[:, :, 1, :], ALU.mult)
                            vec.tensor_tensor(Wk[:, :, 0, :], k4[:, :, 0, :], S4[:, :, 0, :], ALU.mult).then_inc(*VEC(f"W{k}"))

                        weights(0)
                        weights(1)
                        vec.wait_ge(*PE["glu_a"])
                        vec.wait_ge(*ACT["glu_b"])
                        vec.tensor_tensor(tok3(glu[:, :]), bank3(0), tok3(sgb[:, :]), ALU.mult).then_inc(*VEC("glu"))
                        T0 = P - META
                        NW = T2 - T0

                        def tap(n):
                            src = glu[:, T0 - (TAPS - 1) + n:T0 - (TAPS - 1) + n + NW]
                            w = params[:, ds(i * TAPS + (at_w + n), 1)]
                            vec.wait_ge(*VEC["glu" if n == 0 else f"tap{n - 1}"])
                            if n == 0:
                                vec.tensor_scalar(cv[:, T0:], src, w, params[:, ds(i + P2_AT["conv_b"][0], 1)], ALU.mult,
                                                  ALU.add).then_inc(*VEC("tap0"))
                            else:
                                vec.scalar_tensor_tensor(out=cv[:, T0:], in0=src, scalar=w, in1=cv[:, T0:], op0=ALU.mult,
                                                         op1=ALU.add).then_inc(*VEC(f"tap{n}"))
                        done = 0
                        for n in range(NLEV + 1):
                            vec.wait_ge(*PE[f"pairs{n}"])
                            mask = ident if n == 0 else cst("up", n - 1)
                            for b in range(3):
                                q = vec.copy_predicated(at[:, b * THIRD:(b + 1) * THIRD].rearrange("p (t n) -> p t n", n=P),
                                                        rep(mask, 3).bitcast(U32),
                                                        ps[:, b, 0:THIRD].rearrange("p (t n) -> p t n", n=P))
                            q.then_inc(*VEC(f"kept{n}"))
                            if 2 <= n + 1 < NLEV:
                                weights(n + 1)
                            for _ in range(2):
                                tap(done)
                                done += 1
                        vec.wait_ge(*POOL[f"R{NLEV - 1}"])
                        vec.tensor_tensor(kS[:, :], k_[:, :], Sp[:, :], ALU.mult).then_inc(*VEC("kS"))
                        vec.wait_ge(*PE["pairs0"])
                        vec.tensor_tensor(q_[:, :], q_[:, :], Rp[:, :], ALU.mult).then_inc(*VEC("qR"))
                        for _ in range(4):
                            tap(done)
                            done += 1
                        vec.wait_ge(*PE["kv"])
                        for t in range(NT2 - 1):
                            if t:
                                vec.wait_ge(*VEC[f"state{t - 1}"])
                            vec.scalar_tensor_tensor(out=Sst[:, t + 1, :], in0=Sst[:, t, :], scalar=Rp[:, (t + 1) * P - 1:(t + 1) * P],
                                                     in1=ps[:, t // 4, (t % 4) * P:(t % 4 + 1) * P], op0=ALU.mult, op1=ALU.add).then_inc(*VEC(f"state{t}"))
                        while done < TAPS:
                            tap(done)
                            done += 1
                        vec.wait_ge(*ACT["o_rs"])
                        vec.tensor_tensor(orec[:, :], orec[:, :], osq[:, :], ALU.mult).then_inc(*VEC("o_normed"))
                        vec.wait_ge(*VEC["o_normed"])
                        vec.scalar_tensor_tensor(out=orec[:, :], in0=orec[:, :], scalar=params[:, ds(i + P2_AT["gnorm"][0], 1)],
                                                 in1=sgg[:, :], op0=ALU.mult, op1=ALU.mult).then_inc(*VEC("orec"))
                clear()

        merged_stack = ExitStack()
        cz = sbuf(merged_stack, "cz", [P, KD, T2])
        rec = sbuf(merged_stack, "rec", [P, KD, T2])
        merged = sbuf(merged_stack, "merged", [P, KD, T2])
        with ExitStack() as st:
            wz = sbuf(st, "wz", [P, KD, P])
            mu = sbuf(st, "mu", [P, T2])
            sq = sbuf(st, "sq_l", [P, 2, T2])
            zs = sbuf(st, "zs", [P, T2])
            begin("ln")
            with nc.Block() as block:
                @block.sync
                def _(sp):
                    sp.dma_start(wz[:, :, :], w_rows(w_in2[:, 2 * DM:2 * DM + P])).then_inc(*DMA("wz"))
                    sp.dma_start(cz[:, :, :], conv_hbm.rearrange("k p n -> p k n")).then_inc(*DMA("cz"))
                    sp.dma_start(rec[:, :, :], rec_hbm.rearrange("k p n -> p k n")).then_inc(*DMA("rec"))
                    sp.wait_ge(*DMA["rec"])
                    sp.wait_ge(*DMA["wz"])

                @block.tensor
                def _(pe):
                    pe.wait_ge(*DMA["cz"])
                    for b in range(3):
                        for k in range(KD):
                            q = pe.matmul(ps[:, b, 0:THIRD], lhsT=ones, rhs=cz[:, k, b * THIRD:(b + 1) * THIRD], start=(k == 0), stop=(k == KD - 1))
                    q.then_inc(*PE("sum"))
                    for k in range(KD):
                        pe.wait_ge(*ACT[f"sq{k}"])
                        for b in range(3):
                            q = pe.matmul(ps[:, 3 + b, 0:THIRD], lhsT=ones, rhs=sq[:, k % 2, b * THIRD:(b + 1) * THIRD], start=(k == 0),
                                          stop=(k == KD - 1))
                        q.then_inc(*PE(f"sumsq{k}"))

                @block.scalar
                def _(act):
                    act.wait_ge(*PE["sum"])
                    act.mul(tok3(mu[:, :]), bank3(0), 1.0 / DM).then_inc(*ACT("mu"))
                    for k in range(KD):
                        act.wait_ge(*VEC[f"centred{k}"])
                        if k >= 2:
                            act.wait_ge(*PE[f"sumsq{k - 2}"])
                        act.activation(sq[:, k % 2, :], cz[:, k, :], FN.Square).then_inc(*ACT(f"sq{k}"))
                    act.wait_ge(*PE[f"sumsq{KD - 1}"])
                    act.activation(tok3(zs[:, :]), bank3(3), FN.Ln, bias=cst("eps"), scale=1.0 / DM).then_inc(*ACT("ln"))
                    act.wait_ge(*ACT["ln"])
                    act.activation(zs[:, :], zs[:, :], FN.Exp, scale=-0.5).then_inc(*ACT("rs"))

                @block.vector
                def _(vec):
                    vec.wait_ge(*ACT["mu"])
                    for k in range(KD):
                        vec.tensor_tensor(cz[:, k, :], cz[:, k, :], mu[:, :], ALU.subtract).then_inc(*VEC(f"centred{k}"))
                    vec.wait_ge(*ACT["rs"])
                    for k in range(KD):
                        vec.tensor_tensor(cz[:, k, :], cz[:, k, :], zs[:, :], ALU.mult).then_inc(*VEC(f"scaled{k}"))
            clear()
            with nc.Fori(0, KD) as i:
                begin("z")
                with nc.Block() as block:
                    @block.sync
                    def _(sp):
                        sp.wait_ge(*PE["z"])
                        sp.dma_start(wz[:, :, :], w_rows(w_in2[:, ds(i * P + (2 * DM + P), P)])).then_inc(*DMA("wz"))
                        sp.wait_ge(*DMA["wz"])

                    @block.tensor
                    def _(pe):
                        project3(pe, 0, wz, hT).then_inc(*PE("z"))

                    @block.scalar
                    def _(act):
                        act.wait_ge(*VEC["affine"])
                        act.activation(mu[:, :], mu[:, :], FN.Silu).then_inc(*ACT("c"))
                        act.wait_ge(*PE["z"])
                        act.activation(tok3(zs[:, :]), bank3(0), FN.Silu).then_inc(*ACT("z"))

                    @block.vector
                    def _(vec):
                        vec.tensor_scalar(mu[:, :], cz[:, ds(i, 1), :], params[:, ds(i + P2_AT["ln_g"][0], 1)],
                                          params[:, ds(i + P2_AT["ln_b"][0], 1)], ALU.mult, ALU.add).then_inc(*VEC("affine"))
                        vec.wait_ge(*ACT["z"])
                        vec.tensor_tensor(cz[:, ds(i, 1), :], mu[:, :], zs[:, :], ALU.mult).then_inc(*VEC("cz"))
                clear()

        with ExitStack() as st:
            wm = {n: sbuf(st, "wm_" + n, [P, KD, P]) for n in ("m_conv", "m_rec", "conv", "rec")}
            src = {"m_conv": (w_in2, 7 * DM), "m_rec": (w_in2, 8 * DM), "conv": (io["w_conv_out_2"], 0), "rec": (io["w_rec_out_2"], 0)}
            gm = sbuf(st, "gm", [P, 2, T2])
            with nc.Fori(0, KD) as i:
                begin("merge")
                with nc.Block() as block:
                    @block.sync
                    def _(sp):
                        for n in ("m_conv", "conv", "m_rec", "rec"):
                            w, c0 = src[n]
                            sp.dma_start(wm[n][:, :, :], w_rows(w[:, ds(i * P + c0, P)])).then_inc(*DMA("w_" + n))

                    @block.tensor
                    def _(pe):
                        pe.wait_ge(*DMA["w_m_conv"])
                        project3(pe, 0, wm["m_conv"], hT).then_inc(*PE("m_conv"))
                        pe.wait_ge(*DMA["w_conv"])
                        project3(pe, 3, wm["conv"], cz).then_inc(*PE("conv"))
                        pe.wait_ge(*DMA["w_m_rec"])
                        pe.wait_ge(*ACT["m_conv"])
                        project3(pe, 0, wm["m_rec"], hT).then_inc(*PE("m_rec"))
                        pe.wait_ge(*DMA["w_rec"])
                        pe.wait_ge(*VEC["conv"])
                        project3(pe, 3, wm["rec"], rec).then_inc(*PE("rec"))

                    @block.scalar
                    def _(act):
                        act.wait_ge(*PE["m_conv"])
                        act.activation(tok3(gm[:, 0, :]), bank3(0), FN.Sigmoid).then_inc(*ACT("m_conv"))
                        act.wait_ge(*PE["m_rec"])
                        act.activation(tok3(gm[:, 1, :]), bank3(0), FN.Sigmoid).then_inc(*ACT("m_rec"))

                    @block.vector
                    def _(vec):
                        vec.wait_ge(*PE["conv"])
                        vec.wait_ge(*ACT["m_conv"])
                        vec.tensor_tensor(tok3(gm[:, 0, :]), tok3(gm[:, 0, :]), bank3(3), ALU.mult).then_inc(*VEC("conv"))
                        vec.wait_ge(*PE["rec"])
                        vec.wait_ge(*ACT["m_rec"])
                        vec.tensor_tensor(tok3(gm[:, 1, :]), tok3(gm[:, 1, :]), bank3(3), ALU.mult).then_inc(*VEC("rec"))
                        vec.wait_ge(*VEC["rec"])
                        vec.tensor_tensor(merged[:, ds(i, 1), :], gm[:, 0, :], gm[:, 1, :], ALU.add).then_inc(*VEC("merged"))
                clear()

        with ExitStack() as st:
            wo = cz[:, :, 0:DM]
            mT = sbuf(st, "mT2", [P, 2, KD, P])
            xt = rec[:, :, :].rearrange("p k n -> p (k n)")[:, 0:4 * DM].rearrange("p (t n) -> p t n", t=4)
            sq = rec[:, :, :].rearrange("p k n -> p (k n)")[:, 4 * DM:8 * DM].rearrange("p (t n) -> p t n", t=4)
            fg = sbuf(st, "fg2", [P, DM])
            ss = sbuf(st, "ss_e", [P, 4])
            rs = sbuf(st, "rs_e", [P, 4])
            begin("end_load")
            with nc.Block() as block:
                @block.sync
                def _(sp):
                    sp.dma_start(wo, w_rows(io["w_out_2"])).then_inc(*DMA("end"))
                    sp.dma_start(fg[:, :], io["final_g_2"]).then_inc(*DMA("end"))
                    sp.wait_ge(*DMA["end"])
            clear()
            with nc.Fori(0, 2) as i:
                begin("end")
                with nc.Block() as block:
                    row = i * (4 * P)

                    @block.sync
                    def _(sp):
                        for t in range(4):
                            sp.dma_start(xt[:, t, :], x_hbm[ds(row + (t + 1) * P, P), :]).then_inc(*DMA(f"x_in{t}"))
                        for t in range(4):
                            sp.wait_ge(*VEC[f"y{t}"])
                            sp.dma_start(io["out"][ds(row + t * P, P), :], sq[:, t, :]).then_inc(*DMA("y_out"))
                        sp.wait_ge(*DMA["y_out"])

                    @block.gpsimd
                    def _(pool):
                        for t in range(4):
                            if t >= 2:
                                pool.wait_ge(*PE[f"o{t - 2}_1"])
                            pool.tensor_copy(mT[:, t % 2, :, :], merged[:, :, ds(row + (t + 1) * P, P)]).then_inc(*POOL(f"mT{t}"))

                    @block.tensor
                    def _(pe):
                        for t in range(4):
                            pe.wait_ge(*POOL[f"mT{t}"])
                            for b in range(2):
                                for k in range(KD):
                                    q = pe.matmul(ps[:, 2 * t + b, :], lhsT=mT[:, t % 2, k, :], rhs=wo[:, k, 512 * b:512 * (b + 1)], start=(k == 0),
                                                  stop=(k == KD - 1))
                                q.then_inc(*PE(f"o{t}_{b}"))

                    @block.vector
                    def _(vec):
                        for t in range(4):
                            vec.wait_ge(*DMA[f"x_in{t}"])
                            for b in range(2):
                                n = slice(512 * b, 512 * (b + 1))
                                vec.wait_ge(*PE[f"o{t}_{b}"])
                                vec.tensor_tensor(xt[:, t, n], xt[:, t, n], ps[:, 2 * t + b, :], ALU.add).then_inc(*VEC(f"x{t}_{b}"))
                        for t in range(4):
                            vec.wait_ge(*ACT["rs"])
                            vec.scalar_tensor_tensor(out=sq[:, t, :], in0=xt[:, t, :], scalar=rs[:, t:t + 1], in1=fg[:, :], op0=ALU.mult,
                                                     op1=ALU.mult).then_inc(*VEC(f"y{t}"))

                    @block.scalar
                    def _(act):
                        for t in range(4):
                            act.wait_ge(*VEC[f"x{t}_1"])
                            act.activation(sq[:, t, :], xt[:, t, :], FN.Square, accum_out=ss[:, t:t + 1]).then_inc(*ACT(f"ss{t}"))
                        act.wait_ge(*ACT["ss3"])
                        act.activation(rs[:, :], ss[:, :], FN.Ln, bias=cst("eps"), scale=1.0 / DM).then_inc(*ACT("ln"))
                        act.wait_ge(*ACT["ln"])
                        act.activation(rs[:, :], rs[:, :], FN.Exp, scale=-0.5).then_inc(*ACT("rs"))
                clear()
        merged_stack.close()


def kernel(**inputs):
    import numpy as _np
    import concourse.bacc as _bacc
    from concourse import mybir as _mybir
    from concourse.bass_utils import run_bass_kernel_spmd as _run

    a = {k: _np.asarray(v) for k, v in inputs.items()}

    def channels(v, n):
        return v.reshape(v.shape[0], n, P).transpose(0, 2, 1)

    def everywhere(v):
        return _np.broadcast_to(v[:, None, :], (v.shape[0], P, v.shape[1]))

    def both(v, n):
        return v.reshape(v.shape[0], v.shape[1], n, P).transpose(0, 3, 1, 2).reshape(v.shape[0], P, -1)

    q_g = _np.zeros((DEPTH, 2 * P), _np.float32)
    q_g[:, :QR] = a["mla_q_norm_g"]
    laid = {
        "norm_g": channels(a["norm_g"], KD),
        "conv": a["gdn_conv"].reshape(DEPTH, CONV, 9, P).transpose(0, 3, 2, 1).reshape(DEPTH, P, -1),
        "a_log": everywhere(a["gdn_a_log"].reshape(DEPTH, -1)), "dt": everywhere(a["gdn_dt_bias"].reshape(DEPTH, -1)),
        "gdn_g": everywhere(a["gdn_norm_g"]), "q_g": channels(q_g, 2), "kv_g": channels(a["mla_kv_norm_g"], 1),
        "mu": a["rwkv_mu"].reshape(DEPTH, 2, 7, P).transpose(0, 3, 2, 1).reshape(DEPTH, P, -1),
        "w0": both(a["rwkv_w0"], 2), "a0": both(a["rwkv_a0"], 2), "k_k": channels(a["rwkv_k_k"], 2),
        "k_a": channels(a["rwkv_k_a"], 2), "r_k": channels(a["rwkv_r_k"].reshape(DEPTH, RW), 2),
        "ln_g": everywhere(a["rwkv_ln_g"]), "ln_b": everywhere(a["rwkv_ln_b"]),
    }
    laid2 = {
        "norm_g": channels(a["norm_g_2"], KD)[0],
        "conv_w": a["conv_w_2"][0].reshape(TAPS, KD, P).transpose(2, 1, 0).reshape(P, -1),
        "conv_b": channels(a["conv_b_2"], KD)[0], "ln_g": channels(a["ln_g_2"], KD)[0], "ln_b": channels(a["ln_b_2"], KD)[0],
        "lb": a["lb_logits_2"].reshape(2, KD, P).transpose(2, 1, 0).reshape(P, -1), "gnorm": channels(a["gnorm_g_2"], KD)[0],
    }
    w2a2 = _np.concatenate([a["rwkv_w2"].transpose(0, 2, 1, 3), a["rwkv_a2"].transpose(0, 2, 1, 3)], 1)
    arrays = {
        "consts": shape_constants(), "positions": a["positions"].reshape(NT, P).T, "x": a["x"].reshape(SEQ, DM),
        "params": _np.concatenate([laid[n] for n, _ in PARAMS], 2), "params2": _np.concatenate([laid2[n] for n, _ in PARAMS2], 1),
        "w_in": a["w_in"], "w_uq": a["mla_w_uq"], "w_ukv": a["mla_w_ukv"], "w2a2": w2a2, "w_out": a["w_out"],
        "final_g": everywhere(a["final_norm_g"][None])[0], "meta": a["meta_tokens_2"], "w_in_2": a["w_in_2"][0],
        "w_conv_out_2": a["w_conv_out_2"][0], "w_rec_out_2": a["w_rec_out_2"][0], "w_out_2": a["w_out_2"][0],
        "final_g_2": everywhere(a["final_g_2"][None])[0],
    }
    arrays = {"in_" + n: _np.ascontiguousarray(v) for n, v in arrays.items()}

    def program(values):
        nc = _bacc.Bacc("TRN2", target_bir_lowering=False, num_devices=1)
        io = {n[3:]: nc.dram_tensor(n, v.shape, _mybir.dt.from_np(v.dtype), kind="ExternalInput").ap() for n, v in arrays.items()}
        io["out"] = nc.dram_tensor("out", (SEQ, DM), F32, kind="ExternalOutput").ap()
        build(nc, io, values)
        return nc

    values = {}
    program(values)
    r = _run(program(values), [arrays], core_ids=[0])
    return r.results[0]["out"].reshape(1, SEQ, DM)
```

```python
from contextlib import ExitStack

import concourse.bass as bass
import numpy as np
from concourse import mybir

F32 = mybir.dt.float32
I32 = mybir.dt.int32
U32 = mybir.dt.uint32
FN = mybir.ActivationFunctionType
ALU = mybir.AluOpType
AX = mybir.AxisListType.X
ds = bass.ds

P = 128
DEPTH, DM, SEQ = 2, 1024, 1024
KD = DM // P
NT = SEQ // P
GH, GD = 6, 64
GW = GH * GD
CONV = 5
MH, NOPE, ROPE, MV = 6, 64, 32, 64
QR, KVR = 192, 128
QK = NOPE + ROPE
RH, RD = 4, 64
RW = RH * RD
N_IN = 3448
COL_GDN, COL_AB, COL_RW = 1024, 2176, 2552
TM_W = COL_RW - COL_AB
NLEV = 7
T2 = SEQ + P
NT2 = T2 // P
META = 16
TAPS = 31
D_IN2 = 9216
NORM_EPS = 1e-6
RWKV_EPS = 64e-5

PARAMS = [("norm_g", KD), ("conv", 9 * CONV), ("a_log", 2 * GH), ("dt", 2 * GH), ("gdn_g", GD), ("q_g", 2), ("kv_g", 1),
          ("mu", 14), ("w0", 4), ("a0", 4), ("k_k", 2), ("k_a", 2), ("r_k", 2), ("ln_g", RW), ("ln_b", RW)]
PARAMS2 = [("norm_g", KD), ("conv_w", KD * TAPS), ("conv_b", KD), ("ln_g", KD), ("ln_b", KD), ("lb", KD * 2),
           ("gnorm", KD)]
CONSTS = [("ident", P), ("tri_f", P), ("tri_b", P), ("aft", P), ("bef", P), ("ones", P), ("blk", P), ("sel", 2),
          ("freq", ROPE // 2), ("eps", 1), ("rw_eps", 1), ("lo", NLEV * P), ("up", NLEV * P)]


def offsets(fields):
    at, out = 0, {}
    for name, n in fields:
        out[name] = (at, n)
        at += n
    return out, at


def shape_constants():
    i = np.arange(P)
    r, c = i[:, None], i[None, :]
    lo = np.stack([((r >> (k + 1)) == (c >> (k + 1))) & (((r >> k) & 1) == 1) & (((c >> k) & 1) == 0) for k in range(NLEV)], 1)
    up = np.stack([((r >> (k + 1)) == (c >> (k + 1))) & (((r >> k) & 1) == 0) & (((c >> k) & 1) == 1) for k in range(NLEV)], 1)
    half = ROPE // 2
    parts = {
        "ident": r == c, "tri_f": r <= c, "tri_b": r >= c, "aft": r > c, "bef": r < c, "ones": np.ones((P, P)),
        "blk": (r // 64) == (c // 64), "sel": (r // 64) == np.arange(2)[None, :],
        "freq": np.broadcast_to(np.float32(10000.0) ** (-np.arange(half, dtype=np.float32) / half), (P, half)),
        "eps": np.full((P, 1), NORM_EPS), "rw_eps": np.full((P, 1), RWKV_EPS),
        "lo": lo.reshape(P, -1), "up": up.reshape(P, -1),
    }
    return np.ascontiguousarray(np.concatenate([np.asarray(parts[n], np.float32) for n, _ in CONSTS], 1))


class Steps:

    def __init__(self, sem, label, unit, values):
        self.sem, self.label, self.unit, self.values = sem, label, unit, values
        self.stage, self.count = "", 0

    def begin(self, stage):
        self.stage, self.count = stage, 0

    def __call__(self, name):
        self.count += self.unit
        self.values[self.stage, self.label, name] = self.count
        return self.sem, self.unit

    def __getitem__(self, name):
        return self.sem, self.values.get((self.stage, self.label, name), 1)


class Transfers:

    def __init__(self, nc, ctx, values):
        self.nc, self.ctx, self.values, self.sems = nc, ctx, values, {}

    def begin(self, stage):
        self.stage, self.counts = stage, {}

    def sem(self, name):
        if name not in self.sems:
            self.sems[name] = self.ctx.enter_context(self.nc.semaphore("dma_" + name))
        return self.sems[name]

    def __call__(self, name):
        self.counts[name] = self.counts.get(name, 0) + 16
        self.values[self.stage, "dma", name] = self.counts[name]
        return self.sem(name), 16

    def __getitem__(self, name):
        return self.sem(name), self.values.get((self.stage, "dma", name), 16)


def build(nc, io, values):
    with ExitStack() as ctx:
        def sem(name):
            return ctx.enter_context(nc.semaphore(name))

        VEC = Steps(sem("vector_steps"), "vec", 1, values)
        ACT = Steps(sem("scalar_steps"), "act", 1, values)
        PE = Steps(sem("tensor_steps"), "pe", 1, values)
        POOL = Steps(sem("gpsimd_steps"), "pool", 1, values)
        DMA = Transfers(nc, ctx, values)

        def begin(stage):
            for s in (VEC, ACT, PE, POOL, DMA):
                s.begin(stage)

        def clear():
            for s in (VEC, ACT, PE, POOL):
                nc.sync.sem_clear(s.sem)
            for name in DMA.counts:
                nc.sync.sem_clear(DMA.sem(name))
            nc.all_engine_barrier()

        def sbuf(stack, name, shape, dt=F32):
            return stack.enter_context(nc.sbuf_tensor(name, shape, dt))

        def rep(ap, n):
            return ap[:, None, :].broadcast_to([ap.shape[0], n, ap.shape[1]])

        def col(ap, m):
            return ap[:, :, None].broadcast_to([ap.shape[0], ap.shape[1], m])

        def hbm(name, shape):
            return nc.dram_tensor(name, shape, F32).ap()

        gate_hbm = hbm("gate_hbm", (SEQ, DM))
        gdn_hbm = hbm("gdn_hbm", (2, SEQ, GW))
        rwkv_hbm = hbm("rwkv_hbm", (3, SEQ, RW))
        mla_hbm = hbm("mla_hbm", (SEQ, GW))
        kb_hbm = hbm("kb_hbm", (P, 2, 2, 2, SEQ))
        x_hbm = hbm("x_hbm", (T2, DM))
        conv_hbm = hbm("conv_hbm", (KD, P, T2))
        rec_hbm = hbm("rec_hbm", (KD, P, T2))
        tm_hbm = hbm("tm_hbm", (SEQ, TM_W))

        C_AT, C_N = offsets(CONSTS)
        P_AT, P_N = offsets(PARAMS)
        P2_AT, P2_N = offsets(PARAMS2)
        consts = sbuf(ctx, "consts", [P, C_N])
        ps = ctx.enter_context(nc.psum_tensor("ps", [P, 8, 512], F32))

        def cst(name, k=None):
            a, n = C_AT[name]
            return consts[:, a:a + n] if k is None else consts[:, a + k * P:a + (k + 1) * P]

        ident, ones, blk = cst("ident"), cst("ones"), cst("blk")
        hT = sbuf(ctx, "hT", [P, KD, T2])
        params = sbuf(ctx, "params", [P, max(P_N, P2_N)])

        def par(name, table=P_AT):
            a, n = table[name]
            return params[:, a:a + n]

        def w_rows(w):
            return w.rearrange("(k p) n -> p k n", p=P)

        def norm_tiles(stage, n, row, g, work, final=None, loads=None):
            X, ss, rs = work["x"], work["ss"], work["rs"]
            rounds = 2 if final is not None else 1
            begin(stage)
            with nc.Block() as block:
                @block.sync
                def _(sp):
                    for j in range(n):
                        sp.dma_start(X[:, j, :], x_hbm[ds(row(j), P), :]).then_inc(*DMA(f"x_tile{j}"))
                    if loads is not None:
                        loads(sp)
                    if final is not None:
                        for j in range(n):
                            sp.wait_ge(*VEC[f"final{j}"])
                            sp.dma_start(x_hbm[ds(row(j), P), :], X[:, j, :]).then_inc(*DMA("x_out"))
                        sp.wait_ge(*DMA["x_out"])

                @block.scalar
                def _(act):
                    for r in range(rounds):
                        for j in range(n):
                            act.wait_ge(*(DMA[f"x_tile{j}"] if r == 0 else VEC[f"final{j}"]))
                            if r + j > 0:
                                act.wait_ge(*(ACT[f"sum{r}_{j - 1}"] if j > 0 else ACT[f"sum0_{n - 1}"]))
                            act.activation(work["sq"][:, :], X[:, j, :], FN.Square, accum_out=ss[:, r, j:j + 1]).then_inc(*ACT(f"sum{r}_{j}"))
                        act.wait_ge(*ACT[f"sum{r}_{n - 1}"])
                        act.activation(rs[:, r, 0:n], ss[:, r, 0:n], FN.Ln, bias=cst("eps"), scale=1.0 / DM).then_inc(*ACT(f"ln{r}"))
                        act.wait_ge(*ACT[f"ln{r}"])
                        act.activation(rs[:, r, 0:n], rs[:, r, 0:n], FN.Exp, scale=-0.5).then_inc(*ACT(f"rs{r}"))

                @block.vector
                def _(vec):
                    if final is not None:
                        for j in range(n):
                            vec.wait_ge(*ACT["rs0"])
                            vec.scalar_tensor_tensor(out=X[:, j, :], in0=X[:, j, :], scalar=rs[:, 0, j:j + 1], in1=final, op0=ALU.mult,
                                                     op1=ALU.mult).then_inc(*VEC(f"final{j}"))
                    for j in range(n + 1):
                        if j < n:
                            vec.wait_ge(*ACT[f"rs{rounds - 1}"])
                            vec.tensor_scalar(work["xn"][:, j % 2, :], X[:, j, :], rs[:, rounds - 1, j:j + 1], None,
                                              ALU.mult).then_inc(*VEC(f"normed{j}"))
                        if j > 0:
                            for b in range(2):
                                vec.wait_ge(*PE[f"turned{j - 1}_{b}"])
                                bank = (2 * (j - 1) + b) % 8
                                vec.tensor_tensor(hT[:, 4 * b:4 * b + 4, ds(row(j - 1), P)], ps[:, bank, :].rearrange("p (k n) -> p k n", k=4),
                                                  col(g[:, 4 * b:4 * b + 4], P), ALU.mult).then_inc(*VEC(f"h{j - 1}_{b}"))

                @block.tensor
                def _(pe):
                    for j in range(n):
                        pe.wait_ge(*VEC[f"normed{j}"])
                        for b in range(2):
                            for k in range(4):
                                q = pe.transpose(ps[:, (2 * j + b) % 8, k * P:(k + 1) * P], work["xn"][:, j % 2, (4 * b + k) * P:(4 * b + k + 1) * P], ident)
                            q.then_inc(*PE(f"turned{j}_{b}"))
            clear()

        def norm_buffers(stack, tag, n):
            return {"x": sbuf(stack, "x" + tag, [P, n, DM]), "sq": sbuf(stack, "sq" + tag, [P, DM]), "xn": sbuf(stack, "xn" + tag, [P, 2, DM]),
                    "ss": sbuf(stack, "ss" + tag, [P, 2, n]), "rs": sbuf(stack, "rs" + tag, [P, 2, n])}

        first = ExitStack()
        cs = sbuf(first, "cos_sin", [P, NT, 2, ROPE // 2])
        begin("load")
        with ExitStack() as st, nc.Block() as block:
            pos_i = sbuf(st, "pos_i", [P, NT], I32)
            pos = sbuf(st, "pos", [P, NT])
            ang = sbuf(st, "ang", [P, 2, NT, ROPE // 2])
            turns = sbuf(st, "turns", [P, 2, NT, ROPE // 2])
            whole = sbuf(st, "whole", [P, 2, NT, ROPE // 2])
            meta = sbuf(st, "meta", [P, DM])

            @block.sync
            def _(sp):
                sp.dma_start(consts[:, :], io["consts"]).then_inc(*DMA("consts"))
                sp.dma_start(pos_i[:, :], io["positions"]).then_inc(*DMA("positions"))
                sp.dma_start(x_hbm[P:T2, :], io["x"]).then_inc(*DMA("x"))
                sp.wait_ge(*VEC["zero"])
                sp.dma_start(meta[P - META:P, :], io["meta"]).then_inc(*DMA("meta"))
                sp.wait_ge(*DMA["meta"])
                sp.dma_start(x_hbm[0:P, :], meta[:, :]).then_inc(*DMA("meta_out"))
                sp.wait_ge(*DMA["meta_out"])
                sp.wait_ge(*DMA["x"])

            @block.vector
            def _(vec):
                vec.memset(meta[:, :], 0.0).then_inc(*VEC("zero"))
                two_pi = 2 * np.pi
                c1 = float(np.float32(6.28125))
                c2 = float(np.float32(np.round((two_pi - c1) * 2**19) / 2**19))
                c3 = float(np.float32(two_pi - c1 - c2))
                magic = float(np.float32(1.5 * 2**23))
                vec.wait_ge(*DMA["positions"])
                vec.tensor_copy(pos[:, :], pos_i[:, :]).then_inc(*VEC("pos"))
                vec.wait_ge(*DMA["consts"])
                vec.wait_ge(*VEC["pos"])
                vec.tensor_tensor(ang[:, 1, :, :], col(pos[:, :], ROPE // 2), rep(cst("freq"), NT), ALU.mult).then_inc(*VEC("ang"))
                vec.wait_ge(*VEC["ang"])
                vec.tensor_scalar(turns[:, 1], ang[:, 1], 1.0 / two_pi, magic, ALU.mult, ALU.add).then_inc(*VEC("turns1"))
                vec.tensor_scalar(turns[:, 0], ang[:, 1], 1.0 / two_pi, 0.25, ALU.mult, ALU.add).then_inc(*VEC("turns0a"))
                vec.wait_ge(*VEC["turns0a"])
                vec.tensor_scalar(turns[:, 0], turns[:, 0], magic, None, ALU.add).then_inc(*VEC("turns0"))
                vec.wait_ge(*VEC["turns0"])
                vec.tensor_scalar(whole[:, :], turns[:, :], magic, None, ALU.subtract).then_inc(*VEC("whole"))
                vec.tensor_copy(ang[:, 0], ang[:, 1]).then_inc(*VEC("ang0"))
                for n, c in enumerate((c1, c2, c3)):
                    vec.wait_ge(*VEC["ang0" if n == 0 else f"cut{n - 1}"])
                    vec.scalar_tensor_tensor(out=ang[:, :], in0=whole[:, :], scalar=-c, in1=ang[:, :], op0=ALU.mult,
                                             op1=ALU.add).then_inc(*VEC(f"cut{n}"))
                vec.wait_ge(*VEC["cut2"])
                vec.tensor_scalar(ang[:, 0], ang[:, 0], float(np.float32(np.pi / 2)), None, ALU.add).then_inc(*VEC("quarter"))
                vec.wait_ge(*VEC["quarter"])
                vec.tensor_scalar(ang[:, :], ang[:, :], 3.1415925, -3.1415925, ALU.min, ALU.max).then_inc(*VEC("range"))

            @block.scalar
            def _(act):
                act.wait_ge(*VEC["range"])
                act.activation(cs[:, :, :, :].rearrange("p t c f -> p c t f"), ang[:, :, :, :], FN.Sin).then_inc(*ACT("cos_sin"))
        clear()

        with nc.Fori(0, DEPTH) as L:
            w_in = io["w_in"][ds(L, 1)].rearrange("a r n -> (a r) n")
            w_uq = io["w_uq"][ds(L, 1)].rearrange("a r n -> (a r) n")

            with ExitStack() as st:
                wg = sbuf(st, "w_gate", [P, KD, DM])
                wt = sbuf(st, "w_tm", [P, KD, TM_W])
                with ExitStack() as st2:
                    work = norm_buffers(st2, "_1", 4)
                    begin("load1")
                    with nc.Block() as block:
                        @block.sync
                        def _(sp):
                            sp.dma_start(params[:, 0:P_N], io["params"][ds(L, 1)].rearrange("a p n -> (a p) n")).then_inc(*DMA("params"))
                            sp.wait_ge(*DMA["params"])
                    clear()
                    with nc.Fori(0, 2) as i:
                        def load_gate(sp):
                            sp.dma_start(wg[:, ds(i * (KD // 2), KD // 2), :], w_rows(w_in[ds(i * (DM // 2), DM // 2), 0:DM])).then_inc(*DMA("w"))
                            sp.dma_start(wt[:, ds(i * (KD // 2), KD // 2), :], w_rows(w_in[ds(i * (DM // 2), DM // 2), COL_AB:COL_RW])).then_inc(*DMA("w"))
                            sp.wait_ge(*DMA["w"])
                        norm_tiles("norm1", 4, lambda j: i * (4 * P) + (j + 1) * P, par("norm_g"), work, loads=load_gate)

                def token_major(stage, w, columns, out, dst):
                    begin(stage)
                    with nc.Block() as block:
                        @block.tensor
                        def _(pe):
                            for t in range(NT):
                                for k in range(KD):
                                    q = pe.matmul(ps[:, t, 0:columns], lhsT=hT[:, k, (t + 1) * P:(t + 2) * P], rhs=w(k), start=(k == 0),
                                                  stop=(k == KD - 1))
                                q.then_inc(*PE(f"tile{t}"))

                        @block.scalar
                        def _(act):
                            for t in range(0, NT, 2):
                                act.wait_ge(*PE[f"tile{t}"])
                                act.copy(out[:, t, 0:columns], ps[:, t, 0:columns]).then_inc(*ACT(f"tile{t}"))

                        @block.vector
                        def _(vec):
                            for t in range(1, NT, 2):
                                vec.wait_ge(*PE[f"tile{t}"])
                                vec.tensor_copy(out[:, t, 0:columns], ps[:, t, 0:columns]).then_inc(*VEC(f"tile{t}"))

                        @block.sync
                        def _(sp):
                            for t in range(NT):
                                sp.wait_ge(*(VEC if t % 2 else ACT)[f"tile{t}"])
                                sp.dma_start(dst(t), out[:, t, 0:columns]).then_inc(*DMA("out"))
                            sp.wait_ge(*DMA["out"])
                    clear()

                tm_out = sbuf(st, "tm_out", [P, NT, 512])
                token_major("tm", lambda k: wt[:, k, :], TM_W, tm_out, lambda t: tm_hbm[t * P:(t + 1) * P, :])
                with nc.Fori(0, 2) as i:
                    token_major("gate", lambda k: wg[:, k, ds(i * 512, 512)], 512, tm_out,
                                lambda t: gate_hbm[t * P:(t + 1) * P, ds(i * 512, 512)])

            def project_tensor(pe, wc, n):
                for b in range(2):
                    if n >= 3:
                        pe.wait_ge(*ACT[f"proj{n - 3}_{b}"])
                    for k in range(KD):
                        m = pe.matmul(ps[:, 2 * (n % 3) + b, :], lhsT=wc[:, k, :], rhs=hT[:, k, P + b * 512:P + (b + 1) * 512],
                                      start=(k == 0), stop=(k == KD - 1))
                    m.then_inc(*PE(f"proj{n}_{b}"))

            def project_copy(act, xp, n, left):
                if n >= 2:
                    act.wait_ge(*VEC[left])
                for b in range(2):
                    act.wait_ge(*PE[f"proj{n}_{b}"])
                    act.copy(xp[:, n % 2, 2 + b * 512:2 + (b + 1) * 512], ps[:, 2 * (n % 3) + b, :]).then_inc(*ACT(f"proj{n}_{b}"))

            def load_columns(wc, columns):
                begin("columns")
                with nc.Block() as block:
                    @block.sync
                    def _(sp):
                        for s, column in enumerate(columns):
                            sp.dma_start(wc[:, s, :, :], w_rows(w_in[:, column:column + P])).then_inc(*DMA("w_cols"))
                        sp.wait_ge(*DMA["w_cols"])
                clear()

            def side(ap, k, g):
                if len(ap.shape) == 2:
                    return ap.rearrange("p (a s n) -> p a s n", s=2, n=1 << k)[:, :, g, :]
                return ap.rearrange("p u (a s n) -> p u a s n", s=2, n=1 << k)[:, :, :, g, :]

            def products(b, k, g, n, width):
                ap = ps[:, b:b + (n * width + 511) // 512, :].rearrange("p b n -> p (b n)")[:, 0:n * width]
                if width == P:
                    return side(ap.rearrange("p (u n) -> p u n", u=n), k, g)
                return ap.rearrange("p (u a n) -> p u a n", u=n, n=1 << k)

            def unit_bank(b, w, width):
                per = 512 // width
                return ps[:, b + w // per, (w % per) * width:(w % per + 1) * width]

            def invert_tensor(pe, s, n, width, bank, turn_bank, AT, X, Y, Pm, beside):
                def product(k, g):
                    pe.wait_ge(*(ACT if k == 1 else VEC)[f"X{s}_{k - 1}_{g}"])
                    for w in range(n):
                        u = n * g + w
                        q = pe.matmul(unit_bank(bank(g), w, width), lhsT=AT(u), rhs=X[:, u, :] if width == P else side(X[:, u, :], k, g),
                                      start=True, stop=True)
                    q.then_inc(*PE(f"P{s}_{k}_{g}"))

                def turn(k, g, of):
                    for w in range(n):
                        q = pe.transpose(unit_bank(turn_bank(g), w, P), of[:, n * g + w, :], ident)
                    q.then_inc(*PE(f"turn{s}_{k}_{g}"))
                beside(0)
                for g in range(2):
                    pe.wait_ge(*VEC[f"Y{s}_0_{g}"])
                    turn(0, g, Y)
                for g in range(2):
                    product(1, g)
                for k in range(1, NLEV):
                    beside(k)
                    for g in range(2):
                        pe.wait_ge(*VEC[f"P{s}_{k}_{g}"])
                        if k > 1:
                            pe.wait_ge(*ACT[f"Y{s}_{k - 1}_{g}"])
                        for w in range(n):
                            u = n * g + w
                            q = pe.matmul(unit_bank(bank(g), w, width), lhsT=Y[:, u, :], rhs=Pm[:, u, :], start=True, stop=True)
                        q.then_inc(*PE(f"Xd{s}_{k}_{g}"))
                    for g in range(2):
                        if k + 1 < NLEV:
                            product(k + 1, g)
                        pe.wait_ge(*VEC[f"X{s}_{k}_{g}"])
                        turn(k, g, X)

            def invert_vector(vec, s, n, width, bank, ready, AT, X, Y, Pm, beside):
                vec.wait_ge(*VEC[ready])
                for g in range(2):
                    us = slice(n * g, n * g + n)
                    vec.tensor_tensor(Y[:, us, :], AT[:, us], rep(cst("up" if g == 0 else "lo", 0), n), ALU.mult).then_inc(*VEC(f"A{s}_{g}"))
                for g in range(2):
                    us = slice(n * g, n * g + n)
                    vec.wait_ge(*VEC[f"A{s}_{g}"])
                    vec.tensor_tensor(Y[:, us, :], rep(ident, n), Y[:, us, :], ALU.subtract).then_inc(*VEC(f"Y{s}_0_{g}"))
                beside(0)
                for k in range(1, NLEV):
                    for g in range(2):
                        us = slice(n * g, n * g + n)
                        pm = side(Pm[:, us, :], k, g) if width == P else Pm[:, us, :].rearrange("p u (a n) -> p u a n", n=1 << k)
                        mask = side(cst("lo" if g == 0 else "up", k), k, g)
                        vec.wait_ge(*PE[f"P{s}_{k}_{g}"])
                        vec.tensor_tensor(pm, products(bank(g), k, g, n, width),
                                          mask[:, None, :, :].broadcast_to([P, n, 64 >> k, 1 << k]), ALU.mult).then_inc(*VEC(f"P{s}_{k}_{g}"))
                    for g in range(2):
                        us = slice(n * g, n * g + n)
                        vec.wait_ge(*PE[f"Xd{s}_{k}_{g}"])
                        vec.tensor_tensor(side(X[:, us, :], k, g), side(X[:, us, :], k, g), products(bank(g), k, g, n, width),
                                          ALU.subtract).then_inc(*VEC(f"X{s}_{k}_{g}"))
                    beside(k)

            def invert_scalar(act, s, n, turn_bank, X, Y, beside):
                for k in range(NLEV):
                    beside(k)
                    for g in range(2):
                        act.wait_ge(*PE[f"turn{s}_{k}_{g}"])
                        banks = ps[:, turn_bank(g):turn_bank(g) + (n + 3) // 4, :].rearrange("p b n -> p (b n)")[:, 0:n * P]
                        to, name = (Y, "Y") if k else (X, "X")
                        act.copy(to[:, n * g:n * g + n, :].rearrange("p u n -> p (u n)"), banks).then_inc(*ACT(f"{name}{s}_{k}_{g}"))

            with ExitStack() as st:
                rw = sbuf(st, "rw", [P, 7, SEQ])
                dec = sbuf(st, "dec", [P, 2, 2, SEQ])
                bonus_sum = sbuf(st, "bonus_sum", [P, NT, 4])
                with ExitStack() as st2:
                    wc = sbuf(st2, "w_cols", [P, 2, KD, P])
                    xp = sbuf(st2, "x_pad", [P, 2, SEQ + 4])
                    acc = sbuf(st2, "acc", [P, 2, SEQ])
                    mu0 = sbuf(st2, "mu0", [P, 7])
                    load_columns(wc, [COL_RW, COL_RW + P])
                    begin("rw_zero")
                    with nc.Block() as block:
                        @block.vector
                        def _(vec):
                            vec.memset(xp[:, :, :], 0.0).then_inc(*VEC("pad"))
                            mu = par("mu").rearrange("p (i c) -> p i c", c=2)
                            vec.tensor_tensor(mu0[:, :], mu[:, :, 0], mu[:, :, 1], ALU.add).then_inc(*VEC("mu_sum"))
                            vec.wait_ge(*VEC["mu_sum"])
                            vec.tensor_scalar(mu0[:, :], mu0[:, :], -1.0, 1.0, ALU.mult, ALU.add).then_inc(*VEC("mu0"))
                    clear()
                    begin("rw_proj")
                    with nc.Block() as block:
                        @block.tensor
                        def _(pe):
                            for i in range(7):
                                if i >= 2:
                                    pe.wait_ge(*DMA[f"w_cols{i}"])
                                project_tensor(pe, wc[:, i % 2], i)

                        @block.scalar
                        def _(act):
                            for i in range(7):
                                project_copy(act, xp, i, f"after{i - 2}")

                        @block.sync
                        def _(sp):
                            for i in range(2, 7):
                                sp.wait_ge(*PE[f"proj{i - 2}_1"])
                                sp.dma_start(wc[:, i % 2, :, :], w_rows(w_in[:, COL_RW + i * P:COL_RW + (i + 1) * P])).then_inc(*DMA(f"w_cols{i}"))

                        @block.vector
                        def _(vec):
                            mu_at = P_AT["mu"][0]
                            for i in range(7):
                                x, a = xp[:, i % 2, :], acc[:, i % 2, :]
                                vec.wait_ge(*ACT[f"proj{i}_1"])
                                vec.tensor_scalar(a, x[:, 2:2 + SEQ], mu0[:, i:i + 1], None, ALU.mult).then_inc(*VEC(f"centre{i}"))
                                vec.wait_ge(*VEC[f"centre{i}"])
                                vec.scalar_tensor_tensor(out=a, in0=x[:, 1:1 + SEQ], scalar=params[:, 2 * i + mu_at:2 * i + mu_at + 1],
                                                         in1=a, op0=ALU.mult, op1=ALU.add).then_inc(*VEC(f"before{i}"))
                                vec.wait_ge(*VEC[f"before{i}"])
                                vec.scalar_tensor_tensor(out=rw[:, i, :], in0=x[:, 3:3 + SEQ], scalar=params[:, 2 * i + mu_at + 1:2 * i + mu_at + 2],
                                                         in1=a, op0=ALU.mult, op1=ALU.add).then_inc(*VEC(f"after{i}"))
                    clear()

                begin("rw_feat")
                with ExitStack() as st2, nc.Block() as block:
                    th = sbuf(st2, "th", [64, SEQ])
                    kx = sbuf(st2, "kx", [P, 2, SEQ])
                    a_all = sbuf(st2, "a_all", [P, 2, 2, SEQ])
                    sq = sbuf(st2, "sq_f", [P, SEQ])
                    ksum = sbuf(st2, "ksum", [P, SEQ])
                    omka = sbuf(st2, "omka", [P, 2])
                    w2a2 = sbuf(st2, "w2a2", [P, 2, RW])
                    kmod = sbuf(st2, "kmod", [P, 2, 2, SEQ])
                    bb = sbuf(st2, "bb", [P, 2, 2, SEQ])
                    bonus = sbuf(st2, "bonus", [P, 2, SEQ])
                    PAIRS = [(e, m) for e in range(2) for m in range(2)]

                    @block.sync
                    def _(sp):
                        sp.dma_start(w2a2[:, :, :], io["w2a2"][ds(L, 1)].rearrange("a p e n -> (a p) e n")).then_inc(*DMA("w2a2"))
                        for n, (e, m) in enumerate(PAIRS):
                            sp.wait_ge(*VEC[f"km{n}"])
                            sp.dma_start(kb_hbm[:, e, 1, m, :], kmod[:, e, m, :]).then_inc(*DMA("kb_out"))
                        for m in range(2):
                            for e in range(2):
                                sp.wait_ge(*VEC[f"b{e}{m}"])
                                sp.dma_start(kb_hbm[:, e, 0, m, :], bb[:, e, m, :]).then_inc(*DMA("kb_out"))
                        sp.wait_ge(*DMA["kb_out"])

                    @block.tensor
                    def _(pe):
                        pe.wait_ge(*DMA["w2a2"])
                        pe.wait_ge(*ACT["tanh"])
                        for n, (e, m) in enumerate(PAIRS):
                            if n:
                                pe.wait_ge(*ACT[f"dec{n - 1}"])
                            for b in range(2):
                                t = slice(b * 512, (b + 1) * 512)
                                q = pe.matmul(ps[:, b, :], lhsT=w2a2[0:64, e, m * P:(m + 1) * P], rhs=th[:, t], start=True, stop=True)
                            q.then_inc(*PE(f"dec{n}"))
                            if n:
                                pe.wait_ge(*ACT[f"rate{n - 1}"])
                            for b in range(2):
                                t = slice(b * 512, (b + 1) * 512)
                                q = pe.matmul(ps[:, 2 + b, :], lhsT=w2a2[64:128, e, m * P:(m + 1) * P], rhs=rw[64:128, 6, t],
                                              start=True, stop=True)
                            q.then_inc(*PE(f"rate{n}"))
                        for m in range(2):
                            pe.wait_ge(*VEC[f"sq{m}"])
                            if m:
                                pe.wait_ge(*ACT["kk_ln0"])
                            for b in range(2):
                                q = pe.matmul(ps[:, 4 + b, :], lhsT=blk, rhs=sq[:, b * 512:(b + 1) * 512], start=True, stop=True)
                            q.then_inc(*PE(f"sumsq{m}"))
                        for m in range(2):
                            pe.wait_ge(*VEC[f"bo{m}"])
                        for t in range(NT):
                            for m in range(2):
                                q = pe.matmul(ps[:, 6, 4 * t + 2 * m:4 * t + 2 * m + 2], lhsT=bonus[:, m, t * P:(t + 1) * P], rhs=cst("sel"), start=True, stop=True)
                        q.then_inc(*PE("bonus"))

                    @block.scalar
                    def _(act):
                        act.activation(th[:, :], rw[0:64, 6, :], FN.Tanh).then_inc(*ACT("tanh"))
                        for n, (e, m) in enumerate(PAIRS):
                            c = P_AT["w0"][0] + 2 * e + m
                            act.wait_ge(*PE[f"dec{n}"])
                            act.activation(dec[:, e, m, :].rearrange("p (b n) -> p b n", b=2), ps[:, 0:2, :], FN.Sigmoid,
                                           bias=params[:, c:c + 1]).then_inc(*ACT(f"dec{n}"))
                            c = P_AT["a0"][0] + 2 * e + m
                            act.wait_ge(*PE[f"rate{n}"])
                            act.activation(a_all[:, e, m, :].rearrange("p (b n) -> p b n", b=2), ps[:, 2:4, :], FN.Sigmoid,
                                           bias=params[:, c:c + 1]).then_inc(*ACT(f"rate{n}"))
                        act.wait_ge(*ACT["dec3"])
                        act.activation(dec[:, :, :, :], dec[:, :, :, :], FN.Exp, scale=-float(np.exp(-0.5))).then_inc(*ACT("decay"))
                        for m in range(2):
                            act.wait_ge(*PE[f"sumsq{m}"])
                            if m:
                                act.wait_ge(*VEC["kk0"])
                            act.activation(ksum[:, :].rearrange("p (b n) -> p b n", b=2), ps[:, 4:6, :], FN.Ln,
                                           bias=cst("eps")).then_inc(*ACT(f"kk_ln{m}"))
                            act.wait_ge(*ACT[f"kk_ln{m}"])
                            act.activation(ksum[:, :], ksum[:, :], FN.Exp, scale=-0.5).then_inc(*ACT(f"kk_rs{m}"))
                        act.wait_ge(*PE["bonus"])
                        act.copy(bonus_sum[:, :, :], ps[:, 6, 0:4 * NT].rearrange("p (t n) -> p t n", n=4)).then_inc(*ACT("bonus"))

                    @block.vector
                    def _(vec):
                        vec.tensor_scalar(omka[:, :], par("k_a"), -1.0, 1.0, ALU.mult, ALU.add).then_inc(*VEC("omka"))
                        for m in range(2):
                            c = P_AT["k_k"][0] + m
                            vec.tensor_scalar(kx[:, m, :], rw[:, 2 + m, :], params[:, c:c + 1], None, ALU.mult).then_inc(*VEC(f"kx{m}"))
                        for m in range(2):
                            vec.wait_ge(*VEC[f"kx{m}"])
                            if m:
                                vec.wait_ge(*PE["sumsq0"])
                            vec.tensor_tensor(sq[:, :], kx[:, m, :], kx[:, m, :], ALU.mult).then_inc(*VEC(f"sq{m}"))
                        for n, (e, m) in enumerate(PAIRS):
                            c = P_AT["k_a"][0] + m
                            vec.wait_ge(*ACT[f"rate{n}"])
                            vec.wait_ge(*VEC["omka"])
                            vec.tensor_scalar(kmod[:, e, m, :], a_all[:, e, m, :], params[:, c:c + 1], omka[:, m:m + 1],
                                              ALU.mult, ALU.add).then_inc(*VEC(f"kf{n}"))
                            vec.wait_ge(*VEC[f"kf{n}"])
                            vec.tensor_tensor(kmod[:, e, m, :], kmod[:, e, m, :], rw[:, 2 + m, :], ALU.mult).then_inc(*VEC(f"km{n}"))
                        for m in range(2):
                            c = P_AT["r_k"][0] + m
                            vec.wait_ge(*VEC[f"km{2 + m}"])
                            vec.tensor_tensor(bonus[:, m, :], kmod[:, 0, m, :], kmod[:, 1, m, :], ALU.add).then_inc(*VEC(f"bo{m}a"))
                            vec.wait_ge(*VEC[f"bo{m}a"])
                            vec.scalar_tensor_tensor(out=bonus[:, m, :], in0=bonus[:, m, :], scalar=0.5, in1=rw[:, m, :],
                                                     op0=ALU.mult, op1=ALU.mult).then_inc(*VEC(f"bo{m}b"))
                            vec.wait_ge(*VEC[f"bo{m}b"])
                            vec.tensor_scalar(bonus[:, m, :], bonus[:, m, :], params[:, c:c + 1], None, ALU.mult).then_inc(*VEC(f"bo{m}"))
                        for m in range(2):
                            vec.wait_ge(*ACT[f"kk_rs{m}"])
                            vec.tensor_tensor(rw[:, 2 + m, :], kx[:, m, :], ksum[:, :], ALU.mult).then_inc(*VEC(f"kk{m}"))
                            for e in range(2):
                                vec.wait_ge(*VEC[f"kk{m}"])
                                vec.tensor_tensor(bb[:, e, m, :], a_all[:, e, m, :], rw[:, 2 + m, :], ALU.mult).then_inc(*VEC(f"b{e}{m}"))
                clear()

                with ExitStack() as st2:
                    dch = sbuf(st2, "dch", [P, 4, P])
                    vs = sbuf(st2, "vs", [P, 4, P])
                    pp = sbuf(st2, "pp", [P, 4, P + 1])
                    pc = sbuf(st2, "pc", [P, 4, P + 1])
                    ip = sbuf(st2, "ip", [P, 4, P + 1])
                    mid = sbuf(st2, "mid", [P, 2, 4])
                    last = sbuf(st2, "last", [P, 2, 4])
                    cinv = sbuf(st2, "cinv", [P, 2, 4])
                    wcm = sbuf(st2, "wcm", [P, 4])
                    KR = sbuf(st2, "KR", [P, 2, 4, 2, P])
                    KB = sbuf(st2, "KB", [P, 2, 2, 2, P])
                    KBt = sbuf(st2, "KBt", [P, 2, 4, 2, P])
                    vt = sbuf(st2, "vt", [P, 2, 4, P])
                    MT = sbuf(st2, "MT", [P, 2, 8, 4, P])
                    X = sbuf(st2, "X", [P, 2, 8, P])
                    Y = sbuf(st2, "Y", [P, 2, 8, P])
                    Pm = sbuf(st2, "Pm", [P, 8, P])
                    Rs = sbuf(st2, "Rs", [P, 4, P])
                    sa = sbuf(st2, "sa", [P, 4, P])
                    yo = sbuf(st2, "yo", [P, 2, 3, RW])
                    Z = sbuf(st2, "Z", [P, 4, P])
                    Zc = sbuf(st2, "Zc", [P, 4, P])
                    Zt = sbuf(st2, "Zt", [P, 4, P])
                    bon = sbuf(st2, "bon", [P, 2, 4])
                    zero = sbuf(st2, "zero", [P, P])
                    begin("rw_state")
                    with nc.Block() as block:
                        @block.vector
                        def _(vec):
                            vec.memset(Z[:, :, :], 0.0).then_inc(*VEC("z"))
                            vec.memset(zero[:, :], 0.0).then_inc(*VEC("zero"))
                            vec.memset(Pm[:, :, :], 0.0).then_inc(*VEC("pm"))
                            vec.memset(pp[:, :, :], 1.0).then_inc(*VEC("edges"))
                    clear()
                    MID = P // 2

                    def bank(g):
                        return g

                    def turn_bank(g):
                        return 2 + g

                    def pair_bank(s, u):
                        return 4 + u % 4 if s or u < 4 else u - 4

                    def spans(e):
                        return (slice(1, P + 1), slice(0, P)) if e == 0 else (slice(0, P), slice(1, P + 1))

                    with nc.Fori(0, NT // 2) as c:
                        begin("rw_chunk")
                        with nc.Block() as block:
                            off = [[c * (2 * P) + s * P, (NT - 1 - s) * P - c * (2 * P)] for s in range(2)]

                            @block.scalar
                            def _(act):
                                def begin_front(s):
                                    if s:
                                        act.wait_ge(*VEC["scan0_1"])
                                    for e in range(2):
                                        act.copy(dch[:, 2 * e:2 * e + 2, :], dec[:, e, :, ds(off[s][e], P)]).then_inc(*ACT(f"dch{s}_{e}"))
                                    if s:
                                        act.wait_ge(*PE["vt0"])
                                    for e in range(2):
                                        act.copy(vs[:, 2 * e:2 * e + 2, :], rw[:, 4:6, ds(off[s][e], P)]).then_inc(*ACT(f"vs{s}_{e}"))

                                def front(s, k):
                                    if k == 0:
                                        act.wait_ge(*PE[f"vt{s}"])
                                        act.copy(vt[:, s, :, :], ps[:, 4, :].rearrange("p (u n) -> p u n", u=4)).then_inc(*ACT(f"vt{s}"))
                                    elif k == 6:
                                        for e in range(2):
                                            act.wait_ge(*PE[f"KBt{s}_{e}"])
                                            act.copy(KBt[:, s, 2 * e:2 * e + 2, :, :].rearrange("p a k n -> p (a k) n"),
                                                     ps[:, 4 + e, :].rearrange("p (u n) -> p u n", u=4)).then_inc(*ACT(f"KBt{s}_{e}"))

                                def tail(s, k):
                                    if k == 0:
                                        act.wait_ge(*PE[f"R{s}"])
                                        act.mul(Rs[:, :, :], ps[:, 4, :].rearrange("p (u n) -> p u n", u=4), -1.0).then_inc(*ACT(f"R{s}"))
                                    elif k == 1:
                                        act.wait_ge(*PE[f"sa{s}"])
                                        act.copy(sa[:, :, :], ps[:, 5, :].rearrange("p (u n) -> p u n", u=4)).then_inc(*ACT(f"sa{s}"))
                                    elif k == 2:
                                        act.wait_ge(*PE[f"y{s}"])
                                        act.copy(yo[:, s, 0:2, :], ps[:, 6, :].rearrange("p (u n) -> p u n", u=2)).then_inc(*ACT(f"y{s}"))
                                    elif k == 6 and s == 0:
                                        tail(1, 0)
                                begin_front(0)
                                front(0, 0)
                                front(0, 6)
                                begin_front(1)
                                invert_scalar(act, 0, 4, turn_bank, X[:, 0], Y[:, 0], lambda k: front(1, k))
                                invert_scalar(act, 1, 4, turn_bank, X[:, 1], Y[:, 1], lambda k: tail(0, k))
                                tail(1, 1)
                                tail(1, 2)

                            @block.gpsimd
                            def _(pool):
                                for s in range(2):
                                    pool.wait_ge(*VEC[f"pc{s}"])
                                    for e in range(2):
                                        u = slice(2 * e, 2 * e + 2)
                                        inc, exc = spans(e)
                                        pool.tensor_tensor(KR[:, s, u, 0, :], rw[:, 2:4, ds(off[s][e], P)], pc[:, u, exc], ALU.mult)
                                        pool.tensor_tensor(KR[:, s, u, 1, :], rw[:, 0:2, ds(off[s][e], P)], pc[:, u, inc], ALU.mult).then_inc(*POOL(f"KR{s}_{e}"))

                            @block.vector
                            def _(vec):
                                def masks(s, u):
                                    e = u // 4
                                    vec.wait_ge(*PE[f"pairs{s}_{u}"])
                                    bank = ps[:, pair_bank(s, u), :].rearrange("p (a b n) -> p a b n", a=2, b=2)
                                    before = cst("bef" if e == 0 else "aft")
                                    upto = cst("tri_f" if e == 0 else "tri_b")
                                    M4 = MT[:, s, u, :, :].rearrange("p (a b) n -> p a b n", a=2)
                                    vec.tensor_tensor(M4[:, :, 0, :], bank[:, :, 0, :], rep(before, 2), ALU.mult)
                                    vec.tensor_tensor(M4[:, :, 1, :], bank[:, :, 1, :], rep(upto, 2), ALU.mult).then_inc(*VEC(f"MT{s}_{u}"))

                                def inverse_products(s, e):
                                    u = slice(2 * e, 2 * e + 2)
                                    vec.wait_ge(*VEC[f"pc{s}"])
                                    vec.reciprocal(ip[:, u, :], pc[:, u, :]).then_inc(*VEC(f"ip{s}_{e}"))
                                    vec.wait_ge(*VEC[f"ip{s}_{e}"])
                                    vec.wait_ge(*DMA[f"kb{s}"])
                                    vec.tensor_tensor(KB[:, e], KB[:, e], ip[:, u, spans(e)[0]][:, None, :, :].broadcast_to([P, 2, 2, P]),
                                                      ALU.mult).then_inc(*VEC(f"KB{s}_{e}"))

                                def front(s, k):
                                    if k == 0:
                                        if s:
                                            vec.wait_ge(*POOL["KR0_1"])
                                        for e in range(2):
                                            vec.wait_ge(*ACT[f"dch{s}_{e}"])
                                            for m in range(2):
                                                u = 2 * e + m
                                                if e == 0:
                                                    o, d = pp[:, u, 1:P + 1], dch[:, u, :]
                                                else:
                                                    o, d = pp[:, u, 0:P][:, ::-1], dch[:, u, :][:, ::-1]
                                                q = vec.tensor_tensor_scan(o, d, zero[:, :], 1.0, ALU.mult, ALU.add)
                                            q.then_inc(*VEC(f"scan{s}_{e}"))
                                        vec.wait_ge(*VEC[f"scan{s}_0"])
                                        vec.wait_ge(*VEC[f"scan{s}_1"])
                                        vec.tensor_copy(mid[:, s, :], pp[:, :, MID])
                                        for e in range(2):
                                            vec.tensor_copy(last[:, s, 2 * e:2 * e + 2], pp[:, 2 * e:2 * e + 2, 0 if e else P])
                                        vec.reciprocal(cinv[:, s, :], pp[:, :, MID]).then_inc(*VEC(f"cinv{s}"))
                                        vec.wait_ge(*VEC[f"cinv{s}"])
                                        vec.tensor_tensor(pc[:, :, :], pp[:, :, :], col(cinv[:, s, :], P + 1), ALU.mult).then_inc(*VEC(f"pc{s}"))
                                    elif k == 1:
                                        inverse_products(s, 0)
                                    elif k == 2:
                                        inverse_products(s, 1)
                                        masks(s, 0)
                                        masks(s, 1)
                                    elif k < 6:
                                        masks(s, 2 * (k - 2))
                                        masks(s, 2 * (k - 2) + 1)

                                def scale_state(s):
                                    vec.tensor_tensor(Zc[:, :, :], Z[:, :, :], col(mid[:, s, :], P), ALU.mult).then_inc(*VEC(f"Zc{s}"))

                                def tail(s, k):
                                    if k == 0:
                                        vec.tensor_copy(bon[:, s:s + 1, :], bonus_sum[:, ds(c * 2 + s, 1), :]).then_inc(*VEC(f"bon{s}"))
                                        vec.wait_ge(*VEC[f"bon{s}"])
                                        vec.wait_ge(*ACT[f"vt{s}"])
                                        vec.tensor_tensor(yo[:, s, 2, :].rearrange("p (h n) -> p h n", h=4),
                                                          vt[:, s, 0:2, :].rearrange("p m (h n) -> p (m h) n", h=2), col(bon[:, s, :], RD),
                                                          ALU.mult).then_inc(*VEC(f"bonus{s}"))
                                    elif k == 1:
                                        vec.tensor_tensor(wcm[:, :], last[:, s, :], cinv[:, s, :], ALU.mult).then_inc(*VEC(f"wcm{s}"))
                                        vec.wait_ge(*VEC[f"Zc{s}"])
                                        vec.tensor_tensor(Z[:, :, :], Z[:, :, :], col(last[:, s, :], P), ALU.mult).then_inc(*VEC(f"Zdec{s}"))
                                    elif k == 3:
                                        vec.wait_ge(*PE[f"Zn{s}"])
                                        vec.tensor_tensor(Zt[:, :, :], ps[:, 7, :].rearrange("p (u n) -> p u n", u=4), rep(blk, 4), ALU.mult).then_inc(*VEC(f"Zt{s}"))
                                        vec.wait_ge(*VEC[f"wcm{s}"])
                                        vec.wait_ge(*VEC[f"Zt{s}"])
                                        vec.tensor_tensor(Zt[:, :, :], Zt[:, :, :], col(wcm[:, :], P), ALU.mult).then_inc(*VEC(f"Zt{s}b"))
                                        vec.wait_ge(*VEC[f"Zt{s}b"])
                                        vec.tensor_tensor(Z[:, :, :], Z[:, :, :], Zt[:, :, :], ALU.add).then_inc(*VEC(f"Z{s}"))
                                        if s == 0:
                                            vec.wait_ge(*VEC["Z0"])
                                            scale_state(1)
                                for k in range(6):
                                    front(0, k)
                                scale_state(0)
                                invert_vector(vec, 0, 4, P, bank, "MT0_7", MT[:, 0, :, 0, :], X[:, 0], Y[:, 0], Pm, lambda k: front(1, k))
                                invert_vector(vec, 1, 4, P, bank, "MT1_7", MT[:, 1, :, 0, :], X[:, 1], Y[:, 1], Pm, lambda k: tail(0, k))
                                for k in range(4):
                                    tail(1, k)

                            @block.tensor
                            def _(pe):
                                def front(s, k):
                                    if k == 0:
                                        pe.wait_ge(*ACT[f"vs{s}_1"])
                                        if s:
                                            pe.wait_ge(*ACT["KBt0_1"])
                                        for u in range(4):
                                            q = pe.transpose(ps[:, 4, u * P:(u + 1) * P], vs[:, u, :], ident)
                                        q.then_inc(*PE(f"vt{s}"))
                                    elif 2 <= k < 6:
                                        e, m = (k - 2) // 2, k % 2
                                        pe.wait_ge(*POOL[f"KR{s}_{e}"])
                                        pe.wait_ge(*VEC[f"KB{s}_{e}"])
                                        if k == 2:
                                            pe.wait_ge(*ACT[f"vt{s}"])
                                        for h in range(2):
                                            u, c0 = 4 * e + 2 * m + h, slice(64 * h, 64 * h + 64)
                                            if s and u >= 4:
                                                pe.wait_ge(*VEC[f"MT{s}_{u - 4}"])
                                            for kb in range(2):
                                                q = pe.matmul(ps[:, pair_bank(s, u), 256 * kb:256 * kb + 256], lhsT=KB[c0, e, kb, m, :],
                                                              rhs=KR[c0, s, 2 * e + m, :, :], start=True, stop=True)
                                            q.then_inc(*PE(f"pairs{s}_{u}"))
                                    elif k == 6:
                                        for e in range(2):
                                            pe.wait_ge(*VEC[f"MT{s}_{4 * s + e}"])
                                            for m in range(2):
                                                for kb in range(2):
                                                    n = (2 * m + kb) * P
                                                    q = pe.transpose(ps[:, 4 + e, n:n + P], KB[:, e, kb, m, :], ident)
                                            q.then_inc(*PE(f"KBt{s}_{e}"))

                                def tail(s, k):
                                    if k == 0:
                                        pe.wait_ge(*VEC[f"Zc{s}"])
                                        if s == 0:
                                            pe.wait_ge(*ACT[f"Y0_{NLEV - 1}_1"])
                                            pe.wait_ge(*ACT["KBt1_1"])
                                        for em in range(4):
                                            pe.matmul(ps[:, 4, em * P:(em + 1) * P], lhsT=KR[:, s, em, 0, :], rhs=Zc[:, em, :], start=True, stop=False,
                                                      skip_group_check=True)
                                            for h in range(2):
                                                n = slice(em * P + 64 * h, em * P + 64 * h + 64)
                                                q = pe.matmul(ps[:, 4, n], lhsT=MT[:, s, 2 * em + h, 2, :], rhs=vt[:, s, em, 64 * h:64 * h + 64],
                                                              start=False, stop=True, skip_group_check=True)
                                        q.then_inc(*PE(f"R{s}"))
                                    elif k == 1:
                                        pe.wait_ge(*ACT[f"Y{s}_{NLEV - 1}_1"])
                                        pe.wait_ge(*ACT[f"R{s}"])
                                        for u in range(8):
                                            n = slice(64 * u, 64 * u + 64)
                                            q = pe.matmul(ps[:, 5, n], lhsT=Y[:, s, u, :], rhs=Rs[:, u // 2, 64 * (u % 2):64 * (u % 2) + 64], start=True, stop=True)
                                        q.then_inc(*PE(f"sa{s}"))
                                    elif k == 2:
                                        pe.wait_ge(*ACT[f"sa{s}"])
                                        for em in range(4):
                                            pe.matmul(ps[:, 6, em * P:(em + 1) * P], lhsT=KR[:, s, em, 1, :], rhs=Zc[:, em, :], start=True, stop=False,
                                                      skip_group_check=True)
                                            for h in range(2):
                                                n, hs = slice(em * P + 64 * h, em * P + 64 * h + 64), slice(64 * h, 64 * h + 64)
                                                pe.matmul(ps[:, 6, n], lhsT=MT[:, s, 2 * em + h, 1, :], rhs=sa[:, em, hs], start=False, stop=False,
                                                          skip_group_check=True)
                                                q = pe.matmul(ps[:, 6, n], lhsT=MT[:, s, 2 * em + h, 3, :], rhs=vt[:, s, em, hs], start=False, stop=True,
                                                              skip_group_check=True)
                                        q.then_inc(*PE(f"y{s}"))
                                    elif k == 3:
                                        for em in range(4):
                                            pe.matmul(ps[:, 7, em * P:(em + 1) * P], lhsT=KBt[:, s, em, 0, :], rhs=sa[:, em, :], start=True, stop=False)
                                            q = pe.matmul(ps[:, 7, em * P:(em + 1) * P], lhsT=KBt[:, s, em, 1, :], rhs=vt[:, s, em, :], start=False, stop=True)
                                        q.then_inc(*PE(f"Zn{s}"))
                                    elif k == 6 and s == 0:
                                        tail(1, 0)
                                for k in range(7):
                                    front(0, k)
                                invert_tensor(pe, 0, 4, P, bank, turn_bank, lambda u: MT[:, 0, u, 0, :], X[:, 0], Y[:, 0], Pm, lambda k: front(1, k))
                                invert_tensor(pe, 1, 4, P, bank, turn_bank, lambda u: MT[:, 1, u, 0, :], X[:, 1], Y[:, 1], Pm, lambda k: tail(0, k))
                                for k in range(1, 4):
                                    tail(1, k)

                            @block.sync
                            def _(sp):
                                for s in range(2):
                                    if s:
                                        sp.wait_ge(*PE["KBt0_1"])
                                    for e in range(2):
                                        sp.dma_start(KB[:, e].rearrange("p k m n -> p (k m) n"),
                                                     kb_hbm[:, e, :, :, ds(off[s][e], P)].rearrange("p k m n -> p (k m) n")).then_inc(*DMA(f"kb{s}"))
                                for s in range(2):
                                    sp.wait_ge(*VEC[f"bonus{s}"])
                                    sp.dma_start(rwkv_hbm[2, ds(off[s][0], P), :], yo[:, s, 2, :]).then_inc(*DMA("y_out"))
                                    sp.wait_ge(*ACT[f"y{s}"])
                                    for e in range(2):
                                        sp.dma_start(rwkv_hbm[e, ds(off[s][e], P), :], yo[:, s, e, :]).then_inc(*DMA("y_out"))
                                sp.wait_ge(*DMA["y_out"])
                        clear()

            with ExitStack() as st:
                gq = sbuf(st, "gq", [P, 9, SEQ])
                with ExitStack() as st2:
                    wc = sbuf(st2, "w_cols_g", [P, 3, KD, P])
                    xp = sbuf(st2, "x_pad_g", [P, 2, SEQ + 4])
                    acc = sbuf(st2, "acc_g", [P, 2, SEQ])
                    act_out = sbuf(st2, "act_out", [P, 2, SEQ])
                    sq = sbuf(st2, "sq_g", [P, 2, SEQ])
                    rs = sbuf(st2, "rs_g", [P, 2, SEQ])
                    load_columns(wc, [COL_GDN, COL_GDN + P, COL_GDN + 6 * P])
                    begin("gdn_zero")
                    with nc.Block() as block:
                        @block.vector
                        def _(vec):
                            vec.memset(xp[:, :, :], 0.0).then_inc(*VEC("pad"))
                    clear()
                    with nc.Fori(0, 3) as j:
                        tile = [2 * j, 2 * j + 1, j + 6]
                        begin("gdn_proj")
                        with nc.Block() as block:
                            @block.tensor
                            def _(pe):
                                def sums(n):
                                    for b in range(2):
                                        pe.wait_ge(*POOL[f"sq{n}_{b}"])
                                        if n == 1:
                                            pe.wait_ge(*ACT[f"ln0_{b}"])
                                        pe.matmul(ps[:, 6 + b, :], lhsT=blk, rhs=sq[:, n, b * 512:(b + 1) * 512], start=True,
                                                  stop=True).then_inc(*PE(f"sumsq{n}_{b}"))
                                project_tensor(pe, wc[:, 0], 0)
                                project_tensor(pe, wc[:, 1], 1)
                                sums(0)
                                project_tensor(pe, wc[:, 2], 2)
                                sums(1)

                            @block.sync
                            def _(sp):
                                for n in range(3):
                                    sp.wait_ge(*PE[f"proj{n}_1"])
                                    step = (2, 2, 1)[n]
                                    first_next = (step + (0, 1, 6)[n]) * P + COL_GDN
                                    sp.dma_start(wc[:, n, :, :], w_rows(w_in[:, ds(j * (step * P) + first_next, P)])).then_inc(*DMA("w_cols"))
                                sp.wait_ge(*DMA["w_cols"])

                            @block.scalar
                            def _(act):
                                def log_norms(n):
                                    for b in range(2):
                                        act.wait_ge(*PE[f"sumsq{n}_{b}"])
                                        act.activation(rs[:, n, b * 512:(b + 1) * 512], ps[:, 6 + b, :], FN.Ln, bias=cst("eps")).then_inc(*ACT(f"ln{n}_{b}"))
                                for n in range(2):
                                    project_copy(act, xp, n, None)
                                    act.wait_ge(*VEC[f"tap{n}_{CONV - 1}"])
                                    act.activation(act_out[:, n, :], acc[:, n, :], FN.Silu).then_inc(*ACT(f"silu{n}"))
                                log_norms(0)
                                project_copy(act, xp, 2, f"tap0_{CONV - 1}")
                                log_norms(1)
                                act.wait_ge(*ACT["ln1_1"])
                                act.activation(rs[:, :, :], rs[:, :, :], FN.Exp, scale=-0.5).then_inc(*ACT("rs"))
                                act.wait_ge(*VEC[f"tap2_{CONV - 1}"])
                                act.activation(gq[:, ds(tile[2], 1), :], acc[:, 0, :], FN.Silu).then_inc(*ACT("silu2"))

                            @block.vector
                            def _(vec):
                                at = P_AT["conv"][0]
                                for n in range(3):
                                    x, a = xp[:, n % 2, :], acc[:, n % 2, :]
                                    base, step = (0, CONV, 6 * CONV)[n] + at, (2, 2, 1)[n] * CONV
                                    vec.wait_ge(*ACT[f"proj{n}_1"])
                                    if n == 2:
                                        vec.wait_ge(*ACT["silu0"])
                                    vec.tensor_scalar(a, x[:, 0:SEQ], params[:, ds(j * step + base, 1)], None, ALU.mult).then_inc(*VEC(f"tap{n}_0"))
                                    for m in range(1, CONV):
                                        vec.wait_ge(*VEC[f"tap{n}_{m - 1}"])
                                        vec.scalar_tensor_tensor(out=a, in0=x[:, m:m + SEQ], scalar=params[:, ds(j * step + (base + m), 1)],
                                                                 in1=a, op0=ALU.mult, op1=ALU.add).then_inc(*VEC(f"tap{n}_{m}"))
                                vec.wait_ge(*ACT["rs"])
                                vec.tensor_tensor(gq[:, ds(tile[0], 2), :], act_out[:, :, :], rs[:, :, :], ALU.mult).then_inc(*VEC("normed"))

                            @block.gpsimd
                            def _(pool):
                                for n in range(2):
                                    pool.wait_ge(*ACT[f"silu{n}"])
                                    for b in range(2):
                                        t = slice(b * 512, (b + 1) * 512)
                                        pool.tensor_tensor(sq[:, n, t], act_out[:, n, t], act_out[:, n, t], ALU.mult).then_inc(*POOL(f"sq{n}_{b}"))
                        clear()

                G2 = 2 * GH
                tm_ab = sbuf(st, "tm_ab", [P, NT, 2 * G2])
                gb = sbuf(st, "gb", [P, NT, 2, G2])
                begin("gdn_gates")
                with ExitStack() as st2, nc.Block() as block:
                    pre = sbuf(st2, "pre", [P, NT, G2])
                    mag = sbuf(st2, "mag", [P, NT, G2])
                    soft = sbuf(st2, "soft", [P, NT, G2])
                    rate = sbuf(st2, "rate", [P, G2])

                    @block.sync
                    def _(sp):
                        sp.dma_start(tm_ab[:, :, :], tm_hbm[:, 0:2 * G2].rearrange("(t p) n -> p t n", p=P)).then_inc(*DMA("ab"))
                        sp.wait_ge(*DMA["ab"])

                    @block.vector
                    def _(vec):
                        vec.wait_ge(*DMA["ab"])
                        vec.tensor_tensor(pre[:, :, :], tm_ab[:, :, 0:G2], rep(par("dt"), NT), ALU.add).then_inc(*VEC("pre"))
                        vec.wait_ge(*VEC["pre"])
                        vec.scalar_tensor_tensor(out=mag[:, :, :], in0=pre[:, :, :], scalar=-1.0, in1=pre[:, :, :], op0=ALU.mult,
                                                 op1=ALU.max).then_inc(*VEC("mag"))
                        vec.wait_ge(*ACT["soft"])
                        vec.scalar_tensor_tensor(out=soft[:, :, :], in0=pre[:, :, :], scalar=0.0, in1=soft[:, :, :], op0=ALU.max,
                                                 op1=ALU.add).then_inc(*VEC("soft"))
                        vec.wait_ge(*VEC["soft"])
                        vec.wait_ge(*ACT["rate"])
                        vec.tensor_tensor(soft[:, :, :], soft[:, :, :], rep(rate[:, :], NT), ALU.mult).then_inc(*VEC("soft2"))
                        vec.wait_ge(*VEC["soft2"])
                        vec.tensor_scalar(gb[:, :, 0, :], soft[:, :, :], -1.0, None, ALU.mult).then_inc(*VEC("g"))

                    @block.scalar
                    def _(act):
                        act.activation(rate[:, :], par("a_log"), FN.Exp).then_inc(*ACT("rate"))
                        act.wait_ge(*VEC["mag"])
                        act.activation(soft[:, :, :], mag[:, :, :], FN.Exp, scale=-1.0).then_inc(*ACT("exp"))
                        act.wait_ge(*ACT["exp"])
                        act.activation(soft[:, :, :], soft[:, :, :], FN.Ln, bias=1.0).then_inc(*ACT("soft"))
                        act.activation(gb[:, :, 1, :], tm_ab[:, :, G2:2 * G2], FN.Sigmoid).then_inc(*ACT("beta"))
                clear()

                with ExitStack() as st2:
                    kq = sbuf(st2, "kq", [P, 2, 6, 2, P])
                    vs = sbuf(st2, "vs_g", [P, 6, P])
                    gch = sbuf(st2, "gch", [P, 2, 2, 2, GH])
                    Gm = sbuf(st2, "Gm", [P, 12, P])
                    DT = sbuf(st2, "DT", [P, 12, P])
                    DTb = sbuf(st2, "DTb", [P, 12, P])
                    gx = sbuf(st2, "gx", [P, 2, 2, 3, GH])
                    AT = sbuf(st2, "AT", [P, 2, 12, P])
                    PT = sbuf(st2, "PT", [P, 2, 12, P])
                    kt = sbuf(st2, "kt", [P, 2, 2, GW])
                    vt = sbuf(st2, "vt_g", [P, 2, 2, GW])
                    X = sbuf(st2, "X_g", [P, 2, 12, P])
                    Y = sbuf(st2, "Y_g", [P, 2, 12, P])
                    Pm = sbuf(st2, "Pm_g", [P, 12, P // 2])
                    R = sbuf(st2, "R_g", [P, 2, GW])
                    U = sbuf(st2, "U_g", [P, 2, GW])
                    Ur = sbuf(st2, "Ur_g", [P, 2, GW])
                    o = sbuf(st2, "o_g", [P, 2, 2, GW])
                    S = sbuf(st2, "S_g", [P, 6, P])
                    St = vs
                    begin("gdn_state")
                    with nc.Block() as block:
                        @block.vector
                        def _(vec):
                            vec.memset(S[:, :, :], 0.0).then_inc(*VEC("s"))
                    clear()

                    def heads(ap):
                        return ap.rearrange("p (h n) -> p h n", n=GD)

                    def units(b0, n, w):
                        return ps[:, b0:b0 + (n * w + 511) // 512, :].rearrange("p b n -> p (b n)")[:, 0:n * w].rearrange("p (u n) -> p u n", u=n)

                    def bank(g):
                        return g

                    def turn_bank(g):
                        return 2 + 2 * g
                    FRONT_AT = ((0, 2, 6, 4, 0, 2, 4), (6,) * 7)
                    TAIL_AT = ((6, 6, 6, 6), (6, 0, 2, 4))

                    with nc.Fori(0, NT // 2) as c:
                        begin("gdn_chunk")
                        with nc.Block() as block:
                            chunk = [[c * 2 + s, (NT - 1 - s) - c * 2] for s in range(2)]
                            off = [[c * (2 * P) + s * P, (NT - 1 - s) * P - c * (2 * P)] for s in range(2)]

                            @block.scalar
                            def _(act):
                                def begin_front(s):
                                    if s:
                                        act.wait_ge(*PE["turned0_1"])
                                    act.copy(kq[:, s, 0:3, 0, :], gq[:, 3:6, ds(off[s][0], P)])
                                    act.copy(kq[:, s, 0:3, 1, :], gq[:, 0:3, ds(off[s][0], P)])
                                    act.copy(vs[:, 0:3, :], gq[:, 6:9, ds(off[s][0], P)]).then_inc(*ACT(f"v{s}"))

                                def front(s, k):
                                    at = FRONT_AT[s][k]
                                    if k < 2:
                                        act.wait_ge(*PE[f"diff{s}_{k}"])
                                        act.activation(DT[:, 6 * k:6 * k + 6, :], units(at, 6, P), FN.Exp).then_inc(*ACT(f"DT{s}_{k}"))
                                    elif k < 4:
                                        e = k - 2
                                        act.wait_ge(*PE[f"turned{s}_{e}"])
                                        if e == 0:
                                            act.activation(gx[:, s, :, :, :].rearrange("p e a h -> p (e a h)"), ps[:, at + 1, GW:GW + 36], FN.Exp).then_inc(*ACT(f"gx{s}"))
                                        act.copy(kt[:, s, e, :], ps[:, at, 0:GW]).then_inc(*ACT(f"kt{s}_{e}"))
                                        act.copy(vt[:, s, e, :], ps[:, at + 1, 0:GW]).then_inc(*ACT(f"vt{s}_{e}"))
                                begin_front(0)
                                for k in range(4):
                                    front(0, k)
                                begin_front(1)
                                invert_scalar(act, 0, 6, turn_bank, X[:, 0], Y[:, 0], lambda k: front(1, k))
                                invert_scalar(act, 1, 6, turn_bank, X[:, 1], Y[:, 1], lambda k: None)

                            @block.gpsimd
                            def _(pool):
                                for s in range(2):
                                    pool.wait_ge(*VEC[f"gch{s}"])
                                    pool.tensor_tensor(Gm[:, 6:12, :], col(gch[:, s, 1, 0, :], P), rep(cst("tri_b"), 6), ALU.mult).then_inc(*POOL(f"Gm{s}"))
                                    pool.wait_ge(*ACT[f"DT{s}_1"])
                                    pool.tensor_tensor(DT[:, 6:12, :], DT[:, 6:12, :], rep(cst("tri_b"), 6), ALU.mult).then_inc(*POOL(f"DTm{s}"))

                            @block.tensor
                            def _(pe):
                                def front(s, k):
                                    at = FRONT_AT[s][k]
                                    if k < 2:
                                        pe.wait_ge(*(POOL[f"Gm{s}"] if k else VEC[f"Gm{s}"]))
                                        if s:
                                            pe.wait_ge(*(ACT["DT1_0"] if k else VEC["gkS0"]))
                                        g = Gm[:, 6 * k:6 * k + 6, :].rearrange("p u n -> p (u n)")
                                        behind = cst("bef" if k else "aft")
                                        pe.matmul(ps[:, at, :], lhsT=behind, rhs=g[:, 0:512], start=True, stop=True)
                                        pe.matmul(ps[:, at + 1, 0:256], lhsT=behind, rhs=g[:, 512:768], start=True, stop=True).then_inc(*PE(f"diff{s}_{k}"))
                                    elif k < 4:
                                        e = k - 2
                                        pe.wait_ge(*(VEC if e else ACT)[f"v{s}"])
                                        if s:
                                            pe.wait_ge(*(ACT["vt1_0"] if e else ACT["DT1_1"]))
                                        for m in range(3):
                                            pe.transpose(ps[:, at, m * P:(m + 1) * P], kq[:, s, 3 * e + m, 0, :], ident)
                                            q = pe.transpose(ps[:, at + 1, m * P:(m + 1) * P], vs[:, 3 * e + m, :], ident)
                                        if e == 0:
                                            for d in range(2):
                                                mats = (cst("tri_b"), cst("bef"), ones) if d else (cst("tri_f"), cst("aft"), ones)
                                                for n, mat in enumerate(mats):
                                                    i = GW + (3 * d + n) * GH
                                                    q = pe.matmul(ps[:, at + 1, i:i + GH], lhsT=mat, rhs=gch[:, s, d, 0, :], start=True, stop=True)
                                        q.then_inc(*PE(f"turned{s}_{e}"))
                                    else:
                                        pe.wait_ge(*(ACT[f"vt{s}_1"] if k == 4 or s == 0 else VEC[f"PT{s}_{k - 1}"]))
                                        for em in (2 * (k - 4), 2 * (k - 4) + 1):
                                            for h in range(2):
                                                c0 = slice(64 * h, 64 * h + 64)
                                                q = pe.matmul(ps[:, at + h, 256 * (em % 2):256 * (em % 2) + 256], lhsT=kq[c0, s, em, 0, :],
                                                              rhs=kq[c0, s, em, :, :], start=True, stop=True)
                                                q.then_inc(*PE(f"pairs{s}_{em}_{h}"))

                                def keys_on_state(s):
                                    pe.wait_ge(*(VEC["S0"] if s else ACT["vt0_0"]))
                                    if s:
                                        pe.wait_ge(*ACT["vt1_1"])
                                    for e in range(2):
                                        for m in range(3):
                                            q = pe.matmul(ps[:, 6 + e, m * P:(m + 1) * P], lhsT=kq[:, s, 3 * e + m, 0, :], rhs=S[:, 3 * e + m, :], start=True, stop=True)
                                    q.then_inc(*PE(f"kS{s}"))

                                def tail(s, k):
                                    at = TAIL_AT[s][k] if k < 4 else None
                                    if k == 0:
                                        pe.wait_ge(*VEC[f"R{s}"])
                                        pe.wait_ge(*ACT[f"Y{s}_{NLEV - 1}_1"])
                                        if s == 0:
                                            pe.wait_ge(*VEC["PT1_6"])
                                        for u in range(12):
                                            e, n = u // 6, slice(64 * (u % 6), 64 * (u % 6) + 64)
                                            q = pe.matmul(ps[:, at + e, n], lhsT=Y[:, s, u, :], rhs=R[:, e, n], start=True, stop=True)
                                        q.then_inc(*PE(f"w{s}"))
                                    elif k == 1:
                                        if s == 0:
                                            pe.wait_ge(*VEC["U0"])
                                        for e in range(2):
                                            for m in range(3):
                                                q = pe.matmul(ps[:, at + e, m * P:(m + 1) * P], lhsT=kq[:, s, 3 * e + m, 1, :], rhs=S[:, 3 * e + m, :], start=True, stop=True)
                                        q.then_inc(*PE(f"qS{s}"))
                                    elif k == 2:
                                        pe.wait_ge(*VEC[f"U{s}"])
                                        if s == 0:
                                            pe.wait_ge(*VEC["gqS0"])
                                        for u in range(12):
                                            e, n = u // 6, slice(64 * (u % 6), 64 * (u % 6) + 64)
                                            q = pe.matmul(ps[:, at + e, n], lhsT=PT[:, s, u, :], rhs=U[:, e, n], start=True, stop=True)
                                        q.then_inc(*PE(f"PU{s}"))
                                    elif k == 3:
                                        pe.wait_ge(*VEC[f"Ur{s}"])
                                        if s == 0:
                                            pe.wait_ge(*VEC["o0"])
                                        for e in range(2):
                                            for m in range(3):
                                                n = slice(m * P, (m + 1) * P)
                                                q = pe.matmul(ps[:, at + e, n], lhsT=kt[:, s, e, n], rhs=Ur[:, e, n], start=True, stop=True)
                                        q.then_inc(*PE(f"Sn{s}"))
                                    elif k == 6 and s == 0:
                                        keys_on_state(1)
                                for k in range(4):
                                    front(0, k)
                                keys_on_state(0)
                                for k in range(4, 7):
                                    front(0, k)
                                invert_tensor(pe, 0, 6, P // 2, bank, turn_bank, lambda u: AT[:, 0, u, :], X[:, 0], Y[:, 0], Pm, lambda k: front(1, k))
                                invert_tensor(pe, 1, 6, P // 2, bank, turn_bank, lambda u: AT[:, 1, u, :], X[:, 1], Y[:, 1], Pm, lambda k: tail(0, k))
                                for k in range(4):
                                    tail(1, k)

                            @block.vector
                            def _(vec):
                                def begin_front(s):
                                    for e in range(2):
                                        q = vec.tensor_copy(gch[:, s, e, :, :], gb[:, ds(chunk[s][e], 1), :, GH * e:GH * e + GH])
                                    q.then_inc(*VEC(f"gch{s}"))
                                    vec.wait_ge(*VEC[f"gch{s}"])
                                    vec.tensor_tensor(Gm[:, 0:6, :], col(gch[:, s, 0, 0, :], P), rep(cst("tri_f"), 6), ALU.mult).then_inc(*VEC(f"Gm{s}"))
                                    vec.tensor_copy(kq[:, s, 3:6, 0, :], gq[:, 3:6, ds(off[s][1], P)])
                                    vec.tensor_copy(kq[:, s, 3:6, 1, :], gq[:, 0:3, ds(off[s][1], P)])
                                    vec.tensor_copy(vs[:, 3:6, :], gq[:, 6:9, ds(off[s][1], P)]).then_inc(*VEC(f"v{s}"))

                                def front(s, k):
                                    if k == 1:
                                        vec.wait_ge(*ACT[f"DT{s}_0"])
                                        vec.tensor_tensor(DT[:, 0:6, :], DT[:, 0:6, :], rep(cst("tri_f"), 6), ALU.mult).then_inc(*VEC(f"DTm{s}"))
                                    elif k in (2, 3):
                                        e = k - 2
                                        vec.wait_ge(*(POOL if e else VEC)[f"DTm{s}"])
                                        vec.tensor_tensor(DTb[:, 6 * e:6 * e + 6, :], DT[:, 6 * e:6 * e + 6, :], col(gch[:, s, e, 1, :], P), ALU.mult).then_inc(*VEC(f"DTb{s}_{e}"))
                                    elif k > 3:
                                        at = FRONT_AT[s][k]
                                        if k == 4:
                                            vec.wait_ge(*VEC[f"DTb{s}_1"])
                                        for h in range(2):
                                            bank = ps[:, at + h, :].rearrange("p (u k n) -> p u k n", k=2, n=P)
                                            vec.wait_ge(*PE[f"pairs{s}_{2 * (k - 4) + 1}_{h}"])

                                            def of_head(ap):
                                                return ap[:, 4 * (k - 4):4 * (k - 3), :].rearrange("p (u h) n -> p u h n", h=2)[:, :, h, :]
                                            vec.tensor_tensor(of_head(AT[:, s]), bank[:, :, 0, :], of_head(DTb), ALU.mult)
                                            q = vec.scalar_tensor_tensor(out=of_head(PT[:, s]), in0=bank[:, :, 1, :], scalar=GD ** -0.5,
                                                                         in1=of_head(DT), op0=ALU.mult, op1=ALU.mult)
                                        q.then_inc(*VEC(f"PT{s}_{k}"))

                                def right_side(s):
                                    vec.wait_ge(*PE[f"kS{s}"])
                                    vec.wait_ge(*ACT[f"vt{s}_1"])
                                    for e in range(2):
                                        q = vec.tensor_tensor(heads(R[:, e, :]), heads(ps[:, 6 + e, 0:GW]), col(gx[:, s, e, 0, :], GD), ALU.mult)
                                    q.then_inc(*VEC(f"gkS{s}"))
                                    vec.wait_ge(*VEC[f"gkS{s}"])
                                    vec.tensor_tensor(R[:, :, :], vt[:, s, :, :], R[:, :, :], ALU.subtract).then_inc(*VEC(f"R{s}"))

                                def tail(s, k):
                                    at = TAIL_AT[s][k] if k < 4 else None
                                    if k == 0:
                                        vec.wait_ge(*PE[f"w{s}"])
                                        for e in range(2):
                                            q = vec.tensor_tensor(heads(U[:, e, :]), heads(ps[:, at + e, 0:GW]), col(gch[:, s, e, 1, :], GD), ALU.mult)
                                        q.then_inc(*VEC(f"U{s}"))
                                        vec.wait_ge(*VEC[f"U{s}"])
                                        for e in range(2):
                                            q = vec.tensor_tensor(heads(Ur[:, e, :]), heads(U[:, e, :]), col(gx[:, s, e, 1, :], GD), ALU.mult)
                                        q.then_inc(*VEC(f"Ur{s}"))
                                    elif k == 1:
                                        vec.wait_ge(*PE[f"qS{s}"])
                                        for e in range(2):
                                            q = vec.tensor_tensor(heads(o[:, s, e, :]), heads(ps[:, at + e, 0:GW]), col(gx[:, s, e, 0, :], GD), ALU.mult)
                                        q.then_inc(*VEC(f"gqS{s}"))
                                    elif k == 2:
                                        vec.wait_ge(*VEC[f"gqS{s}"])
                                        vec.wait_ge(*PE[f"PU{s}"])
                                        vec.scalar_tensor_tensor(out=o[:, s, :, :], in0=o[:, s, :, :], scalar=GD ** -0.5, in1=ps[:, at:at + 2, 0:GW],
                                                                 op0=ALU.mult, op1=ALU.add).then_inc(*VEC(f"o{s}"))
                                        for e in range(2):
                                            su = S[:, 3 * e:3 * e + 3, :].rearrange("p m (h n) -> p (m h) n", h=2)
                                            q = vec.tensor_tensor(su, su, col(gx[:, s, e, 2, :], GD), ALU.mult)
                                        q.then_inc(*VEC(f"Sdec{s}"))
                                    elif k == 3:
                                        vec.wait_ge(*PE[f"Sn{s}"])
                                        for e in range(2):
                                            q = vec.tensor_tensor(St[:, 3 * e:3 * e + 3, :], ps[:, at + e, 0:GW].rearrange("p (m n) -> p m n", n=P), rep(blk, 3), ALU.mult)
                                        q.then_inc(*VEC(f"St{s}"))
                                        vec.wait_ge(*VEC[f"St{s}"])
                                        vec.tensor_tensor(S[:, :, :], S[:, :, :], St[:, :, :], ALU.add).then_inc(*VEC(f"S{s}"))
                                    elif k == 6 and s == 0:
                                        right_side(1)
                                begin_front(0)
                                for k in range(4):
                                    front(0, k)
                                right_side(0)
                                for k in range(4, 7):
                                    front(0, k)
                                begin_front(1)
                                invert_vector(vec, 0, 6, P // 2, bank, "PT0_6", AT[:, 0], X[:, 0], Y[:, 0], Pm, lambda k: front(1, k))
                                invert_vector(vec, 1, 6, P // 2, bank, "PT1_6", AT[:, 1], X[:, 1], Y[:, 1], Pm, lambda k: tail(0, k))
                                for k in range(4):
                                    tail(1, k)

                            @block.sync
                            def _(sp):
                                for s in range(2):
                                    sp.wait_ge(*VEC[f"o{s}"])
                                    for e in range(2):
                                        sp.dma_start(gdn_hbm[e, ds(off[s][e], P), :], o[:, s, e, :]).then_inc(*DMA("o_out"))
                                sp.wait_ge(*DMA["o_out"])
                        clear()

            with ExitStack() as st:
                qT = sbuf(st, "qT", [QK, MH, SEQ])
                kT = sbuf(st, "kT", [QK, MH, SEQ])
                V = sbuf(st, "V", [P, NT, MH, MV])
                with ExitStack() as st2:
                    wq = sbuf(st2, "w_uq", [P, 2, MH * QK])
                    wkv = sbuf(st2, "w_ukv", [P, MH * (NOPE + MV)])
                    begin("mla_load")
                    with nc.Block() as block:
                        @block.sync
                        def _(sp):
                            sp.dma_start(wq[:, 0, :], w_uq[0:P, :]).then_inc(*DMA("w_mla"))
                            sp.dma_start(wq[0:QR - P, 1, :], w_uq[P:QR, :]).then_inc(*DMA("w_mla"))
                            sp.dma_start(wkv[:, :], io["w_ukv"][ds(L, 1)].rearrange("a r n -> (a r) n")).then_inc(*DMA("w_mla"))
                            sp.wait_ge(*DMA["w_mla"])
                    clear()
                    lat = sbuf(st2, "lat", [P, 2, QR + KVR + ROPE])
                    junk = sbuf(st2, "junk", [P, 2, 2, QR])
                    ss = sbuf(st2, "ss_m", [P, 2, 2])
                    rs = sbuf(st2, "rs_m", [P, 2, 2])
                    cn = sbuf(st2, "cn", [P, 2, QR + KVR])
                    cT = sbuf(st2, "cT", [P, 2, 3, P])
                    qk = sbuf(st2, "qk", [P, 2, 2 * MH, QK])
                    tr = sbuf(st2, "tr", [P, 2, 2, MH, ROPE])
                    tk = sbuf(st2, "tk", [P, 2, 2, ROPE])
                    kr = sbuf(st2, "kr", [P, 2, ROPE])
                    csn = sbuf(st2, "csn", [P, 2, 2, ROPE // 2])
                    H2 = ROPE // 2
                    with nc.Fori(0, NT // 2) as t:
                        begin("mla_up")
                        with nc.Block() as block:
                            def tokens(n):
                                return ds(t * (2 * P) + n * P, P)

                            @block.sync
                            def _(sp):
                                for n in range(2):
                                    sp.dma_start(lat[:, n, :], tm_hbm[tokens(n), 4 * GH:TM_W]).then_inc(*DMA(f"lat{n}"))

                            @block.scalar
                            def _(act):
                                for n in range(2):
                                    act.wait_ge(*DMA[f"lat{n}"])
                                    act.activation(junk[:, n, 0, :], lat[:, n, 0:QR], FN.Square, accum_out=ss[:, 0, n:n + 1]).then_inc(*ACT(f"ss0_{n}"))
                                    act.activation(junk[:, n, 1, 0:KVR], lat[:, n, QR:QR + KVR], FN.Square, accum_out=ss[:, 1, n:n + 1]).then_inc(*ACT(f"ss1_{n}"))
                                act.wait_ge(*ACT["ss1_1"])
                                act.activation(rs[:, 0, :], ss[:, 0, :], FN.Ln, bias=cst("eps"), scale=1.0 / QR).then_inc(*ACT("ln0"))
                                act.activation(rs[:, 1, :], ss[:, 1, :], FN.Ln, bias=cst("eps"), scale=1.0 / KVR).then_inc(*ACT("ln1"))
                                act.wait_ge(*ACT["ln1"])
                                act.activation(rs[:, :, :], rs[:, :, :], FN.Exp, scale=-0.5).then_inc(*ACT("rs"))
                                for n in range(2):
                                    for b in range(2):
                                        act.wait_ge(*PE[f"q{n}_{b}"])
                                        act.copy(qk[:, n, 3 * b:3 * b + 3, :], ps[:, 1 + b, 0:3 * QK].rearrange("p (h n) -> p h n", n=QK)).then_inc(*ACT(f"q{n}_{b}"))
                                    for b in range(2):
                                        act.wait_ge(*PE[f"kv{n}_{b}"])
                                        kv = ps[:, 3 + b, 0:3 * (NOPE + MV)].rearrange("p (h n) -> p h n", h=3)
                                        act.copy(qk[:, n, MH + 3 * b:MH + 3 * b + 3, 0:NOPE], kv[:, :, 0:NOPE]).then_inc(*ACT(f"k{n}_{b}"))
                                for n in range(2):
                                    act.wait_ge(*PE[f"qkT{n}_0"])
                                    act.copy(qT[:, 0:4, tokens(n)], ps[0:QK, 5, :].rearrange("p (h n) -> p h n", h=4)).then_inc(*ACT(f"qT{n}_0"))
                                    act.wait_ge(*PE[f"qkT{n}_1"])
                                    act.copy(qT[:, 4:6, tokens(n)], ps[0:QK, 6, 0:256].rearrange("p (h n) -> p h n", h=2)).then_inc(*ACT(f"qT{n}_1"))

                            @block.vector
                            def _(vec):
                                vec.tensor_copy(csn[:, :, :, :], cs[:, ds(t * 2, 2), :, :]).then_inc(*VEC("cos_sin"))
                                vec.wait_ge(*ACT["rs"])
                                for n in range(2):
                                    vec.tensor_scalar(cn[:, n, 0:QR], lat[:, n, 0:QR], rs[:, 0, n:n + 1], None, ALU.mult)
                                    vec.tensor_scalar(cn[:, n, QR:QR + KVR], lat[:, n, QR:QR + KVR], rs[:, 1, n:n + 1], None, ALU.mult).then_inc(*VEC(f"cn{n}"))
                                g = P_AT["q_g"][0]
                                for n in range(2):
                                    vec.wait_ge(*PE[f"cT{n}"])
                                    vec.tensor_scalar(cT[:, n, 0, :], ps[:, 5 * n, 0:P], params[:, g:g + 1], None, ALU.mult)
                                    vec.tensor_scalar(cT[0:QR - P, n, 1, :], ps[0:QR - P, 5 * n, P:2 * P], params[0:QR - P, g + 1:g + 2], None, ALU.mult)
                                    vec.tensor_scalar(cT[:, n, 2, :], ps[:, 5 * n, 2 * P:3 * P], par("kv_g"), None, ALU.mult).then_inc(*VEC(f"cT{n}"))
                                vec.wait_ge(*VEC["cos_sin"])
                                for n in range(2):
                                    cos1, sin1 = csn[:, n, 0, :], csn[:, n, 1, :]
                                    k1, k2 = lat[:, n, QR + KVR:QR + KVR + H2], lat[:, n, QR + KVR + H2:]
                                    vec.tensor_tensor(tk[:, n, 0, 0:H2], k1, cos1, ALU.mult)
                                    vec.tensor_tensor(tk[:, n, 1, 0:H2], k2, sin1, ALU.mult)
                                    vec.tensor_tensor(tk[:, n, 0, H2:], k2, cos1, ALU.mult)
                                    vec.tensor_tensor(tk[:, n, 1, H2:], k1, sin1, ALU.mult).then_inc(*VEC(f"tk{n}"))
                                for n in range(2):
                                    vec.wait_ge(*VEC[f"tk{n}"])
                                    vec.tensor_tensor(kr[:, n, 0:H2], tk[:, n, 0, 0:H2], tk[:, n, 1, 0:H2], ALU.subtract)
                                    vec.tensor_tensor(kr[:, n, H2:], tk[:, n, 0, H2:], tk[:, n, 1, H2:], ALU.add).then_inc(*VEC(f"kr{n}"))
                                for n in range(2):
                                    vec.wait_ge(*VEC[f"kr{n}"])
                                    vec.tensor_copy(qk[:, n, MH:2 * MH, NOPE:QK], rep(kr[:, n, :], MH)).then_inc(*VEC(f"k_rot{n}"))
                                for n in range(2):
                                    cos1, sin1 = csn[:, n, 0, :], csn[:, n, 1, :]
                                    vec.wait_ge(*ACT[f"q{n}_1"])
                                    q1, q2 = qk[:, n, 0:MH, NOPE:NOPE + H2], qk[:, n, 0:MH, NOPE + H2:QK]
                                    vec.tensor_tensor(tr[:, n, 0, :, 0:H2], q1, rep(cos1, MH), ALU.mult)
                                    vec.tensor_tensor(tr[:, n, 1, :, 0:H2], q2, rep(sin1, MH), ALU.mult)
                                    vec.tensor_tensor(tr[:, n, 0, :, H2:], q2, rep(cos1, MH), ALU.mult)
                                    vec.tensor_tensor(tr[:, n, 1, :, H2:], q1, rep(sin1, MH), ALU.mult).then_inc(*VEC(f"tr{n}"))
                                    vec.wait_ge(*VEC[f"tr{n}"])
                                    vec.tensor_tensor(q1, tr[:, n, 0, :, 0:H2], tr[:, n, 1, :, 0:H2], ALU.subtract)
                                    vec.tensor_tensor(q2, tr[:, n, 0, :, H2:], tr[:, n, 1, :, H2:], ALU.add).then_inc(*VEC(f"q_rot{n}"))
                                    for b in range(2):
                                        vec.wait_ge(*PE[f"kv{n}_{b}"])
                                        vec.wait_ge(*ACT[f"k{n}_{b}"])
                                        kv = ps[:, 3 + b, 0:3 * (NOPE + MV)].rearrange("p (h n) -> p h n", h=3)
                                        vec.tensor_copy(V[:, ds(t * 2 + n, 1), 3 * b:3 * b + 3, :], kv[:, None, :, NOPE:NOPE + MV]).then_inc(*VEC(f"v{n}_{b}"))
                                for n in range(2):
                                    vec.wait_ge(*ACT[f"qT{n}_1"])
                                    vec.tensor_copy(kT[:, 0:2, tokens(n)], ps[0:QK, 6, 256:512].rearrange("p (h n) -> p h n", h=2)).then_inc(*VEC(f"kT{n}_1"))
                                    vec.wait_ge(*PE[f"qkT{n}_2"])
                                    vec.tensor_copy(kT[:, 2:6, tokens(n)], ps[0:QK, 7, :].rearrange("p (h n) -> p h n", h=4)).then_inc(*VEC(f"kT{n}_2"))

                            @block.tensor
                            def _(pe):
                                for n in range(2):
                                    pe.wait_ge(*VEC[f"cn{n}"])
                                    pe.transpose(ps[:, 5 * n, 0:P], cn[:, n, 0:P], ident)
                                    pe.transpose(ps[0:QR - P, 5 * n, P:2 * P], cn[:, n, P:QR], ident)
                                    pe.transpose(ps[:, 5 * n, 2 * P:3 * P], cn[:, n, QR:QR + KVR], ident).then_inc(*PE(f"cT{n}"))
                                for n in range(2):
                                    pe.wait_ge(*VEC[f"cT{n}"])
                                    for b in range(2):
                                        if n:
                                            pe.wait_ge(*ACT[f"q0_{b}"])
                                        c = slice(3 * QK * b, 3 * QK * (b + 1))
                                        pe.matmul(ps[:, 1 + b, 0:3 * QK], lhsT=cT[:, n, 0, :], rhs=wq[:, 0, c], start=True, stop=False)
                                        pe.matmul(ps[:, 1 + b, 0:3 * QK], lhsT=cT[0:QR - P, n, 1, :], rhs=wq[0:QR - P, 1, c], start=False,
                                                  stop=True).then_inc(*PE(f"q{n}_{b}"))
                                    for b in range(2):
                                        if n:
                                            pe.wait_ge(*VEC[f"v0_{b}"])
                                        w = 3 * (NOPE + MV)
                                        pe.matmul(ps[:, 3 + b, 0:w], lhsT=cT[:, n, 2, :], rhs=wkv[:, w * b:w * (b + 1)], start=True,
                                                  stop=True).then_inc(*PE(f"kv{n}_{b}"))
                                for n in range(2):
                                    pe.wait_ge(*VEC[f"q_rot{n}"])
                                    pe.wait_ge(*ACT[f"k{n}_1"])
                                    for b in range(3):
                                        if n:
                                            if b < 2:
                                                pe.wait_ge(*ACT[f"qT0_{b}"])
                                            if b:
                                                pe.wait_ge(*VEC[f"kT0_{b}"])
                                        for u in range(4):
                                            q = pe.transpose(ps[0:QK, 5 + b, u * P:(u + 1) * P], qk[:, n, 4 * b + u, :], ident)
                                        q.then_inc(*PE(f"qkT{n}_{b}"))
                        clear()

                with ExitStack() as st2:
                    NU = 2 * MH
                    qs = sbuf(st2, "qs", [QK, NU, P])
                    pr = sbuf(st2, "pr", [P, 2, SEQ])
                    pT = sbuf(st2, "pT", [P, 2, NT, P])
                    mx = sbuf(st2, "mx", [P, NU])
                    nm = sbuf(st2, "nm", [P, NU])
                    den = sbuf(st2, "den", [P, NU])
                    inv = sbuf(st2, "inv", [P, NU])
                    om = sbuf(st2, "om", [P, 2, GW])
                    SC = QK ** -0.5
                    with nc.Fori(0, NT // 2) as t:
                        begin("attend")
                        with nc.Block() as block:
                            @block.tensor
                            def _(pe):
                                def scores(j):
                                    pe.wait_ge(*(VEC if j < MH else ACT)[f"qs{j // MH}"])
                                    if j >= 2:
                                        pe.wait_ge(*ACT[f"p{j - 2}"])
                                    for b in range(2):
                                        q = pe.matmul(ps[:, 2 * (j % 2) + b, :], lhsT=qs[:, j, :], rhs=kT[:, j % MH, b * 512:(b + 1) * 512],
                                                      start=True, stop=True)
                                    q.then_inc(*PE(f"s{j}"))
                                scores(0)
                                scores(1)
                                for j in range(NU):
                                    s = j % 2
                                    pe.wait_ge(*ACT[f"p{j}"])
                                    if j >= 1:
                                        pe.wait_ge(*VEC[f"pT{j - 1}"])
                                        pe.wait_ge(*ACT[f"pT{j - 1}"])
                                    for b in range(2):
                                        for n in range(4):
                                            q = pe.transpose(ps[:, 4 + b, n * P:(n + 1) * P], pr[:, s, (4 * b + n) * P:(4 * b + n + 1) * P], ident)
                                        q.then_inc(*PE(f"t{j}_{b}"))
                                    if j + 2 < NU:
                                        scores(j + 2)
                                    pe.wait_ge(*VEC[f"pT{j}"])
                                    pe.wait_ge(*ACT[f"pT{j}"])
                                    if j >= 2:
                                        pe.wait_ge(*VEC[f"o{j - 2}"])
                                    for k in range(NT):
                                        q = pe.matmul(ps[:, 6 + s, 0:MV], lhsT=pT[:, s, k, :], rhs=V[:, k, j % MH, :], start=(k == 0), stop=(k == NT - 1))
                                    q.then_inc(*PE(f"o{j}"))

                            @block.scalar
                            def _(act):
                                def expo(j):
                                    s = j % 2
                                    act.wait_ge(*VEC[f"nm{j}"])
                                    if j >= 2:
                                        act.wait_ge(*PE[f"t{j - 2}_1"])
                                    act.activation(pr[:, s, :].rearrange("p (b n) -> p b n", b=2), ps[:, 2 * s:2 * s + 2, :], FN.Exp,
                                                   bias=nm[:, j:j + 1], scale=SC, accum_out=den[:, j:j + 1]).then_inc(*ACT(f"p{j}"))
                                act.copy(qs[:, MH:NU, :], qT[:, :, ds(t * (2 * P) + P, P)]).then_inc(*ACT("qs1"))
                                expo(0)
                                expo(1)
                                for j in range(NU):
                                    act.wait_ge(*PE[f"t{j}_1"])
                                    if j >= 2:
                                        act.wait_ge(*PE[f"o{j - 2}"])
                                    act.copy(pT[:, j % 2, 4:8, :], ps[:, 5, :].rearrange("p (k n) -> p k n", k=4)).then_inc(*ACT(f"pT{j}"))
                                    if j + 2 < NU:
                                        expo(j + 2)

                            @block.vector
                            def _(vec):
                                def top(j):
                                    s = j % 2
                                    vec.wait_ge(*PE[f"s{j}"])
                                    vec.tensor_reduce(mx[:, j:j + 1], ps[:, 2 * s:2 * s + 2, :].rearrange("p b n -> p (b n)"), AX, ALU.max).then_inc(*VEC(f"mx{j}"))
                                    vec.wait_ge(*VEC[f"mx{j}"])
                                    vec.tensor_scalar(nm[:, j:j + 1], mx[:, j:j + 1], -SC, None, ALU.mult).then_inc(*VEC(f"nm{j}"))

                                def scale(j):
                                    vec.wait_ge(*PE[f"o{j}"])
                                    vec.tensor_scalar(om[:, j // MH, (j % MH) * MV:(j % MH + 1) * MV], ps[:, 6 + j % 2, 0:MV], inv[:, j:j + 1], None,
                                                      ALU.mult).then_inc(*VEC(f"o{j}"))
                                vec.tensor_copy(qs[:, 0:MH, :], qT[:, :, ds(t * (2 * P), P)]).then_inc(*VEC("qs0"))
                                top(0)
                                top(1)
                                for j in range(NU):
                                    vec.wait_ge(*PE[f"t{j}_0"])
                                    if j >= 2:
                                        vec.wait_ge(*PE[f"o{j - 2}"])
                                    vec.tensor_copy(pT[:, j % 2, 0:4, :], ps[:, 4, :].rearrange("p (k n) -> p k n", k=4)).then_inc(*VEC(f"pT{j}"))
                                    vec.wait_ge(*ACT[f"p{j}"])
                                    vec.reciprocal(inv[:, j:j + 1], den[:, j:j + 1]).then_inc(*VEC(f"inv{j}"))
                                    if j + 2 < NU:
                                        top(j + 2)
                                    if j >= 1:
                                        vec.wait_ge(*VEC[f"inv{j - 1}"])
                                        scale(j - 1)
                                vec.wait_ge(*VEC[f"inv{NU - 1}"])
                                scale(NU - 1)

                            @block.sync
                            def _(sp):
                                for n in range(2):
                                    sp.wait_ge(*VEC[f"o{MH * n + MH - 1}"])
                                    sp.dma_start(mla_hbm[ds(t * (2 * P) + n * P, P), :], om[:, n, :]).then_inc(*DMA("o_out"))
                                sp.wait_ge(*DMA["o_out"])
                        clear()

            with ExitStack() as st:
                wo = sbuf(st, "w_out", [P, KD, DM])
                gi = sbuf(st, "gi", [P, 2, 2, GW])
                ri = sbuf(st, "ri", [P, 2, 3, 2, RW])
                gate = sbuf(st, "gate_in", [P, 2, 2, DM])
                mix = sbuf(st, "mix", [P, 2, 2, DM])
                mT = sbuf(st, "mT", [P, 2, KD, P])
                xt = sbuf(st, "x_t", [P, 4, DM])
                s = sbuf(st, "s_sum", [P, 2, GW])
                y = sbuf(st, "y_sum", [P, 2, RW])
                sq = sbuf(st, "sq_o", [P, 2, GW])
                gi2 = sbuf(st, "gi2", [P, 2, 2, GW])
                g_ss = sbuf(st, "g_ss", [P, 2 * GH])
                r_ss = sbuf(st, "r_ss", [P, 2 * RH])
                mean = sbuf(st, "mean", [P, 2 * RH])
                g_rs = sbuf(st, "g_rs", [P, 2 * GH])
                r_rs = sbuf(st, "r_rs", [P, 2 * RH])
                begin("out_load")
                with nc.Block() as block:
                    @block.sync
                    def _(sp):
                        sp.dma_start(wo[:, :, :], w_rows(io["w_out"][ds(L, 1)].rearrange("a r n -> (a r) n"))).then_inc(*DMA("w_out"))
                        sp.wait_ge(*DMA["w_out"])
                clear()
                with nc.Fori(0, 2) as i:
                    begin("out")
                    with nc.Block() as block:
                        def h64(ap):
                            return ap.rearrange("p t (h n) -> p (t h) n", n=GD)

                        @block.sync
                        def _(sp):
                            for p in range(2):
                                row = i * (4 * P) + 2 * P * p

                                def rows(ap):
                                    return ap.rearrange("(t p) n -> p t n", p=P)
                                for e, dst in enumerate((gi, gi2)):
                                    sp.dma_start(dst[:, p, :, :], rows(gdn_hbm[e, ds(row, 2 * P), :])).then_inc(*DMA(f"gdn_in{p}"))
                                for e in range(3):
                                    sp.dma_start(ri[:, p, e, :, :], rows(rwkv_hbm[e, ds(row, 2 * P), :])).then_inc(*DMA(f"rwkv_in{p}"))
                                sp.dma_start(gate[:, p, :, :], rows(gate_hbm[ds(row, 2 * P), :])).then_inc(*DMA(f"gate_in{p}"))
                                sp.dma_start(mix[:, p, :, GW:2 * GW], rows(mla_hbm[ds(row, 2 * P), :])).then_inc(*DMA(f"mla_in{p}"))
                                sp.dma_start(xt[:, 2 * p:2 * p + 2, :], rows(x_hbm[ds(row + P, 2 * P), :])).then_inc(*DMA(f"x_in{p}"))
                            for t in range(4):
                                sp.wait_ge(*VEC[f"x{t}_1"])
                                sp.dma_start(x_hbm[ds(i * (4 * P) + (t + 1) * P, P), :], xt[:, t, :]).then_inc(*DMA("x_out"))
                            sp.wait_ge(*DMA["x_out"])

                        @block.scalar
                        def _(act):
                            for p in range(2):
                                act.wait_ge(*DMA[f"gate_in{p}"])
                                act.activation(gate[:, p, :, :], gate[:, p, :, :], FN.Silu).then_inc(*ACT(f"gate{p}"))
                            for p in range(2):
                                act.wait_ge(*VEC[f"gss{p}"])
                                act.activation(g_rs[:, :], g_ss[:, :], FN.Ln, bias=cst("eps"), scale=1.0 / GD).then_inc(*ACT(f"ln_g{p}"))
                                act.wait_ge(*VEC[f"rss{p}"])
                                act.activation(r_rs[:, :], r_ss[:, :], FN.Ln, bias=cst("rw_eps"), scale=1.0 / RD).then_inc(*ACT(f"ln_r{p}"))
                                act.wait_ge(*ACT[f"ln_g{p}"])
                                act.activation(g_rs[:, :], g_rs[:, :], FN.Exp, scale=-0.5).then_inc(*ACT(f"g_rs{p}"))
                                act.wait_ge(*ACT[f"ln_r{p}"])
                                act.activation(r_rs[:, :], r_rs[:, :], FN.Exp, scale=-0.5).then_inc(*ACT(f"rs{p}"))
                            for t in range(4):
                                for b in range(2):
                                    act.wait_ge(*PE[f"mT{t}_{b}"])
                                    act.copy(mT[:, t % 2, 4 * b:4 * b + 4, :], ps[:, b, :].rearrange("p (k n) -> p k n", k=4)).then_inc(*ACT(f"mT{t}_{b}"))

                        @block.vector
                        def _(vec):
                            for p in range(2):
                                if p:
                                    vec.wait_ge(*ACT["rs0"])
                                vec.wait_ge(*DMA[f"gdn_in{p}"])
                                vec.tensor_tensor(s[:, :, :], gi[:, p, :, :], gi2[:, p, :, :], ALU.add).then_inc(*VEC(f"s{p}"))
                                vec.wait_ge(*DMA[f"rwkv_in{p}"])
                                vec.tensor_tensor(y[:, :, :], ri[:, p, 0, :, :], ri[:, p, 1, :, :], ALU.add).then_inc(*VEC(f"y{p}"))
                                vec.wait_ge(*VEC[f"s{p}"])
                                vec.tensor_tensor(sq[:, :, :], s[:, :, :], s[:, :, :], ALU.mult).then_inc(*VEC(f"gsq{p}"))
                                vec.wait_ge(*VEC[f"y{p}"])
                                vec.tensor_reduce(mean[:, :], h64(y[:, :, :]), AX, ALU.add).then_inc(*VEC(f"ysum{p}"))
                                vec.wait_ge(*VEC[f"gsq{p}"])
                                vec.tensor_reduce(g_ss[:, :], h64(sq[:, :, :]), AX, ALU.add).then_inc(*VEC(f"gss{p}"))
                                vec.wait_ge(*VEC[f"ysum{p}"])
                                vec.tensor_scalar(mean[:, :], mean[:, :], 1.0 / RD, None, ALU.mult).then_inc(*VEC(f"mean{p}"))
                                vec.wait_ge(*VEC[f"mean{p}"])
                                vec.tensor_tensor(h64(y[:, :, :]), h64(y[:, :, :]), col(mean[:, :], RD), ALU.subtract).then_inc(*VEC(f"yc{p}"))
                                vec.wait_ge(*VEC[f"yc{p}"])
                                vec.wait_ge(*VEC[f"gss{p}"])
                                vec.tensor_tensor(sq[:, :, 0:RW], y[:, :, :], y[:, :, :], ALU.mult).then_inc(*VEC(f"rsq{p}"))
                                vec.wait_ge(*VEC[f"rsq{p}"])
                                vec.tensor_reduce(r_ss[:, :], sq[:, :, 0:RW].rearrange("p t (h n) -> p t h n", n=RD), AX, ALU.add).then_inc(*VEC(f"rss{p}"))
                                vec.tensor_tensor(ri[:, p, 2, :, :], ri[:, p, 2, :, :], rep(par("ln_b"), 2), ALU.add).then_inc(*VEC(f"r3{p}"))
                                vec.wait_ge(*ACT[f"g_rs{p}"])
                                vec.tensor_tensor(h64(s[:, :, :]), h64(s[:, :, :]), col(g_rs[:, :], GD), ALU.mult).then_inc(*VEC(f"g1{p}"))
                                vec.wait_ge(*ACT[f"rs{p}"])
                                vec.tensor_tensor(h64(y[:, :, :]), h64(y[:, :, :]), col(r_rs[:, :], RD), ALU.mult).then_inc(*VEC(f"r1{p}"))
                                vec.wait_ge(*VEC[f"g1{p}"])
                                for t in range(2):
                                    q = vec.tensor_tensor(mix[:, p, t, 0:GW].rearrange("p (h n) -> p h n", n=GD), s[:, t, :].rearrange("p (h n) -> p h n", n=GD),
                                                          rep(par("gdn_g"), GH), ALU.mult)
                                q.then_inc(*VEC(f"g2{p}"))
                                vec.wait_ge(*VEC[f"r1{p}"])
                                vec.tensor_tensor(y[:, :, :], y[:, :, :], rep(par("ln_g"), 2), ALU.mult).then_inc(*VEC(f"r2{p}"))
                                vec.wait_ge(*VEC[f"r3{p}"])
                                vec.wait_ge(*VEC[f"r2{p}"])
                                vec.tensor_tensor(mix[:, p, :, 2 * GW:], y[:, :, :], ri[:, p, 2, :, :], ALU.add).then_inc(*VEC(f"r4{p}"))
                                vec.wait_ge(*VEC[f"r4{p}"])
                                vec.wait_ge(*DMA[f"mla_in{p}"])
                                vec.wait_ge(*ACT[f"gate{p}"])
                                vec.tensor_tensor(mix[:, p, :, :], mix[:, p, :, :], gate[:, p, :, :], ALU.mult).then_inc(*VEC(f"mix{p}"))
                            for t in range(4):
                                vec.wait_ge(*DMA[f"x_in{t // 2}"])
                                for b in range(2):
                                    n = slice(512 * b, 512 * (b + 1))
                                    vec.wait_ge(*PE[f"o{t}_{b}"])
                                    vec.tensor_tensor(xt[:, t, n], xt[:, t, n], ps[:, 2 + (2 * t + b) % 6, :], ALU.add).then_inc(*VEC(f"x{t}_{b}"))

                        @block.tensor
                        def _(pe):
                            def turn(t):
                                pe.wait_ge(*VEC[f"mix{t // 2}"])
                                for b in range(2):
                                    if t >= 1:
                                        pe.wait_ge(*ACT[f"mT{t - 1}_{b}"])
                                    for k in range(4):
                                        q = pe.transpose(ps[:, b, k * P:(k + 1) * P], mix[:, t // 2, t % 2, (4 * b + k) * P:(4 * b + k + 1) * P], ident)
                                    q.then_inc(*PE(f"mT{t}_{b}"))
                            turn(0)
                            for t in range(4):
                                if t == 0:
                                    turn(1)
                                pe.wait_ge(*ACT[f"mT{t}_1"])
                                for b in range(2):
                                    if 2 * t + b >= 6:
                                        pe.wait_ge(*VEC[f"x{(2 * t + b - 6) // 2}_{b}"])
                                    for k in range(KD):
                                        q = pe.matmul(ps[:, 2 + (2 * t + b) % 6, :], lhsT=mT[:, t % 2, k, :], rhs=wo[:, k, 512 * b:512 * (b + 1)],
                                                      start=(k == 0), stop=(k == KD - 1))
                                    q.then_inc(*PE(f"o{t}_{b}"))
                                if t + 2 < 4:
                                    turn(t + 2)
                    clear()
        first.close()

        with ExitStack() as st:
            work = norm_buffers(st, "_2", 4)
            fg = sbuf(st, "fg", [P, DM])
            begin("load2")
            with nc.Block() as block:
                @block.sync
                def _(sp):
                    sp.dma_start(params[:, 0:P2_N], io["params2"]).then_inc(*DMA("params2"))
                    sp.dma_start(fg[:, :], io["final_g"]).then_inc(*DMA("final_g"))
                    sp.wait_ge(*DMA["params2"])
                    sp.wait_ge(*DMA["final_g"])
            clear()
            with nc.Fori(0, 2) as i:
                norm_tiles("norm2", 4, lambda j: i * (4 * P) + (j + 1) * P, par("norm_g", P2_AT), work, final=fg[:, :])
            norm_tiles("norm_meta", 1, lambda j: 0, par("norm_g", P2_AT), work)

        w_in2 = io["w_in_2"]
        THIRD = T2 // 3

        def project3(pe, banks, w, x_in):
            for b in range(3):
                for k in range(KD):
                    q = pe.matmul(ps[:, banks + b, 0:THIRD], lhsT=w[:, k, :], rhs=x_in[:, k, b * THIRD:(b + 1) * THIRD],
                                  start=(k == 0), stop=(k == KD - 1))
            return q

        def bank3(banks):
            return ps[:, banks:banks + 3, 0:THIRD]

        def tok3(ap):
            return ap.rearrange("p (b n) -> p b n", b=3)

        def tiles(ap):
            return ap.rearrange("p (t n) -> p t n", n=P)

        with ExitStack() as st:
            NAMES = ("glu_a", "glu_b", "q", "f", "i", "g")
            COLS = dict(zip(NAMES, (0, DM, 3 * DM, 4 * DM, 5 * DM, 6 * DM)))
            wt = {n: sbuf(st, "w2_" + n, [P, KD, P]) for n in NAMES}
            glu = sbuf(st, "glu", [P, T2])
            sgb = sbuf(st, "sgb", [P, T2])
            cv = sbuf(st, "cv", [P, T2])
            q_ = sbuf(st, "q_", [P, T2])
            k_ = sbuf(st, "k_", [P, T2])
            Rp = sbuf(st, "Rp", [P, T2])
            Sp = sbuf(st, "Sp", [P, T2])
            W = sbuf(st, "W", [P, 2, T2])
            v = sbuf(st, "v2", [P, T2])
            kS = sbuf(st, "kS", [P, T2])
            at = sbuf(st, "attn", [P, T2])
            Sst = sbuf(st, "Sst", [P, NT2, P])
            sgg = sbuf(st, "sgg", [P, T2])
            orec = sbuf(st, "orec", [P, T2])
            osq = sbuf(st, "osq", [P, T2])
            lb = sbuf(st, "lb", [P, KD])
            omlb = sbuf(st, "omlb", [P, KD])
            diff = sbuf(st, "lb_diff", [P, KD])
            begin("hg_load")
            with nc.Block() as block:
                @block.sync
                def _(sp):
                    for n in NAMES:
                        sp.dma_start(wt[n][:, :, :], w_rows(w_in2[:, COLS[n]:COLS[n] + P])).then_inc(*DMA("w2"))
                    sp.wait_ge(*DMA["w2"])

                @block.vector
                def _(vec):
                    l = par("lb", P2_AT).rearrange("p (k c) -> p k c", c=2)
                    mxl, e2 = Sp[:, 0:KD], Rp[:, 0:2 * KD].rearrange("p (c k) -> p c k", c=2)
                    vec.tensor_tensor(mxl, l[:, :, 0], l[:, :, 1], ALU.max).then_inc(*VEC("lb_max"))
                    vec.wait_ge(*VEC["lb_max"])
                    vec.tensor_tensor(e2[:, 0, :], l[:, :, 0], mxl, ALU.subtract)
                    vec.tensor_tensor(e2[:, 1, :], l[:, :, 1], mxl, ALU.subtract).then_inc(*VEC("lb_shift"))
                    vec.wait_ge(*ACT["lb_exp"])
                    vec.tensor_tensor(diff[:, :], e2[:, 0, :], e2[:, 1, :], ALU.add).then_inc(*VEC("lb_sum"))
                    vec.wait_ge(*VEC["lb_sum"])
                    vec.reciprocal(diff[:, :], diff[:, :]).then_inc(*VEC("lb_inv"))
                    vec.wait_ge(*VEC["lb_inv"])
                    vec.tensor_tensor(lb[:, :], e2[:, 0, :], diff[:, :], ALU.mult).then_inc(*VEC("lb"))
                    vec.wait_ge(*VEC["lb"])
                    vec.tensor_scalar(omlb[:, :], lb[:, :], -1.0, 1.0, ALU.mult, ALU.add).then_inc(*VEC("omlb"))
                    vec.memset(at[:, :], 0.0).then_inc(*VEC("attn0"))
                    vec.memset(cv[:, :], 0.0).then_inc(*VEC("cv0"))
                    vec.memset(Sst[:, 0, :], 0.0).then_inc(*VEC("state0"))

                @block.scalar
                def _(act):
                    act.wait_ge(*VEC["lb_shift"])
                    act.activation(Rp[:, 0:2 * KD], Rp[:, 0:2 * KD], FN.Exp).then_inc(*ACT("lb_exp"))
            clear()

            def level(ap, k):
                return ap.rearrange("p (a s n) -> p a s n", s=2, n=1 << k)

            with nc.Fori(0, KD) as i:
                begin("hg")
                with nc.Block() as block:
                    at_w = P2_AT["conv_w"][0]

                    @block.sync
                    def _(sp):
                        for n, used in (("f", "f"), ("glu_b", "glu_b"), ("q", "q"), ("glu_a", "glu_a"), ("i", "v"), ("g", "g")):
                            sp.wait_ge(*PE[used])
                            sp.dma_start(wt[n][:, :, :], w_rows(w_in2[:, ds(i * P + (COLS[n] + P), P)])).then_inc(*DMA("w2"))
                        sp.wait_ge(*VEC[f"tap{TAPS - 1}"])
                        sp.dma_start(conv_hbm[ds(i, 1)].rearrange("a p n -> (a p) n"), cv[:, :]).then_inc(*DMA("out2"))
                        sp.wait_ge(*VEC["orec"])
                        sp.dma_start(rec_hbm[ds(i, 1)].rearrange("a p n -> (a p) n"), orec[:, :]).then_inc(*DMA("out2"))
                        sp.wait_ge(*DMA["w2"])
                        sp.wait_ge(*DMA["out2"])

                    @block.tensor
                    def _(pe):
                        project3(pe, 0, wt["f"], hT).then_inc(*PE("f"))
                        project3(pe, 3, wt["glu_b"], hT).then_inc(*PE("glu_b"))
                        pe.wait_ge(*ACT["f"])
                        project3(pe, 0, wt["q"], hT).then_inc(*PE("q"))
                        pe.wait_ge(*ACT["glu_b"])
                        project3(pe, 3, wt["glu_a"], hT).then_inc(*PE("glu_a"))

                        def values(tiles):
                            for t in tiles:
                                for k in range(KD):
                                    q = pe.matmul(ps[:, 3 + t // 3, (t % 3) * P:(t % 3 + 1) * P], lhsT=hT[:, k, t * P:(t + 1) * P], rhs=wt["i"][:, k, :],
                                                  start=(k == 0), stop=(k == KD - 1))
                            return q
                        for n in range(NLEV + 1):
                            if n == 0:
                                pe.wait_ge(*VEC["k"])
                                pe.wait_ge(*ACT["q"])
                            else:
                                pe.wait_ge(*VEC[f"kept{n - 1}"])
                                pe.wait_ge(*VEC[f"W{n - 1}"])
                            for t in range(NT2):
                                u = slice(t * P, (t + 1) * P)
                                a, b = (k_[:, u], q_[:, u]) if n == 0 else (W[:, (n - 1) % 2, u],) * 2
                                q = pe.matmul(ps[:, t // 3, (t % 3) * P:(t % 3 + 1) * P], lhsT=a, rhs=b, start=True, stop=True)
                            q.then_inc(*PE(f"pairs{n}"))
                            if n < 4:
                                if n == 0:
                                    pe.wait_ge(*VEC["glu"])
                                q = values(range(NT2 * n // 4, NT2 * (n + 1) // 4))
                                if n == 3:
                                    q.then_inc(*PE("v"))
                            elif n < 7:
                                if n == 4:
                                    pe.wait_ge(*ACT["v"])
                                b = n - 4
                                for k in range(KD):
                                    q = pe.matmul(ps[:, 3 + b, 0:THIRD], lhsT=wt["g"][:, k, :], rhs=hT[:, k, b * THIRD:(b + 1) * THIRD],
                                                  start=(k == 0), stop=(k == KD - 1))
                                if n == 6:
                                    q.then_inc(*PE("g"))
                        pe.wait_ge(*VEC["kS"])
                        pe.wait_ge(*ACT["g"])
                        for t in range(NT2):
                            q = pe.transpose(ps[:, 3 + t // 3, (t % 3) * P:(t % 3 + 1) * P], kS[:, t * P:(t + 1) * P], ident)
                        q.then_inc(*PE("kS"))
                        pe.wait_ge(*ACT["kS"])
                        pe.wait_ge(*VEC[f"kept{NLEV}"])
                        for t in range(NT2 - 1):
                            q = pe.matmul(ps[:, t // 4, (t % 4) * P:(t % 4 + 1) * P], lhsT=kS[:, t * P:(t + 1) * P], rhs=v[:, t * P:(t + 1) * P],
                                          start=True, stop=True)
                        q.then_inc(*PE("kv"))
                        pe.wait_ge(*VEC[f"state{NT2 - 2}"])
                        pe.wait_ge(*VEC["qR"])
                        for t in range(NT2):
                            u = slice(t * P, (t + 1) * P)
                            o_ap = ps[:, 3 + t // 3, (t % 3) * P:(t % 3 + 1) * P]
                            pe.matmul(o_ap, lhsT=v[:, u], rhs=at[:, u], start=True, stop=False)
                            q = pe.matmul(o_ap, lhsT=Sst[:, t, :], rhs=q_[:, u], start=False, stop=True)
                        q.then_inc(*PE("o"))
                        pe.wait_ge(*ACT["osq"])
                        for b in range(3):
                            q = pe.matmul(ps[:, b, 0:THIRD], lhsT=ones, rhs=osq[:, b * THIRD:(b + 1) * THIRD], start=True, stop=True)
                        q.then_inc(*PE("oss"))

                    @block.scalar
                    def _(act):
                        act.wait_ge(*PE["f"])
                        act.activation(tok3(sgb[:, :]), bank3(0), FN.Sigmoid).then_inc(*ACT("f"))
                        act.wait_ge(*PE["glu_b"])
                        act.wait_ge(*VEC["f"])
                        act.activation(tok3(sgb[:, :]), bank3(3), FN.Sigmoid).then_inc(*ACT("glu_b"))
                        act.wait_ge(*PE["q"])
                        act.activation(tok3(q_[:, :]), bank3(0), FN.Silu).then_inc(*ACT("q"))
                        act.wait_ge(*PE["v"])
                        act.copy(tok3(v[:, :]), bank3(3)).then_inc(*ACT("v"))
                        act.wait_ge(*PE["g"])
                        act.activation(tok3(sgg[:, :]), bank3(3), FN.Silu).then_inc(*ACT("g"))
                        act.wait_ge(*PE["kS"])
                        act.copy(tok3(kS[:, :]), bank3(3)).then_inc(*ACT("kS"))
                        act.wait_ge(*PE["o"])
                        act.activation(tok3(osq[:, :]), bank3(3), FN.Square).then_inc(*ACT("osq"))
                        act.copy(tok3(orec[:, :]), bank3(3)).then_inc(*ACT("o"))
                        act.wait_ge(*PE["oss"])
                        act.activation(tok3(osq[:, :]), bank3(0), FN.Ln, bias=cst("eps"), scale=1.0 / P).then_inc(*ACT("o_ln"))
                        act.wait_ge(*ACT["o_ln"])
                        act.activation(osq[:, :], osq[:, :], FN.Exp, scale=-0.5).then_inc(*ACT("o_rs"))

                    @block.gpsimd
                    def _(pool):
                        pool.memset(Sp[:, :], 1.0).then_inc(*POOL("S_"))
                        for k in range(NLEV):
                            R4, S4 = level(Rp[:, :], k), level(Sp[:, :], k)
                            n = T2 >> (k + 1)
                            pool.wait_ge(*POOL["S_"] if k == 0 else POOL[f"R{k - 1}"])
                            pool.wait_ge(*VEC[f"W{k}"])
                            pool.tensor_tensor(S4[:, :, 0, :], S4[:, :, 0, :], R4[:, :, 1, (1 << k) - 1:1 << k].broadcast_to([P, n, 1 << k]),
                                               ALU.mult).then_inc(*POOL(f"S{k}"))
                            pool.wait_ge(*POOL[f"S{k}"])
                            pool.tensor_tensor(R4[:, :, 1, :], R4[:, :, 1, :], R4[:, :, 0, (1 << k) - 1:1 << k].broadcast_to([P, n, 1 << k]),
                                               ALU.mult).then_inc(*POOL(f"R{k}"))

                    @block.vector
                    def _(vec):
                        vec.wait_ge(*ACT["f"])
                        vec.tensor_scalar(Rp[:, :], sgb[:, :], omlb[:, ds(i, 1)], lb[:, ds(i, 1)], ALU.mult, ALU.add).then_inc(*VEC("f"))
                        vec.wait_ge(*VEC["f"])
                        vec.tensor_scalar(k_[:, :], Rp[:, :], -1.0, 1.0, ALU.mult, ALU.add).then_inc(*VEC("k"))
                        vec.wait_ge(*ACT["q"])
                        vec.wait_ge(*VEC["k"])
                        vec.wait_ge(*POOL["S_"])

                        def weights(k):
                            Wk, q4, k4, R4, S4 = (level(a, k) for a in (W[:, k % 2, :], q_[:, :], k_[:, :], Rp[:, :], Sp[:, :]))
                            if k >= 1:
                                vec.wait_ge(*POOL[f"R{k - 1}"])
                            if k >= 2:
                                vec.wait_ge(*PE[f"pairs{k - 1}"])
                            vec.tensor_tensor(Wk[:, :, 1, :], q4[:, :, 1, :], R4[:, :, 1, :], ALU.mult)
                            vec.tensor_tensor(Wk[:, :, 0, :], k4[:, :, 0, :], S4[:, :, 0, :], ALU.mult).then_inc(*VEC(f"W{k}"))

                        weights(0)
                        weights(1)
                        vec.wait_ge(*PE["glu_a"])
                        vec.wait_ge(*ACT["glu_b"])
                        vec.tensor_tensor(tok3(glu[:, :]), bank3(3), tok3(sgb[:, :]), ALU.mult).then_inc(*VEC("glu"))
                        T0 = P - META
                        NW = T2 - T0

                        def tap(n):
                            src = glu[:, T0 - (TAPS - 1) + n:T0 - (TAPS - 1) + n + NW]
                            w = params[:, ds(i * TAPS + (at_w + n), 1)]
                            vec.wait_ge(*VEC["glu" if n == 0 else f"tap{n - 1}"])
                            if n == 0:
                                vec.tensor_scalar(cv[:, T0:], src, w, params[:, ds(i + P2_AT["conv_b"][0], 1)], ALU.mult,
                                                  ALU.add).then_inc(*VEC("tap0"))
                            else:
                                vec.scalar_tensor_tensor(out=cv[:, T0:], in0=src, scalar=w, in1=cv[:, T0:], op0=ALU.mult,
                                                         op1=ALU.add).then_inc(*VEC(f"tap{n}"))
                        done = 0
                        for n in range(NLEV + 1):
                            vec.wait_ge(*PE[f"pairs{n}"])
                            mask = ident if n == 0 else cst("up", n - 1)
                            for b in range(3):
                                q = vec.copy_predicated(at[:, b * THIRD:(b + 1) * THIRD].rearrange("p (t n) -> p t n", n=P),
                                                        rep(mask, 3).bitcast(U32),
                                                        ps[:, b, 0:THIRD].rearrange("p (t n) -> p t n", n=P))
                            q.then_inc(*VEC(f"kept{n}"))
                            if 2 <= n + 1 < NLEV:
                                weights(n + 1)
                            for _ in range(2):
                                tap(done)
                                done += 1
                        vec.wait_ge(*POOL[f"R{NLEV - 1}"])
                        vec.tensor_tensor(kS[:, :], k_[:, :], Sp[:, :], ALU.mult).then_inc(*VEC("kS"))
                        vec.wait_ge(*PE["pairs0"])
                        vec.tensor_tensor(q_[:, :], q_[:, :], Rp[:, :], ALU.mult).then_inc(*VEC("qR"))
                        for _ in range(4):
                            tap(done)
                            done += 1
                        vec.wait_ge(*PE["kv"])
                        for t in range(NT2 - 1):
                            if t:
                                vec.wait_ge(*VEC[f"state{t - 1}"])
                            vec.scalar_tensor_tensor(out=Sst[:, t + 1, :], in0=Sst[:, t, :], scalar=Rp[:, (t + 1) * P - 1:(t + 1) * P],
                                                     in1=ps[:, t // 4, (t % 4) * P:(t % 4 + 1) * P], op0=ALU.mult, op1=ALU.add).then_inc(*VEC(f"state{t}"))
                        while done < TAPS:
                            tap(done)
                            done += 1
                        vec.wait_ge(*ACT["o_rs"])
                        vec.tensor_tensor(orec[:, :], orec[:, :], osq[:, :], ALU.mult).then_inc(*VEC("o_normed"))
                        vec.wait_ge(*VEC["o_normed"])
                        vec.scalar_tensor_tensor(out=orec[:, :], in0=orec[:, :], scalar=params[:, ds(i + P2_AT["gnorm"][0], 1)],
                                                 in1=sgg[:, :], op0=ALU.mult, op1=ALU.mult).then_inc(*VEC("orec"))
                clear()

        merged_stack = ExitStack()
        cz = sbuf(merged_stack, "cz", [P, KD, T2])
        rec = sbuf(merged_stack, "rec", [P, KD, T2])
        merged = sbuf(merged_stack, "merged", [P, KD, T2])
        with ExitStack() as st:
            wz = sbuf(st, "wz", [P, KD, P])
            mu = sbuf(st, "mu", [P, T2])
            sq = sbuf(st, "sq_l", [P, 2, T2])
            zs = sbuf(st, "zs", [P, T2])
            begin("ln")
            with nc.Block() as block:
                @block.sync
                def _(sp):
                    sp.dma_start(wz[:, :, :], w_rows(w_in2[:, 2 * DM:2 * DM + P])).then_inc(*DMA("wz"))
                    sp.dma_start(cz[:, :, :], conv_hbm.rearrange("k p n -> p k n")).then_inc(*DMA("cz"))
                    sp.dma_start(rec[:, :, :], rec_hbm.rearrange("k p n -> p k n")).then_inc(*DMA("rec"))
                    sp.wait_ge(*DMA["rec"])
                    sp.wait_ge(*DMA["wz"])

                @block.tensor
                def _(pe):
                    pe.wait_ge(*DMA["cz"])
                    for b in range(3):
                        for k in range(KD):
                            q = pe.matmul(ps[:, b, 0:THIRD], lhsT=ones, rhs=cz[:, k, b * THIRD:(b + 1) * THIRD], start=(k == 0), stop=(k == KD - 1))
                    q.then_inc(*PE("sum"))
                    for k in range(KD):
                        pe.wait_ge(*ACT[f"sq{k}"])
                        for b in range(3):
                            q = pe.matmul(ps[:, 3 + b, 0:THIRD], lhsT=ones, rhs=sq[:, k % 2, b * THIRD:(b + 1) * THIRD], start=(k == 0),
                                          stop=(k == KD - 1))
                        q.then_inc(*PE(f"sumsq{k}"))

                @block.scalar
                def _(act):
                    act.wait_ge(*PE["sum"])
                    act.mul(tok3(mu[:, :]), bank3(0), 1.0 / DM).then_inc(*ACT("mu"))
                    for k in range(KD):
                        act.wait_ge(*VEC[f"centred{k}"])
                        if k >= 2:
                            act.wait_ge(*PE[f"sumsq{k - 2}"])
                        act.activation(sq[:, k % 2, :], cz[:, k, :], FN.Square).then_inc(*ACT(f"sq{k}"))
                    act.wait_ge(*PE[f"sumsq{KD - 1}"])
                    act.activation(tok3(zs[:, :]), bank3(3), FN.Ln, bias=cst("eps"), scale=1.0 / DM).then_inc(*ACT("ln"))
                    act.wait_ge(*ACT["ln"])
                    act.activation(zs[:, :], zs[:, :], FN.Exp, scale=-0.5).then_inc(*ACT("rs"))

                @block.vector
                def _(vec):
                    vec.wait_ge(*ACT["mu"])
                    for k in range(KD):
                        vec.tensor_tensor(cz[:, k, :], cz[:, k, :], mu[:, :], ALU.subtract).then_inc(*VEC(f"centred{k}"))
                    vec.wait_ge(*ACT["rs"])
                    for k in range(KD):
                        vec.tensor_tensor(cz[:, k, :], cz[:, k, :], zs[:, :], ALU.mult).then_inc(*VEC(f"scaled{k}"))
            clear()
            with nc.Fori(0, KD) as i:
                begin("z")
                with nc.Block() as block:
                    @block.sync
                    def _(sp):
                        sp.wait_ge(*PE["z"])
                        sp.dma_start(wz[:, :, :], w_rows(w_in2[:, ds(i * P + (2 * DM + P), P)])).then_inc(*DMA("wz"))
                        sp.wait_ge(*DMA["wz"])

                    @block.tensor
                    def _(pe):
                        project3(pe, 0, wz, hT).then_inc(*PE("z"))

                    @block.scalar
                    def _(act):
                        act.wait_ge(*VEC["affine"])
                        act.activation(mu[:, :], mu[:, :], FN.Silu).then_inc(*ACT("c"))
                        act.wait_ge(*PE["z"])
                        act.activation(tok3(zs[:, :]), bank3(0), FN.Silu).then_inc(*ACT("z"))

                    @block.vector
                    def _(vec):
                        vec.tensor_scalar(mu[:, :], cz[:, ds(i, 1), :], params[:, ds(i + P2_AT["ln_g"][0], 1)],
                                          params[:, ds(i + P2_AT["ln_b"][0], 1)], ALU.mult, ALU.add).then_inc(*VEC("affine"))
                        vec.wait_ge(*ACT["z"])
                        vec.tensor_tensor(cz[:, ds(i, 1), :], mu[:, :], zs[:, :], ALU.mult).then_inc(*VEC("cz"))
                clear()

        with ExitStack() as st:
            wm = {n: sbuf(st, "wm_" + n, [P, KD, P]) for n in ("m_conv", "m_rec", "conv", "rec")}
            src = {"m_conv": (w_in2, 7 * DM), "m_rec": (w_in2, 8 * DM), "conv": (io["w_conv_out_2"], 0), "rec": (io["w_rec_out_2"], 0)}
            gm = sbuf(st, "gm", [P, 2, T2])
            with nc.Fori(0, KD) as i:
                begin("merge")
                with nc.Block() as block:
                    @block.sync
                    def _(sp):
                        for n in ("m_conv", "conv", "m_rec", "rec"):
                            w, c0 = src[n]
                            sp.dma_start(wm[n][:, :, :], w_rows(w[:, ds(i * P + c0, P)])).then_inc(*DMA("w_" + n))

                    @block.tensor
                    def _(pe):
                        pe.wait_ge(*DMA["w_m_conv"])
                        project3(pe, 0, wm["m_conv"], hT).then_inc(*PE("m_conv"))
                        pe.wait_ge(*DMA["w_conv"])
                        project3(pe, 3, wm["conv"], cz).then_inc(*PE("conv"))
                        pe.wait_ge(*DMA["w_m_rec"])
                        pe.wait_ge(*ACT["m_conv"])
                        project3(pe, 0, wm["m_rec"], hT).then_inc(*PE("m_rec"))
                        pe.wait_ge(*DMA["w_rec"])
                        pe.wait_ge(*VEC["conv"])
                        project3(pe, 3, wm["rec"], rec).then_inc(*PE("rec"))

                    @block.scalar
                    def _(act):
                        act.wait_ge(*PE["m_conv"])
                        act.activation(tok3(gm[:, 0, :]), bank3(0), FN.Sigmoid).then_inc(*ACT("m_conv"))
                        act.wait_ge(*PE["m_rec"])
                        act.activation(tok3(gm[:, 1, :]), bank3(0), FN.Sigmoid).then_inc(*ACT("m_rec"))

                    @block.vector
                    def _(vec):
                        vec.wait_ge(*PE["conv"])
                        vec.wait_ge(*ACT["m_conv"])
                        vec.tensor_tensor(tok3(gm[:, 0, :]), tok3(gm[:, 0, :]), bank3(3), ALU.mult).then_inc(*VEC("conv"))
                        vec.wait_ge(*PE["rec"])
                        vec.wait_ge(*ACT["m_rec"])
                        vec.tensor_tensor(tok3(gm[:, 1, :]), tok3(gm[:, 1, :]), bank3(3), ALU.mult).then_inc(*VEC("rec"))
                        vec.wait_ge(*VEC["rec"])
                        vec.tensor_tensor(merged[:, ds(i, 1), :], gm[:, 0, :], gm[:, 1, :], ALU.add).then_inc(*VEC("merged"))
                clear()

        with ExitStack() as st:
            wo = cz[:, :, 0:DM]
            mT = sbuf(st, "mT2", [P, 2, KD, P])
            xt = rec[:, :, :].rearrange("p k n -> p (k n)")[:, 0:4 * DM].rearrange("p (t n) -> p t n", t=4)
            sq = rec[:, :, :].rearrange("p k n -> p (k n)")[:, 4 * DM:8 * DM].rearrange("p (t n) -> p t n", t=4)
            fg = sbuf(st, "fg2", [P, DM])
            ss = sbuf(st, "ss_e", [P, 4])
            rs = sbuf(st, "rs_e", [P, 4])
            begin("end_load")
            with nc.Block() as block:
                @block.sync
                def _(sp):
                    sp.dma_start(wo, w_rows(io["w_out_2"])).then_inc(*DMA("end"))
                    sp.dma_start(fg[:, :], io["final_g_2"]).then_inc(*DMA("end"))
                    sp.wait_ge(*DMA["end"])
            clear()
            with nc.Fori(0, 2) as i:
                begin("end")
                with nc.Block() as block:
                    row = i * (4 * P)

                    @block.sync
                    def _(sp):
                        for t in range(4):
                            sp.dma_start(xt[:, t, :], x_hbm[ds(row + (t + 1) * P, P), :]).then_inc(*DMA(f"x_in{t}"))
                        for t in range(4):
                            sp.wait_ge(*VEC[f"y{t}"])
                            sp.dma_start(io["out"][ds(row + t * P, P), :], sq[:, t, :]).then_inc(*DMA("y_out"))
                        sp.wait_ge(*DMA["y_out"])

                    @block.gpsimd
                    def _(pool):
                        for t in range(4):
                            if t >= 2:
                                pool.wait_ge(*PE[f"o{t - 2}_1"])
                            pool.tensor_copy(mT[:, t % 2, :, :], merged[:, :, ds(row + (t + 1) * P, P)]).then_inc(*POOL(f"mT{t}"))

                    @block.tensor
                    def _(pe):
                        for t in range(4):
                            pe.wait_ge(*POOL[f"mT{t}"])
                            for b in range(2):
                                for k in range(KD):
                                    q = pe.matmul(ps[:, 2 * t + b, :], lhsT=mT[:, t % 2, k, :], rhs=wo[:, k, 512 * b:512 * (b + 1)], start=(k == 0),
                                                  stop=(k == KD - 1))
                                q.then_inc(*PE(f"o{t}_{b}"))

                    @block.vector
                    def _(vec):
                        for t in range(4):
                            vec.wait_ge(*DMA[f"x_in{t}"])
                            for b in range(2):
                                n = slice(512 * b, 512 * (b + 1))
                                vec.wait_ge(*PE[f"o{t}_{b}"])
                                vec.tensor_tensor(xt[:, t, n], xt[:, t, n], ps[:, 2 * t + b, :], ALU.add).then_inc(*VEC(f"x{t}_{b}"))
                        for t in range(4):
                            vec.wait_ge(*ACT["rs"])
                            vec.scalar_tensor_tensor(out=sq[:, t, :], in0=xt[:, t, :], scalar=rs[:, t:t + 1], in1=fg[:, :], op0=ALU.mult,
                                                     op1=ALU.mult).then_inc(*VEC(f"y{t}"))

                    @block.scalar
                    def _(act):
                        for t in range(4):
                            act.wait_ge(*VEC[f"x{t}_1"])
                            act.activation(sq[:, t, :], xt[:, t, :], FN.Square, accum_out=ss[:, t:t + 1]).then_inc(*ACT(f"ss{t}"))
                        act.wait_ge(*ACT["ss3"])
                        act.activation(rs[:, :], ss[:, :], FN.Ln, bias=cst("eps"), scale=1.0 / DM).then_inc(*ACT("ln"))
                        act.wait_ge(*ACT["ln"])
                        act.activation(rs[:, :], rs[:, :], FN.Exp, scale=-0.5).then_inc(*ACT("rs"))
                clear()
        merged_stack.close()


def kernel(**inputs):
    import numpy as _np
    import concourse.bacc as _bacc
    from concourse import mybir as _mybir
    from concourse.bass_utils import run_bass_kernel_spmd as _run

    a = {k: _np.asarray(v) for k, v in inputs.items()}

    def channels(v, n):
        return v.reshape(v.shape[0], n, P).transpose(0, 2, 1)

    def everywhere(v):
        return _np.broadcast_to(v[:, None, :], (v.shape[0], P, v.shape[1]))

    def both(v, n):
        return v.reshape(v.shape[0], v.shape[1], n, P).transpose(0, 3, 1, 2).reshape(v.shape[0], P, -1)

    q_g = _np.zeros((DEPTH, 2 * P), _np.float32)
    q_g[:, :QR] = a["mla_q_norm_g"]
    laid = {
        "norm_g": channels(a["norm_g"], KD),
        "conv": a["gdn_conv"].reshape(DEPTH, CONV, 9, P).transpose(0, 3, 2, 1).reshape(DEPTH, P, -1),
        "a_log": everywhere(a["gdn_a_log"].reshape(DEPTH, -1)), "dt": everywhere(a["gdn_dt_bias"].reshape(DEPTH, -1)),
        "gdn_g": everywhere(a["gdn_norm_g"]), "q_g": channels(q_g, 2), "kv_g": channels(a["mla_kv_norm_g"], 1),
        "mu": a["rwkv_mu"].reshape(DEPTH, 2, 7, P).transpose(0, 3, 2, 1).reshape(DEPTH, P, -1),
        "w0": both(a["rwkv_w0"], 2), "a0": both(a["rwkv_a0"], 2), "k_k": channels(a["rwkv_k_k"], 2),
        "k_a": channels(a["rwkv_k_a"], 2), "r_k": channels(a["rwkv_r_k"].reshape(DEPTH, RW), 2),
        "ln_g": everywhere(a["rwkv_ln_g"]), "ln_b": everywhere(a["rwkv_ln_b"]),
    }
    laid2 = {
        "norm_g": channels(a["norm_g_2"], KD)[0],
        "conv_w": a["conv_w_2"][0].reshape(TAPS, KD, P).transpose(2, 1, 0).reshape(P, -1),
        "conv_b": channels(a["conv_b_2"], KD)[0], "ln_g": channels(a["ln_g_2"], KD)[0], "ln_b": channels(a["ln_b_2"], KD)[0],
        "lb": a["lb_logits_2"].reshape(2, KD, P).transpose(2, 1, 0).reshape(P, -1), "gnorm": channels(a["gnorm_g_2"], KD)[0],
    }
    w2a2 = _np.concatenate([a["rwkv_w2"].transpose(0, 2, 1, 3), a["rwkv_a2"].transpose(0, 2, 1, 3)], 1)
    arrays = {
        "consts": shape_constants(), "positions": a["positions"].reshape(NT, P).T, "x": a["x"].reshape(SEQ, DM),
        "params": _np.concatenate([laid[n] for n, _ in PARAMS], 2), "params2": _np.concatenate([laid2[n] for n, _ in PARAMS2], 1),
        "w_in": a["w_in"], "w_uq": a["mla_w_uq"], "w_ukv": a["mla_w_ukv"], "w2a2": w2a2, "w_out": a["w_out"],
        "final_g": everywhere(a["final_norm_g"][None])[0], "meta": a["meta_tokens_2"], "w_in_2": a["w_in_2"][0],
        "w_conv_out_2": a["w_conv_out_2"][0], "w_rec_out_2": a["w_rec_out_2"][0], "w_out_2": a["w_out_2"][0],
        "final_g_2": everywhere(a["final_g_2"][None])[0],
    }
    arrays = {"in_" + n: _np.ascontiguousarray(v) for n, v in arrays.items()}

    def program(values):
        nc = _bacc.Bacc("TRN2", target_bir_lowering=False, num_devices=1)
        io = {n[3:]: nc.dram_tensor(n, v.shape, _mybir.dt.from_np(v.dtype), kind="ExternalInput").ap() for n, v in arrays.items()}
        io["out"] = nc.dram_tensor("out", (SEQ, DM), F32, kind="ExternalOutput").ap()
        build(nc, io, values)
        return nc

    values = {}
    program(values)
    r = _run(program(values), [arrays], core_ids=[0])
    return r.results[0]["out"].reshape(1, SEQ, DM)
```
